# Optimizing a Trainium2 kernel written in Bass

```python
import jax, jax.numpy as jnp
from jax import lax
import numpy as np
import jax
import jax.numpy as jnp

D_MODEL = 1024
BATCH = 1
SEQ = 512
DEPTH = 1

MIX_WIDTH = D_MODEL
HGRN_WIDTH = MIX_WIDTH // 2
CONV_WIDTH = MIX_WIDTH - HGRN_WIDTH
HGRN_HEAD_DIM = 128
HGRN_HEADS = HGRN_WIDTH // HGRN_HEAD_DIM
CONV_GROUPS = 4
CONV_GROUP_DIM = CONV_WIDTH // CONV_GROUPS
CONV_TAPS = 3
CHUNK = 64
IN_COLS = 4 * HGRN_WIDTH + 3 * CONV_WIDTH
PEER_HEADS = 8
PEER_NKEYS = 128
PEER_EXPERTS = PEER_NKEYS * PEER_NKEYS
PEER_QDIM = 256
PEER_HALF = PEER_QDIM // 2
PEER_TOPK = 16
TOKEN_BLOCK = 128
EPS = 1e-6


def rmsnorm(x, w):
    xf = x.astype(jnp.float32)
    y = xf * lax.rsqrt(jnp.mean(xf * xf, axis=-1, keepdims=True) + EPS)
    return (y * w.astype(jnp.float32)).astype(x.dtype)

def group_rmsnorm(x, w, groups):
    shp = x.shape
    xg = x.reshape(shp[:-1] + (groups, shp[-1] // groups))
    return rmsnorm(xg, w.reshape(groups, shp[-1] // groups)).reshape(shp)

def hgrn2_chunkwise(q, k, v, log_f):
    B, H, S, DK = q.shape
    DV = v.shape[-1]
    n = S // CHUNK

    def to_chunks(t):
        return t.reshape(B, H, n, CHUNK, t.shape[-1]).transpose(2, 0, 1, 3, 4)

    qc, kc, vc, gc = to_chunks(q), to_chunks(k), to_chunks(v), to_chunks(log_f)
    causal = jnp.tril(jnp.ones((CHUNK, CHUNK), dtype=bool))[:, :, None]

    def step(state, inp):
        qb, kb, vb, gb = inp
        b = jnp.cumsum(gb, axis=2)
        diff = b[:, :, :, None, :] - b[:, :, None, :, :]
        decay = jnp.exp(jnp.where(causal, diff, -jnp.inf))
        scores = jnp.einsum('bhtd,bhsd,bhtsd->bhts', qb, kb, decay)
        o = (jnp.einsum('bhts,bhsv->bhtv', scores, vb)
             + jnp.einsum('bhtd,bhdv->bhtv', qb * jnp.exp(b), state))
        b_last = b[:, :, -1:, :]
        new_state = (jnp.exp(b_last[:, :, 0, :])[..., None] * state
                     + jnp.einsum('bhsd,bhsv->bhdv', kb * jnp.exp(b_last - b), vb))
        return new_state, o

    s0 = jnp.zeros((B, H, DK, DV), jnp.float32)
    _, o = lax.scan(step, s0, (qc, kc, vc, gc))
    return o.transpose(1, 2, 0, 3, 4).reshape(B, H, S, DV)

def hgrn2_group(p, lb, onorm_w):
    B, S, _ = p.shape
    pf = p.astype(jnp.float32)
    q, f_raw, i, g = jnp.split(pf, 4, axis=-1)
    f = lb + (1.0 - lb) * jax.nn.sigmoid(f_raw)
    log_f = jnp.log(f)
    k = (1.0 - lb) * jax.nn.sigmoid(-f_raw)

    def heads(t):
        return t.reshape(B, S, HGRN_HEADS, HGRN_HEAD_DIM).transpose(0, 2, 1, 3)

    o = hgrn2_chunkwise(heads(q), heads(k), heads(i), heads(log_f))
    o = o.transpose(0, 2, 1, 3).reshape(B, S, HGRN_WIDTH)
    o = group_rmsnorm(o, onorm_w, HGRN_HEADS) * jax.nn.silu(g)
    return o.astype(p.dtype)

def short_conv_group(p, conv_w, onorm_w):
    b_gate, c_gate, xin = jnp.split(p, 3, axis=-1)
    u = c_gate * xin
    y = lax.conv_general_dilated(
        u, conv_w[:, None, :].astype(u.dtype), window_strides=(1,),
        padding=[(CONV_TAPS - 1, 0)], dimension_numbers=('NWC', 'WIO', 'NWC'),
        feature_group_count=CONV_WIDTH)
    y = b_gate * y
    return group_rmsnorm(y, onorm_w, CONV_GROUPS)

def peer(h, w_query, sub_keys, expert_u, expert_v):
    B, S, D = h.shape
    hb = h.reshape(B * S // TOKEN_BLOCK, TOKEN_BLOCK, D)

    def block(xb):
        T = xb.shape[0]
        q = (xb @ w_query).reshape(T, PEER_HEADS, 2, PEER_HALF)
        s = jnp.einsum('thpk,hpnk->thpn', q, sub_keys).astype(jnp.float32)
        top_s, top_i = lax.top_k(s, PEER_TOPK)
        cand_s = top_s[:, :, 0, :, None] + top_s[:, :, 1, None, :]
        cand_i = top_i[:, :, 0, :, None] * PEER_NKEYS + top_i[:, :, 1, None, :]
        best_s, best_pos = lax.top_k(cand_s.reshape(T, PEER_HEADS, PEER_TOPK * PEER_TOPK), PEER_TOPK)
        idx = jnp.take_along_axis(cand_i.reshape(T, PEER_HEADS, PEER_TOPK * PEER_TOPK), best_pos, axis=-1)
        gate = jax.nn.softmax(best_s, axis=-1)
        u = expert_u[idx]
        v = expert_v[idx]
        act = jax.nn.gelu(jnp.einsum('td,thkd->thk', xb, u).astype(jnp.float32), approximate=False)
        return jnp.einsum('thk,thkd->td', (gate * act).astype(xb.dtype), v)

    return lax.map(block, hb).reshape(B, S, D)

def first_inputs(seed: int = 0) -> dict:
    key = jax.random.key(seed)
    ks = jax.random.split(key, 17)
    f32 = jnp.float32
    D = D_MODEL
    return {
        "x": jax.random.normal(ks[0], (BATCH, SEQ, D), f32),
        "c": jax.random.normal(ks[1], (BATCH, D), f32),
        "w_ada": jax.random.normal(ks[2], (DEPTH, D, 6 * D), f32) * (0.5 * D ** -0.5),
        "b_ada": jax.random.normal(ks[3], (DEPTH, 6 * D), f32) * 0.02,
        "norm1_w": 1.0 + 0.02 * jax.random.normal(ks[4], (DEPTH, D), f32),
        "w_in": jax.random.normal(ks[5], (DEPTH, D, IN_COLS), f32) * D ** -0.5,
        "hgrn_lb_logits": jax.random.normal(ks[6], (DEPTH + 1, HGRN_WIDTH), f32) * 0.5,
        "hgrn_onorm_w": 1.0 + 0.02 * jax.random.normal(ks[7], (DEPTH, HGRN_WIDTH), f32),
        "conv_w": jax.random.normal(ks[8], (DEPTH, CONV_TAPS, CONV_WIDTH), f32) * CONV_TAPS ** -0.5,
        "conv_onorm_w": 1.0 + 0.02 * jax.random.normal(ks[9], (DEPTH, CONV_WIDTH), f32),
        "w_out": jax.random.normal(ks[10], (DEPTH, MIX_WIDTH, D), f32) * MIX_WIDTH ** -0.5,
        "norm2_w": 1.0 + 0.02 * jax.random.normal(ks[11], (DEPTH, D), f32),
        "peer_w_query": jax.random.normal(ks[12], (DEPTH, D, PEER_HEADS * PEER_QDIM), f32) * D ** -0.5,
        "peer_sub_keys": jax.random.normal(ks[13], (DEPTH, PEER_HEADS, 2, PEER_NKEYS, PEER_HALF), f32) * PEER_HALF ** -0.5,
        "peer_u": jax.random.normal(ks[14], (DEPTH, PEER_EXPERTS, D), f32) * D ** -0.5,
        "peer_v": jax.random.normal(ks[15], (DEPTH, PEER_EXPERTS, D), f32),
        "final_norm_w": 1.0 + 0.02 * jax.random.normal(ks[16], (D,), f32),
    }

def first_block(x, c, w_ada, b_ada, norm1_w, w_in, hgrn_lb_logits, hgrn_onorm_w, conv_w,
              conv_onorm_w, w_out, norm2_w, peer_w_query, peer_sub_keys, peer_u, peer_v,
              final_norm_w):
    lower_bounds = jnp.cumsum(jax.nn.softmax(hgrn_lb_logits.astype(jnp.float32), axis=0), axis=0)
    c_act = jax.nn.silu(c)
    for l in range(DEPTH):
        mod = (c_act @ w_ada[l] + b_ada[l])[:, None, :]
        shift1, scale1, gate1, shift2, scale2, gate2 = jnp.split(mod, 6, axis=-1)

        h = rmsnorm(x, norm1_w[l]) * (1.0 + scale1) + shift1
        proj = h @ w_in[l]
        y_a = hgrn2_group(proj[..., :4 * HGRN_WIDTH], lower_bounds[l], hgrn_onorm_w[l])
        y_b = short_conv_group(proj[..., 4 * HGRN_WIDTH:], conv_w[l], conv_onorm_w[l])
        mix = jnp.concatenate([y_a, y_b], axis=-1) @ w_out[l]
        x = x + gate1 * mix

        h = rmsnorm(x, norm2_w[l]) * (1.0 + scale2) + shift2
        x = x + gate2 * peer(h, peer_w_query[l], peer_sub_keys[l], peer_u[l], peer_v[l])
    return rmsnorm(x, final_norm_w)


NORM_EPS = 1e-6

RWKV_HEAD = 64
RWKV_WIDTH = D_MODEL
RWKV_HEADS = RWKV_WIDTH // RWKV_HEAD
DECAY_LORA = 64
AAA_LORA = 64
GATE_LORA = 128
RWKV_GN_EPS = 64e-5
RWKV_SPLITS = (RWKV_WIDTH, 2 * RWKV_WIDTH, 3 * RWKV_WIDTH, 3 * RWKV_WIDTH + DECAY_LORA, 3 * RWKV_WIDTH + DECAY_LORA + AAA_LORA)
RWKV_COLS = 3 * RWKV_WIDTH + DECAY_LORA + AAA_LORA + GATE_LORA

SSD_WIDTH = 2 * D_MODEL
SSD_HEAD = 64
SSD_HEADS = SSD_WIDTH // SSD_HEAD
SSD_GROUPS = 4
SSD_HEADS_PER_GROUP = SSD_HEADS // SSD_GROUPS
SSD_STATE = 128
SSD_CONV = 4
SSD_CONV_CH = SSD_WIDTH + 2 * SSD_GROUPS * SSD_STATE
SSD_COLS = SSD_WIDTH + SSD_CONV_CH + SSD_HEADS

N_BRANCH = 2
GATE_COLS = N_BRANCH * D_MODEL
IN_COLS_2 = RWKV_COLS + SSD_COLS + GATE_COLS

N_GROUPS = 4
EXP_PER_GROUP = 8
N_EXPERTS = N_GROUPS * EXP_PER_GROUP
TOP_K = 2
D_EXPERT = 512
MOE_BLOCK = 128


def rmsnorm_2(x, g):
    xf = x.astype(jnp.float32)
    y = xf * lax.rsqrt(jnp.mean(xf * xf, axis=-1, keepdims=True) + NORM_EPS)
    return (y * g.astype(jnp.float32)).astype(x.dtype)

def token_shift(u):
    return jnp.pad(u[:, :-1], ((0, 0), (1, 0), (0, 0)))

def rwkv7_mix(p, mu, w0, w_decay, a0, w_a, w_g, k_k, k_a, r_k, ln_g, ln_b):
    B_, S_, _ = p.shape
    f32 = jnp.float32
    u = p + mu * (token_shift(p) - p)
    r, k, v, zw, za, zg = jnp.split(u, RWKV_SPLITS, axis=-1)
    w = -jax.nn.softplus(-(w0 + jnp.tanh(zw) @ w_decay)) - 0.5
    decay = jnp.exp(-jnp.exp(w.astype(f32)))
    a = jax.nn.sigmoid(a0 + za @ w_a)
    g = jax.nn.sigmoid(zg) @ w_g

    def heads(t):
        return t.astype(f32).reshape(B_, S_, RWKV_HEADS, RWKV_HEAD)

    kk = heads(k * k_k)
    kk = kk / jnp.maximum(jnp.sqrt(jnp.sum(kk * kk, axis=-1, keepdims=True)), 1e-12)
    k = k * (1.0 + (a - 1.0) * k_a)
    r_h, k_h, v_h, a_h, w_h = heads(r), heads(k), heads(v), heads(a), heads(decay)

    def step(state, inp):
        r_t, w_t, k_t, v_t, kk_t, a_t = inp
        sa = jnp.einsum('bhij,bhj->bhi', state, -kk_t)
        state = (state * w_t[:, :, None, :]
                 + sa[..., None] * (kk_t * a_t)[:, :, None, :]
                 + v_t[..., None] * k_t[:, :, None, :])
        y_t = jnp.einsum('bhij,bhj->bhi', state, r_t)
        return state, y_t

    xs = tuple(jnp.moveaxis(t, 1, 0) for t in (r_h, w_h, k_h, v_h, kk, a_h))
    state0 = jnp.zeros((B_, RWKV_HEADS, RWKV_HEAD, RWKV_HEAD), f32)
    _, ys = lax.scan(step, state0, xs)
    y = jnp.moveaxis(ys, 0, 1)

    mean = jnp.mean(y, axis=-1, keepdims=True)
    var = jnp.mean(jnp.square(y - mean), axis=-1, keepdims=True)
    y = ((y - mean) * lax.rsqrt(var + RWKV_GN_EPS)).reshape(B_, S_, RWKV_WIDTH)
    y = y * ln_g + ln_b
    bonus = jnp.sum(r_h * k_h * r_k, axis=-1, keepdims=True) * v_h
    out = (y + bonus.reshape(B_, S_, RWKV_WIDTH)) * g
    return out.astype(p.dtype)

def causal_dwconv(u, w, b):
    c = u.shape[-1]
    y = lax.conv_general_dilated(u, w[:, None, :], window_strides=(1,), padding=[(SSD_CONV - 1, 0)],
                                 dimension_numbers=('NWC', 'WIO', 'NWC'), feature_group_count=c)
    return y + b

def ssd_chunked(xs, dt, A, Bm, Cm):
    f32 = jnp.float32
    B_, S_, _ = xs.shape
    nc = S_ // CHUNK
    G, Hg, P, N = SSD_GROUPS, SSD_HEADS_PER_GROUP, SSD_HEAD, SSD_STATE
    x = xs.astype(f32).reshape(B_, nc, CHUNK, G, Hg, P)
    dt = dt.reshape(B_, nc, CHUNK, G, Hg)
    Bc = Bm.astype(f32).reshape(B_, nc, CHUNK, G, N)
    Cc = Cm.astype(f32).reshape(B_, nc, CHUNK, G, N)
    a_dt = dt * A.reshape(G, Hg)
    a_cs = jnp.cumsum(a_dt, axis=2)
    xdt = x * dt[..., None]

    seg = a_cs[:, :, :, None] - a_cs[:, :, None, :]
    tril = jnp.tril(jnp.ones((CHUNK, CHUNK), dtype=bool))[None, None, :, :, None, None]
    decay_in = jnp.exp(jnp.where(tril, seg, -jnp.inf))
    cb = jnp.einsum('bclgn,bcsgn->bclsg', Cc, Bc)
    y_diag = jnp.einsum('bclsgh,bcsghp->bclghp', cb[..., None] * decay_in, xdt)

    decay_st = jnp.exp(a_cs[:, :, -1:] - a_cs)
    states = jnp.einsum('bcsgn,bcsghp->bcghpn', Bc, xdt * decay_st[..., None])
    chunk_decay = jnp.exp(a_cs[:, :, -1])

    def step(h, inp):
        s_c, d_c = inp
        return h * d_c[..., None, None] + s_c, h

    h0 = jnp.zeros((B_, G, Hg, P, N), f32)
    _, prev = lax.scan(step, h0, (jnp.moveaxis(states, 1, 0), jnp.moveaxis(chunk_decay, 1, 0)))
    prev = jnp.moveaxis(prev, 0, 1)
    y_off = jnp.einsum('bclgn,bcghpn->bclghp', Cc, prev) * jnp.exp(a_cs)[..., None]
    return (y_diag + y_off).reshape(B_, S_, SSD_WIDTH)

def ssd_mix(p, conv_w, conv_b, dt_bias, a_log, d_skip, norm_g):
    B_, S_, _ = p.shape
    f32 = jnp.float32
    z = p[..., :SSD_WIDTH]
    xbc = p[..., SSD_WIDTH:SSD_WIDTH + SSD_CONV_CH]
    dt_raw = p[..., SSD_WIDTH + SSD_CONV_CH:]
    xbc = jax.nn.silu(causal_dwconv(xbc, conv_w, conv_b))
    xs = xbc[..., :SSD_WIDTH]
    Bm = xbc[..., SSD_WIDTH:SSD_WIDTH + SSD_GROUPS * SSD_STATE]
    Cm = xbc[..., SSD_WIDTH + SSD_GROUPS * SSD_STATE:]
    dt = jax.nn.softplus(dt_raw.astype(f32) + dt_bias.astype(f32))
    A = -jnp.exp(a_log.astype(f32))
    y = ssd_chunked(xs, dt, A, Bm, Cm)
    y = y + (xs.astype(f32).reshape(B_, S_, SSD_HEADS, SSD_HEAD) * d_skip[:, None]).reshape(B_, S_, SSD_WIDTH)
    u = y * jax.nn.silu(z.astype(f32))
    u = u.reshape(B_, S_, SSD_GROUPS, SSD_WIDTH // SSD_GROUPS)
    u = u * lax.rsqrt(jnp.mean(u * u, axis=-1, keepdims=True) + NORM_EPS)
    u = u.reshape(B_, S_, SSD_WIDTH) * norm_g
    return u.astype(p.dtype)

def hier_moe(h, w_rg, b_rg, w_re, b_re, w_gate, w_up, w_down):
    B_, S_, D = h.shape
    T = B_ * S_
    f32 = jnp.float32
    ht = h.reshape(T, D)
    g_logits = (ht @ w_rg + b_rg).astype(f32)
    g_prob = jax.nn.softmax(g_logits, axis=-1)
    grp = jnp.argmax(g_logits, axis=-1)
    g_w = jnp.take_along_axis(g_prob, grp[:, None], axis=1)[:, 0]
    e_logits = (ht @ w_re + b_re).astype(f32).reshape(T, N_GROUPS, EXP_PER_GROUP)
    e_logits = jnp.take_along_axis(e_logits, grp[:, None, None], axis=1)[:, 0]
    e_prob = jax.nn.softmax(e_logits, axis=-1)
    top_p, top_i = lax.top_k(e_prob, TOP_K)
    gate = g_w[:, None] * top_p / jnp.sum(top_p, axis=-1, keepdims=True)
    expert = grp[:, None] * EXP_PER_GROUP + top_i

    n_assign = T * TOP_K
    e_flat = expert.reshape(-1)
    tok_flat = jnp.repeat(jnp.arange(T, dtype=jnp.int32), TOP_K)
    w_flat = gate.reshape(-1)
    order = jnp.argsort(e_flat)
    e_sorted, tok_sorted, w_sorted = e_flat[order], tok_flat[order], w_flat[order]
    counts = jnp.bincount(e_flat, length=N_EXPERTS)
    starts = jnp.cumsum(counts) - counts
    pad_counts = (counts + MOE_BLOCK - 1) // MOE_BLOCK * MOE_BLOCK
    pad_ends = jnp.cumsum(pad_counts)
    pad_starts = pad_ends - pad_counts
    dest = pad_starts[e_sorted] + (jnp.arange(n_assign) - starts[e_sorted])
    n_blocks = n_assign // MOE_BLOCK + N_EXPERTS
    buf_tok = jnp.zeros((n_blocks * MOE_BLOCK,), jnp.int32).at[dest].set(tok_sorted)
    buf_w = jnp.zeros((n_blocks * MOE_BLOCK,), f32).at[dest].set(w_sorted)
    block_exp = jnp.minimum(jnp.searchsorted(pad_ends, jnp.arange(n_blocks) * MOE_BLOCK, side='right'), N_EXPERTS - 1)

    def run_block(args):
        tok, e = args
        xb = ht[tok]
        hid = jax.nn.silu(xb @ w_gate[e]) * (xb @ w_up[e])
        return hid @ w_down[e]

    y_blocks = lax.map(run_block, (buf_tok.reshape(n_blocks, MOE_BLOCK), block_exp))
    y = jnp.zeros((T, D), f32).at[buf_tok].add(y_blocks.reshape(-1, D).astype(f32) * buf_w[:, None])
    return y.reshape(B_, S_, D).astype(h.dtype)

def second_inputs(seed: int = 0) -> dict:
    key = jax.random.key(seed)
    ks = iter(jax.random.split(key, 40))
    f32 = jnp.float32
    L = DEPTH

    def nrm(shape, scale):
        return jax.random.normal(next(ks), shape, f32) * scale

    def unif(shape, lo, hi):
        return jax.random.uniform(next(ks), shape, f32, lo, hi)

    x = nrm((BATCH, SEQ, D_MODEL), 1.0)
    attn_norm_g = 1.0 + nrm((L, D_MODEL), 0.05)
    w_in = nrm((L, D_MODEL, IN_COLS_2), D_MODEL ** -0.5)
    b_gate = nrm((L, GATE_COLS), 0.1)
    rwkv_mu = unif((L, RWKV_COLS), 0.2, 0.8)
    rwkv_w0 = unif((L, RWKV_WIDTH), -6.0, -1.0)
    rwkv_w_decay = nrm((L, DECAY_LORA, RWKV_WIDTH), 0.5 * DECAY_LORA ** -0.5)
    rwkv_a0 = nrm((L, RWKV_WIDTH), 0.5)
    rwkv_w_a = nrm((L, AAA_LORA, RWKV_WIDTH), AAA_LORA ** -0.5)
    rwkv_w_g = nrm((L, GATE_LORA, RWKV_WIDTH), GATE_LORA ** -0.5)
    rwkv_k_k = 0.85 + nrm((L, RWKV_WIDTH), 0.05)
    rwkv_k_a = 1.0 + nrm((L, RWKV_WIDTH), 0.05)
    rwkv_r_k = nrm((L, RWKV_HEADS, RWKV_HEAD), 0.1)
    rwkv_ln_g = 1.0 + nrm((L, RWKV_WIDTH), 0.05)
    rwkv_ln_b = nrm((L, RWKV_WIDTH), 0.05)
    w_up_rwkv = nrm((L, RWKV_WIDTH, D_MODEL), RWKV_WIDTH ** -0.5)
    ssd_conv_w = nrm((L, SSD_CONV, SSD_CONV_CH), SSD_CONV ** -0.5)
    ssd_conv_b = nrm((L, SSD_CONV_CH), 0.05)
    dt0 = jnp.exp(unif((L, SSD_HEADS), float(np.log(1e-3)), float(np.log(1e-1))))
    ssd_dt_bias = dt0 + jnp.log(-jnp.expm1(-dt0))
    ssd_a_log = jnp.log(unif((L, SSD_HEADS), 1.0, 16.0))
    ssd_d = 1.0 + nrm((L, SSD_HEADS), 0.1)
    ssd_norm_g = 1.0 + nrm((L, SSD_WIDTH), 0.05)
    w_up_ssd = nrm((L, SSD_WIDTH, D_MODEL), SSD_WIDTH ** -0.5)
    w_out = nrm((L, D_MODEL, D_MODEL), D_MODEL ** -0.5)
    ffn_norm_g = 1.0 + nrm((L, D_MODEL), 0.05)
    w_router_group = nrm((L, D_MODEL, N_GROUPS), D_MODEL ** -0.5)
    b_router_group = nrm((L, N_GROUPS), 0.01)
    w_router_expert = nrm((L, D_MODEL, N_EXPERTS), D_MODEL ** -0.5)
    b_router_expert = nrm((L, N_EXPERTS), 0.01)
    w_exp_gate = nrm((L, N_EXPERTS, D_MODEL, D_EXPERT), D_MODEL ** -0.5)
    w_exp_up = nrm((L, N_EXPERTS, D_MODEL, D_EXPERT), D_MODEL ** -0.5)
    w_exp_down = nrm((L, N_EXPERTS, D_EXPERT, D_MODEL), D_EXPERT ** -0.5)
    final_norm_g = 1.0 + nrm((D_MODEL,), 0.05)
    return {'x': x, 'attn_norm_g': attn_norm_g, 'w_in': w_in, 'b_gate': b_gate,
            'rwkv_mu': rwkv_mu, 'rwkv_w0': rwkv_w0, 'rwkv_w_decay': rwkv_w_decay, 'rwkv_a0': rwkv_a0,
            'rwkv_w_a': rwkv_w_a, 'rwkv_w_g': rwkv_w_g, 'rwkv_k_k': rwkv_k_k, 'rwkv_k_a': rwkv_k_a,
            'rwkv_r_k': rwkv_r_k, 'rwkv_ln_g': rwkv_ln_g, 'rwkv_ln_b': rwkv_ln_b, 'w_up_rwkv': w_up_rwkv,
            'ssd_conv_w': ssd_conv_w, 'ssd_conv_b': ssd_conv_b, 'ssd_dt_bias': ssd_dt_bias,
            'ssd_a_log': ssd_a_log, 'ssd_d': ssd_d, 'ssd_norm_g': ssd_norm_g, 'w_up_ssd': w_up_ssd,
            'w_out': w_out, 'ffn_norm_g': ffn_norm_g, 'w_router_group': w_router_group,
            'b_router_group': b_router_group, 'w_router_expert': w_router_expert,
            'b_router_expert': b_router_expert, 'w_exp_gate': w_exp_gate, 'w_exp_up': w_exp_up,
            'w_exp_down': w_exp_down, 'final_norm_g': final_norm_g}

def second_block(x, attn_norm_g, w_in, b_gate, rwkv_mu, rwkv_w0, rwkv_w_decay, rwkv_a0, rwkv_w_a, rwkv_w_g,
              rwkv_k_k, rwkv_k_a, rwkv_r_k, rwkv_ln_g, rwkv_ln_b, w_up_rwkv, ssd_conv_w, ssd_conv_b,
              ssd_dt_bias, ssd_a_log, ssd_d, ssd_norm_g, w_up_ssd, w_out, ffn_norm_g, w_router_group,
              b_router_group, w_router_expert, b_router_expert, w_exp_gate, w_exp_up, w_exp_down,
              final_norm_g):
    for l in range(DEPTH):
        h = rmsnorm_2(x, attn_norm_g[l])
        proj = h @ w_in[l]
        p_rwkv = proj[..., :RWKV_COLS]
        p_ssd = proj[..., RWKV_COLS:RWKV_COLS + SSD_COLS]
        p_gate = proj[..., RWKV_COLS + SSD_COLS:] + b_gate[l]
        y_a = rwkv7_mix(p_rwkv, rwkv_mu[l], rwkv_w0[l], rwkv_w_decay[l], rwkv_a0[l], rwkv_w_a[l], rwkv_w_g[l],
                        rwkv_k_k[l], rwkv_k_a[l], rwkv_r_k[l], rwkv_ln_g[l], rwkv_ln_b[l])
        y_b = ssd_mix(p_ssd, ssd_conv_w[l], ssd_conv_b[l], ssd_dt_bias[l], ssd_a_log[l], ssd_d[l], ssd_norm_g[l])
        gates = jax.nn.sigmoid(p_gate)
        g_a = gates[..., :D_MODEL]
        g_b = gates[..., D_MODEL:]
        merged = g_a * (y_a @ w_up_rwkv[l]) + g_b * (y_b @ w_up_ssd[l])
        x = x + merged @ w_out[l]
        h2 = rmsnorm_2(x, ffn_norm_g[l])
        x = x + hier_moe(h2, w_router_group[l], b_router_group[l], w_router_expert[l], b_router_expert[l],
                         w_exp_gate[l], w_exp_up[l], w_exp_down[l])
    return rmsnorm_2(x, final_norm_g)


def setup_inputs(seed=0):
    out = dict(first_inputs(seed))
    for name, value in second_inputs(seed + 1).items():
        if name != "x":
            out[name + "_2"] = value
    return out


def reference(
    x, c, w_ada, b_ada, norm1_w, w_in, hgrn_lb_logits, hgrn_onorm_w, conv_w, conv_onorm_w,
    w_out, norm2_w, peer_w_query, peer_sub_keys, peer_u, peer_v, final_norm_w, attn_norm_g_2,
    w_in_2, b_gate_2, rwkv_mu_2, rwkv_w0_2, rwkv_w_decay_2, rwkv_a0_2, rwkv_w_a_2, rwkv_w_g_2,
    rwkv_k_k_2, rwkv_k_a_2, rwkv_r_k_2, rwkv_ln_g_2, rwkv_ln_b_2, w_up_rwkv_2, ssd_conv_w_2,
    ssd_conv_b_2, ssd_dt_bias_2, ssd_a_log_2, ssd_d_2, ssd_norm_g_2, w_up_ssd_2, w_out_2,
    ffn_norm_g_2, w_router_group_2, b_router_group_2, w_router_expert_2, b_router_expert_2,
    w_exp_gate_2, w_exp_up_2, w_exp_down_2, final_norm_g_2,
):
    x = first_block(
        x, c, w_ada, b_ada, norm1_w, w_in, hgrn_lb_logits, hgrn_onorm_w, conv_w, conv_onorm_w,
        w_out, norm2_w, peer_w_query, peer_sub_keys, peer_u, peer_v, final_norm_w,
    )
    return second_block(
        x, attn_norm_g_2, w_in_2, b_gate_2, rwkv_mu_2, rwkv_w0_2, rwkv_w_decay_2, rwkv_a0_2,
        rwkv_w_a_2, rwkv_w_g_2, rwkv_k_k_2, rwkv_k_a_2, rwkv_r_k_2, rwkv_ln_g_2, rwkv_ln_b_2,
        w_up_rwkv_2, ssd_conv_w_2, ssd_conv_b_2, ssd_dt_bias_2, ssd_a_log_2, ssd_d_2,
        ssd_norm_g_2, w_up_ssd_2, w_out_2, ffn_norm_g_2, w_router_group_2, b_router_group_2,
        w_router_expert_2, b_router_expert_2, w_exp_gate_2, w_exp_up_2, w_exp_down_2,
        final_norm_g_2,
    )


_drawn_inputs = setup_inputs


def setup_inputs(seed=0):
    import zlib

    import numpy as np

    out = dict(_drawn_inputs(seed))
    spreads = {}
    factors = {'hgrn_onorm_w': 2.888,
     'rwkv_w_decay_2': 3.844,
     'rwkv_ln_b_2': 2.68,
     'b_router_group_2': 3.583,
     'b_router_expert_2': 4.95}
    for name, (base, spread) in spreads.items():
        noise = np.random.default_rng([zlib.crc32(name.encode()), seed]).standard_normal(out[name].shape)
        drawn = base * np.exp(spread * noise) if base else spread * noise
        out[name] = jnp.asarray(drawn.astype(out[name].dtype))
    for name, factor in factors.items():
        out[name] = (out[name] * factor).astype(out[name].dtype)
    return out
```

```python
from contextlib import ExitStack, contextmanager

import concourse.bass as bass
from concourse import mybir

P = 128
F32 = mybir.dt.float32
I32 = mybir.dt.int32
U32 = mybir.dt.uint32
ALU = mybir.AluOpType
ACT = mybir.ActivationFunctionType
AX = mybir.AxisListType
EPS = 1e-6

T = 512
D = 1024
KT = D // P
TT = T // P
HG = 4
HC = 128
CG = 4
HGRN_LEVELS = 7
SLOTS = 4
SLOT_COLS = 256


class Chain:

    def __init__(self, sem):
        self.sem = sem
        self.n = 0
        self.off = 0

    def link(self, eng, ins):
        self.mark(ins)
        self.wait(eng)

    def mark(self, ins):
        ins.then_inc(self.sem, 1)
        self.n += 1

    def wait(self, eng):
        eng.wait_ge(self.sem, self.off + self.n)

    def enter(self, i, steps):
        self.base = self.n
        self.steps = steps
        self.off = i * steps

    def leave(self, turns):
        assert self.n - self.base == self.steps, (self.n, self.base, self.steps)
        self.off = 0
        self.n = self.base + self.steps * turns


class Mem:
    pass


def setup(nc, ctx):
    m = Mem()
    m.nc = nc
    m.ctx = ctx
    m.ps = [ctx.enter_context(nc.psum_tensor(f"bank{i}", [P, 512], F32)) for i in range(8)]
    m.sem = lambda name: ctx.enter_context(nc.semaphore(name))
    m.dve = Chain(m.sem("dve_steps"))
    m.act = Chain(m.sem("act_steps"))
    m.pool = Chain(m.sem("pool_steps"))
    m.pe = Chain(m.sem("pe_steps"))
    sb = lambda name, shape, dt=F32: ctx.enter_context(nc.sbuf_tensor(name, shape, dt))
    m.sb = sb
    m.ready = m.sem("constants_ready")
    m.ident = sb("ident", [P, P])
    m.ones = sb("ones", [P, P])
    m.half_ones = sb("half_ones", [P, P])
    m.weights = sb("weights", [P, SLOTS, KT, SLOT_COLS])
    m.xT = sb("xT", [P, KT, T])
    m.hT = sb("hT", [P, KT, T])
    m.w_landed = [m.sem(f"w_landed{i}") for i in range(SLOTS)]
    m.w_landed_n = [0] * SLOTS
    m.tile_made = m.sem("tile_made")
    m.tile_made_n = 0
    m.tile_kept = m.sem("tile_kept")
    m.tile_kept_n = 0
    m.sq_made = m.sem("sq_made")
    m.sq_made_n = 0
    m.sq_summed = m.sem("sq_summed")
    m.sq_summed_n = 0
    m.rstd_made = m.sem("rstd_made")
    m.rstd_made_n = 0
    m.scaled = m.sem("scaled")
    m.scaled_n = 0
    return m


@contextmanager
def stage(m):
    nc, outer, taken = m.nc, m.sem, []
    with ExitStack() as own:
        def sem(name):
            taken.append(own.enter_context(nc.semaphore(name)))
            return taken[-1]

        m.sem = sem
        yield
        m.sem = outer
        with nc.Block() as block:

            @block.gpsimd
            def _(pool):
                for s in taken:
                    pool.sem_clear(s)


def constants(m):
    nc = m.nc
    with nc.Block() as block:

        @block.gpsimd
        def _(pool):
            c = m.pool
            c.mark(pool.memset(m.ones[:], 1.0))
            c.mark(pool.memset(m.half_ones[:], 1.0))
            c.mark(pool.memset(m.ident[:], 0.0))
            c.wait(pool)
            c.link(pool, pool.affine_select(out=m.ident[:], in_=m.ident[:], compare_op=ALU.not_equal, fill=1.0,
                                            base=0, pattern=[[-1, P]], channel_multiplier=1))
            c.link(pool, pool.memset(m.half_ones[0:64, 64:P], 0.0))
            c.link(pool, pool.memset(m.half_ones[64:P, 0:64], 0.0))
            pool.sem_inc(m.ready, 1)


def column_rows(m, name, rows):
    nc = m.nc
    n = sum(ap.shape[0] for _, ap in rows)
    assert n <= P
    cols = m.sb(name, [P, n])
    at = {}
    landed = m.sem(f"{name}_landed")
    with ExitStack() as own:
        raw = own.enter_context(nc.sbuf_tensor(f"{name}_raw", [P, P], F32))
        with nc.Block() as block:

            @block.sync
            def _(sp):
                r = 0
                for key, ap in rows:
                    at[key] = r
                    sp.dma_start(raw[r:r + ap.shape[0], :], ap).then_inc(landed, 16)
                    r += ap.shape[0]

            @block.tensor
            def _(pe):
                pe.wait_ge(landed, 16 * len(rows))
                m.pe.mark(pe.transpose(m.ps[0][:, 0:n], raw[0:n, :], m.ident[0:n, 0:n]))

            @block.vector
            def _(dve):
                m.pe.wait(dve)
                m.dve.mark(dve.tensor_copy(cols[:, :], m.ps[0][:, 0:n]))
    return cols, at


def project(m, w, n_tiles, rhs, k_tiles, keep, other=None, setup=None, col0=0):
    nc = m.nc
    wv = w.rearrange("(k p) n -> p k n", p=P)
    per_slot = SLOT_COLS // P
    chunks = n_tiles // per_slot
    turns = chunks // SLOTS
    assert n_tiles % per_slot == 0
    made0, kept0 = m.tile_made_n, m.tile_kept_n
    landed0 = list(m.w_landed_n)
    per_turn = SLOTS * per_slot

    def turns_of(eng, body, first=0):
        if turns > first:
            with eng.Fori(first, turns) as i:
                body(i, SLOTS)
        if chunks % SLOTS:
            body(turns, chunks % SLOTS)

    with nc.Block() as block:

        @block.sync
        def _(sp):
            def load(i, s):
                sp.dma_start(m.weights[:, s, 0:k_tiles, :],
                             wv[:, :, bass.ds((i * SLOTS + s) * SLOT_COLS + col0, SLOT_COLS)]).then_inc(m.w_landed[s], 16)

            def body(i, slots):
                for s in range(slots):
                    sp.wait_ge(m.tile_made, made0 + (i - 1) * per_turn + (s + 1) * per_slot)
                    load(i, s)

            for s in range(min(SLOTS, chunks)):
                load(0, s)
            if turns >= 1:
                turns_of(sp, body, first=1)

        @block.tensor
        def _(pe):
            def body(i, slots, first_turn=False):
                for s in range(slots):
                    pe.wait_ge(m.w_landed[s], landed0[s] + 16 * i + 16)
                    for c in range(per_slot):
                        b = s * per_slot + c
                        if not first_turn:
                            pe.wait_ge(m.tile_kept, kept0 + (i - 1) * per_turn + b + 1)
                        for k in range(k_tiles):
                            ins = pe.matmul(m.ps[b][:, :], m.weights[:, s, k, c * P:(c + 1) * P], rhs(k),
                                            start=(k == 0), stop=(k == k_tiles - 1))
                        ins.then_inc(m.tile_made, 1)

            if turns >= 1:
                body(0, SLOTS, first_turn=True)
                turns_of(pe, body, first=1)
            else:
                body(0, chunks, first_turn=True)

        @block.vector
        def _(dve):
            def body(i, slots):
                for b in range(slots * per_slot):
                    dve.wait_ge(m.tile_made, made0 + i * per_turn + b + 1)
                    keep(dve, i * per_turn + b, m.ps[b]).then_inc(m.tile_kept, 1)

            if setup:
                setup(dve)
            turns_of(dve, body)

        if other:
            other(block)

    m.tile_made_n += n_tiles
    m.tile_kept_n += n_tiles
    for s in range(SLOTS):
        m.w_landed_n[s] += 16 * len([c for c in range(chunks) if c % SLOTS == s])


def norm(m, src, dst, scale, shift=None, sq=None):
    nc = m.nc
    sq = dst if sq is None else sq
    made0, summed0, rstd0, scaled0 = m.sq_made_n, m.sq_summed_n, m.rstd_made_n, m.scaled_n
    with ExitStack() as own:
        rstd = own.enter_context(nc.sbuf_tensor(f"rstd{made0}", [P, T], F32))
        with nc.Block() as block:

            @block.scalar
            def _(act):
                for k in range(KT):
                    act.activation(sq[:, k, :], src[:, k, :], ACT.Square).then_inc(m.sq_made, 1)
                act.wait_ge(m.rstd_made, rstd0 + 1)
                act.activation(rstd[:, :], rstd[:, :], ACT.Sqrt).then_inc(m.rstd_made, 1)
                if shift is not None:
                    for k in range(KT):
                        act.wait_ge(m.scaled, scaled0 + k + 1)
                        m.act.mark(act.activation(dst[:, k, :], dst[:, k, :], ACT.Identity, bias=shift[:, k:k + 1]))

            @block.tensor
            def _(pe):
                for k in range(KT):
                    pe.wait_ge(m.sq_made, made0 + k + 1)
                    ins = pe.matmul(m.ps[0][:, :], m.ones[:, :], sq[:, k, :], start=(k == 0), stop=(k == KT - 1))
                ins.then_inc(m.sq_summed, 1)

            @block.vector
            def _(dve):
                dve.wait_ge(m.sq_summed, summed0 + 1)
                dve.tensor_scalar(rstd[:, :], m.ps[0][:, :], 1.0 / D, EPS, ALU.mult, ALU.add).then_inc(m.rstd_made, 1)
                dve.wait_ge(m.rstd_made, rstd0 + 2)
                m.dve.link(dve, dve.reciprocal(rstd[:, :], rstd[:, :]))
                for k in range(KT):
                    dve.scalar_tensor_tensor(out=dst[:, k, :], in0=src[:, k, :], scalar=scale[:, k:k + 1],
                                             in1=rstd[:, :], op0=ALU.mult, op1=ALU.mult).then_inc(m.scaled, 1)

    m.sq_made_n += KT
    m.sq_summed_n += 1
    m.rstd_made_n += 2
    m.scaled_n += KT


def load_tokens(m, x):
    nc = m.nc
    landed = m.sem("x_landed")
    turned = m.sem("x_turned")
    with ExitStack() as own:
        rows = own.enter_context(nc.sbuf_tensor("x_rows", [P, TT, D], F32))
        with nc.Block() as block:

            @block.sync
            def _(sp):
                sp.dma_start(rows[:, :, :], x.rearrange("(t p) d -> p t d", p=P)).then_inc(landed, 16)

            @block.tensor
            def _(pe):
                pe.wait_ge(landed, 16)
                for k in range(KT):
                    for t in range(TT):
                        ins = pe.transpose(m.ps[k][:, t * P:(t + 1) * P], rows[:, t, k * P:(k + 1) * P], m.ident[:, :])
                    ins.then_inc(turned, 1)

            @block.vector
            def _(dve):
                for k in range(KT):
                    dve.wait_ge(turned, k + 1)
                    m.dve.mark(dve.tensor_copy(m.xT[:, k, :], m.ps[k][:, :]))


def modulation(m, w_ada, cols, at, mod, lead):
    nc = m.nc
    n_tiles = w_ada.shape[1] // P
    per_slot = SLOT_COLS // P
    per_turn = SLOTS * per_slot
    turns = n_tiles // per_turn
    wv = w_ada.rearrange("(k p) n -> p k n", p=P)
    made0 = m.tile_made_n
    with nc.Block() as block:

        @block.sync
        def _(sp):
            def load(i, s):
                sp.dma_start(m.weights[:, s, :, :],
                             wv[:, :, bass.ds((i * SLOTS + s) * SLOT_COLS, SLOT_COLS)]).then_inc(m.w_landed[s], 16)

            for s in range(SLOTS):
                load(0, s)
            with sp.Fori(1, turns) as i:
                for s in range(SLOTS):
                    sp.wait_ge(m.tile_made, made0 + (i - 1) * per_turn + (s + 1) * per_slot)
                    load(i, s)

        @block.scalar
        def _(act):
            m.act.mark(act.activation(lead[:, :], cols[:, at["c"]:at["c"] + KT], ACT.Silu))

        @block.tensor
        def _(pe):
            m.act.wait(pe)
            with pe.Fori(0, turns) as i:
                for s in range(SLOTS):
                    pe.wait_ge(m.w_landed[s], m.w_landed_n[s] + 16 * i + 16)
                    for c in range(per_slot):
                        b = s * per_slot + c
                        for k in range(KT):
                            ins = pe.matmul(m.ps[0][:, bass.ds(i * per_turn + b, 1)],
                                            m.weights[:, s, k, c * P:(c + 1) * P], lead[:, k:k + 1],
                                            start=(k == 0), stop=(k == KT - 1))
                        ins.then_inc(m.tile_made, 1)

        @block.vector
        def _(dve):
            dve.wait_ge(m.tile_made, made0 + n_tiles)
            b0 = at["b_ada"]
            m.dve.mark(dve.tensor_tensor(mod[:, :], m.ps[0][:, 0:n_tiles], cols[:, b0:b0 + n_tiles], ALU.add))

    m.tile_made_n += n_tiles
    for s in range(SLOTS):
        m.w_landed_n[s] += 16 * turns


def level_masks(m, own, name, n, levels):
    nc = m.nc
    masks = own.enter_context(nc.sbuf_tensor(name, [P, levels + 1, n], I32))
    with ExitStack() as own:
        s_of = own.enter_context(nc.sbuf_tensor(f"{name}_s", [P, n], I32))
        t_of = own.enter_context(nc.sbuf_tensor(f"{name}_t", [P, n], I32))
        late = own.enter_context(nc.sbuf_tensor(f"{name}_late", [P, n], I32))
        x = own.enter_context(nc.sbuf_tensor(f"{name}_x", [P, n], I32))
        with nc.Block() as block:

            @block.gpsimd
            def _(pool):
                c = m.pool
                for h in range(P // n):
                    c.mark(pool.iota(s_of[h * n:(h + 1) * n, :], [[0, n]], base=0, channel_multiplier=1))
                c.mark(pool.iota(t_of[:, :], [[1, n]], base=0, channel_multiplier=0))

            @block.vector
            def _(dve):
                c = m.dve
                m.pool.wait(dve)
                c.mark(dve.tensor_tensor(late[:, :], t_of[:, :], s_of[:, :], ALU.is_gt))
                c.mark(dve.tensor_tensor(masks[:, levels, :], t_of[:, :], s_of[:, :], ALU.is_equal))
                c.link(dve, dve.tensor_tensor(x[:, :], t_of[:, :], s_of[:, :], ALU.bitwise_xor))
                c.link(dve, dve.tensor_tensor(x[:, :], x[:, :], late[:, :], ALU.mult))
                for l in range(levels):
                    c.link(dve, dve.tensor_scalar(s_of[:, :], x[:, :], l, None, ALU.logical_shift_right))
                    c.link(dve, dve.tensor_scalar(masks[:, l, :], s_of[:, :], 1, None, ALU.is_equal))
    return masks


def group_norm(m, src, dst, w, groups, per_group, ones, mean_of, eps=EPS, gate=None):
    nc = m.nc
    made0, summed0, rstd0, scaled0 = m.sq_made_n, m.sq_summed_n, m.rstd_made_n, m.scaled_n
    turns = groups
    with ExitStack() as own:
        sq = own.enter_context(nc.sbuf_tensor(f"gn_sq{made0}", [P, 2, per_group, T], F32))
        rstd = own.enter_context(nc.sbuf_tensor(f"gn_rstd{made0}", [P, 2, T], F32))
        with nc.Block() as block:

            @block.scalar
            def _(act):
                def root(g):
                    act.wait_ge(m.rstd_made, rstd0 + 2 * g + 1)
                    act.activation(rstd[:, g % 2, :], rstd[:, g % 2, :], ACT.Sqrt).then_inc(m.rstd_made, 1)

                for g in range(turns):
                    if g >= 2:
                        act.wait_ge(m.sq_summed, summed0 + g - 1)
                    for j in range(per_group):
                        act.activation(sq[:, g % 2, j, :], src[:, g * per_group + j, :], ACT.Square).then_inc(m.sq_made, 1)
                    if g >= 1:
                        root(g - 1)
                root(turns - 1)

            @block.tensor
            def _(pe):
                for g in range(turns):
                    pe.wait_ge(m.sq_made, made0 + (g + 1) * per_group)
                    if g >= 2:
                        pe.wait_ge(m.rstd_made, rstd0 + 2 * g - 3)
                    for j in range(per_group):
                        ins = pe.matmul(m.ps[g % 2][:, :], ones[:, :], sq[:, g % 2, j, :],
                                        start=(j == 0), stop=(j == per_group - 1))
                    ins.then_inc(m.sq_summed, 1)

            @block.vector
            def _(dve):
                c = m.dve
                for g in range(turns):
                    dve.wait_ge(m.sq_summed, summed0 + g + 1)
                    if g >= 1:
                        dve.wait_ge(m.rstd_made, rstd0 + 2 * g)
                        c.wait(dve)
                    dve.tensor_scalar(rstd[:, g % 2, :], m.ps[g % 2][:, :], 1.0 / mean_of, eps,
                                      ALU.mult, ALU.add).then_inc(m.rstd_made, 1)
                    dve.wait_ge(m.rstd_made, rstd0 + 2 * g + 2)
                    c.link(dve, dve.reciprocal(rstd[:, g % 2, :], rstd[:, g % 2, :]))
                    for j in range(per_group):
                        t = g * per_group + j
                        c.mark(dve.scalar_tensor_tensor(out=dst[:, t, :], in0=src[:, t, :], scalar=w[:, t:t + 1],
                                                        in1=rstd[:, g % 2, :], op0=ALU.mult, op1=ALU.mult))
                        if gate is not None:
                            c.wait(dve)
                            c.mark(dve.tensor_tensor(dst[:, t, :], dst[:, t, :], gate[:, t, :], ALU.mult))

    m.sq_made_n += turns * per_group
    m.sq_summed_n += turns
    m.rstd_made_n += 2 * turns


def hgrn(m, cols, at, proj, yT, masks):
    nc = m.nc
    H, C = HG, HC
    NCH = T // C
    W = H * T
    L = HGRN_LEVELS
    flat = lambda ap: ap.rearrange("p h t -> p (h t)")
    q, f_raw, v, g = (proj[:, j * H:(j + 1) * H, :] for j in range(4))
    with ExitStack() as own:
        sb = lambda name, shape, dt=F32: own.enter_context(nc.sbuf_tensor(name, shape, dt))
        lb = sb("hg_lb", [P, H])
        lb1 = sb("hg_lb1", [P, H])
        kk = sb("hg_k", [P, H, T])
        b = sb("hg_b", [P, H, T])
        pair = sb("hg_pair", [P, 2, H, T])
        scores = sb("hg_scores", [P, H, T])
        dist = sb("hg_dist", [P, 2, H, T])
        keep = dist[:, 0]
        f = dist[:, 1]

        diff_made, sig_made, f_made, ready = (m.sem(f"hg_{x}") for x in ("diff", "sig", "f", "ready"))
        with nc.Block() as block:

            @block.gpsimd
            def _(pool):
                m.pool.mark(pool.memset(scores[:, :, :], 0.0))
                m.pool.link(pool, pool.memset(keep[:, :, :], 1.0))
                k4 = flat(keep).rearrange("p (n c) -> p n c", c=C)
                pool.memset(k4[:, :, 0:1], 0.0).then_inc(ready, 1)

            @block.scalar
            def _(act):
                act.wait_ge(diff_made, 1)
                act.activation(lb[:, :], lb1[:, :], ACT.Sigmoid).then_inc(sig_made, 1)
                act.activation(flat(f), flat(f_raw), ACT.Sigmoid).then_inc(sig_made, 1)
                act.activation(flat(kk), flat(f_raw), ACT.Sigmoid, scale=-1.0).then_inc(sig_made, 1)
                act.wait_ge(f_made, H)
                act.activation(flat(f), flat(f), ACT.Ln).then_inc(sig_made, 1)

            @block.vector
            def _(dve):
                c = m.dve
                a0 = at["lb"]
                dve.tensor_tensor(lb1[:, :], cols[:, a0:a0 + H], cols[:, a0 + H:a0 + 2 * H], ALU.subtract).then_inc(diff_made, 1)
                dve.wait_ge(sig_made, 1)
                c.link(dve, dve.tensor_scalar(lb1[:, :], lb[:, :], -1.0, 1.0, ALU.mult, ALU.add))
                dve.wait_ge(sig_made, 3)
                for h in range(H):
                    dve.tensor_scalar(f[:, h, :], f[:, h, :], lb1[:, h:h + 1], lb[:, h:h + 1],
                                      ALU.mult, ALU.add).then_inc(f_made, 1)
                for h in range(H):
                    c.mark(dve.tensor_scalar(kk[:, h, :], kk[:, h, :], lb1[:, h:h + 1], None, ALU.mult))
                dve.wait_ge(sig_made, 4)
                dve.wait_ge(ready, 1)
                c.mark(dve.tensor_tensor_scan(flat(b), flat(keep), flat(f), 0.0, ALU.mult, ALU.add))

        dist_made, decay_made, pair_made, level_made, folded = (
            m.sem(f"hg_{x}") for x in ("dist_made", "decay_made", "pair_made", "level_made", "folded"))
        blocks = lambda ap, l: flat(ap).rearrange("p (n c) -> p n c", c=2 << l)
        halves = lambda ap, l, j: flat(ap).rearrange("p (n j c) -> p n j c", j=2, c=1 << l)[:, :, j, :]
        with nc.Block() as block:

            @block.scalar
            def _(act):
                for l in range(L):
                    act.wait_ge(dist_made, l + 1)
                    act.activation(flat(dist[:, l % 2]), flat(dist[:, l % 2]), ACT.Abs).then_inc(decay_made, 1)
                    act.wait_ge(decay_made, 2 * l + 1)
                    act.activation(flat(dist[:, l % 2]), flat(dist[:, l % 2]), ACT.Exp, scale=-1.0).then_inc(decay_made, 1)

            @block.tensor
            def _(pe):
                for l in range(L + 1):
                    if l < L:
                        pe.wait_ge(pair_made, 2 * l + 2)
                    if l >= 2:
                        pe.wait_ge(folded, H * (l - 1))
                    for h in range(H):
                        for n in range(NCH):
                            t = slice(n * C, (n + 1) * C)
                            k_, q_ = (pair[:, l % 2, h, t],) * 2 if l < L else (kk[:, h, t], q[:, h, t])
                            ins = pe.matmul(m.ps[4 * (l % 2) + h][:, t], k_, q_, start=True, stop=True)
                    ins.then_inc(level_made, 1)

            @block.vector
            def _(dve):
                for l in range(L + 3):
                    if l < L:
                        if l >= 2:
                            dve.wait_ge(pair_made, 2 * l - 2)
                        mid = blocks(b, l)[:, :, (1 << l) - 1:1 << l].to_broadcast([P, W // (2 << l), 2 << l])
                        dve.tensor_tensor(blocks(dist[:, l % 2], l), blocks(b, l), mid, ALU.subtract).then_inc(dist_made, 1)
                    if 1 <= l <= L:
                        p = l - 1
                        dve.wait_ge(decay_made, 2 * p + 2)
                        if p >= 2:
                            dve.wait_ge(level_made, p - 1)
                        for j, src in enumerate((kk, q)):
                            dve.tensor_tensor(halves(pair[:, p % 2], p, j), halves(dist[:, p % 2], p, j),
                                              halves(src, p, j), ALU.mult).then_inc(pair_made, 1)
                    if l >= 2:
                        p = l - 2
                        dve.wait_ge(level_made, p + 1)
                        if p >= 1:
                            dve.wait_ge(folded, H * p)
                        for h in range(H):
                            mask = masks[:, p:p + 1, :].to_broadcast([P, NCH, C])
                            dve.copy_predicated(scores[:, h, :].rearrange("p (n t) -> p n t", t=C), mask,
                                                m.ps[4 * (p % 2) + h][:, :].rearrange("p (n t) -> p n t", t=C)).then_inc(folded, 1)

        vrow, krow = dist[:, 0], dist[:, 1]
        with ExitStack() as last:
            elast = last.enter_context(nc.sbuf_tensor("hg_elast", [P, H, NCH], F32))
            state = last.enter_context(nc.sbuf_tensor("hg_state", [P, H, P], F32))
            eb = m.hT[:, 0:H, :]
            v_turned, k_turned, e_made, k_decayed, rows_kept, update_made, state_made, out_kept = (
                m.sem(f"hg_{x}") for x in ("v_turned", "k_turned", "e_made", "k_decayed", "rows_kept", "update_made",
                                           "state_made", "out_kept"))
            with nc.Block() as block:

                @block.scalar
                def _(act):
                    act.activation(flat(eb), flat(b), ACT.Exp).then_inc(e_made, 1)
                    act.activation(elast[:, :, :], b[:, :, C - 1:T:C], ACT.Exp).then_inc(e_made, 1)
                    act.wait_ge(k_decayed, 1)
                    act.activation(flat(pair[:, 1]), flat(pair[:, 1]), ACT.Exp, scale=-1.0).then_inc(e_made, 1)
                    for h in range(H):
                        act.wait_ge(v_turned, h + 1)
                        act.copy(vrow[:, h, :], m.ps[h][:, :]).then_inc(rows_kept, 1)
                    for h in range(H):
                        act.wait_ge(k_turned, h + 1)
                        act.copy(krow[:, h, :], m.ps[4 + h][:, :]).then_inc(rows_kept, 1)
                    m.act.mark(act.activation(flat(kk), flat(g), ACT.Silu))

                @block.tensor
                def _(pe):
                    for h in range(H):
                        for n in range(NCH):
                            ins = pe.transpose(m.ps[h][:, n * C:(n + 1) * C], v[:, h, n * C:(n + 1) * C], m.ident[:, :])
                        ins.then_inc(v_turned, 1)
                    pe.wait_ge(k_decayed, 3)
                    for h in range(H):
                        for n in range(NCH):
                            ins = pe.transpose(m.ps[4 + h][:, n * C:(n + 1) * C], pair[:, 1, h, n * C:(n + 1) * C], m.ident[:, :])
                        ins.then_inc(k_turned, 1)
                    pe.wait_ge(rows_kept, 2 * H)
                    for n in range(NCH):
                        t = slice(n * C, (n + 1) * C)
                        for h in range(H):
                            pe.matmul(m.ps[h][:, t], vrow[:, h, t], scores[:, h, t], start=True, stop=(n == 0))
                            if n > 0:
                                pe.wait_ge(state_made, (n - 1) * H + h + 1)
                                ins = pe.matmul(m.ps[h][:, t], state[:, h, :], pair[:, 0, h, t], start=False, stop=True)
                            if n < NCH - 1:
                                ins = pe.matmul(m.ps[4 + h][:, t], krow[:, h, t], vrow[:, h, t], start=True, stop=True)
                            ins.then_inc(update_made, 1)

                @block.vector
                def _(dve):
                    bv = flat(b).rearrange("p (n c) -> p n c", c=C)
                    last_b = bv[:, :, C - 1:C].to_broadcast([P, H * NCH, C])
                    kd = flat(pair[:, 1])
                    dve.tensor_tensor(kd.rearrange("p (n c) -> p n c", c=C), bv, last_b, ALU.subtract).then_inc(k_decayed, 1)
                    dve.wait_ge(e_made, 2)
                    dve.tensor_tensor(flat(pair[:, 0]), flat(eb), flat(q), ALU.mult).then_inc(k_decayed, 1)
                    dve.wait_ge(e_made, 3)
                    dve.tensor_tensor(kd, kd, flat(kk), ALU.mult).then_inc(k_decayed, 1)
                    for n in range(NCH - 1):
                        for h in range(H):
                            u = m.ps[4 + h][:, n * C:(n + 1) * C]
                            dve.wait_ge(update_made, n * H + h + 1)
                            if n == 0:
                                dve.tensor_copy(state[:, h, :], u).then_inc(state_made, 1)
                            else:
                                dve.wait_ge(state_made, (n - 1) * H + h + 1)
                                dve.scalar_tensor_tensor(out=state[:, h, :], in0=state[:, h, :], scalar=elast[:, h, n:n + 1],
                                                         in1=u, op0=ALU.mult, op1=ALU.add).then_inc(state_made, 1)
                    for h in range(H):
                        dve.wait_ge(update_made, (NCH - 1) * H + h + 1)
                        m.dve.mark(dve.tensor_copy(b[:, h, :], m.ps[h][:, :]))

        w0 = at["hgrn_w"]
        group_norm(m, b, yT, cols[:, w0:w0 + H], H, 1, m.ones, P, gate=kk)


def short_conv(m, cols, at, proj, yT):
    nc = m.nc
    bg, cg, xin = (proj[:, 16 + 4 * j:20 + 4 * j, :] for j in range(3))
    c0 = at["conv_w"]
    with nc.Block() as block:

        @block.vector
        def _(dve):
            c = m.dve
            c.link(dve, dve.tensor_tensor(xin, cg, xin, ALU.mult))
            for g in range(CG):
                tap = lambda j: cols[:, c0 + j * CG + g:c0 + j * CG + g + 1]
                u, y = xin[:, g, :], cg[:, g, :]
                c.link(dve, dve.tensor_scalar(y, u, tap(2), None, ALU.mult))
                for j in (1, 0):
                    d = 2 - j
                    c.link(dve, dve.scalar_tensor_tensor(out=y[:, d:], in0=u[:, :T - d], scalar=tap(j), in1=y[:, d:],
                                                         op0=ALU.mult, op1=ALU.add))
            c.mark(dve.tensor_tensor(bg, cg, bg, ALU.mult))
    w0 = at["conv_norm"]
    group_norm(m, bg, yT[:, HG:HG + CG, :], cols[:, w0:w0 + CG], CG, 1, m.ones, P)


def first_mixer(m, x, c, w_ada, b_ada, norm1_w, w_in, lb_logits, hgrn_w, conv_w, conv_norm_w, w_out, norm2_w, final_norm_w):
    nc = m.nc
    row = lambda ap: ap.rearrange("(k p) -> k p", p=P)
    load_tokens(m, x[0])
    cols, at = column_rows(m, "cols1", [
        ("c", row(c[0])), ("b_ada", row(b_ada[0])), ("norm1", row(norm1_w[0])),
        ("lb", lb_logits.rearrange("l (k p) -> (l k) p", p=P)), ("hgrn_w", row(hgrn_w[0])),
        ("conv_w", conv_w[0].rearrange("j (k p) -> (j k) p", p=P)), ("conv_norm", row(conv_norm_w[0])),
        ("norm2", row(norm2_w[0])), ("final", row(final_norm_w))])
    mod = m.sb("mod", [P, 6 * KT])
    m.mod = mod
    scale1 = m.sb("scale1", [P, KT])
    m.scale2 = m.sb("scale2", [P, KT])
    silu_c = m.sb("silu_c", [P, KT])
    modulation(m, w_ada[0], cols, at, mod, silu_c)
    with nc.Block() as block:

        @block.vector
        def _(dve):
            for j, key, dst in ((1, "norm1", scale1), (4, "norm2", m.scale2)):
                m.dve.mark(dve.scalar_tensor_tensor(out=dst[:, :], in0=mod[:, j * KT:(j + 1) * KT], scalar=1.0,
                                                    in1=cols[:, at[key]:at[key] + KT], op0=ALU.add, op1=ALU.mult))
    norm(m, m.xT, m.hT, scale1, mod[:, 0:KT])
    with ExitStack() as own:
        proj = own.enter_context(nc.sbuf_tensor("proj1", [P, 28, T], F32))
        yT = own.enter_context(nc.sbuf_tensor("y1T", [P, KT, T], F32))
        project(m, w_in[0], 28, lambda k: m.hT[:, k, :], KT,
                lambda dve, t, bank: dve.tensor_copy(at_tile(proj, t), bank[:, :]))
        with ExitStack() as own2:
            masks = level_masks(m, own2, "pairs128", HC, HGRN_LEVELS)
            hgrn(m, cols, at, proj, yT, masks)
        short_conv(m, cols, at, proj, yT)
        add_projected(m, w_out[0], yT, KT, mod[:, 2 * KT:3 * KT])
    return cols, at


def at_tile(t3, t):
    return t3[:, t, :] if isinstance(t, int) else t3[:, bass.ds(t, 1), :].rearrange("p a t -> p (a t)")


def add_projected(m, w, rhs, k_tiles, gate):
    def keep(dve, t, bank):
        scalar = gate[:, t:t + 1] if isinstance(t, int) else gate[:, bass.ds(t, 1)]
        x = at_tile(m.xT, t)
        return dve.scalar_tensor_tensor(out=x, in0=bank[:, :], scalar=scalar, in1=x, op0=ALU.mult, op1=ALU.add)
    project(m, w, KT, lambda k: rhs[:, k, :], k_tiles, keep)


PH = 8
NK = 128
TOPK = 16
PICKS = PH * TOPK
RING = 16
GROUP = 4
GROUPS = PICKS // GROUP
BUFS = 2 * RING // GROUP
LOWEST = -3.0e38


def turn_back(m, src, dst, name):
    nc = m.nc
    turned = m.sem(f"{name}_turned")
    kept = m.sem(f"{name}_kept")
    halves = D // 512
    with nc.Block() as block:

        @block.tensor
        def _(pe):
            for t in range(TT):
                for h in range(halves):
                    for j in range(4):
                        ins = pe.transpose(m.ps[t * halves + h][:, j * P:(j + 1) * P],
                                           src[:, 4 * h + j, t * P:(t + 1) * P], m.ident[:, :])
                    ins.then_inc(turned, 1)

        @block.vector
        def _(dve):
            for n in range(TT * halves):
                dve.wait_ge(turned, n + 1)
                m.dve.mark(dve.tensor_copy(dst[:, n // halves, (n % halves) * 512:(n % halves + 1) * 512], m.ps[n][:, :]))


def turn_forward(m, src, name, keep):
    nc = m.nc
    turned = m.sem(f"{name}_turned")
    with nc.Block() as block:

        @block.tensor
        def _(pe):
            for k in range(KT):
                for t in range(TT):
                    ins = pe.transpose(m.ps[k][:, t * P:(t + 1) * P], src[:, t, k * P:(k + 1) * P], m.ident[:, :])
                ins.then_inc(turned, 1)

        @block.vector
        def _(dve):
            for k in range(KT):
                dve.wait_ge(turned, k + 1)
                m.dve.mark(keep(dve, k, m.ps[k]))


def key_scores(m, sub_keys, qT, s_all):
    nc = m.nc
    HP = 2 * PH
    landed, turned, kept, made, s_kept = (m.sem(f"keys_{x}") for x in ("landed", "turned", "kept", "made", "s_kept"))
    with ExitStack() as own:
        raw = own.enter_context(nc.sbuf_tensor("keys_raw", [P, HP, P], F32))
        kT = own.enter_context(nc.sbuf_tensor("keysT", [P, HP, P], F32))
        with nc.Block() as block:

            @block.sync
            def _(sp):
                keys = sub_keys.rearrange("h j n k -> n (h j) k")
                for b in range(4):
                    sp.dma_start(raw[:, 4 * b:4 * b + 4, :], keys[:, 4 * b:4 * b + 4, :]).then_inc(landed, 16)

            @block.tensor
            def _(pe):
                pe.wait_ge(landed, 64)
                for b in range(4):
                    for j in range(4):
                        ins = pe.transpose(m.ps[b][:, j * P:(j + 1) * P], raw[:, 4 * b + j, :], m.ident[:, :])
                    ins.then_inc(turned, 1)
                pe.wait_ge(kept, 4)
                for t in range(TT):
                    for b in range(4):
                        n = t * 4 + b
                        if n >= 8:
                            pe.wait_ge(s_kept, n - 7)
                        for j in range(4):
                            hp = 4 * b + j
                            ins = pe.matmul(m.ps[n % 8][:, j * P:(j + 1) * P], qT[:, hp, t * P:(t + 1) * P], kT[:, hp, :],
                                            start=True, stop=True)
                        ins.then_inc(made, 1)

            @block.vector
            def _(dve):
                for b in range(4):
                    dve.wait_ge(turned, b + 1)
                    dve.tensor_copy(kT[:, 4 * b:4 * b + 4, :].rearrange("p j n -> p (j n)"), m.ps[b][:, :]).then_inc(kept, 1)
                for n in range(4 * TT):
                    dve.wait_ge(made, n + 1)
                    dve.tensor_copy(s_all[:, n // 4, (n % 4) * 512:(n % 4 + 1) * 512], m.ps[n % 8][:, :]).then_inc(s_kept, 1)


def pick_experts(m, s_all, index, gate):
    nc = m.nc
    HP = 2 * PH
    shifted, exps = m.sem("gate_shifted"), m.sem("gate_exps")
    with ExitStack() as own:
        sb = lambda name, shape, dt=F32: own.enter_context(nc.sbuf_tensor(name, shape, dt))
        s = sb("pk_s", [P, HP, NK])
        s2 = sb("pk_s2", [P, HP, NK])
        val = sb("pk_val", [P, HP, TOPK])
        ind = sb("pk_ind", [P, HP, TOPK], U32)
        indf = sb("pk_indf", [P, HP, TOPK])
        cand = sb("pk_cand", [P, PH, TOPK * TOPK])
        cand2 = sb("pk_cand2", [P, PH, TOPK * TOPK])
        best = sb("pk_best", [P, PH, TOPK])
        pos = sb("pk_pos", [P, PH, TOPK], U32)
        digit = sb("pk_digit", [P, 2, PH * TOPK], U32)
        digitf = sb("pk_digitf", [P, 2, PH * TOPK])
        which = sb("pk_which", [P, PH, TOPK, TOPK])
        found = sb("pk_found", [P, 2, PH * TOPK])
        count = sb("pk_count", [P, TOPK])
        total = sb("pk_total", [P, PH])
        ex = sb("pk_ex", [P, PH, TOPK])
        pad = sb("pk_pad", [P, 1])

        def top16(dve, src, spare, vals, inds, n):
            c = m.dve
            c.mark(dve.memset(pad[:, :], 0.0))
            for r in range(n):
                c.mark(dve.max(vals[:, r, 0:8], src[:, r, :]))
            c.wait(dve)
            c.mark(dve.memset(pad[:, :], 0.0))
            for r in range(n):
                c.mark(dve.max_index(inds[:, r, 0:8], vals[:, r, 0:8], src[:, r, :]))
                c.mark(dve.match_replace(spare[:, r, :], vals[:, r, 0:8], src[:, r, :], LOWEST))
            c.wait(dve)
            c.mark(dve.memset(pad[:, :], 0.0))
            for r in range(n):
                c.mark(dve.max(vals[:, r, 8:16], spare[:, r, :]))
            c.wait(dve)
            c.mark(dve.memset(pad[:, :], 0.0))
            for r in range(n):
                c.mark(dve.max_index(inds[:, r, 8:16], vals[:, r, 8:16], spare[:, r, :]))
            c.wait(dve)

        STEPS = 1 + (5 * HP + 4) + 2 + (5 * PH + 4) + 3 + 2 * 3 + 1 + 3
        with nc.Block() as block:

            @block.gpsimd
            def _(pool):
                m.pool.mark(pool.memset(index[:, TT, :], 0))
                m.pool.mark(pool.iota(count[:, :], [[1, TOPK]], base=0, channel_multiplier=0,
                                      allow_small_or_imprecise_dtypes=True))

            @block.scalar
            def _(act):
                with act.Fori(0, TT) as i:
                    act.wait_ge(shifted, i + 1)
                    act.activation(ex[:, :, :], ex[:, :, :], ACT.Exp).then_inc(exps, 1)

            @block.vector
            def _(dve):
                c = m.dve
                m.pool.wait(dve)
                with dve.Fori(0, TT) as i:
                    c.enter(i, STEPS)
                    c.link(dve, dve.tensor_copy(s[:, :, :].rearrange("p h n -> p (h n)"),
                                                s_all[:, bass.ds(i, 1), :].rearrange("p a n -> p (a n)")))
                    top16(dve, s, s2, val, ind, HP)
                    c.mark(dve.tensor_copy(indf[:, :, :], ind[:, :, :]))
                    v4 = val[:, :, :].rearrange("p (h j) k -> p h j k", j=2)
                    c.link(dve, dve.tensor_tensor(
                        cand[:, :, :].rearrange("p h (a b) -> p h a b", b=TOPK),
                        v4[:, :, 0, :].unsqueeze(3).to_broadcast([P, PH, TOPK, TOPK]),
                        v4[:, :, 1, :].unsqueeze(2).to_broadcast([P, PH, TOPK, TOPK]), ALU.add))
                    top16(dve, cand, cand2, best, pos, PH)
                    flat_pos = pos[:, :, :].rearrange("p h k -> p (h k)")
                    c.mark(dve.tensor_scalar(digit[:, 0, :], flat_pos, 4, None, ALU.logical_shift_right))
                    c.mark(dve.tensor_scalar(digit[:, 1, :], flat_pos, 15, None, ALU.bitwise_and))
                    dve.tensor_tensor(ex[:, :, :], best[:, :, :], best[:, :, 0:1].to_broadcast([P, PH, TOPK]),
                                      ALU.subtract).then_inc(shifted, 1)
                    c.wait(dve)
                    c.link(dve, dve.tensor_copy(digitf[:, :, :], digit[:, :, :]))
                    i4 = indf[:, :, :].rearrange("p (h j) k -> p h j k", j=2)
                    for j in range(2):
                        w3 = which[:, :, :, :].rearrange("p h k n -> p (h k) n")
                        c.link(dve, dve.tensor_tensor(w3, count[:, :].unsqueeze(1).to_broadcast([P, PH * TOPK, TOPK]),
                                                      digitf[:, j, :].unsqueeze(2).to_broadcast([P, PH * TOPK, TOPK]),
                                                      ALU.is_equal))
                        c.link(dve, dve.tensor_tensor(which[:, :, :, :], which[:, :, :, :],
                                                      i4[:, :, j, :].unsqueeze(2).to_broadcast([P, PH, TOPK, TOPK]),
                                                      ALU.mult))
                        c.link(dve, dve.tensor_reduce(found[:, j, :], w3, AX.X, ALU.add))
                    c.mark(dve.scalar_tensor_tensor(out=index[:, bass.ds(i, 1), :].rearrange("p a n -> p (a n)"),
                                                    in0=found[:, 0, :], scalar=float(NK), in1=found[:, 1, :],
                                                    op0=ALU.mult, op1=ALU.add))
                    dve.wait_ge(exps, i + 1)
                    c.link(dve, dve.tensor_reduce(total[:, :], ex[:, :, :], AX.X, ALU.add))
                    c.link(dve, dve.reciprocal(total[:, :], total[:, :]))
                    c.mark(dve.tensor_tensor(gate[:, bass.ds(i, 1), :].rearrange("p a (h k) -> p (a h) k", k=TOPK),
                                             ex[:, :, :], total[:, :].unsqueeze(2).to_broadcast([P, PH, TOPK]), ALU.mult))
                    c.leave(TT)


def apply_experts(m, table_u, table_v, rows, index, gate, out):
    nc = m.nc
    TURNS = PICKS // RING
    landed = [m.sem(f"row_landed{s}") for s in range(RING)]
    free, index_set, dots_made, act_made, coef_made = (
        m.sem(x) for x in ("rows_free", "index_set", "dots_made", "act_made", "coef_made"))
    with ExitStack() as own:
        sb = lambda name, shape, dt=F32: own.enter_context(nc.sbuf_tensor(name, shape, dt))
        ring = sb("ring", [P, RING, D])
        now = sb("index_now", [P, BUFS, GROUP], U32)
        flat_index = index[:, :, :].rearrange("p t n -> p (t n)")
        dots = sb("dots", [P, PICKS])
        coef = sb("coef", [P, PICKS])
        acc = sb("acc", [P, D])
        pad = sb("pad", [P, 1])
        one = lambda ap3, i: ap3[:, bass.ds(i, 1), :].rearrange("p a n -> p (a n)")
        with nc.Block() as block:

            @block.gpsimd
            def _(pool):
                pool.tensor_copy(now[:, 0, :], flat_index[:, 0:GROUP]).then_inc(index_set, 1)
                with pool.Fori(0, TT) as i:
                    for half, table in enumerate((table_u, table_v)):
                        with pool.Fori(0, GROUPS // BUFS) as body:
                            for b in range(BUFS):
                                g = body * BUFS + b
                                n = (i * 2 + half) * GROUPS + g
                                pool.wait_ge(index_set, n + 1)
                                pool.wait_ge(free, (n + 1) * GROUP)
                                after = i * PICKS + g * GROUP + GROUP
                                if b == BUFS - 1 and half == 0:
                                    after = i * PICKS + (body + 1) % (GROUPS // BUFS) * (BUFS * GROUP)
                                pool.tensor_copy(now[:, (b + 1) % BUFS, :],
                                                 flat_index[:, bass.ds(after, GROUP)]).then_inc(index_set, 1)
                                for j in range(GROUP):
                                    s = (b * GROUP + j) % RING
                                    pool.indirect_dma_start(
                                        out=ring[:, s, :], out_offset=None, in_=table,
                                        in_offset=bass.IndirectOffsetOnAxis(ap=now[:, b, j:j + 1], axis=0)).then_inc(landed[s], 16)

            @block.scalar
            def _(act):
                with act.Fori(0, TT) as i:
                    act.wait_ge(dots_made, (i + 1) * PICKS)
                    act.activation(coef[:, :], dots[:, :], ACT.Gelu).then_inc(act_made, 1)

            @block.vector
            def _(dve):
                c = m.dve
                dve.sem_inc(free, RING)
                with dve.Fori(0, TT) as i:
                    c.enter(i, 4)
                    with dve.Fori(0, TURNS) as g:
                        for s in range(RING):
                            dve.wait_ge(landed[s], (i * (2 * TURNS) + g + 1) * 16)
                            dve.scalar_tensor_tensor(out=ring[:, s, :], in0=ring[:, s, :], scalar=1.0, in1=one(rows, i),
                                                     op0=ALU.mult, op1=ALU.mult,
                                                     accum_out=dots[:, bass.ds(g * RING + s, 1)]).then_inc(free, 1)
                    dve.wait_ge(free, RING + (i * (2 * TURNS) + TURNS) * RING)
                    dve.nop().then_inc(dots_made, PICKS)
                    dve.wait_ge(act_made, i + 1)
                    c.mark(dve.tensor_tensor(coef[:, :], coef[:, :], one(gate, i), ALU.mult))
                    c.mark(dve.memset(acc[:, :], 0.0))
                    c.wait(dve)
                    c.mark(dve.memset(pad[:, :], 0.0))
                    v0 = i * (2 * TURNS) + TURNS
                    with dve.Fori(0, TURNS) as g:
                        for s in range(RING):
                            dve.wait_ge(landed[s], (v0 + g + 1) * 16)
                            if s:
                                dve.wait_ge(free, (v0 + g + 1) * RING + s)
                            else:
                                dve.wait_ge(free, (v0 + g + 1) * RING)
                            dve.scalar_tensor_tensor(out=acc[:, :], in0=ring[:, s, :],
                                                     scalar=coef[:, bass.ds(g * RING + s, 1)], in1=acc[:, :],
                                                     op0=ALU.mult, op1=ALU.add).then_inc(free, 1)
                    dve.wait_ge(free, (v0 + TURNS + 1) * RING)
                    c.mark(dve.tensor_copy(one(out, i), acc[:, :]))
                    c.leave(TT)


def first_experts(m, w_query, sub_keys, table_u, table_v, cols, at):
    nc = m.nc
    norm(m, m.xT, m.hT, m.scale2, m.mod[:, 3 * KT:4 * KT])
    with ExitStack() as own:
        index = own.enter_context(nc.sbuf_tensor("index", [P, TT + 1, PICKS], U32))
        gate = own.enter_context(nc.sbuf_tensor("gate", [P, TT, PICKS], F32))
        rows = own.enter_context(nc.sbuf_tensor("h_rows", [P, TT, D], F32))
        turn_back(m, m.hT, rows, "h2")
        with ExitStack() as own2:
            s_all = own2.enter_context(nc.sbuf_tensor("s_all", [P, TT, 2 * PH * NK], F32))
            with ExitStack() as own3:
                qT = own3.enter_context(nc.sbuf_tensor("qT", [P, 2 * PH, T], F32))
                project(m, w_query[0], 2 * PH, lambda k: m.hT[:, k, :], KT,
                        lambda dve, t, bank: dve.tensor_copy(at_tile(qT, t), bank[:, :]))
                key_scores(m, sub_keys[0], qT, s_all)
            pick_experts(m, s_all, index, gate)
        out = own.enter_context(nc.sbuf_tensor("peer_out", [P, TT, D], F32))
        apply_experts(m, table_u[0], table_v[0], rows, index, gate, out)
        g0 = 5 * KT
        turn_forward(m, out, "peer", lambda dve, k, bank: dve.scalar_tensor_tensor(
            out=m.xT[:, k, :], in0=bank[:, :], scalar=m.mod[:, g0 + k:g0 + k + 1], in1=m.xT[:, k, :],
            op0=ALU.mult, op1=ALU.add))
    norm(m, m.xT, m.xT, cols[:, at["final"]:at["final"] + KT], sq=m.hT)


RH = 64
RC = 64
RT = 8
RN = T // RC
R_TILES = 3 * RT + 2
R_LEVELS = 6
E_HALF = 0.6065306597126334


def rwkv_masks(m, own):
    nc = m.nc
    sb = lambda ctx, name, shape, dt=F32: ctx.enter_context(nc.sbuf_tensor(name, shape, dt))
    lower = sb(own, "rk_lower", [P, R_LEVELS, RC])
    first = sb(own, "rk_first", [P, RC])
    after = sb(own, "rk_after", [P, RC])
    upto = sb(own, "rk_upto", [P, RC])
    eye = sb(own, "rk_eye", [P, RC])
    with ExitStack() as tmp:
        a = sb(tmp, "rk_a", [P, RC], I32)
        b = sb(tmp, "rk_b", [P, RC], I32)
        x = sb(tmp, "rk_x", [P, RC], I32)
        y = sb(tmp, "rk_y", [P, RC], I32)
        z = sb(tmp, "rk_z", [P, RC], I32)
        with nc.Block() as block:

            @block.gpsimd
            def _(pool):
                for h in range(2):
                    m.pool.link(pool, pool.iota(a[h * RC:(h + 1) * RC, :], [[0, RC]], base=0, channel_multiplier=1))
                m.pool.mark(pool.iota(b[:, :], [[1, RC]], base=0, channel_multiplier=0))

            @block.vector
            def _(dve):
                c = m.dve
                m.pool.wait(dve)
                c.mark(dve.tensor_tensor(after[:, :], b[:, :], a[:, :], ALU.is_gt))
                c.mark(dve.tensor_tensor(upto[:, :], b[:, :], a[:, :], ALU.is_ge))
                c.mark(dve.tensor_tensor(eye[:, :], b[:, :], a[:, :], ALU.is_equal))
                c.mark(dve.tensor_tensor(y[:, :], a[:, :], b[:, :], ALU.is_gt))
                c.link(dve, dve.tensor_tensor(x[:, :], a[:, :], b[:, :], ALU.bitwise_xor))
                c.link(dve, dve.tensor_scalar(z[:, :], x[:, :], 1, None, ALU.is_equal))
                c.link(dve, dve.tensor_tensor(first[:, :], z[:, :], after[:, :], ALU.mult))
                c.link(dve, dve.tensor_tensor(x[:, :], x[:, :], y[:, :], ALU.mult))
                for l in range(R_LEVELS):
                    c.link(dve, dve.tensor_scalar(z[:, :], x[:, :], l, None, ALU.logical_shift_right))
                    c.link(dve, dve.tensor_scalar(lower[:, l, :], z[:, :], 1, None, ALU.is_equal))
    return lower, first, after, upto, eye


def rwkv(m, cols, at, p, yT, w_decay, w_a, w_g):
    nc = m.nc
    flat = lambda ap: ap.rearrange("p h t -> p (h t)")
    r, k, v = (p[:, j * RT:(j + 1) * RT, :] for j in range(3))
    col = lambda key, t: cols[:, at[key] + t:at[key] + t + 1]
    wflat = m.weights[:, :, :, :].rearrange("p s k c -> p (s k c)")
    w0 = wflat[:, 0:RT * T].rearrange("p (h t) -> p h t", t=T)
    w1 = wflat[:, RT * T:2 * RT * T].rearrange("p (h t) -> p h t", t=T)
    a_bank = lambda n: m.ps[n % 8]
    with ExitStack() as own:
        sb = lambda name, shape, dt=F32: own.enter_context(nc.sbuf_tensor(name, shape, dt))
        A, KK = (sb(f"rk_{x}", [P, RT, T]) for x in ("A", "KK"))
        S, BON = m.hT, m.xT
        elast = sb("rk_elast", [P, RT, RN])
        state = sb("rk_state", [P, RT, RH])
        early = ExitStack()
        ranks = early.enter_context(nc.sbuf_tensor("rk_ranks", [P, D], F32))
        B = early.enter_context(nc.sbuf_tensor("rk_B", [P, RT, T], F32))

        lora_landed = m.sem("rk_lora_landed")
        with nc.Block() as block:

            @block.sync
            def _(sp):
                sp.dma_start(ranks[0:RH, :], w_decay).then_inc(lora_landed, 16)
                sp.dma_start(ranks[RH:P, :], w_a).then_inc(lora_landed, 16)

            @block.gpsimd
            def _(pool):
                m.pool.link(pool, pool.memset(w0[:, :, :], 1.0))
                k4 = flat(w0).rearrange("p (n c) -> p n c", c=RC)
                m.pool.link(pool, pool.memset(k4[:, :, 0:1], 0.0))
                m.pool.mark(pool.memset(state[:, :, :], 0.0))

            @block.vector
            def _(dve):
                c = m.dve
                for j in range(0, R_TILES, RT):
                    n = min(RT, R_TILES - j)
                    c.mark(dve.tensor_tensor(w1[:, 0:n, 1:T], p[:, j:j + n, 0:T - 1], p[:, j:j + n, 1:T], ALU.subtract))
                    c.mark(dve.tensor_scalar(w1[:, 0:n, 0:1], p[:, j:j + n, 0:1], -1.0, None, ALU.mult))
                    c.wait(dve)
                    for t in range(n):
                        c.mark(dve.scalar_tensor_tensor(out=p[:, j + t, :], in0=w1[:, t, :], scalar=col("mu", j + t),
                                                        in1=p[:, j + t, :], op0=ALU.mult, op1=ALU.add))
                    c.wait(dve)

        low, lora_made, lora_kept = m.sem("rk_low"), m.sem("rk_lora_made"), m.sem("rk_lora_kept")
        with nc.Block() as block:

            @block.scalar
            def _(act):
                act.activation(p[0:RH, 24, :], p[0:RH, 24, :], ACT.Tanh).then_inc(low, 1)
                for n in range(2 * RT):
                    t = n % RT
                    act.wait_ge(lora_made, n + 1)
                    act.activation((S if n < RT else A)[:, t, :], a_bank(n)[:, :], ACT.Sigmoid,
                                   bias=col("w0" if n < RT else "a0", t)).then_inc(lora_kept, 1)
                m.act.mark(act.activation(p[:, 25, :], p[:, 25, :], ACT.Sigmoid))

            @block.tensor
            def _(pe):
                pe.wait_ge(lora_landed, 32)
                pe.wait_ge(low, 1)
                for n in range(2 * RT):
                    h, t = n // RT, n % RT
                    if n >= 8:
                        pe.wait_ge(lora_kept, n - 7)
                    q = slice(h * RH, (h + 1) * RH)
                    pe.matmul(a_bank(n)[:, :], ranks[q, t * P:(t + 1) * P], p[q, 24, :],
                              start=True, stop=True).then_inc(lora_made, 1)

            @block.vector
            def _(dve):
                c = m.dve
                dve.wait_ge(lora_kept, RT)
                c.link(dve, dve.tensor_scalar(flat(S), flat(S), -E_HALF, None, ALU.mult))
                c.mark(dve.tensor_tensor_scan(flat(B), flat(w0), flat(S), 0.0, ALU.mult, ALU.add))

        kk_sq, kk_sum, kk_root, bon_in, bon_sum, bon_out = (
            m.sem(f"rk_{x}") for x in ("kk_sq", "kk_sum", "kk_root", "bon_in", "bon_sum", "bon_out"))
        with nc.Block() as block:

            @block.scalar
            def _(act):
                for t in range(RT):
                    act.wait_ge(kk_sq, 2 * t + 1)
                    act.activation(w1[:, t, :], KK[:, t, :], ACT.Square).then_inc(kk_sq, 1)
                for t in range(RT):
                    act.wait_ge(kk_sum, t + 1)
                    act.activation(w0[:, t, :], m.ps[t][:, :], ACT.Sqrt).then_inc(kk_root, 1)

            @block.tensor
            def _(pe):
                for t in range(RT):
                    pe.wait_ge(kk_sq, 2 * t + 2)
                    pe.matmul(m.ps[t][:, :], m.half_ones[:, :], w1[:, t, :], start=True, stop=True).then_inc(kk_sum, 1)
                for t in range(RT):
                    pe.wait_ge(bon_in, t + 1)
                    pe.wait_ge(kk_root, t + 1)
                    pe.matmul(m.ps[t][:, :], m.half_ones[:, :], w1[:, t, :], start=True, stop=True).then_inc(bon_sum, 1)

            @block.vector
            def _(dve):
                c = m.dve
                for t in range(RT):
                    if t:
                        dve.wait_ge(kk_sq, 2 * t)
                    dve.tensor_scalar(KK[:, t, :], k[:, t, :], col("k_k", t), None, ALU.mult).then_inc(kk_sq, 1)
                for t in range(RT):
                    dve.wait_ge(kk_root, t + 1)
                    c.mark(dve.tensor_scalar(w0[:, t, :], w0[:, t, :], 1e-12, None, ALU.max))
                c.wait(dve)
                c.link(dve, dve.reciprocal(flat(w0), flat(w0)))
                c.link(dve, dve.tensor_tensor(flat(KK), flat(KK), flat(w0), ALU.mult))
                for t in range(RT):
                    c.mark(dve.tensor_scalar(w0[:, t, :], A[:, t, :], 1.0, col("k_a", t), ALU.subtract, ALU.mult))
                c.wait(dve)
                c.link(dve, dve.scalar_tensor_tensor(out=flat(k), in0=flat(w0), scalar=1.0, in1=flat(k),
                                                     op0=ALU.add, op1=ALU.mult))
                c.mark(dve.tensor_tensor(flat(KK) if False else flat(A), flat(KK), flat(A), ALU.mult))
                for t in range(RT):
                    dve.scalar_tensor_tensor(out=w1[:, t, :], in0=r[:, t, :], scalar=col("r_k", t), in1=k[:, t, :],
                                             op0=ALU.mult, op1=ALU.mult).then_inc(bon_in, 1)
                for t in range(RT):
                    dve.wait_ge(bon_sum, t + 1)
                    c.mark(dve.tensor_tensor(BON[:, t, :], m.ps[t][:, :], v[:, t, :], ALU.mult))

        exps, shifted = m.sem("rk_exps"), m.sem("rk_shifted")
        with nc.Block() as block:

            @block.scalar
            def _(act):
                act.activation(flat(w0), flat(B), ACT.Exp).then_inc(exps, 1)
                act.activation(elast[:, :, :], B[:, :, RC - 1:T:RC], ACT.Exp).then_inc(exps, 1)
                act.wait_ge(shifted, 1)
                act.activation(flat(w1), flat(w1), ACT.Exp).then_inc(exps, 1)
                act.activation(flat(S), flat(B), ACT.Exp, scale=-1.0).then_inc(exps, 1)

            @block.vector
            def _(dve):
                dve.tensor_tensor(flat(w1), flat(B), flat(S), ALU.subtract).then_inc(shifted, 1)

        early.close()
        with ExitStack() as late:
            rwkv_chunks(m, late, KK, A, k, r, v, w0, w1, S, elast, state, w0)
        gates = sb("rk_gates", [P, D])
        B = w0

        head_sum, g_made, gates_landed = m.sem("rk_head_sum"), m.sem("rk_g_made"), m.sem("rk_gates_landed")
        with nc.Block() as block:

            @block.sync
            def _(sp):
                sp.dma_start(gates[:, :], w_g).then_inc(gates_landed, 16)

            @block.tensor
            def _(pe):
                for t in range(RT):
                    pe.matmul(m.ps[t][:, :], m.half_ones[:, :], B[:, t, :], start=True, stop=True).then_inc(head_sum, 1)

            @block.vector
            def _(dve):
                for t in range(RT):
                    dve.wait_ge(head_sum, t + 1)
                    m.dve.mark(dve.scalar_tensor_tensor(out=B[:, t, :], in0=m.ps[t][:, :], scalar=-1.0 / RH,
                                                        in1=B[:, t, :], op0=ALU.mult, op1=ALU.add))
        g0 = at["ln_g"]
        group_norm(m, B, yT, cols[:, g0:g0 + RT], RT, 1, m.half_ones, RH, eps=64e-5)
        with nc.Block() as block:

            @block.tensor
            def _(pe):
                pe.wait_ge(gates_landed, 16)
                for t in range(RT):
                    pe.matmul(m.ps[t][:, :], gates[:, t * P:(t + 1) * P], p[:, 25, :], start=True, stop=True).then_inc(g_made, 1)

            @block.vector
            def _(dve):
                c = m.dve
                for t in range(RT):
                    c.mark(dve.scalar_tensor_tensor(out=BON[:, t, :], in0=BON[:, t, :], scalar=col("ln_b", t),
                                                    in1=yT[:, t, :], op0=ALU.add, op1=ALU.add))
                c.wait(dve)
                for t in range(RT):
                    dve.wait_ge(g_made, t + 1)
                    c.mark(dve.tensor_tensor(yT[:, t, :], m.ps[t][:, :], BON[:, t, :], ALU.mult))


def rwkv_chunks(m, own, KK, KA, k, r, v, e, ex, ei, elast, state, out):
    nc = m.nc
    lower, first, after, upto, eye = rwkv_masks(m, own)
    names = ("alpha", "beta", "kappa", "rho", "v")
    with ExitStack() as tmp:
        sb = lambda name: tmp.enter_context(nc.sbuf_tensor(f"rc_{name}", [P, RT, RC], F32))
        st = {x: sb(x) for x in names}
        X, Y, TM, R, U, GAK, GRB, GRK, VT, BT, KT_ = (
            sb(x) for x in ("X", "Y", "TM", "R", "U", "gak", "grb", "grk", "vT", "betaT", "kappaT"))
        NL = tmp.enter_context(nc.sbuf_tensor("rc_NL", [P, R_LEVELS - 1, RT, RC], F32))
        f2 = lambda ap: ap.rearrange("p h t -> p (h t)")
        staged, made, masked, turned_kept, t_made, t_kept, xy_made, xy_kept, tail_made, tail_kept, state_kept = (
            m.sem(f"rc_{x}") for x in ("staged", "products", "masked", "turned_kept", "t_made", "t_kept", "xy_made",
                                       "xy_kept", "tail_made", "tail_kept", "state_kept"))
        over = lambda mask: mask.unsqueeze(1).to_broadcast([P, RT, RC])
        bank3 = lambda b: m.ps[b][:, :].rearrange("p (h t) -> p h t", t=RC)

        def heads(pe, bank, *terms):
            for t in range(RT):
                for h in range(2):
                    q = slice(h * RH, (h + 1) * RH)
                    for n, (lhs, rhs) in enumerate(terms):
                        o, l = bank[q, t * RC:(t + 1) * RC], lhs[q, t, :]
                        rr = rhs[q, t, :] if len(rhs.shape) == 3 else rhs[q, h * RH:(h + 1) * RH]
                        if t == h == n == 0:
                            wide = lhs[q, 0:2, :].rearrange("p a t -> p (a t)")
                            ins = pe.matmul(bank[:, 0:RC], wide, rr, start=True, stop=True)
                            if len(terms) == 1:
                                continue
                        ins = pe.matmul(o, l, rr, start=(n == 0), stop=(n == len(terms) - 1))
            return ins

        with nc.Block() as block:

            @block.vector
            def _(dve):
                with dve.Fori(0, RN) as c:
                    now = lambda ap: ap[:, :, bass.ds(c * RC, RC)]
                    dve.wait_ge(tail_made, 4 * c)
                    dve.wait_ge(tail_kept, 3 * c)
                    dve.wait_ge(state_kept, 2 * c)
                    dve.scalar_tensor_tensor(out=st["alpha"][:, :, :], in0=now(KK), scalar=-1.0, in1=now(ex),
                                             op0=ALU.mult, op1=ALU.mult).then_inc(staged, 1)
                    dve.tensor_tensor(st["beta"][:, :, :], now(KA), now(ei), ALU.mult).then_inc(staged, 1)
                    dve.tensor_tensor(st["kappa"][:, :, :], now(k), now(ei), ALU.mult).then_inc(staged, 1)
                    dve.tensor_tensor(st["rho"][:, :, :], now(r), now(e), ALU.mult).then_inc(staged, 1)
                    dve.tensor_copy(st["v"][:, :, :], now(v)).then_inc(staged, 1)
                    dve.wait_ge(made, 8 * c + 1)
                    dve.tensor_tensor(Y[:, :, :], bank3(0), over(first[:, :]), ALU.mult).then_inc(masked, 1)
                    dve.wait_ge(made, 8 * c + 2)
                    dve.tensor_tensor(X[:, :, :], bank3(1), over(lower[:, 0, :]), ALU.mult).then_inc(masked, 1)
                    dve.wait_ge(masked, 8 * c + 2)
                    dve.tensor_tensor(Y[:, :, :], Y[:, :, :], over(eye[:, :]), ALU.add).then_inc(masked, 1)
                    dve.tensor_tensor(X[:, :, :], X[:, :, :], over(eye[:, :]), ALU.add).then_inc(masked, 1)
                    dve.tensor_tensor(NL[:, :, :, :], bank3(1).unsqueeze(1).to_broadcast([P, R_LEVELS - 1, RT, RC]),
                                      lower[:, 1:R_LEVELS, :].unsqueeze(2).to_broadcast([P, R_LEVELS - 1, RT, RC]),
                                      ALU.mult).then_inc(masked, 1)
                    for n, (dst, mask) in enumerate(((GAK, after[:, :]), (GRB, upto[:, :]), (GRK, upto[:, :]))):
                        dve.wait_ge(made, 8 * c + 3 + n)
                        dve.tensor_tensor(dst[:, :, :], bank3(2 + n), over(mask), ALU.mult).then_inc(masked, 1)
                    for l in range(1, R_LEVELS):
                        for j, dst in enumerate((Y, X)[:2 if l < R_LEVELS - 1 else 1]):
                            dve.wait_ge(xy_made, (2 * R_LEVELS - 3) * c + 2 * (l - 1) + j + 1)
                            dve.tensor_tensor(dst[:, :, :], dst[:, :, :], bank3(5 + j), ALU.add).then_inc(xy_kept, 1)
                    dve.wait_ge(tail_made, 4 * c + 4)
                    dve.tensor_tensor(state[:, :, :], state[:, :, :], bank3(2), ALU.add).then_inc(state_kept, 1)
                    dve.wait_ge(state_kept, 2 * c + 1)
                    dve.tensor_tensor(state[:, :, :], state[:, :, :],
                                      elast[:, :, bass.ds(c, 1)].to_broadcast([P, RT, RH]), ALU.mult).then_inc(state_kept, 1)

            @block.scalar
            def _(act):
                with act.Fori(0, RN) as c:
                    for n, dst in enumerate((VT, BT, KT_)):
                        act.wait_ge(made, 8 * c + 6 + n)
                        act.copy(f2(dst), m.ps[5 + n][:, :]).then_inc(turned_kept, 1)
                    act.wait_ge(tail_made, 4 * c + 1)
                    act.copy(f2(R), m.ps[7][:, :]).then_inc(tail_kept, 1)
                    for l in range(1, R_LEVELS):
                        act.wait_ge(t_made, (R_LEVELS - 1) * c + l)
                        act.copy(f2(TM), m.ps[0][:, :]).then_inc(t_kept, 1)
                    act.wait_ge(tail_made, 4 * c + 2)
                    act.copy(f2(U), m.ps[0][:, :]).then_inc(tail_kept, 1)
                    act.wait_ge(tail_made, 4 * c + 3)
                    act.copy(out[:, :, bass.ds(c * RC, RC)], bank3(1)).then_inc(tail_kept, 1)

            @block.tensor
            def _(pe):
                A, B, K, R_, V = (st[x] for x in names)
                XY = 2 * R_LEVELS - 3
                with pe.Fori(0, RN) as c:
                    pe.wait_ge(staged, 5 * c + 5)
                    for b, (l, rr) in enumerate(((B, A), (A, B), (K, A), (B, R_), (K, R_),
                                                 (V, m.ident), (B, m.ident), (K, m.ident))):
                        heads(pe, m.ps[b], (l, rr)).then_inc(made, 1)
                    pe.wait_ge(masked, 8 * c + 6)
                    pe.wait_ge(turned_kept, 3 * c + 3)
                    heads(pe, m.ps[7], (A, state), (GAK, VT)).then_inc(tail_made, 1)
                    for l in range(1, R_LEVELS):
                        if l == 1:
                            pe.wait_ge(masked, 8 * c + 5)
                        else:
                            pe.wait_ge(xy_kept, XY * c + 2 * (l - 1))
                        heads(pe, m.ps[0], (NL[:, l - 1], Y)).then_inc(t_made, 1)
                        pe.wait_ge(t_kept, (R_LEVELS - 1) * c + l)
                        heads(pe, m.ps[5], (X, TM)).then_inc(xy_made, 1)
                        if l < R_LEVELS - 1:
                            heads(pe, m.ps[6], (TM, X)).then_inc(xy_made, 1)
                    pe.wait_ge(xy_kept, XY * (c + 1))
                    pe.wait_ge(tail_kept, 3 * c + 1)
                    heads(pe, m.ps[0], (Y, R)).then_inc(tail_made, 1)
                    pe.wait_ge(masked, 8 * c + 8)
                    pe.wait_ge(tail_kept, 3 * c + 2)
                    heads(pe, m.ps[1], (state, R_), (U, GRB), (VT, GRK)).then_inc(tail_made, 1)
                    heads(pe, m.ps[2], (BT, U), (KT_, VT)).then_inc(tail_made, 1)


def second_columns(m, attn_norm, mu, w0, a0, k_k, k_a, r_k, ln_g, ln_b):
    row = lambda ap: ap.rearrange("(k p) -> k p", p=P)
    return column_rows(m, "cols2", [
        ("attn_norm", row(attn_norm[0])), ("mu", row(mu[0])), ("w0", row(w0[0])), ("a0", row(a0[0])),
        ("k_k", row(k_k[0])), ("k_a", row(k_a[0])),
        ("r_k", r_k[0].rearrange("(k j) c -> k (j c)", j=2)), ("ln_g", row(ln_g[0])), ("ln_b", row(ln_b[0]))])


def copy_out(m, name, pairs):
    done = m.sem(name)
    with m.nc.Block() as block:

        @block.sync
        def _(sp):
            for dst, src in pairs:
                sp.dma_start(dst, src).then_inc(done, 16)
            sp.wait_ge(done, 16 * len(pairs))


def second_rwkv(m, w_in, cols, at, w_decay, w_a, w_g, x_kept, y_kept):
    nc = m.nc
    n0 = at["attn_norm"]
    norm(m, m.xT, m.hT, cols[:, n0:n0 + KT])
    copy_out(m, "x_kept", [(x_kept, m.xT[:, :, :])])
    with ExitStack() as own:
        p = own.enter_context(nc.sbuf_tensor("proj_rk", [P, R_TILES, T], F32))
        project(m, w_in[0], R_TILES, lambda k: m.hT[:, k, :], KT,
                lambda dve, t, bank: dve.tensor_copy(at_tile(p, t), bank[:, :]))
        yT = p[:, 0:RT, :]
        rwkv(m, cols, at, p, yT, w_decay[0], w_a[0], w_g[0])
        copy_out(m, "y_kept", [(y_kept, yT)])


SH = 32
SG = 4
SC = 128
SN = T // SC
S_TILES = 16
X_TILES = S_TILES + 2 * SG
TAPS = 4
GH = SH // SG


def ssd_conv(m, p, cols, at):
    nc = m.nc
    conved, silued = m.sem("sd_conved"), m.sem("sd_silued")
    with ExitStack() as own:
        tmp = own.enter_context(nc.sbuf_tensor("sd_conv", [P, 2, 4, T], F32))
        with nc.Block() as block:

            @block.vector
            def _(dve):
                c = m.dve
                for g in range(X_TILES // 4):
                    if g >= 2:
                        dve.wait_ge(silued, g - 1)
                    for d in range(TAPS):
                        for j in range(4):
                            t = 4 * g + j
                            tap = cols[:, at["conv"] + (TAPS - 1 - d) * X_TILES + t:][:, 0:1]
                            y = tmp[:, g % 2, j, d:]
                            if d == 0:
                                c.mark(dve.tensor_scalar(y, p[:, t, :], tap, cols[:, at["conv_b"] + t:][:, 0:1],
                                                         ALU.mult, ALU.add))
                            else:
                                ins = dve.scalar_tensor_tensor(out=y, in0=p[:, t, :T - d], scalar=tap, in1=y,
                                                               op0=ALU.mult, op1=ALU.add)
                                if d < TAPS - 1:
                                    c.mark(ins)
                                else:
                                    ins.then_inc(conved, 1)
                        c.wait(dve)

            @block.scalar
            def _(act):
                for g in range(X_TILES // 4):
                    act.wait_ge(conved, 4 * (g + 1))
                    act.activation(p[:, 4 * g:4 * g + 4, :], tmp[:, g % 2], ACT.Silu).then_inc(silued, 1)


def ssd(m, p, w_in_dt, dt_bias, a_log, d_skip):
    nc = m.nc
    with ExitStack() as own:
        sb = lambda name, shape, dt=F32: own.enter_context(nc.sbuf_tensor(name, shape, dt))
        w_dt = sb("sd_w_dt", [P, KT, SH])
        small = sb("sd_small", [SH, 4])
        dt, pos, acs, keep = (sb(f"sd_{x}", [SH, T]) for x in ("dt", "pos", "acs", "keep"))
        tok = sb("sd_tok", [P, 2, SN, SH])
        left = sb("sd_left", [P, SN, SH])
        whole = sb("sd_whole", [P, SN, SH])
        last_row = sb("sd_last_row", [P, P])
        upto = sb("sd_upto", [P, SC])
        d_col = sb("sd_d", [P, S_TILES])

        landed, made, soft, turned = (m.sem(f"sd_{x}") for x in ("landed", "dt_made", "soft", "turned"))
        with nc.Block() as block:

            @block.sync
            def _(sp):
                sp.dma_start(w_dt[:, :, :], w_in_dt.rearrange("(k p) n -> p k n", p=P)).then_inc(landed, 16)
                sp.dma_start(small[:, 0:1], dt_bias.rearrange("(h a) -> h a", a=1)).then_inc(landed, 16)
                sp.dma_start(small[:, 1:2], a_log.rearrange("(h a) -> h a", a=1)).then_inc(landed, 16)
                for h in range(2):
                    src = d_skip.rearrange("(a t j) -> a t j", a=1, j=2)[:, :, h]
                    with nc.allow_non_contiguous_dma(reason="32 numbers"):
                        sp.dma_start(d_col[h * RH:(h + 1) * RH, :], src.to_broadcast([RH, S_TILES])).then_inc(landed, 16)

            @block.gpsimd
            def _(pool):
                c = m.pool
                c.mark(pool.memset(keep[:, :], 1.0))
                c.mark(pool.memset(last_row[:, :], 1.0))
                c.mark(pool.memset(upto[:, :], 1.0))
                c.wait(pool)
                c.link(pool, pool.memset(keep[:, 0:T:SC], 0.0))
                c.link(pool, pool.affine_select(out=last_row[:, :], in_=last_row[:, :], compare_op=ALU.is_ge, fill=0.0,
                                                base=-(P - 1), pattern=[[0, P]], channel_multiplier=1))
                c.link(pool, pool.affine_select(out=upto[:, :], in_=upto[:, :], compare_op=ALU.is_ge, fill=0.0,
                                                base=0, pattern=[[1, SC]], channel_multiplier=-1))

            @block.tensor
            def _(pe):
                pe.wait_ge(landed, 80)
                for k in range(KT):
                    ins = pe.matmul(m.ps[0][0:SH, :], w_dt[:, k, :], m.hT[:, k, :], start=(k == 0), stop=(k == KT - 1))
                ins.then_inc(made, 1)
                pe.wait_ge(soft, 9)
                for j, src in enumerate((dt, acs)):
                    for n in range(SN):
                        ins = pe.transpose(m.ps[1][:, (j * SN + n) * SH:(j * SN + n + 1) * SH],
                                           src[:, n * SC:(n + 1) * SC], m.ident[0:SH, 0:SH])
                ins.then_inc(turned, 1)
                pe.wait_ge(soft, 10)
                pe.matmul(m.ps[2][:, 0:SN * SH], last_row[:, :], tok[:, 1].rearrange("p n h -> p (n h)"),
                          start=True, stop=True).then_inc(turned, 1)

            @block.scalar
            def _(act):
                act.wait_ge(landed, 80)
                act.activation(small[:, 2:3], small[:, 1:2], ACT.Exp).then_inc(soft, 1)
                act.wait_ge(soft, 3)
                act.activation(dt[:, :], dt[:, :], ACT.Abs).then_inc(soft, 1)
                act.wait_ge(soft, 4)
                act.activation(dt[:, :], dt[:, :], ACT.Exp, scale=-1.0).then_inc(soft, 1)
                act.wait_ge(soft, 5)
                act.activation(dt[:, :], dt[:, :], ACT.Ln, bias=1.0).then_inc(soft, 1)
                act.wait_ge(soft, 12)
                act.activation(left[:, :, :], left[:, :, :], ACT.Exp).then_inc(soft, 1)
                act.activation(whole[:, :, :], whole[:, :, :], ACT.Exp).then_inc(soft, 1)

            @block.vector
            def _(dve):
                dve.wait_ge(made, 1)
                dve.wait_ge(soft, 1)
                dve.tensor_scalar(dt[:, :], m.ps[0][0:SH, :], small[:, 0:1], None, ALU.add).then_inc(soft, 1)
                dve.tensor_scalar(pos[:, :], m.ps[0][0:SH, :], small[:, 0:1], 0.0, ALU.add, ALU.max).then_inc(soft, 1)
                dve.wait_ge(soft, 6)
                dve.tensor_tensor(dt[:, :], dt[:, :], pos[:, :], ALU.add).then_inc(soft, 1)
                dve.wait_ge(soft, 7)
                dve.tensor_scalar(pos[:, :], dt[:, :], small[:, 2:3], -1.0, ALU.mult, ALU.mult).then_inc(soft, 1)
                dve.wait_ge(soft, 8)
                m.pool.wait(dve)
                dve.tensor_tensor_scan(acs[:, :], keep[:, :], pos[:, :], 0.0, ALU.mult, ALU.add).then_inc(soft, 1)
                dve.wait_ge(turned, 1)
                dve.tensor_copy(tok[:, :, :, :].rearrange("p a n h -> p (a n h)"), m.ps[1][:, 0:2 * SN * SH]).then_inc(soft, 1)
                dve.wait_ge(turned, 2)
                b3 = m.ps[2][:, 0:SN * SH].rearrange("p (n h) -> p n h", h=SH)
                dve.tensor_tensor(left[:, :, :], b3, tok[:, 1], ALU.subtract).then_inc(soft, 1)
                dve.tensor_copy(whole[:, :, :], b3).then_inc(soft, 1)

        state = sb("sd_state", [P, SH * RH])
        xdt = sb("sd_xdt", [P, SH * RH])
        xdts = sb("sd_xdts", [P, SH * RH])
        bt = sb("sd_bt", [P, SG, SC])
        cb = sb("sd_cb", [P, SG, SC])
        dec = sb("sd_dec", [P, 2, GH, SC])
        inn = sb("sd_inn", [P, 2, GH, SC])
        names = ("x_turned", "rows_kept", "cb_made", "spread", "exps", "seg", "scores", "y_made", "y_kept", "s_made", "s_kept", "s_read")
        x_turned, rows_kept, cb_made, spread, exps, seg_made, scores, y_made, y_kept, s_made, s_kept, s_read = (
            m.sem(f"sd_{x}_n") for x in names)
        h3 = lambda ap: ap.rearrange("p (h c) -> p h c", c=RH)

        with nc.Block() as block:

            @block.tensor
            def _(pe):
                for n in range(SN):
                    t = slice(n * SC, (n + 1) * SC)
                    if n:
                        pe.wait_ge(y_kept, 4 * SG * n)
                        pe.wait_ge(s_kept, 2 * SG * n)
                    for b in range(4):
                        for j in range(4):
                            ins = pe.transpose(m.ps[b][:, j * P:(j + 1) * P], p[:, 4 * b + j, t], m.ident[:, :])
                        ins.then_inc(x_turned, 1)
                    for g in range(SG):
                        ins = pe.transpose(m.ps[4][:, g * P:(g + 1) * P], p[:, S_TILES + g, t], m.ident[:, :])
                    ins.then_inc(x_turned, 1)
                    for g in range(SG):
                        ins = pe.matmul(m.ps[5][:, g * P:(g + 1) * P], p[:, S_TILES + g, t], p[:, S_TILES + SG + g, t],
                                        start=True, stop=True)
                    ins.then_inc(x_turned, 1)
                    pe.wait_ge(rows_kept, 14 * (n + 1))
                    for g in range(SG + 1):
                        if g < SG:
                            i = n * SG + g
                            if i >= 2:
                                pe.wait_ge(exps, 3 * (i - 1))
                            for h in range(GH):
                                b = 2 * (i % 2) + h // 4
                                ins = pe.matmul(m.ps[b][:, (h % 4) * SC:(h % 4 + 1) * SC],
                                                m.ident[0:SH, g * GH + h:g * GH + h + 1].to_broadcast([SH, P]), acs[:, t],
                                                start=True, stop=True)
                                if h % 4 == 3:
                                    ins.then_inc(spread, 1)
                        if g >= 1:
                            i = n * SG + g - 1
                            gp = g - 1
                            bank = m.ps[4 + i % 2]
                            pe.wait_ge(scores, 2 * (i + 1))
                            if i >= 2:
                                pe.wait_ge(y_kept, 4 * (i - 1))
                            for h in range(GH):
                                hh = gp * GH + h
                                o = bank[(h % 2) * RH:(h % 2 + 1) * RH, (h // 2) * SC:(h // 2 + 1) * SC]
                                ins = pe.matmul(o, xdt[:, hh * RH:(hh + 1) * RH], dec[:, i % 2, h, :],
                                                start=True, stop=(n == 0))
                                if n:
                                    ins = pe.matmul(o, state[:, hh * RH:(hh + 1) * RH], inn[:, i % 2, h, :],
                                                    start=False, stop=True)
                            ins.then_inc(y_made, 1)
                            if i >= 2:
                                pe.wait_ge(s_kept, 2 * (i - 1))
                            pe.matmul(m.ps[6 + i % 2][:, :], bt[:, gp, :], xdts[:, gp * 512:(gp + 1) * 512],
                                      start=True, stop=True).then_inc(s_made, 1)

            @block.scalar
            def _(act):
                for n in range(SN):
                    for g in range(SG):
                        i = n * SG + g
                        if i >= 2:
                            act.wait_ge(y_made, i - 1)
                        for b in range(2):
                            act.wait_ge(seg_made, GH * i + 4 * (b + 1))
                            bank = m.ps[2 * (i % 2) + b]
                            act.activation(inn[:, i % 2, 4 * b:4 * b + 4, :].rearrange("p h l -> p (h l)"), bank[:, :],
                                           ACT.Exp).then_inc(exps, 1)
                        act.wait_ge(seg_made, GH * (i + 1))
                        act.activation(dec[:, i % 2], dec[:, i % 2], ACT.Exp).then_inc(exps, 1)

            @block.vector
            def _(dve):
                def keep_y(i):
                    n, g = i // SG, i % SG
                    t = slice(n * SC, (n + 1) * SC)
                    bank = m.ps[4 + i % 2]
                    dve.wait_ge(y_made, i + 1)
                    for j in range(4):
                        x = p[:, 4 * g + j, t]
                        dve.scalar_tensor_tensor(out=x, in0=x, scalar=d_col[:, 4 * g + j:4 * g + j + 1],
                                                 in1=bank[:, j * SC:(j + 1) * SC], op0=ALU.mult,
                                                 op1=ALU.add).then_inc(y_kept, 1)
                    dve.wait_ge(s_made, i + 1)
                    s = state[:, g * 512:(g + 1) * 512]
                    if n == 0:
                        dve.tensor_copy(s, m.ps[6 + i % 2][:, :]).then_inc(s_kept, 2)
                    else:
                        dve.tensor_tensor(h3(s), h3(s), whole[:, n, g * GH:(g + 1) * GH].unsqueeze(2)
                                          .to_broadcast([P, GH, RH]), ALU.mult).then_inc(s_kept, 1)
                        dve.wait_ge(s_kept, 2 * i + 1)
                        dve.tensor_tensor(s, s, m.ps[6 + i % 2][:, :], ALU.add).then_inc(s_kept, 1)

                for n in range(SN):
                    if n:
                        dve.wait_ge(y_kept, 4 * SG * n)
                    for b in range(4):
                        q = slice(b * 512, (b + 1) * 512)
                        wide = lambda ap: ap[:, n, b * GH:(b + 1) * GH].unsqueeze(2).to_broadcast([P, GH, RH])
                        dve.wait_ge(x_turned, 6 * n + b + 1)
                        dve.tensor_tensor(h3(xdt[:, q]), h3(m.ps[b][:, :]), wide(tok[:, 0]), ALU.mult).then_inc(rows_kept, 1)
                        dve.wait_ge(rows_kept, 14 * n + 2 * b + 1)
                        dve.tensor_tensor(h3(xdts[:, q]), h3(xdt[:, q]), wide(left), ALU.mult).then_inc(rows_kept, 1)
                    dve.wait_ge(x_turned, 6 * n + 5)
                    dve.tensor_copy(bt[:, :, :].rearrange("p g s -> p (g s)"), m.ps[4][:, :]).then_inc(rows_kept, 1)
                    dve.wait_ge(x_turned, 6 * n + 6)
                    dve.tensor_tensor(cb[:, :, :], m.ps[5][:, :].rearrange("p (g l) -> p g l", l=SC),
                                      upto[:, :].unsqueeze(1).to_broadcast([P, SG, SC]), ALU.mult).then_inc(rows_kept, 5)
                    for g in range(SG):
                        i = n * SG + g
                        if i >= 2:
                            dve.wait_ge(y_made, i - 1)
                        for h in range(GH):
                            if h % 4 == 0:
                                dve.wait_ge(spread, 2 * i + h // 4 + 1)
                            hh = g * GH + h
                            dve.tensor_scalar(dec[:, i % 2, h, :], m.ps[2 * (i % 2) + h // 4][:, (h % 4) * SC:(h % 4 + 1) * SC],
                                              tok[:, 1, n, hh:hh + 1], 0.0, ALU.subtract, ALU.min).then_inc(seg_made, 1)
                        if g >= 1:
                            keep_y(i - 1)
                        dve.wait_ge(exps, 3 * (i + 1))
                        dve.wait_ge(rows_kept, 14 * (n + 1))
                        d = dec[:, i % 2]
                        dve.tensor_tensor(d, d, cb[:, g, :].unsqueeze(1).to_broadcast([P, GH, SC]),
                                          ALU.mult).then_inc(scores, 1)
                        dve.tensor_tensor(inn[:, i % 2], inn[:, i % 2],
                                          p[:, S_TILES + SG + g, n * SC:(n + 1) * SC].unsqueeze(1).to_broadcast([P, GH, SC]),
                                          ALU.mult).then_inc(scores, 1)
                    keep_y(n * SG + SG - 1)


def second_ssd(m, w_in, cols, at, norms, norms_at, dt_bias, a_log, d_skip, y):
    nc = m.nc
    c0 = 3 * D + 2 * P
    w = w_in[0]
    project(m, w, X_TILES, lambda k: m.hT[:, k, :], KT,
            lambda dve, t, bank: dve.tensor_copy(at_tile(y, t), bank[:, :]), col0=c0 + S_TILES * P)
    ssd_conv(m, y, cols, at)
    ssd(m, y, w[:, c0 + (S_TILES + X_TILES) * P:c0 + (S_TILES + X_TILES) * P + SH], dt_bias[0], a_log[0], d_skip[0])
    with ExitStack() as own:
        z = own.enter_context(nc.sbuf_tensor("sd_z", [P, S_TILES, T], F32))
        project(m, w, S_TILES, lambda k: m.hT[:, k, :], KT,
                lambda dve, t, bank: dve.tensor_copy(at_tile(z, t), bank[:, :]), col0=c0)
        z_silued = m.sem("sd_z_silued")
        with nc.Block() as block:

            @block.scalar
            def _(act):
                for j in range(SG):
                    act.activation(z[:, 4 * j:4 * j + 4, :], z[:, 4 * j:4 * j + 4, :], ACT.Silu).then_inc(z_silued, 1)

            @block.vector
            def _(dve):
                for j in range(SG):
                    dve.wait_ge(z_silued, j + 1)
                    q = slice(4 * j, 4 * j + 4)
                    m.dve.mark(dve.tensor_tensor(y[:, q, :], y[:, q, :], z[:, q, :], ALU.mult))
    n0 = norms_at["norm_g"]
    group_norm(m, y, y, norms[:, n0:n0 + S_TILES], SG, S_TILES // SG, m.ones, D // 2)


def second_merge(m, w_in, cols, at, y, w_up_rwkv, w_up_ssd, w_out, x_kept, y_kept):
    nc = m.nc
    g0 = 3 * D + 2 * P + (S_TILES + X_TILES) * P + SH
    copy_out(m, "ya_back", [(m.xT[:, :, :], y_kept)])
    with ExitStack() as own:
        sb = lambda name, shape, dt=F32: own.enter_context(nc.sbuf_tensor(name, shape, dt))
        up_a = sb("up_a", [P, KT, T])
        gates = sb("mix_gates", [P, KT, T])
        g_made = m.sem("mix_gate")

        def gated(half, dst, name):
            made = m.sem(f"{name}_gate_sigmoid")
            project(m, w_in[0], KT, lambda k: m.hT[:, k, :], KT,
                    lambda dve, t, bank: dve.tensor_copy(at_tile(gates, t), bank[:, :]), col0=g0 + half * D)
            with nc.Block() as block:

                @block.scalar
                def _(act):
                    for t in range(KT):
                        b = at["b_gate"] + half * KT + t
                        act.activation(gates[:, t, :], gates[:, t, :], ACT.Sigmoid, bias=cols[:, b:b + 1]).then_inc(made, 1)

                @block.vector
                def _(dve):
                    for t in range(KT):
                        dve.wait_ge(made, t + 1)
                        m.dve.mark(dve.tensor_tensor(dst[:, t, :], dst[:, t, :], gates[:, t, :], ALU.mult))

        project(m, w_up_rwkv[0], KT, lambda k: m.xT[:, k, :], KT,
                lambda dve, t, bank: dve.tensor_copy(at_tile(up_a, t), bank[:, :]))
        up_b = m.xT
        project(m, w_up_ssd[0][0:D, :], KT, lambda k: y[:, k, :], KT,
                lambda dve, t, bank: dve.tensor_copy(at_tile(up_b, t), bank[:, :]))
        project(m, w_up_ssd[0][D:2 * D, :], KT, lambda k: y[:, KT + k, :], KT,
                lambda dve, t, bank: dve.tensor_tensor(at_tile(up_b, t), bank[:, :], at_tile(up_b, t), ALU.add))
        gated(0, up_a, "a")
        gated(1, up_b, "b")
        with nc.Block() as block:

            @block.vector
            def _(dve):
                m.dve.mark(dve.tensor_tensor(up_a[:, :, :], up_a[:, :, :], up_b[:, :, :], ALU.add))
        copy_out(m, "x_back", [(m.xT[:, :, :], x_kept)])

        def keep(dve, t, bank):
            return dve.tensor_tensor(at_tile(m.xT, t), bank[:, :], at_tile(m.xT, t), ALU.add)
        project(m, w_out[0], KT, lambda k: up_a[:, k, :], KT, keep)


NG = 4
EG = 8
NE = NG * EG
DE = 512
TOP = 2
EXTRA = T * TOP // P - 1
BLOCKS = NE + EXTRA


def load_router(m, own, w_rg, b_rg, w_re, b_re):
    w = own.enter_context(m.nc.sbuf_tensor("mo_w", [P, KT, NG + NE], F32))
    b = own.enter_context(m.nc.sbuf_tensor("mo_b", [P, NG + NE], F32))
    parts = []
    for src, bias, c, n in ((w_rg, b_rg, 0, NG), (w_re, b_re, NG, NE)):
        parts.append((w[:, :, c:c + n], src.rearrange("(k p) n -> p k n", p=P)))
        parts.append((b[:, c:c + n], bias.rearrange("(a n) -> a n", a=1).to_broadcast([P, n])))
    copy_out(m, "router_landed", parts)
    return w, b


def route(m, w, bias, gate, dest, extra_expert, slot_token):
    nc = m.nc
    with ExitStack() as tmp:
        sb = lambda name, shape, dt=F32: tmp.enter_context(nc.sbuf_tensor(name, shape, dt))
        logit = sb("mo_logit", [P, TT, NG + NE])
        top = sb("mo_top", [P, TT, 1])
        ex = sb("mo_ex", [P, TT, NG])
        total = sb("mo_total", [P, TT, 1])
        eq = sb("mo_eq", [P, TT, NG])
        grp = sb("mo_grp", [P, TT, 1])
        hot = sb("mo_hot", [P, TT, NG])
        mix = sb("mo_mix", [P, TT, NG, EG])
        sel = sb("mo_sel", [P, TT, EG])
        val8 = sb("mo_val8", [P, TT, 8])
        ind8 = sb("mo_ind8", [P, TT, 8], U32)
        indf = sb("mo_indf", [P, TT, 8])
        e2 = sb("mo_e2", [P, TT, 1])
        inv = sb("mo_inv", [P, TT, 1])
        expert = sb("mo_expert", [P, TT, TOP])
        mask = sb("mo_mask", [P, TT, TOP, NE])
        both = sb("mo_both", [P, TT, NE])
        rank = sb("mo_rank", [P, TT, NE])
        pick = sb("mo_pick", [P, TT, TOP, NE])
        rk = sb("mo_rk", [P, TT, TOP])
        st = sb("mo_st", [P, TT, TOP])
        over = sb("mo_over", [P, TT, TOP])
        base = sb("mo_base", [P, TT, TOP])
        count = sb("mo_count", [P, NE])
        more = sb("mo_more", [P, NE])
        tmp32 = sb("mo_tmp32", [P, NE])
        ends = sb("mo_ends", [P, NE])
        starts = sb("mo_starts", [P, NE])
        ones32 = sb("mo_ones32", [P, NE])
        down4 = sb("mo_down4", [P, NG])
        up32 = sb("mo_up32", [P, NE])
        before = sb("mo_before", [P, P])
        token = sb("mo_token", [P, TT])
        xe = sb("mo_xe", [P, EXTRA, NE])
        upx = sb("mo_upx", [P, EXTRA])
        xf = sb("mo_xf", [P, EXTRA + 1])
        zero = sb("mo_zero", [BLOCKS, P])
        logits_made, ex_made, counted, zeroed, ready, scattered, dest_made = (
            m.sem(f"mo_{x}") for x in ("logits", "exps", "counted", "zeroed", "iotas", "scattered", "dest_made"))
        with nc.Block() as block:

            @block.gpsimd
            def _(pool):
                c = m.pool
                iota = lambda ap, pat, b, cm: c.link(pool, pool.iota(ap, pat, base=b, channel_multiplier=cm,
                                                                     allow_small_or_imprecise_dtypes=True))
                c.link(pool, pool.memset(zero[:, :], 0.0))
                iota(down4[:, :], [[-1, NG]], NG, 0)
                iota(up32[:, :], [[1, NE]], 0, 0)
                iota(upx[:, :], [[1, EXTRA]], 0, 0)
                iota(token[:, :], [[P, TT]], 0, 1)
                c.link(pool, pool.memset(ones32[:, :], 1.0))
                c.link(pool, pool.memset(before[:, :], 1.0))
                pool.affine_select(out=before[:, :], in_=before[:, :], compare_op=ALU.is_gt, fill=0.0, base=0,
                                   pattern=[[1, P]], channel_multiplier=-1).then_inc(ready, 1)
                pool.wait_ge(ready, 1)
                pool.dma_start(slot_token, zero[:, :]).then_inc(zeroed, 16)
                pool.wait_ge(zeroed, 16)
                pool.wait_ge(dest_made, 1)
                for t in range(TT):
                    for j in range(TOP):
                        n = t * TOP + j
                        pool.indirect_dma_start(
                            out=slot_token.rearrange("b (s a) -> (b s) a", a=1),
                            out_offset=bass.IndirectOffsetOnAxis(ap=dest[:, n:n + 1], axis=0),
                            in_=token[:, t:t + 1], in_offset=None).then_inc(scattered, 16)
                pool.wait_ge(scattered, 16 * TT * TOP)

            @block.tensor
            def _(pe):
                for t in range(TT):
                    for k in range(KT):
                        ins = pe.matmul(m.ps[0][:, t * 64:t * 64 + NG + NE], m.hT[:, k, t * P:(t + 1) * P], w[:, k, :],
                                        start=(k == 0), stop=(k == KT - 1))
                ins.then_inc(logits_made, 1)
                pe.wait_ge(ready, 1)
                pe.wait_ge(counted, 1)
                for t in range(TT):
                    for u in range(t + 1):
                        ins = pe.matmul(m.ps[1][:, t * NE:(t + 1) * NE], (before if u == t else m.ones)[:, :], both[:, u, :],
                                        start=(u == 0), stop=(u == t))
                for u in range(TT):
                    ins = pe.matmul(m.ps[2][:, 0:NE], m.ones[:, :], both[:, u, :], start=(u == 0), stop=(u == TT - 1))
                ins.then_inc(counted, 1)

            @block.scalar
            def _(act):
                act.wait_ge(ex_made, 1)
                act.activation(ex[:, :, :], ex[:, :, :], ACT.Exp).then_inc(ex_made, 1)
                act.wait_ge(ex_made, 3)
                act.activation(e2[:, :, :], e2[:, :, :], ACT.Exp).then_inc(ex_made, 1)

            @block.vector
            def _(dve):
                c = m.dve
                L = lambda ins: c.link(dve, ins)
                bc = lambda ap, shape: ap.to_broadcast(shape)
                dve.wait_ge(ready, 1)
                dve.wait_ge(logits_made, 1)
                b3 = m.ps[0][:, 0:TT * 64].rearrange("p (t n) -> p t n", n=64)[:, :, 0:NG + NE]
                L(dve.tensor_tensor(logit[:, :, :], b3, bias[:, :].unsqueeze(1).to_broadcast([P, TT, NG + NE]), ALU.add))
                g, e = logit[:, :, 0:NG], logit[:, :, NG:NG + NE]
                L(dve.tensor_reduce(top[:, :, :], g, AX.X, ALU.max))
                dve.tensor_tensor(ex[:, :, :], g, bc(top[:, :, :], [P, TT, NG]), ALU.subtract).then_inc(ex_made, 1)
                L(dve.tensor_tensor(eq[:, :, :], g, bc(top[:, :, :], [P, TT, NG]), ALU.is_equal))
                L(dve.tensor_tensor(eq[:, :, :], eq[:, :, :], down4[:, :].unsqueeze(1).to_broadcast([P, TT, NG]), ALU.mult))
                L(dve.tensor_reduce(grp[:, :, :], eq[:, :, :], AX.X, ALU.max))
                L(dve.tensor_tensor(hot[:, :, :], down4[:, :].unsqueeze(1).to_broadcast([P, TT, NG]),
                                    bc(grp[:, :, :], [P, TT, NG]), ALU.is_equal))
                L(dve.tensor_scalar(grp[:, :, :], grp[:, :, :], -1.0, float(NG), ALU.mult, ALU.add))
                L(dve.tensor_tensor(mix[:, :, :, :], e.rearrange("p t (g n) -> p t g n", n=EG),
                                    hot[:, :, :].unsqueeze(3).to_broadcast([P, TT, NG, EG]), ALU.mult))
                L(dve.tensor_reduce(sel[:, :, :], mix[:, :, :, :].rearrange("p t g n -> p t n g"), AX.X, ALU.add))
                for t in range(TT):
                    c.mark(dve.max(val8[:, t, :], sel[:, t, :]))
                c.wait(dve)
                for t in range(TT):
                    c.mark(dve.max_index(ind8[:, t, :], val8[:, t, :], sel[:, t, :]))
                dve.wait_ge(ex_made, 2)
                dve.tensor_tensor(e2[:, :, :], val8[:, :, 1:2], val8[:, :, 0:1], ALU.subtract).then_inc(ex_made, 1)
                L(dve.tensor_reduce(total[:, :, :], ex[:, :, :], AX.X, ALU.add))
                L(dve.tensor_copy(indf[:, :, :], ind8[:, :, :]))
                dve.wait_ge(ex_made, 4)
                L(dve.tensor_scalar(inv[:, :, :], e2[:, :, :], 1.0, None, ALU.add))
                L(dve.tensor_tensor(inv[:, :, :], inv[:, :, :], total[:, :, :], ALU.mult))
                L(dve.reciprocal(inv[:, :, :], inv[:, :, :]))
                g3 = gate[:, :].rearrange("p (t j) -> p t j", j=TOP)
                c.mark(dve.tensor_copy(g3[:, :, 0:1], inv[:, :, :]))
                c.mark(dve.tensor_tensor(g3[:, :, 1:2], inv[:, :, :], e2[:, :, :], ALU.mult))
                L(dve.scalar_tensor_tensor(out=expert[:, :, 0:1], in0=grp[:, :, :], scalar=float(EG), in1=indf[:, :, 0:1],
                                           op0=ALU.mult, op1=ALU.add))
                L(dve.scalar_tensor_tensor(out=expert[:, :, 1:2], in0=grp[:, :, :], scalar=float(EG), in1=indf[:, :, 1:2],
                                           op0=ALU.mult, op1=ALU.add))
                for j in range(TOP):
                    c.mark(dve.tensor_tensor(mask[:, :, j, :], up32[:, :].unsqueeze(1).to_broadcast([P, TT, NE]),
                                             bc(expert[:, :, j:j + 1], [P, TT, NE]), ALU.is_equal))
                c.wait(dve)
                dve.tensor_tensor(both[:, :, :], mask[:, :, 0, :], mask[:, :, 1, :], ALU.add).then_inc(counted, 1)
                dve.wait_ge(counted, 2)
                c.mark(dve.tensor_copy(rank[:, :, :], m.ps[1][:, 0:TT * NE].rearrange("p (t n) -> p t n", n=NE)))
                L(dve.tensor_copy(count[:, :], m.ps[2][:, 0:NE]))
                L(dve.tensor_scalar(more[:, :], count[:, :], float(P), None, ALU.is_gt))
                for q in range(2, T // P):
                    L(dve.tensor_scalar(tmp32[:, :], count[:, :], float(q * P), None, ALU.is_gt))
                    L(dve.tensor_tensor(more[:, :], more[:, :], tmp32[:, :], ALU.add))
                L(dve.tensor_tensor_scan(ends[:, :], ones32[:, :], more[:, :], 0.0, ALU.mult, ALU.add))
                L(dve.tensor_tensor(starts[:, :], ends[:, :], more[:, :], ALU.subtract))
                L(dve.tensor_tensor(xe[:, :, :], ends[:, :].unsqueeze(1).to_broadcast([P, EXTRA, NE]),
                                    upx[:, :].unsqueeze(2).to_broadcast([P, EXTRA, NE]), ALU.is_le))
                L(dve.tensor_reduce(xf[:, 0:EXTRA], xe[:, :, :], AX.X, ALU.add))
                L(dve.tensor_scalar(xf[:, 0:EXTRA], xf[:, 0:EXTRA], float(NE - 1), None, ALU.min))
                L(dve.tensor_copy(xf[:, EXTRA:EXTRA + 1], ends[:, NE - 1:NE]))
                L(dve.tensor_copy(extra_expert[:, :], xf[:, :]))
                for dst, src in ((rk, rank[:, :, :]), (st, starts[:, :].unsqueeze(1).to_broadcast([P, TT, NE]))):
                    for j in range(TOP):
                        c.mark(dve.tensor_tensor(pick[:, :, j, :], mask[:, :, j, :], src, ALU.mult))
                    c.wait(dve)
                    L(dve.tensor_reduce(dst[:, :, :], pick[:, :, :, :], AX.X, ALU.add))
                L(dve.tensor_scalar(over[:, :, :], rk[:, :, :], float(P), None, ALU.is_ge))
                L(dve.tensor_scalar(expert[:, :, :], expert[:, :, :], float(P), None, ALU.mult))
                L(dve.tensor_scalar(base[:, :, :], st[:, :, :], float(P), float((NE - 1) * P), ALU.mult, ALU.add))
                L(dve.tensor_tensor(base[:, :, :], base[:, :, :], expert[:, :, :], ALU.subtract))
                L(dve.tensor_tensor(base[:, :, :], base[:, :, :], over[:, :, :], ALU.mult))
                L(dve.tensor_tensor(base[:, :, :], base[:, :, :], expert[:, :, :], ALU.add))
                dve.tensor_tensor(dest[:, :], base[:, :, :].rearrange("p t j -> p (t j)"),
                                  rk[:, :, :].rearrange("p t j -> p (t j)"), ALU.add).then_inc(dest_made, 1)


def slot_columns(m, slot_token, columns):
    nc = m.nc
    landed, turned = m.sem("slots_landed"), m.sem("slots_turned")
    with ExitStack() as own:
        rows = own.enter_context(nc.sbuf_tensor("slot_rows", [BLOCKS, P], F32))
        with nc.Block() as block:

            @block.sync
            def _(sp):
                sp.dma_start(rows[:, :], slot_token).then_inc(landed, 16)

            @block.tensor
            def _(pe):
                pe.wait_ge(landed, 16)
                pe.transpose(m.ps[0][:, 0:BLOCKS], rows[:, :], m.ident[0:BLOCKS, 0:BLOCKS]).then_inc(turned, 1)

            @block.vector
            def _(dve):
                dve.wait_ge(turned, 1)
                m.dve.mark(dve.memset(columns[:, BLOCKS:BLOCKS + 1], 0))
                m.dve.mark(dve.tensor_copy(columns[:, 0:BLOCKS], m.ps[0][:, 0:BLOCKS]))


def wait(eng, sem, value):
    if not isinstance(value, int) or value > 0:
        eng.wait_ge(sem, value)


class Experts:

    def __init__(self, m, tag, w_gate, w_up, w_down, h_rows, y_rows, bufs):
        self.m, self.h_rows, self.y_rows = m, h_rows, y_rows
        self.w = (w_gate.rearrange("e (p k) n -> e p (k n)", k=KT), w_up.rearrange("e (p k) n -> e p (k n)", k=KT),
                  w_down.rearrange("e (p k) n -> e p (k n)", k=DE // P))
        self.gu, self.dn, self.xr, self.xT, self.hs, self.hid, self.hidT, self.yb, self.now = bufs
        sem = lambda x: m.sem(f"{tag}_{x}")
        self.w_landed = [[sem(f"w{j}_landed{s}") for s in range(2)] for j in range(3)]
        self.x_landed = [sem(f"x_landed{s}") for s in range(2)]
        self.y_stored = [sem(f"y_stored{s}") for s in range(2)]
        (self.index_set, self.x_turned, self.x_kept_act, self.x_kept_dve, self.g_made, self.u_made, self.silu_made,
         self.h_made, self.h_turned, self.h_kept, self.y_made, self.y_kept) = (sem(x) for x in (
             "index_set", "x_turned", "x_kept_act", "x_kept_dve", "g_made", "u_made", "silu_made", "h_made", "h_turned",
             "h_kept", "y_made", "y_kept"))

    def load(self, sp, e, n, s, reuse=True):
        for j, (done, k) in enumerate(((self.g_made, 1), (self.u_made, 1), (self.y_made, 2))):
            if reuse:
                wait(sp, done, k * (n - 1))
            dst = self.gu[:, s, j, :] if j < 2 else self.dn[:, s, :]
            src = self.w[j][e] if isinstance(e, int) else self.w[j][bass.ds(e, 1)].rearrange("a p n -> p (a n)")
            sp.dma_start(dst, src).then_inc(self.w_landed[j][s], 16)

    def gather(self, pool, columns, n, slot, s, reuse=True):
        wait(pool, self.index_set, n + 1)
        if reuse:
            wait(pool, self.x_turned, 2 * (n - 1))
        pool.tensor_copy(self.now[:, (slot + 1) % 4:(slot + 1) % 4 + 1],
                         columns[:, bass.ds(n + 1, 1)]).then_inc(self.index_set, 1)
        pool.indirect_dma_start(out=self.xr[:, s, :], out_offset=None, in_=self.h_rows,
                                in_offset=bass.IndirectOffsetOnAxis(ap=self.now[:, slot:slot + 1], axis=0)
                                ).then_inc(self.x_landed[s], 16)

    def turn_x(self, pe, n, s, u):
        m = self.m
        wait(pe, self.x_landed[s], 16 * (u + 1))
        wait(pe, self.x_kept_act, n)
        wait(pe, self.x_kept_dve, n)
        for b in range(2):
            for j in range(4):
                k = 4 * b + j
                ins = pe.transpose(m.ps[b][:, j * P:(j + 1) * P], self.xr[:, s, k:D:KT], m.ident[:, :])
            ins.then_inc(self.x_turned, 1)

    def up(self, pe, n, s, u):
        m = self.m
        wait(pe, self.x_kept_act, n + 1)
        wait(pe, self.x_kept_dve, n + 1)
        wait(pe, self.h_made, n)
        for j, made in enumerate((self.g_made, self.u_made)):
            wait(pe, self.w_landed[j][s], 16 * (u + 1))
            for k in range(KT):
                ins = pe.matmul(m.ps[2 + j][:, :], self.xT[:, k, :], self.gu[:, s, j, k * DE:(k + 1) * DE],
                                start=(k == 0), stop=(k == KT - 1))
            ins.then_inc(made, 1)

    def down(self, pe, n, s, u):
        m = self.m
        wait(pe, self.h_made, n + 1)
        wait(pe, self.h_kept, n)
        for k in range(DE // P):
            ins = pe.transpose(m.ps[4][:, k * P:(k + 1) * P], self.hid[:, k:DE:DE // P], m.ident[:, :])
        ins.then_inc(self.h_turned, 1)
        wait(pe, self.h_kept, n + 1)
        wait(pe, self.y_kept, 2 * n)
        wait(pe, self.w_landed[2][s], 16 * (u + 1))
        for b in range(2):
            for k in range(DE // P):
                ins = pe.matmul(m.ps[5 + b][:, :], self.hidT[:, k, :], self.dn[:, s, k * D + b * 512:k * D + b * 512 + 512],
                                start=(k == 0), stop=(k == DE // P - 1))
            ins.then_inc(self.y_made, 1)

    def act_x(self, act, n):
        wait(act, self.x_turned, 2 * n + 1)
        act.copy(self.xT[:, 0:4, :].rearrange("p k r -> p (k r)"), self.m.ps[0][:, :]).then_inc(self.x_kept_act, 1)

    def act_silu(self, act, n):
        wait(act, self.h_made, n)
        wait(act, self.g_made, n + 1)
        act.activation(self.hs[:, :], self.m.ps[2][:, :], ACT.Silu).then_inc(self.silu_made, 1)

    def act_down(self, act, n, s, u, row):
        wait(act, self.y_stored[s], 16 * u)
        for b in range(2):
            wait(act, self.y_made, 2 * n + b + 1)
            act.copy(self.yb[:, s, b * 512:(b + 1) * 512], self.m.ps[5 + b][:, :]).then_inc(self.y_kept, 1)
        wait(act, self.y_kept, 2 * n + 2)
        act.dma_start(self.y_rows[bass.ds(row, P), :], self.yb[:, s, :]).then_inc(self.y_stored[s], 16)

    def dve_x(self, dve, n):
        wait(dve, self.x_turned, 2 * n + 2)
        dve.tensor_copy(self.xT[:, 4:8, :].rearrange("p k r -> p (k r)"), self.m.ps[1][:, :]).then_inc(self.x_kept_dve, 1)

    def dve_hidden(self, dve, n):
        wait(dve, self.h_turned, n)
        wait(dve, self.silu_made, n + 1)
        wait(dve, self.u_made, n + 1)
        dve.tensor_tensor(self.hid[:, :], self.hs[:, :], self.m.ps[3][:, :], ALU.mult).then_inc(self.h_made, 1)

    def dve_down(self, dve, n):
        wait(dve, self.h_turned, n + 1)
        dve.tensor_copy(self.hidT[:, :, :].rearrange("p k r -> p (k r)"), self.m.ps[4][:, :]).then_inc(self.h_kept, 1)


def run_experts(m, w_gate, w_up, w_down, columns, extra_expert, h_rows, y_rows):
    nc = m.nc
    with ExitStack() as own:
        sb = lambda name, shape, dt=F32: own.enter_context(nc.sbuf_tensor(name, shape, dt))
        bufs = (sb("xp_gu", [P, 2, 2, KT * DE]), sb("xp_dn", [P, 2, (DE // P) * D]), sb("xp_xr", [P, 2, D]),
                sb("xp_xT", [P, KT, P]), sb("xp_hs", [P, DE]), sb("xp_hid", [P, DE]), sb("xp_hidT", [P, DE // P, P]),
                sb("xp_yb", [P, 2, D]), sb("xp_now", [P, 4], U32))
        x = Experts(m, "xp", w_gate, w_up, w_down, h_rows, y_rows, bufs)
        zero = sb("xp_zero", [P, D])
        zero_set, zero_stored = m.sem("xp_zero_set"), m.sem("xp_zero_stored")
        with nc.Block() as block:

            @block.sync
            def _(sp):
                x.load(sp, 0, 0, 0, reuse=False)
                x.load(sp, 1, 1, 1, reuse=False)
                sp.wait_ge(zero_set, 1)
                for q in range(EXTRA):
                    sp.dma_start(y_rows[(NE + q) * P:(NE + q + 1) * P, :], zero[:, :]).then_inc(zero_stored, 16)
                with sp.Fori(1, NE // 2) as i:
                    for s in range(2):
                        x.load(sp, 2 * i + s, 2 * i + s, s)
                sp.wait_ge(zero_stored, 16 * EXTRA)

            @block.gpsimd
            def _(pool):
                pool.tensor_copy(x.now[:, 0:1], columns[:, 0:1]).then_inc(x.index_set, 1)
                for e in range(4):
                    x.gather(pool, columns, e, e, e % 2, reuse=(e >= 2))
                with pool.Fori(1, NE // 4) as i:
                    for b in range(4):
                        x.gather(pool, columns, 4 * i + b, b, b % 2)

            @block.tensor
            def _(pe):
                def step(e, s, u, u1):
                    x.up(pe, e, s, u)
                    x.turn_x(pe, e + 1, 1 - s, u1)
                    x.down(pe, e - 1, 1 - s, u1 - 1)

                def turn(i):
                    step(2 * i + 1, 1, i, i + 1)
                    step(2 * i + 2, 0, i + 1, i + 1)

                x.turn_x(pe, 0, 0, 0)
                x.up(pe, 0, 0, 0)
                x.turn_x(pe, 1, 1, 0)
                turn(0)
                with pe.Fori(1, NE // 2 - 1) as i:
                    turn(i)
                last = NE // 2 - 1
                x.up(pe, NE - 1, 1, last)
                x.down(pe, NE - 2, 0, last)
                x.down(pe, NE - 1, 1, last)

            @block.scalar
            def _(act):
                def turn(i):
                    for s in range(2):
                        e = 2 * i + s
                        x.act_silu(act, e + 1)
                        x.act_x(act, e + 2)
                        x.act_down(act, e, s, i, (2 * P) * i + s * P)

                x.act_x(act, 0)
                x.act_silu(act, 0)
                x.act_x(act, 1)
                turn(0)
                with act.Fori(1, NE // 2 - 1) as i:
                    turn(i)
                last = NE // 2 - 1
                x.act_silu(act, NE - 1)
                x.act_down(act, NE - 2, 0, last, (NE - 2) * P)
                x.act_down(act, NE - 1, 1, last, (NE - 1) * P)
                for s in range(2):
                    act.wait_ge(x.y_stored[s], 16 * (NE // 2))

            @block.vector
            def _(dve):
                dve.memset(zero[:, :], 0.0).then_inc(zero_set, 1)
                x.dve_x(dve, 0)
                x.dve_hidden(dve, 0)
                x.dve_x(dve, 1)
                with dve.Fori(0, NE // 2 - 1) as i:
                    for s in range(2):
                        e = 2 * i + s
                        x.dve_x(dve, e + 2)
                        x.dve_down(dve, e)
                        x.dve_hidden(dve, e + 1)
                x.dve_down(dve, NE - 2)
                x.dve_hidden(dve, NE - 1)
                x.dve_down(dve, NE - 1)

        y = Experts(m, "xq", w_gate, w_up, w_down, h_rows, y_rows, bufs)
        some = lambda eng: eng.value_load(extra_expert[0:1, EXTRA:EXTRA + 1], min_val=0, max_val=EXTRA)
        with nc.Block() as block:

            @block.sync
            def _(sp):
                experts = [sp.value_load(extra_expert[0:1, q:q + 1], min_val=0, max_val=NE - 1) for q in range(EXTRA)]
                with sp.If(some(sp) > 0):
                    for q in range(EXTRA):
                        y.load(sp, experts[q], q, q % 2, reuse=(q >= 2))

            @block.gpsimd
            def _(pool):
                with pool.If(some(pool) > 0):
                    for q in range(EXTRA):
                        if q >= 2:
                            pool.wait_ge(y.x_turned, 2 * (q - 1))
                        pool.indirect_dma_start(
                            out=y.xr[:, q % 2, :], out_offset=None, in_=h_rows,
                            in_offset=bass.IndirectOffsetOnAxis(ap=columns[:, NE + q:NE + q + 1], axis=0)
                        ).then_inc(y.x_landed[q % 2], 16)

            @block.tensor
            def _(pe):
                with pe.If(some(pe) > 0):
                    for q in range(EXTRA):
                        y.turn_x(pe, q, q % 2, q // 2)
                        y.up(pe, q, q % 2, q // 2)
                        y.down(pe, q, q % 2, q // 2)

            @block.scalar
            def _(act):
                with act.If(some(act) > 0):
                    for q in range(EXTRA):
                        y.act_x(act, q)
                        y.act_silu(act, q)
                        y.act_down(act, q, q % 2, q // 2, (NE + q) * P)
                    for s in range(2):
                        act.wait_ge(y.y_stored[s], 16 * ((EXTRA + 1 - s) // 2))

            @block.vector
            def _(dve):
                with dve.If(some(dve) > 0):
                    for q in range(EXTRA):
                        y.dve_x(dve, q)
                        y.dve_hidden(dve, q)
                        y.dve_down(dve, q)


def combine(m, gate, dest, x_rows, y_rows, final_norm_g, out):
    nc = m.nc
    with ExitStack() as own:
        sb = lambda name, shape, dt=F32: own.enter_context(nc.sbuf_tensor(name, shape, dt))
        r = sb("cb_r", [P, TT, TOP, D])
        g = sb("cb_g", [P, D])
        sq = sb("cb_sq", [P, D])
        eps = sb("cb_eps", [P, 1])
        mean = sb("cb_mean", [P, TT])
        root = sb("cb_root", [P, TT])
        inv = sb("cb_inv", [P, TT])
        landed = [m.sem(f"cb_landed{n}") for n in range(TT)]
        g_landed, eps_set, summed, squared, rooted, made, stored = (
            m.sem(f"cb_{x}") for x in ("g_landed", "eps_set", "summed", "squared", "rooted", "made", "stored"))
        with nc.Block() as block:

            @block.gpsimd
            def _(pool):
                for t in range(TT):
                    for j in range(TOP):
                        n = t * TOP + j
                        pool.indirect_dma_start(
                            out=r[:, t, j, :], out_offset=None, in_=y_rows,
                            in_offset=bass.IndirectOffsetOnAxis(ap=dest[:, n:n + 1], axis=0)).then_inc(landed[t], 16)

            @block.sync
            def _(sp):
                sp.dma_start(g[:, :], final_norm_g.rearrange("(a n) -> a n", a=1).to_broadcast([P, D])).then_inc(g_landed, 16)
                for t in range(TT):
                    sp.wait_ge(made, t + 1)
                    sp.dma_start(out[t * P:(t + 1) * P, :], x_rows[:, t, :]).then_inc(stored, 16)
                sp.wait_ge(stored, 16 * TT)

            @block.scalar
            def _(act):
                act.wait_ge(eps_set, 1)
                for t in range(TT):
                    act.wait_ge(summed, t + 1)
                    if t:
                        act.wait_ge(squared, t)
                    act.activation(sq[:, :], x_rows[:, t, :], ACT.Square, accum_out=mean[:, t:t + 1]).then_inc(squared, 1)
                act.wait_ge(squared, TT)
                act.activation(root[:, :], mean[:, :], ACT.Sqrt, scale=1.0 / D, bias=eps[:, :]).then_inc(rooted, 1)

            @block.vector
            def _(dve):
                c = m.dve
                dve.memset(eps[:, :], EPS).then_inc(eps_set, 1)
                for t in range(TT):
                    dve.wait_ge(landed[t], 16 * TOP)
                    for j in range(TOP):
                        n = t * TOP + j
                        ins = dve.scalar_tensor_tensor(out=x_rows[:, t, :], in0=r[:, t, j, :], scalar=gate[:, n:n + 1],
                                                       in1=x_rows[:, t, :], op0=ALU.mult, op1=ALU.add)
                        if j < TOP - 1:
                            c.link(dve, ins)
                    ins.then_inc(summed, 1)
                dve.wait_ge(g_landed, 16)
                dve.wait_ge(rooted, 1)
                c.link(dve, dve.reciprocal(inv[:, :], root[:, :]))
                for t in range(TT):
                    dve.scalar_tensor_tensor(out=x_rows[:, t, :], in0=x_rows[:, t, :], scalar=inv[:, t:t + 1], in1=g[:, :],
                                             op0=ALU.mult, op1=ALU.mult).then_inc(made, 1)


def second_experts(m, norm_col, w_rg, b_rg, w_re, b_re, w_gate, w_up, w_down, final_norm_g, h_kept, slot_token, y_rows, out):
    nc = m.nc
    norm(m, m.xT, m.hT, norm_col)
    with ExitStack() as own:
        sb = lambda name, shape, dt=F32: own.enter_context(nc.sbuf_tensor(name, shape, dt))
        gate = sb("mo_gate", [P, TT * TOP])
        dest = sb("mo_dest", [P, TT * TOP], U32)
        extra_expert = sb("mo_extra_expert", [P, EXTRA + 1], I32)
        columns = sb("mo_columns", [P, BLOCKS + 1], U32)
        with ExitStack() as own2:
            w, bias = load_router(m, own2, w_rg, b_rg, w_re, b_re)
            route(m, w, bias, gate, dest, extra_expert, slot_token)
            slot_columns(m, slot_token, columns)
        rows = m.hT[:, :, :].rearrange("p k t -> p (k t)").rearrange("p (t d) -> p t d", t=TT)
        with ExitStack() as own2:
            h_rows = own2.enter_context(nc.sbuf_tensor("mo_h_rows", [P, TT, D], F32))
            turn_back(m, m.hT, h_rows, "h4")
            copy_out(m, "h_stored", [(h_kept.rearrange("(t p) d -> p t d", p=P), h_rows[:, :, :])])
        turn_back(m, m.xT, rows, "x4")
        run_experts(m, w_gate, w_up, w_down, columns, extra_expert, h_kept, y_rows)
        combine(m, gate, dest, rows, y_rows, final_norm_g, out)


def two_blocks(nc, x, c, w_ada, b_ada, norm1_w, w_in, hgrn_lb_logits, hgrn_onorm_w, conv_w, conv_onorm_w, w_out, norm2_w,
               peer_w_query, peer_sub_keys, peer_u, peer_v, final_norm_w, attn_norm_g_2, w_in_2, b_gate_2, rwkv_mu_2,
               rwkv_w0_2, rwkv_w_decay_2, rwkv_a0_2, rwkv_w_a_2, rwkv_w_g_2, rwkv_k_k_2, rwkv_k_a_2, rwkv_r_k_2, rwkv_ln_g_2,
               rwkv_ln_b_2, w_up_rwkv_2, ssd_conv_w_2, ssd_conv_b_2, ssd_dt_bias_2, ssd_a_log_2, ssd_d_2, ssd_norm_g_2,
               w_up_ssd_2, w_out_2, ffn_norm_g_2, w_router_group_2, b_router_group_2, w_router_expert_2, b_router_expert_2,
               w_exp_gate_2, w_exp_up_2, w_exp_down_2, final_norm_g_2, out):
    row = lambda ap: ap.rearrange("(k p) -> k p", p=P)
    kept = lambda name, shape: nc.dram_tensor(name, shape, F32, kind="Internal").ap()
    with ExitStack() as ctx:
        m = setup(nc, ctx)
        constants(m)
        with stage(m):
            cols, at = first_mixer(m, x, c, w_ada, b_ada, norm1_w, w_in, hgrn_lb_logits, hgrn_onorm_w, conv_w,
                                   conv_onorm_w, w_out, norm2_w, final_norm_w)
            first_experts(m, peer_w_query, peer_sub_keys, peer_u, peer_v, cols, at)
        with stage(m):
            x_kept, y_kept = kept("x_kept", [P, KT, T]), kept("ya_kept", [P, KT, T])
            cols, at = second_columns(m, attn_norm_g_2, rwkv_mu_2, rwkv_w0_2, rwkv_a0_2, rwkv_k_k_2, rwkv_k_a_2,
                                      rwkv_r_k_2, rwkv_ln_g_2, rwkv_ln_b_2)
            second_rwkv(m, w_in_2, cols, at, rwkv_w_decay_2, rwkv_w_a_2, rwkv_w_g_2, x_kept, y_kept)
            copy_out(m, "x_back_norm", [(m.xT[:, :, :], x_kept)])
            norm(m, m.xT, m.hT, cols[:, at["attn_norm"]:at["attn_norm"] + KT])
        with stage(m):
            cols3, at3 = column_rows(m, "cols3", [
                ("conv", ssd_conv_w_2[0].rearrange("j (k p) -> (j k) p", p=P)), ("conv_b", row(ssd_conv_b_2[0]))])
            cols4, at4 = column_rows(m, "cols4", [
                ("norm_g", row(ssd_norm_g_2[0])), ("b_gate", row(b_gate_2[0])), ("ffn_norm", row(ffn_norm_g_2[0]))])
            with ExitStack() as own:
                y = own.enter_context(nc.sbuf_tensor("ssd_y", [P, S_TILES + 2 * SG, T], F32))
                second_ssd(m, w_in_2, cols3, at3, cols4, at4, ssd_dt_bias_2, ssd_a_log_2, ssd_d_2, y)
                second_merge(m, w_in_2, cols4, at4, y, w_up_rwkv_2, w_up_ssd_2, w_out_2, x_kept, y_kept)
            second_experts(m, cols4[:, at4["ffn_norm"]:at4["ffn_norm"] + KT], w_router_group_2[0], b_router_group_2[0],
                           w_router_expert_2[0], b_router_expert_2[0], w_exp_gate_2[0], w_exp_up_2[0], w_exp_down_2[0],
                           final_norm_g_2, kept("h_kept", [T, D]), kept("slot_token", [BLOCKS, P]),
                           kept("y_rows", [BLOCKS * P, D]), out[0])


_INS = ['x', 'c', 'w_ada', 'b_ada', 'norm1_w', 'w_in', 'hgrn_lb_logits', 'hgrn_onorm_w', 'conv_w',
        'conv_onorm_w', 'w_out', 'norm2_w', 'peer_w_query', 'peer_sub_keys', 'peer_u', 'peer_v', 'final_norm_w',
        'attn_norm_g_2', 'w_in_2', 'b_gate_2', 'rwkv_mu_2', 'rwkv_w0_2', 'rwkv_w_decay_2', 'rwkv_a0_2',
        'rwkv_w_a_2', 'rwkv_w_g_2', 'rwkv_k_k_2', 'rwkv_k_a_2', 'rwkv_r_k_2', 'rwkv_ln_g_2', 'rwkv_ln_b_2',
        'w_up_rwkv_2', 'ssd_conv_w_2', 'ssd_conv_b_2', 'ssd_dt_bias_2', 'ssd_a_log_2', 'ssd_d_2', 'ssd_norm_g_2',
        'w_up_ssd_2', 'w_out_2', 'ffn_norm_g_2', 'w_router_group_2', 'b_router_group_2', 'w_router_expert_2',
        'b_router_expert_2', 'w_exp_gate_2', 'w_exp_up_2', 'w_exp_down_2', 'final_norm_g_2']


def kernel(**inputs):
    import numpy as _np
    import concourse.bacc as _bacc
    from concourse import mybir as _mybir
    from concourse.bass_utils import run_bass_kernel_spmd as _run

    nc = _bacc.Bacc("TRN2", target_bir_lowering=False, num_devices=1)
    arrays, args = {}, []
    for name in _INS:
        a = _np.ascontiguousarray(inputs[name])
        arrays[f"in_{name}_dram"] = a
        args.append(nc.dram_tensor(f"in_{name}_dram", a.shape, _mybir.dt.from_np(a.dtype), kind="ExternalInput").ap())
    out = nc.dram_tensor("out_0_dram", (1, T, D), F32, kind="ExternalOutput").ap()
    two_blocks(nc, *args, out)
    r = _run(nc, [arrays], core_ids=[0])
    return r.results[0]["out_0_dram"]
```

```python
from contextlib import ExitStack, contextmanager

import concourse.bass as bass
from concourse import mybir

P = 128
F32 = mybir.dt.float32
I32 = mybir.dt.int32
U32 = mybir.dt.uint32
ALU = mybir.AluOpType
ACT = mybir.ActivationFunctionType
AX = mybir.AxisListType
EPS = 1e-6

T = 512
D = 1024
KT = D // P
TT = T // P
HG = 4
HC = 128
CG = 4
HGRN_LEVELS = 7
SLOTS = 4
SLOT_COLS = 256


class Chain:

    def __init__(self, sem):
        self.sem = sem
        self.n = 0
        self.off = 0

    def link(self, eng, ins):
        self.mark(ins)
        self.wait(eng)

    def mark(self, ins):
        ins.then_inc(self.sem, 1)
        self.n += 1

    def wait(self, eng):
        eng.wait_ge(self.sem, self.off + self.n)

    def enter(self, i, steps):
        self.base = self.n
        self.steps = steps
        self.off = i * steps

    def leave(self, turns):
        assert self.n - self.base == self.steps, (self.n, self.base, self.steps)
        self.off = 0
        self.n = self.base + self.steps * turns


class Mem:
    pass


def setup(nc, ctx):
    m = Mem()
    m.nc = nc
    m.ctx = ctx
    m.ps = [ctx.enter_context(nc.psum_tensor(f"bank{i}", [P, 512], F32)) for i in range(8)]
    m.sem = lambda name: ctx.enter_context(nc.semaphore(name))
    m.dve = Chain(m.sem("dve_steps"))
    m.act = Chain(m.sem("act_steps"))
    m.pool = Chain(m.sem("pool_steps"))
    m.pe = Chain(m.sem("pe_steps"))
    sb = lambda name, shape, dt=F32: ctx.enter_context(nc.sbuf_tensor(name, shape, dt))
    m.sb = sb
    m.gathers = [m.sem(f"gathered{s}") for s in range(26)]
    m.ready = m.sem("constants_ready")
    m.ident = sb("ident", [P, P])
    m.ones = sb("ones", [P, P])
    m.half_ones = sb("half_ones", [P, P])
    m.weights = sb("weights", [P, SLOTS, KT, SLOT_COLS])
    m.xT = sb("xT", [P, KT, T])
    m.hT = sb("hT", [P, KT, T])
    m.w_landed = [m.sem(f"w_landed{i}") for i in range(SLOTS)]
    m.w_landed_n = [0] * SLOTS
    m.tile_made = m.sem("tile_made")
    m.tile_made_n = 0
    m.tile_kept = m.sem("tile_kept")
    m.tile_kept_n = 0
    m.sq_made = m.sem("sq_made")
    m.sq_made_n = 0
    m.sq_summed = m.sem("sq_summed")
    m.sq_summed_n = 0
    m.rstd_made = m.sem("rstd_made")
    m.rstd_made_n = 0
    m.scaled = m.sem("scaled")
    m.scaled_n = 0
    return m


@contextmanager
def stage(m):
    nc, outer, taken = m.nc, m.sem, []
    with ExitStack() as own:
        def sem(name):
            taken.append(own.enter_context(nc.semaphore(name)))
            return taken[-1]

        m.sem = sem
        yield
        m.sem = outer
        with nc.Block() as block:

            @block.gpsimd
            def _(pool):
                for s in taken:
                    pool.sem_clear(s)


def constants(m):
    nc = m.nc
    with nc.Block() as block:

        @block.gpsimd
        def _(pool):
            c = m.pool
            c.mark(pool.memset(m.ones[:], 1.0))
            c.mark(pool.memset(m.half_ones[:], 1.0))
            c.mark(pool.memset(m.ident[:], 0.0))
            c.wait(pool)
            c.link(pool, pool.affine_select(out=m.ident[:], in_=m.ident[:], compare_op=ALU.not_equal, fill=1.0,
                                            base=0, pattern=[[-1, P]], channel_multiplier=1))
            c.link(pool, pool.memset(m.half_ones[0:64, 64:P], 0.0))
            c.link(pool, pool.memset(m.half_ones[64:P, 0:64], 0.0))
            pool.sem_inc(m.ready, 1)


def column_rows(m, name, rows):
    nc = m.nc
    n = sum(ap.shape[0] for _, ap in rows)
    assert n <= P
    cols = m.sb(name, [P, n])
    at = {}
    landed = m.sem(f"{name}_landed")
    with ExitStack() as own:
        raw = own.enter_context(nc.sbuf_tensor(f"{name}_raw", [P, P], F32))
        with nc.Block() as block:

            @block.sync
            def _(sp):
                r = 0
                for key, ap in rows:
                    at[key] = r
                    sp.dma_start(raw[r:r + ap.shape[0], :], ap).then_inc(landed, 16)
                    r += ap.shape[0]

            @block.tensor
            def _(pe):
                pe.wait_ge(landed, 16 * len(rows))
                m.pe.mark(pe.transpose(m.ps[0][:, 0:n], raw[0:n, :], m.ident[0:n, 0:n]))

            @block.vector
            def _(dve):
                m.pe.wait(dve)
                m.dve.mark(dve.tensor_copy(cols[:, :], m.ps[0][:, 0:n]))
    return cols, at


def project(m, w, n_tiles, rhs, k_tiles, keep, other=None, setup=None, col0=0):
    nc = m.nc
    wv = w.rearrange("(k p) n -> p k n", p=P)
    per_slot = SLOT_COLS // P
    chunks = n_tiles // per_slot
    turns = chunks // SLOTS
    assert n_tiles % per_slot == 0
    made0, kept0 = m.tile_made_n, m.tile_kept_n
    landed0 = list(m.w_landed_n)
    per_turn = SLOTS * per_slot

    def turns_of(eng, body, first=0):
        if turns > first:
            with eng.Fori(first, turns) as i:
                body(i, SLOTS)
        if chunks % SLOTS:
            body(turns, chunks % SLOTS)

    with nc.Block() as block:

        @block.sync
        def _(sp):
            def load(i, s):
                sp.dma_start(m.weights[:, s, 0:k_tiles, :],
                             wv[:, :, bass.ds((i * SLOTS + s) * SLOT_COLS + col0, SLOT_COLS)]).then_inc(m.w_landed[s], 16)

            def body(i, slots):
                for s in range(slots):
                    sp.wait_ge(m.tile_made, made0 + (i - 1) * per_turn + (s + 1) * per_slot)
                    load(i, s)

            for s in range(min(SLOTS, chunks)):
                load(0, s)
            if turns >= 1:
                turns_of(sp, body, first=1)

        @block.tensor
        def _(pe):
            def body(i, slots, first_turn=False):
                for s in range(slots):
                    pe.wait_ge(m.w_landed[s], landed0[s] + 16 * i + 16)
                    for c in range(per_slot):
                        b = s * per_slot + c
                        if not first_turn:
                            pe.wait_ge(m.tile_kept, kept0 + (i - 1) * per_turn + b + 1)
                        for k in range(k_tiles):
                            ins = pe.matmul(m.ps[b][:, :], m.weights[:, s, k, c * P:(c + 1) * P], rhs(k),
                                            start=(k == 0), stop=(k == k_tiles - 1))
                        ins.then_inc(m.tile_made, 1)

            if turns >= 1:
                body(0, SLOTS, first_turn=True)
                turns_of(pe, body, first=1)
            else:
                body(0, chunks, first_turn=True)

        @block.vector
        def _(dve):
            def body(i, slots):
                for b in range(slots * per_slot):
                    dve.wait_ge(m.tile_made, made0 + i * per_turn + b + 1)
                    keep(dve, i * per_turn + b, m.ps[b]).then_inc(m.tile_kept, 1)

            if setup:
                setup(dve)
            turns_of(dve, body)

        if other:
            other(block)

    m.tile_made_n += n_tiles
    m.tile_kept_n += n_tiles
    for s in range(SLOTS):
        m.w_landed_n[s] += 16 * len([c for c in range(chunks) if c % SLOTS == s])


def norm(m, src, dst, scale, shift=None, sq=None):
    nc = m.nc
    sq = dst if sq is None else sq
    made0, summed0, rstd0, scaled0 = m.sq_made_n, m.sq_summed_n, m.rstd_made_n, m.scaled_n
    with ExitStack() as own:
        rstd = own.enter_context(nc.sbuf_tensor(f"rstd{made0}", [P, T], F32))
        with nc.Block() as block:

            @block.scalar
            def _(act):
                for k in range(KT):
                    act.activation(sq[:, k, :], src[:, k, :], ACT.Square).then_inc(m.sq_made, 1)
                act.wait_ge(m.rstd_made, rstd0 + 1)
                act.activation(rstd[:, :], rstd[:, :], ACT.Sqrt).then_inc(m.rstd_made, 1)
                if shift is not None:
                    for k in range(KT):
                        act.wait_ge(m.scaled, scaled0 + k + 1)
                        m.act.mark(act.activation(dst[:, k, :], dst[:, k, :], ACT.Identity, bias=shift[:, k:k + 1]))

            @block.tensor
            def _(pe):
                for k in range(KT):
                    pe.wait_ge(m.sq_made, made0 + k + 1)
                    ins = pe.matmul(m.ps[0][:, :], m.ones[:, :], sq[:, k, :], start=(k == 0), stop=(k == KT - 1))
                ins.then_inc(m.sq_summed, 1)

            @block.vector
            def _(dve):
                dve.wait_ge(m.sq_summed, summed0 + 1)
                dve.tensor_scalar(rstd[:, :], m.ps[0][:, :], 1.0 / D, EPS, ALU.mult, ALU.add).then_inc(m.rstd_made, 1)
                dve.wait_ge(m.rstd_made, rstd0 + 2)
                m.dve.link(dve, dve.reciprocal(rstd[:, :], rstd[:, :]))
                for k in range(KT):
                    dve.scalar_tensor_tensor(out=dst[:, k, :], in0=src[:, k, :], scalar=scale[:, k:k + 1],
                                             in1=rstd[:, :], op0=ALU.mult, op1=ALU.mult).then_inc(m.scaled, 1)

    m.sq_made_n += KT
    m.sq_summed_n += 1
    m.rstd_made_n += 2
    m.scaled_n += KT


def load_tokens(m, x):
    nc = m.nc
    landed = m.sem("x_landed")
    turned = m.sem("x_turned")
    with ExitStack() as own:
        rows = own.enter_context(nc.sbuf_tensor("x_rows", [P, TT, D], F32))
        with nc.Block() as block:

            @block.sync
            def _(sp):
                sp.dma_start(rows[:, :, :], x.rearrange("(t p) d -> p t d", p=P)).then_inc(landed, 16)

            @block.tensor
            def _(pe):
                pe.wait_ge(landed, 16)
                for k in range(KT):
                    for t in range(TT):
                        ins = pe.transpose(m.ps[k][:, t * P:(t + 1) * P], rows[:, t, k * P:(k + 1) * P], m.ident[:, :])
                    ins.then_inc(turned, 1)

            @block.vector
            def _(dve):
                for k in range(KT):
                    dve.wait_ge(turned, k + 1)
                    m.dve.mark(dve.tensor_copy(m.xT[:, k, :], m.ps[k][:, :]))


def modulation(m, w_ada, cols, at, mod, lead):
    nc = m.nc
    width = w_ada.shape[1]
    n_tiles = width // P
    halves, bufs = 2, 4
    H = width // halves
    landed = [m.sem(f"ada_landed{b}") for b in range(bufs)]
    added, summed = m.sem("ada_added"), m.sem("ada_summed")
    with ExitStack() as own:
        rows = own.enter_context(nc.sbuf_tensor("ada_rows", [P, bufs, H], F32))
        acc = own.enter_context(nc.sbuf_tensor("ada_acc", [P, width], F32))
        with nc.Block() as block:

            @block.sync
            def _(sp):
                for n in range(KT * halves):
                    k, h = n // halves, n % halves
                    if n >= bufs:
                        sp.wait_ge(added, n - bufs + 1)
                    sp.dma_start(rows[:, n % bufs, :], w_ada[k * P:(k + 1) * P, h * H:(h + 1) * H]).then_inc(landed[n % bufs], 16)

            @block.scalar
            def _(act):
                m.act.mark(act.activation(lead[:, :], cols[:, at["c"]:at["c"] + KT], ACT.Silu))

            @block.vector
            def _(dve):
                m.act.wait(dve)
                for n in range(KT * halves):
                    k, h = n // halves, n % halves
                    a, row = acc[:, h * H:(h + 1) * H], rows[:, n % bufs, :]
                    dve.wait_ge(landed[n % bufs], 16 * (n // bufs + 1))
                    if k == 0:
                        ins = dve.tensor_scalar(a, row, lead[:, 0:1], None, ALU.mult)
                    else:
                        dve.wait_ge(added, n - halves + 1)
                        ins = dve.scalar_tensor_tensor(out=a, in0=row, scalar=lead[:, k:k + 1], in1=a,
                                                       op0=ALU.mult, op1=ALU.add)
                    ins.then_inc(added, 1)
                dve.wait_ge(summed, 1)
                b0 = at["b_ada"]
                m.dve.mark(dve.tensor_tensor(mod[:, :], m.ps[0][:, 0:n_tiles], cols[:, b0:b0 + n_tiles], ALU.add))

            @block.tensor
            def _(pe):
                for n in range(n_tiles):
                    if n % (n_tiles // halves) == 0:
                        pe.wait_ge(added, halves * (KT - 1) + n // (n_tiles // halves) + 1)
                    ins = pe.matmul(m.ps[0][:, n:n + 1], acc[:, n * P:(n + 1) * P], m.ones[:, 0:1], start=True, stop=True)
                ins.then_inc(summed, 1)


def level_masks(m, own, name, n, levels):
    nc = m.nc
    masks = own.enter_context(nc.sbuf_tensor(name, [P, levels + 1, n], I32))
    with ExitStack() as own:
        s_of = own.enter_context(nc.sbuf_tensor(f"{name}_s", [P, n], I32))
        t_of = own.enter_context(nc.sbuf_tensor(f"{name}_t", [P, n], I32))
        late = own.enter_context(nc.sbuf_tensor(f"{name}_late", [P, n], I32))
        x = own.enter_context(nc.sbuf_tensor(f"{name}_x", [P, n], I32))
        with nc.Block() as block:

            @block.gpsimd
            def _(pool):
                c = m.pool
                for h in range(P // n):
                    c.mark(pool.iota(s_of[h * n:(h + 1) * n, :], [[0, n]], base=0, channel_multiplier=1))
                c.mark(pool.iota(t_of[:, :], [[1, n]], base=0, channel_multiplier=0))

            @block.vector
            def _(dve):
                c = m.dve
                m.pool.wait(dve)
                c.mark(dve.tensor_tensor(late[:, :], t_of[:, :], s_of[:, :], ALU.is_gt))
                c.mark(dve.tensor_tensor(masks[:, levels, :], t_of[:, :], s_of[:, :], ALU.is_equal))
                c.link(dve, dve.tensor_tensor(x[:, :], t_of[:, :], s_of[:, :], ALU.bitwise_xor))
                c.link(dve, dve.tensor_tensor(x[:, :], x[:, :], late[:, :], ALU.mult))
                for l in range(levels):
                    c.link(dve, dve.tensor_scalar(s_of[:, :], x[:, :], l, None, ALU.logical_shift_right))
                    c.link(dve, dve.tensor_scalar(masks[:, l, :], s_of[:, :], 1, None, ALU.is_equal))
    return masks


def group_norm(m, src, dst, w, groups, per_group, ones, mean_of, eps=EPS, gate=None):
    nc = m.nc
    made0, summed0, rstd0, scaled0 = m.sq_made_n, m.sq_summed_n, m.rstd_made_n, m.scaled_n
    turns = groups
    with ExitStack() as own:
        sq = own.enter_context(nc.sbuf_tensor(f"gn_sq{made0}", [P, 2, per_group, T], F32))
        rstd = own.enter_context(nc.sbuf_tensor(f"gn_rstd{made0}", [P, 2, T], F32))
        with nc.Block() as block:

            @block.scalar
            def _(act):
                def root(g):
                    act.wait_ge(m.rstd_made, rstd0 + 2 * g + 1)
                    act.activation(rstd[:, g % 2, :], rstd[:, g % 2, :], ACT.Sqrt).then_inc(m.rstd_made, 1)

                for g in range(turns):
                    if g >= 2:
                        act.wait_ge(m.sq_summed, summed0 + g - 1)
                    for j in range(per_group):
                        act.activation(sq[:, g % 2, j, :], src[:, g * per_group + j, :], ACT.Square).then_inc(m.sq_made, 1)
                    if g >= 1:
                        root(g - 1)
                root(turns - 1)

            @block.tensor
            def _(pe):
                for g in range(turns):
                    pe.wait_ge(m.sq_made, made0 + (g + 1) * per_group)
                    if g >= 2:
                        pe.wait_ge(m.rstd_made, rstd0 + 2 * g - 3)
                    for j in range(per_group):
                        ins = pe.matmul(m.ps[g % 2][:, :], ones[:, :], sq[:, g % 2, j, :],
                                        start=(j == 0), stop=(j == per_group - 1))
                    ins.then_inc(m.sq_summed, 1)

            @block.vector
            def _(dve):
                c = m.dve
                for g in range(turns):
                    dve.wait_ge(m.sq_summed, summed0 + g + 1)
                    if g >= 1:
                        dve.wait_ge(m.rstd_made, rstd0 + 2 * g)
                        c.wait(dve)
                    dve.tensor_scalar(rstd[:, g % 2, :], m.ps[g % 2][:, :], 1.0 / mean_of, eps,
                                      ALU.mult, ALU.add).then_inc(m.rstd_made, 1)
                    dve.wait_ge(m.rstd_made, rstd0 + 2 * g + 2)
                    c.link(dve, dve.reciprocal(rstd[:, g % 2, :], rstd[:, g % 2, :]))
                    for j in range(per_group):
                        t = g * per_group + j
                        c.mark(dve.scalar_tensor_tensor(out=dst[:, t, :], in0=src[:, t, :], scalar=w[:, t:t + 1],
                                                        in1=rstd[:, g % 2, :], op0=ALU.mult, op1=ALU.mult))
                        if gate is not None:
                            c.wait(dve)
                            c.mark(dve.tensor_tensor(dst[:, t, :], dst[:, t, :], gate[:, t, :], ALU.mult))

    m.sq_made_n += turns * per_group
    m.sq_summed_n += turns
    m.rstd_made_n += 2 * turns


def hgrn(m, cols, at, proj, yT, masks):
    nc = m.nc
    H, C = HG, HC
    NCH = T // C
    W = H * T
    L = HGRN_LEVELS
    flat = lambda ap: ap.rearrange("p h t -> p (h t)")
    q, f_raw, v, g = (proj[:, j * H:(j + 1) * H, :] for j in range(4))
    with ExitStack() as own:
        sb = lambda name, shape, dt=F32: own.enter_context(nc.sbuf_tensor(name, shape, dt))
        lb = sb("hg_lb", [P, H])
        lb1 = sb("hg_lb1", [P, H])
        kk = sb("hg_k", [P, H, T])
        b = sb("hg_b", [P, H, T])
        pair = sb("hg_pair", [P, 2, H, T])
        scores = sb("hg_scores", [P, H, T])
        dist = sb("hg_dist", [P, 2, H, T])
        keep = dist[:, 0]
        f = dist[:, 1]

        diff_made, sig_made, f_made, ready = (m.sem(f"hg_{x}") for x in ("diff", "sig", "f", "ready"))
        with nc.Block() as block:

            @block.gpsimd
            def _(pool):
                m.pool.mark(pool.memset(scores[:, :, :], 0.0))
                m.pool.link(pool, pool.memset(keep[:, :, :], 1.0))
                k4 = flat(keep).rearrange("p (n c) -> p n c", c=C)
                pool.memset(k4[:, :, 0:1], 0.0).then_inc(ready, 1)

            @block.scalar
            def _(act):
                act.wait_ge(diff_made, 1)
                act.activation(lb[:, :], lb1[:, :], ACT.Sigmoid).then_inc(sig_made, 1)
                act.activation(flat(f), flat(f_raw), ACT.Sigmoid).then_inc(sig_made, 1)
                act.activation(flat(kk), flat(f_raw), ACT.Sigmoid, scale=-1.0).then_inc(sig_made, 1)
                act.wait_ge(f_made, H)
                act.activation(flat(f), flat(f), ACT.Ln).then_inc(sig_made, 1)

            @block.vector
            def _(dve):
                c = m.dve
                a0 = at["lb"]
                dve.tensor_tensor(lb1[:, :], cols[:, a0:a0 + H], cols[:, a0 + H:a0 + 2 * H], ALU.subtract).then_inc(diff_made, 1)
                dve.wait_ge(sig_made, 1)
                c.link(dve, dve.tensor_scalar(lb1[:, :], lb[:, :], -1.0, 1.0, ALU.mult, ALU.add))
                dve.wait_ge(sig_made, 3)
                for h in range(H):
                    dve.tensor_scalar(f[:, h, :], f[:, h, :], lb1[:, h:h + 1], lb[:, h:h + 1],
                                      ALU.mult, ALU.add).then_inc(f_made, 1)
                for h in range(H):
                    c.mark(dve.tensor_scalar(kk[:, h, :], kk[:, h, :], lb1[:, h:h + 1], None, ALU.mult))
                dve.wait_ge(sig_made, 4)
                dve.wait_ge(ready, 1)
                c.mark(dve.tensor_tensor_scan(flat(b), flat(keep), flat(f), 0.0, ALU.mult, ALU.add))

        dist_made, decay_made, pair_made, level_made, folded = (
            m.sem(f"hg_{x}") for x in ("dist_made", "decay_made", "pair_made", "level_made", "folded"))
        blocks = lambda ap, l: flat(ap).rearrange("p (n c) -> p n c", c=2 << l)
        halves = lambda ap, l, j: flat(ap).rearrange("p (n j c) -> p n j c", j=2, c=1 << l)[:, :, j, :]
        with nc.Block() as block:

            @block.scalar
            def _(act):
                for l in range(L):
                    act.wait_ge(dist_made, l + 1)
                    act.activation(flat(dist[:, l % 2]), flat(dist[:, l % 2]), ACT.Abs).then_inc(decay_made, 1)
                    act.wait_ge(decay_made, 2 * l + 1)
                    act.activation(flat(dist[:, l % 2]), flat(dist[:, l % 2]), ACT.Exp, scale=-1.0).then_inc(decay_made, 1)

            @block.tensor
            def _(pe):
                for l in range(L + 1):
                    if l < L:
                        pe.wait_ge(pair_made, 2 * l + 2)
                    if l >= 2:
                        pe.wait_ge(folded, H * (l - 1))
                    for h in range(H):
                        for n in range(NCH):
                            t = slice(n * C, (n + 1) * C)
                            k_, q_ = (pair[:, l % 2, h, t],) * 2 if l < L else (kk[:, h, t], q[:, h, t])
                            ins = pe.matmul(m.ps[4 * (l % 2) + h][:, t], k_, q_, start=True, stop=True)
                    ins.then_inc(level_made, 1)

            @block.vector
            def _(dve):
                for l in range(L + 3):
                    if l < L:
                        if l >= 2:
                            dve.wait_ge(pair_made, 2 * l - 2)
                        mid = blocks(b, l)[:, :, (1 << l) - 1:1 << l].to_broadcast([P, W // (2 << l), 2 << l])
                        dve.tensor_tensor(blocks(dist[:, l % 2], l), blocks(b, l), mid, ALU.subtract).then_inc(dist_made, 1)
                    if 1 <= l <= L:
                        p = l - 1
                        dve.wait_ge(decay_made, 2 * p + 2)
                        if p >= 2:
                            dve.wait_ge(level_made, p - 1)
                        for j, src in enumerate((kk, q)):
                            dve.tensor_tensor(halves(pair[:, p % 2], p, j), halves(dist[:, p % 2], p, j),
                                              halves(src, p, j), ALU.mult).then_inc(pair_made, 1)
                    if l >= 2:
                        p = l - 2
                        dve.wait_ge(level_made, p + 1)
                        if p >= 1:
                            dve.wait_ge(folded, H * p)
                        for h in range(H):
                            mask = masks[:, p:p + 1, :].to_broadcast([P, NCH, C])
                            dve.copy_predicated(scores[:, h, :].rearrange("p (n t) -> p n t", t=C), mask,
                                                m.ps[4 * (p % 2) + h][:, :].rearrange("p (n t) -> p n t", t=C)).then_inc(folded, 1)

        vrow, krow = dist[:, 0], dist[:, 1]
        with ExitStack() as last:
            elast = last.enter_context(nc.sbuf_tensor("hg_elast", [P, H, NCH], F32))
            state = last.enter_context(nc.sbuf_tensor("hg_state", [P, H, P], F32))
            eb = m.hT[:, 0:H, :]
            v_turned, k_turned, e_made, k_decayed, rows_kept, update_made, state_made, out_kept = (
                m.sem(f"hg_{x}") for x in ("v_turned", "k_turned", "e_made", "k_decayed", "rows_kept", "update_made",
                                           "state_made", "out_kept"))
            with nc.Block() as block:

                @block.scalar
                def _(act):
                    act.activation(flat(eb), flat(b), ACT.Exp).then_inc(e_made, 1)
                    act.activation(elast[:, :, :], b[:, :, C - 1:T:C], ACT.Exp).then_inc(e_made, 1)
                    act.wait_ge(k_decayed, 1)
                    act.activation(flat(pair[:, 1]), flat(pair[:, 1]), ACT.Exp, scale=-1.0).then_inc(e_made, 1)
                    for h in range(H):
                        act.wait_ge(v_turned, h + 1)
                        act.copy(vrow[:, h, :], m.ps[h][:, :]).then_inc(rows_kept, 1)
                    for h in range(H):
                        act.wait_ge(k_turned, h + 1)
                        act.copy(krow[:, h, :], m.ps[4 + h][:, :]).then_inc(rows_kept, 1)
                    m.act.mark(act.activation(flat(kk), flat(g), ACT.Silu))

                @block.tensor
                def _(pe):
                    for h in range(H):
                        for n in range(NCH):
                            ins = pe.transpose(m.ps[h][:, n * C:(n + 1) * C], v[:, h, n * C:(n + 1) * C], m.ident[:, :])
                        ins.then_inc(v_turned, 1)
                    pe.wait_ge(k_decayed, 3)
                    for h in range(H):
                        for n in range(NCH):
                            ins = pe.transpose(m.ps[4 + h][:, n * C:(n + 1) * C], pair[:, 1, h, n * C:(n + 1) * C], m.ident[:, :])
                        ins.then_inc(k_turned, 1)
                    pe.wait_ge(rows_kept, 2 * H)
                    for n in range(NCH):
                        t = slice(n * C, (n + 1) * C)
                        for h in range(H):
                            pe.matmul(m.ps[h][:, t], vrow[:, h, t], scores[:, h, t], start=True, stop=(n == 0))
                            if n > 0:
                                pe.wait_ge(state_made, (n - 1) * H + h + 1)
                                ins = pe.matmul(m.ps[h][:, t], state[:, h, :], pair[:, 0, h, t], start=False, stop=True)
                            if n < NCH - 1:
                                ins = pe.matmul(m.ps[4 + h][:, t], krow[:, h, t], vrow[:, h, t], start=True, stop=True)
                            ins.then_inc(update_made, 1)

                @block.vector
                def _(dve):
                    bv = flat(b).rearrange("p (n c) -> p n c", c=C)
                    last_b = bv[:, :, C - 1:C].to_broadcast([P, H * NCH, C])
                    kd = flat(pair[:, 1])
                    dve.tensor_tensor(kd.rearrange("p (n c) -> p n c", c=C), bv, last_b, ALU.subtract).then_inc(k_decayed, 1)
                    dve.wait_ge(e_made, 2)
                    dve.tensor_tensor(flat(pair[:, 0]), flat(eb), flat(q), ALU.mult).then_inc(k_decayed, 1)
                    dve.wait_ge(e_made, 3)
                    dve.tensor_tensor(kd, kd, flat(kk), ALU.mult).then_inc(k_decayed, 1)
                    for n in range(NCH - 1):
                        for h in range(H):
                            u = m.ps[4 + h][:, n * C:(n + 1) * C]
                            dve.wait_ge(update_made, n * H + h + 1)
                            if n == 0:
                                dve.tensor_copy(state[:, h, :], u).then_inc(state_made, 1)
                            else:
                                dve.wait_ge(state_made, (n - 1) * H + h + 1)
                                dve.scalar_tensor_tensor(out=state[:, h, :], in0=state[:, h, :], scalar=elast[:, h, n:n + 1],
                                                         in1=u, op0=ALU.mult, op1=ALU.add).then_inc(state_made, 1)
                    for h in range(H):
                        dve.wait_ge(update_made, (NCH - 1) * H + h + 1)
                        m.dve.mark(dve.tensor_copy(b[:, h, :], m.ps[h][:, :]))

        w0 = at["hgrn_w"]
        group_norm(m, b, yT, cols[:, w0:w0 + H], H, 1, m.ones, P, gate=kk)


def short_conv(m, cols, at, proj, yT):
    nc = m.nc
    bg, cg, xin = (proj[:, 16 + 4 * j:20 + 4 * j, :] for j in range(3))
    c0 = at["conv_w"]
    with nc.Block() as block:

        @block.vector
        def _(dve):
            c = m.dve
            c.link(dve, dve.tensor_tensor(xin, cg, xin, ALU.mult))
            for g in range(CG):
                tap = lambda j: cols[:, c0 + j * CG + g:c0 + j * CG + g + 1]
                u, y = xin[:, g, :], cg[:, g, :]
                c.link(dve, dve.tensor_scalar(y, u, tap(2), None, ALU.mult))
                for j in (1, 0):
                    d = 2 - j
                    c.link(dve, dve.scalar_tensor_tensor(out=y[:, d:], in0=u[:, :T - d], scalar=tap(j), in1=y[:, d:],
                                                         op0=ALU.mult, op1=ALU.add))
            c.mark(dve.tensor_tensor(bg, cg, bg, ALU.mult))
    w0 = at["conv_norm"]
    group_norm(m, bg, yT[:, HG:HG + CG, :], cols[:, w0:w0 + CG], CG, 1, m.ones, P)


def first_mixer(m, x, c, w_ada, b_ada, norm1_w, w_in, lb_logits, hgrn_w, conv_w, conv_norm_w, w_out, norm2_w, final_norm_w):
    nc = m.nc
    row = lambda ap: ap.rearrange("(k p) -> k p", p=P)
    load_tokens(m, x[0])
    cols, at = column_rows(m, "cols1", [
        ("c", row(c[0])), ("b_ada", row(b_ada[0])), ("norm1", row(norm1_w[0])),
        ("lb", lb_logits.rearrange("l (k p) -> (l k) p", p=P)), ("hgrn_w", row(hgrn_w[0])),
        ("conv_w", conv_w[0].rearrange("j (k p) -> (j k) p", p=P)), ("conv_norm", row(conv_norm_w[0])),
        ("norm2", row(norm2_w[0])), ("final", row(final_norm_w))])
    mod = m.sb("mod", [P, 6 * KT])
    m.mod = mod
    scale1 = m.sb("scale1", [P, KT])
    m.scale2 = m.sb("scale2", [P, KT])
    silu_c = m.sb("silu_c", [P, KT])
    modulation(m, w_ada[0], cols, at, mod, silu_c)
    with nc.Block() as block:

        @block.vector
        def _(dve):
            for j, key, dst in ((1, "norm1", scale1), (4, "norm2", m.scale2)):
                m.dve.mark(dve.scalar_tensor_tensor(out=dst[:, :], in0=mod[:, j * KT:(j + 1) * KT], scalar=1.0,
                                                    in1=cols[:, at[key]:at[key] + KT], op0=ALU.add, op1=ALU.mult))
    norm(m, m.xT, m.hT, scale1, mod[:, 0:KT])
    with ExitStack() as own:
        proj = own.enter_context(nc.sbuf_tensor("proj1", [P, 28, T], F32))
        yT = own.enter_context(nc.sbuf_tensor("y1T", [P, KT, T], F32))
        project(m, w_in[0], 28, lambda k: m.hT[:, k, :], KT,
                lambda dve, t, bank: dve.tensor_copy(at_tile(proj, t), bank[:, :]))
        with ExitStack() as own2:
            masks = level_masks(m, own2, "pairs128", HC, HGRN_LEVELS)
            hgrn(m, cols, at, proj, yT, masks)
        short_conv(m, cols, at, proj, yT)
        add_projected(m, w_out[0], yT, KT, mod[:, 2 * KT:3 * KT])
    return cols, at


def at_tile(t3, t):
    return t3[:, t, :] if isinstance(t, int) else t3[:, bass.ds(t, 1), :].rearrange("p a t -> p (a t)")


def add_projected(m, w, rhs, k_tiles, gate):
    def keep(dve, t, bank):
        scalar = gate[:, t:t + 1] if isinstance(t, int) else gate[:, bass.ds(t, 1)]
        x = at_tile(m.xT, t)
        return dve.scalar_tensor_tensor(out=x, in0=bank[:, :], scalar=scalar, in1=x, op0=ALU.mult, op1=ALU.add)
    project(m, w, KT, lambda k: rhs[:, k, :], k_tiles, keep)


PH = 8
NK = 128
TOPK = 16
PICKS = PH * TOPK
RING = 16
GROUP = 4
GROUPS = PICKS // GROUP
BUFS = 2 * RING // GROUP
LOWEST = -3.0e38


def turn_back(m, src, dst, name):
    nc = m.nc
    turned = m.sem(f"{name}_turned")
    kept = m.sem(f"{name}_kept")
    halves = D // 512
    with nc.Block() as block:

        @block.tensor
        def _(pe):
            for t in range(TT):
                for h in range(halves):
                    for j in range(4):
                        ins = pe.transpose(m.ps[t * halves + h][:, j * P:(j + 1) * P],
                                           src[:, 4 * h + j, t * P:(t + 1) * P], m.ident[:, :])
                    ins.then_inc(turned, 1)

        @block.vector
        def _(dve):
            for n in range(TT * halves):
                dve.wait_ge(turned, n + 1)
                m.dve.mark(dve.tensor_copy(dst[:, n // halves, (n % halves) * 512:(n % halves + 1) * 512], m.ps[n][:, :]))


def turn_forward(m, src, name, keep):
    nc = m.nc
    turned = m.sem(f"{name}_turned")
    with nc.Block() as block:

        @block.tensor
        def _(pe):
            for k in range(KT):
                for t in range(TT):
                    ins = pe.transpose(m.ps[k][:, t * P:(t + 1) * P], src[:, t, k * P:(k + 1) * P], m.ident[:, :])
                ins.then_inc(turned, 1)

        @block.vector
        def _(dve):
            for k in range(KT):
                dve.wait_ge(turned, k + 1)
                m.dve.mark(keep(dve, k, m.ps[k]))


def key_scores(m, sub_keys, qT, s_all):
    nc = m.nc
    HP = 2 * PH
    landed, turned, kept, made, s_kept = (m.sem(f"keys_{x}") for x in ("landed", "turned", "kept", "made", "s_kept"))
    with ExitStack() as own:
        raw = own.enter_context(nc.sbuf_tensor("keys_raw", [P, HP, P], F32))
        kT = own.enter_context(nc.sbuf_tensor("keysT", [P, HP, P], F32))
        with nc.Block() as block:

            @block.sync
            def _(sp):
                keys = sub_keys.rearrange("h j n k -> n (h j) k")
                for b in range(4):
                    sp.dma_start(raw[:, 4 * b:4 * b + 4, :], keys[:, 4 * b:4 * b + 4, :]).then_inc(landed, 16)

            @block.tensor
            def _(pe):
                pe.wait_ge(landed, 64)
                for b in range(4):
                    for j in range(4):
                        ins = pe.transpose(m.ps[b][:, j * P:(j + 1) * P], raw[:, 4 * b + j, :], m.ident[:, :])
                    ins.then_inc(turned, 1)
                pe.wait_ge(kept, 4)
                for t in range(TT):
                    for b in range(4):
                        n = t * 4 + b
                        if n >= 8:
                            pe.wait_ge(s_kept, n - 7)
                        for j in range(4):
                            hp = 4 * b + j
                            ins = pe.matmul(m.ps[n % 8][:, j * P:(j + 1) * P], qT[:, hp, t * P:(t + 1) * P], kT[:, hp, :],
                                            start=True, stop=True)
                        ins.then_inc(made, 1)

            @block.vector
            def _(dve):
                for b in range(4):
                    dve.wait_ge(turned, b + 1)
                    dve.tensor_copy(kT[:, 4 * b:4 * b + 4, :].rearrange("p j n -> p (j n)"), m.ps[b][:, :]).then_inc(kept, 1)
                for n in range(4 * TT):
                    dve.wait_ge(made, n + 1)
                    dve.tensor_copy(s_all[:, n // 4, (n % 4) * 512:(n % 4 + 1) * 512], m.ps[n % 8][:, :]).then_inc(s_kept, 1)


class Picker:
    PARTS = 14

    def __init__(self, m, own, s_all, index, gate):
        self.m, self.s_all, self.index, self.gate = m, s_all, index, gate
        self.shifted, self.exps, self.picked = m.sem("gate_shifted"), m.sem("gate_exps"), m.sem("tiles_picked")
        HP = 2 * PH
        sb = lambda name, shape, dt=F32: own.enter_context(m.nc.sbuf_tensor(name, shape, dt))
        self.s = sb("pk_s", [P, HP, NK])
        self.s2 = sb("pk_s2", [P, HP, NK])
        self.val = sb("pk_val", [P, HP, TOPK])
        self.ind = sb("pk_ind", [P, HP, TOPK], U32)
        self.indf = sb("pk_indf", [P, HP, TOPK])
        self.cand = sb("pk_cand", [P, PH, TOPK * TOPK])
        self.cand2 = sb("pk_cand2", [P, PH, TOPK * TOPK])
        self.best = sb("pk_best", [P, PH, TOPK])
        self.pos = sb("pk_pos", [P, PH, TOPK], U32)
        self.digit = sb("pk_digit", [P, 2, PH * TOPK], U32)
        self.digitf = sb("pk_digitf", [P, 2, PH * TOPK])
        self.which = sb("pk_which", [P, PH, TOPK, TOPK])
        self.found = sb("pk_found", [P, 2, PH * TOPK])
        self.count = sb("pk_count", [P, TOPK])
        self.total = sb("pk_total", [P, PH])
        self.ex = sb("pk_ex", [P, PH, TOPK])
        self.pad = sb("pk_pad", [P, 1])
        self.STEPS = 1 + (5 * HP + 4) + 2 + (5 * PH + 4) + 3 + 2 * 3 + 1 + 2

    def start(self, pool):
        m = self.m
        m.pool.mark(pool.memset(self.index[:, TT, :], 0))
        m.pool.mark(pool.iota(self.count[:, :], [[1, TOPK]], base=0, channel_multiplier=0,
                              allow_small_or_imprecise_dtypes=True))

    def exp(self, act, i):
        act.wait_ge(self.shifted, i + 1)
        act.activation(self.ex[:, :, :], self.ex[:, :, :], ACT.Exp).then_inc(self.exps, 1)

    def carried(self, dve):
        c = self.m.dve
        c.wait(dve)
        c.mark(dve.memset(self.pad[:, :], 0.0))

    def largest8(self, dve, vals, src, half, n):
        for r in range(n):
            self.m.dve.mark(dve.max(vals[:, r, 8 * half:8 * half + 8], src[:, r, :]))

    def places8(self, dve, inds, vals, src, half, n):
        for r in range(n):
            self.m.dve.mark(dve.max_index(inds[:, r, 8 * half:8 * half + 8], vals[:, r, 8 * half:8 * half + 8], src[:, r, :]))

    def strike8(self, dve, spare, vals, src, n):
        for r in range(n):
            self.m.dve.mark(dve.match_replace(spare[:, r, :], vals[:, r, 0:8], src[:, r, :], LOWEST))

    def look_up(self, dve, j, step):
        c = self.m.dve
        w3 = self.which[:, :, :, :].rearrange("p h k n -> p (h k) n")
        i4 = self.indf[:, :, :].rearrange("p (h j) k -> p h j k", j=2)
        if step == 0:
            c.link(dve, dve.tensor_tensor(w3, self.count[:, :].unsqueeze(1).to_broadcast([P, PH * TOPK, TOPK]),
                                          self.digitf[:, j, :].unsqueeze(2).to_broadcast([P, PH * TOPK, TOPK]),
                                          ALU.is_equal))
        elif step == 1:
            c.link(dve, dve.tensor_tensor(self.which[:, :, :, :], self.which[:, :, :, :],
                                          i4[:, :, j, :].unsqueeze(2).to_broadcast([P, PH, TOPK, TOPK]), ALU.mult))
        else:
            c.link(dve, dve.tensor_reduce(self.found[:, j, :], w3, AX.X, ALU.add))

    def part(self, dve, n, i):
        c, HP = self.m.dve, 2 * PH
        s, s2, val, ind, cand, cand2, best, pos = (
            self.s, self.s2, self.val, self.ind, self.cand, self.cand2, self.best, self.pos)
        if n == 0:
            c.link(dve, dve.tensor_copy(s[:, :, :].rearrange("p h n -> p (h n)"),
                                        self.s_all[:, bass.ds(i, 1), :].rearrange("p a n -> p (a n)")))
            self.carried(dve)
            self.largest8(dve, val, s, 0, HP)
        elif n == 1:
            self.carried(dve)
            self.places8(dve, ind, val, s, 0, HP)
        elif n == 2:
            self.strike8(dve, s2, val, s, HP)
        elif n == 3:
            self.carried(dve)
            self.largest8(dve, val, s2, 1, HP)
        elif n == 4:
            self.carried(dve)
            self.places8(dve, ind, val, s2, 1, HP)
        elif n == 5:
            c.wait(dve)
            c.mark(dve.tensor_copy(self.indf[:, :, :], ind[:, :, :]))
            v4 = val[:, :, :].rearrange("p (h j) k -> p h j k", j=2)
            c.link(dve, dve.tensor_tensor(
                cand[:, :, :].rearrange("p h (a b) -> p h a b", b=TOPK),
                v4[:, :, 0, :].unsqueeze(3).to_broadcast([P, PH, TOPK, TOPK]),
                v4[:, :, 1, :].unsqueeze(2).to_broadcast([P, PH, TOPK, TOPK]), ALU.add))
        elif n == 6:
            self.carried(dve)
            self.largest8(dve, best, cand, 0, PH)
            self.carried(dve)
            self.places8(dve, pos, best, cand, 0, PH)
        elif n == 7:
            self.strike8(dve, cand2, best, cand, PH)
            self.carried(dve)
            self.largest8(dve, best, cand2, 1, PH)
        elif n == 8:
            self.carried(dve)
            self.places8(dve, pos, best, cand2, 1, PH)
            c.wait(dve)
            flat_pos = pos[:, :, :].rearrange("p h k -> p (h k)")
            c.mark(dve.tensor_scalar(self.digit[:, 0, :], flat_pos, 4, None, ALU.logical_shift_right))
            c.mark(dve.tensor_scalar(self.digit[:, 1, :], flat_pos, 15, None, ALU.bitwise_and))
            dve.tensor_tensor(self.ex[:, :, :], best[:, :, :], best[:, :, 0:1].to_broadcast([P, PH, TOPK]),
                              ALU.subtract).then_inc(self.shifted, 1)
            c.wait(dve)
            c.link(dve, dve.tensor_copy(self.digitf[:, :, :], self.digit[:, :, :]))
        elif n == 9:
            self.look_up(dve, 0, 0)
        elif n == 10:
            self.look_up(dve, 0, 1)
            self.look_up(dve, 0, 2)
        elif n == 11:
            self.look_up(dve, 1, 0)
        elif n == 12:
            self.look_up(dve, 1, 1)
            self.look_up(dve, 1, 2)
        else:
            dve.scalar_tensor_tensor(out=self.index[:, bass.ds(i, 1), :].rearrange("p a n -> p (a n)"),
                                     in0=self.found[:, 0, :], scalar=float(NK), in1=self.found[:, 1, :],
                                     op0=ALU.mult, op1=ALU.add).then_inc(self.picked, 1)
            dve.wait_ge(self.exps, i + 1)
            c.link(dve, dve.tensor_reduce(self.total[:, :], self.ex[:, :, :], AX.X, ALU.add))
            c.link(dve, dve.reciprocal(self.total[:, :], self.total[:, :]))
            c.mark(dve.tensor_tensor(self.gate[:, bass.ds(i, 1), :].rearrange("p a (h k) -> p (a h) k", k=TOPK),
                                     self.ex[:, :, :], self.total[:, :].unsqueeze(2).to_broadcast([P, PH, TOPK]), ALU.mult))


def apply_experts(m, table_u, table_v, s_all, rows, index, gate, out):
    nc = m.nc
    TURNS = PICKS // RING
    landed = m.gathers[0:RING]
    free, index_set, dots_made, act_made, coef_made = (
        m.sem(x) for x in ("rows_free", "index_set", "dots_made", "act_made", "coef_made"))
    with ExitStack() as own:
        sb = lambda name, shape, dt=F32: own.enter_context(nc.sbuf_tensor(name, shape, dt))
        ring = sb("ring", [P, RING, D])
        now = sb("index_now", [P, BUFS, GROUP], U32)
        flat_index = index[:, :, :].rearrange("p t n -> p (t n)")
        dots = sb("dots", [P, PICKS])
        coef = sb("coef", [P, PICKS])
        acc = sb("acc", [P, D])
        picker = Picker(m, own, s_all, index, gate)
        one = lambda ap3, i: ap3[:, bass.ds(i, 1), :].rearrange("p a n -> p (a n)")
        with nc.Block() as block:

            @block.gpsimd
            def _(pool):
                def groups(i, half, table, body):
                    for b in range(BUFS):
                        g = body * BUFS + b
                        n = (i * 2 + half) * GROUPS + g
                        pool.wait_ge(index_set, n + 1)
                        pool.wait_ge(free, (n + 1) * GROUP)
                        after = i * PICKS + g * GROUP + GROUP
                        last = b == BUFS - 1
                        if last and half == 0:
                            after = i * PICKS + (body + 1) % (GROUPS // BUFS) * (BUFS * GROUP)
                        if last and half == 1 and isinstance(body, int):
                            pool.wait_ge(picker.picked, i + 2)
                        pool.tensor_copy(now[:, (b + 1) % BUFS, :],
                                         flat_index[:, bass.ds(after, GROUP)]).then_inc(index_set, 1)
                        for j in range(GROUP):
                            s = (b * GROUP + j) % RING
                            pool.indirect_dma_start(
                                out=ring[:, s, :], out_offset=None, in_=table,
                                in_offset=bass.IndirectOffsetOnAxis(ap=now[:, b, j:j + 1], axis=0)).then_inc(landed[s], 16)

                picker.start(pool)
                pool.wait_ge(picker.picked, 1)
                pool.tensor_copy(now[:, 0, :], flat_index[:, 0:GROUP]).then_inc(index_set, 1)
                with pool.Fori(0, TT) as i:
                    with pool.Fori(0, GROUPS // BUFS) as body:
                        groups(i, 0, table_u, body)
                    with pool.Fori(0, GROUPS // BUFS - 1) as body:
                        groups(i, 1, table_v, body)
                    groups(i, 1, table_v, GROUPS // BUFS - 1)

            @block.scalar
            def _(act):
                picker.exp(act, 0)
                with act.Fori(0, TT - 1) as i:
                    act.wait_ge(dots_made, (i + 1) * PICKS)
                    act.activation(coef[:, :], dots[:, :], ACT.Gelu).then_inc(act_made, 1)
                    picker.exp(act, i + 1)
                act.wait_ge(dots_made, TT * PICKS)
                act.activation(coef[:, :], dots[:, :], ACT.Gelu).then_inc(act_made, 1)

            @block.vector
            def _(dve):
                c = m.dve

                def dot(i, g):
                    for s in range(RING):
                        dve.wait_ge(landed[s], (i * (2 * TURNS) + g + 1) * 16)
                        dve.scalar_tensor_tensor(out=ring[:, s, :], in0=ring[:, s, :], scalar=1.0, in1=one(rows, i),
                                                 op0=ALU.mult, op1=ALU.mult,
                                                 accum_out=dots[:, bass.ds(g * RING + s, 1)]).then_inc(free, 1)

                def add(i, g):
                    v0 = i * (2 * TURNS) + TURNS
                    for s in range(RING):
                        dve.wait_ge(landed[s], (v0 + g + 1) * 16)
                        dve.wait_ge(free, (v0 + g + 1) * RING + s)
                        dve.scalar_tensor_tensor(out=acc[:, :], in0=ring[:, s, :],
                                                 scalar=coef[:, bass.ds(g * RING + s, 1)], in1=acc[:, :],
                                                 op0=ALU.mult, op1=ALU.add).then_inc(free, 1)

                def coefficients(i):
                    dve.wait_ge(free, RING + (i * (2 * TURNS) + TURNS) * RING)
                    dve.nop().then_inc(dots_made, PICKS)
                    dve.wait_ge(act_made, i + 1)
                    c.mark(dve.tensor_tensor(coef[:, :], coef[:, :], one(gate, i), ALU.mult))
                    c.mark(dve.memset(acc[:, :], 0.0))
                    c.wait(dve)
                    c.mark(dve.memset(picker.pad[:, :], 0.0))

                def keep(i):
                    dve.wait_ge(free, (i * 2 + 2) * TURNS * RING + RING)
                    c.mark(dve.tensor_copy(one(out, i), acc[:, :]))

                dve.sem_inc(free, RING)
                m.pool.wait(dve)
                for n in range(picker.PARTS):
                    picker.part(dve, n, 0)
                c.wait(dve)
                c.mark(dve.memset(picker.pad[:, :], 0.0))
                with dve.Fori(0, TT - 1) as i:
                    c.enter(i, picker.STEPS + 4)
                    for g in range(TURNS):
                        dot(i, g)
                        picker.part(dve, g, i + 1)
                    coefficients(i)
                    for g in range(TURNS):
                        add(i, g)
                        if TURNS + g < picker.PARTS:
                            picker.part(dve, TURNS + g, i + 1)
                    keep(i)
                    c.leave(TT - 1)
                dve.sem_inc(picker.picked, 1)
                with dve.Fori(0, TURNS) as g:
                    dot(TT - 1, g)
                coefficients(TT - 1)
                with dve.Fori(0, TURNS) as g:
                    add(TT - 1, g)
                keep(TT - 1)


def first_experts(m, w_query, sub_keys, table_u, table_v, cols, at):
    nc = m.nc
    norm(m, m.xT, m.hT, m.scale2, m.mod[:, 3 * KT:4 * KT])
    with ExitStack() as own:
        index = own.enter_context(nc.sbuf_tensor("index", [P, TT + 1, PICKS], U32))
        gate = own.enter_context(nc.sbuf_tensor("gate", [P, TT, PICKS], F32))
        rows = own.enter_context(nc.sbuf_tensor("h_rows", [P, TT, D], F32))
        turn_back(m, m.hT, rows, "h2")
        s_all = m.weights[:, :, :, :].rearrange("p s k c -> p (s k c)").rearrange("p (t n) -> p t n", t=TT)
        out = m.hT[:, :, :].rearrange("p k t -> p (k t)").rearrange("p (t d) -> p t d", t=TT)
        with ExitStack() as own2:
            qT = own2.enter_context(nc.sbuf_tensor("qT", [P, 2 * PH, T], F32))
            project(m, w_query[0], 2 * PH, lambda k: m.hT[:, k, :], KT,
                    lambda dve, t, bank: dve.tensor_copy(at_tile(qT, t), bank[:, :]))
            key_scores(m, sub_keys[0], qT, s_all)
        apply_experts(m, table_u[0], table_v[0], s_all, rows, index, gate, out)
        g0 = 5 * KT
        turn_forward(m, out, "peer", lambda dve, k, bank: dve.scalar_tensor_tensor(
            out=m.xT[:, k, :], in0=bank[:, :], scalar=m.mod[:, g0 + k:g0 + k + 1], in1=m.xT[:, k, :],
            op0=ALU.mult, op1=ALU.add))
    norm(m, m.xT, m.xT, cols[:, at["final"]:at["final"] + KT], sq=m.hT)


RH = 64
RC = 64
RT = 8
RN = T // RC
R_TILES = 3 * RT + 2
R_LEVELS = 6
E_HALF = 0.6065306597126334


def rwkv_masks(m, own):
    nc = m.nc
    sb = lambda ctx, name, shape, dt=F32: ctx.enter_context(nc.sbuf_tensor(name, shape, dt))
    lower = sb(own, "rk_lower", [P, R_LEVELS, RC])
    first = sb(own, "rk_first", [P, RC])
    after = sb(own, "rk_after", [P, RC])
    upto = sb(own, "rk_upto", [P, RC])
    eye = sb(own, "rk_eye", [P, RC])
    with ExitStack() as tmp:
        a = sb(tmp, "rk_a", [P, RC], I32)
        b = sb(tmp, "rk_b", [P, RC], I32)
        x = sb(tmp, "rk_x", [P, RC], I32)
        y = sb(tmp, "rk_y", [P, RC], I32)
        z = sb(tmp, "rk_z", [P, RC], I32)
        with nc.Block() as block:

            @block.gpsimd
            def _(pool):
                for h in range(2):
                    m.pool.link(pool, pool.iota(a[h * RC:(h + 1) * RC, :], [[0, RC]], base=0, channel_multiplier=1))
                m.pool.mark(pool.iota(b[:, :], [[1, RC]], base=0, channel_multiplier=0))

            @block.vector
            def _(dve):
                c = m.dve
                m.pool.wait(dve)
                c.mark(dve.tensor_tensor(after[:, :], b[:, :], a[:, :], ALU.is_gt))
                c.mark(dve.tensor_tensor(upto[:, :], b[:, :], a[:, :], ALU.is_ge))
                c.mark(dve.tensor_tensor(eye[:, :], b[:, :], a[:, :], ALU.is_equal))
                c.mark(dve.tensor_tensor(y[:, :], a[:, :], b[:, :], ALU.is_gt))
                c.link(dve, dve.tensor_tensor(x[:, :], a[:, :], b[:, :], ALU.bitwise_xor))
                c.link(dve, dve.tensor_scalar(z[:, :], x[:, :], 1, None, ALU.is_equal))
                c.link(dve, dve.tensor_tensor(first[:, :], z[:, :], after[:, :], ALU.mult))
                c.link(dve, dve.tensor_tensor(x[:, :], x[:, :], y[:, :], ALU.mult))
                for l in range(R_LEVELS):
                    c.link(dve, dve.tensor_scalar(z[:, :], x[:, :], l, None, ALU.logical_shift_right))
                    c.link(dve, dve.tensor_scalar(lower[:, l, :], z[:, :], 1, None, ALU.is_equal))
    return lower, first, after, upto, eye


class Spare:
    MAIN, GATE = 5, 2
    TILES = MAIN + GATE

    def __init__(self, m, w, main0, gate0, dest, h_kept, bonus_kept):
        self.m, self.main0, self.gate0, self.dest = m, main0, gate0, dest
        self.h_kept, self.bonus_kept = h_kept, bonus_kept
        self.w = w.rearrange("(k p) n -> p k n", p=P)
        self.landed = [m.sem(f"spare_landed{s}") for s in range(2)]
        self.made, self.kept, self.stored = (m.sem(f"spare_{x}") for x in ("made", "kept", "stored"))

    def open(self, own, leaving):
        self.weights = own.enter_context(self.m.nc.sbuf_tensor("spare_weights", [P, 2, KT, P], F32))
        self.leaving = leaving

    def place(self, c, j):
        if j < self.MAIN:
            n = self.MAIN * c + j
            return self.main0 + n * P, n
        n = self.GATE * c + j - self.MAIN
        return self.gate0 + n * P, RN * self.MAIN + n

    def load(self, sp, c, j):
        sp.dma_start(self.weights[:, j % 2], self.w[:, :, bass.ds(self.place(c, j)[0], P)]).then_inc(self.landed[j % 2], 16)

    def store(self, sp, c, j):
        sp.wait_ge(self.kept, self.TILES * c + j + 2)
        n = self.place(c, j)[1]
        dst = self.dest[n] if isinstance(n, int) else self.dest[bass.ds(n, 1)].rearrange("a p t -> p (a t)")
        sp.dma_start(dst, self.leaving).then_inc(self.stored, 16)

    def chunk_loads(self, sp, c, last=False):
        for j in range(self.TILES):
            self.store(sp, c, j)
            if j + 2 < self.TILES:
                self.load(sp, c, j + 2)
            elif not last:
                self.load(sp, c + 1, j % 2)

    def multiply(self, pe, c, i, count):
        for x in range(i, i + count):
            j, k = x // KT, x % KT
            if k == 0:
                use = (self.TILES + 1 - j % 2) // 2 * c + j // 2
                pe.wait_ge(self.landed[j % 2], 16 * (use + 1))
                pe.wait_ge(self.kept, self.TILES * c + 1 + max(0, j - 1))
            ins = pe.matmul(self.m.ps[3 + j % 2][:, :], self.weights[:, j % 2, k, :], self.m.xT[:, k, :],
                            start=(k == 0), stop=(k == KT - 1))
            if k == KT - 1:
                ins.then_inc(self.made, 1)
        return i + count

    def keep(self, act, c, j):
        act.wait_ge(self.made, self.TILES * c + j + 1)
        act.wait_ge(self.stored, 16 * (self.TILES * c + j + 1))
        act.copy(self.leaving, self.m.ps[3 + j % 2][:, :]).then_inc(self.kept, 1)


def rwkv(m, cols, at, p, yT, w_decay, w_a, w_g, spare):
    nc = m.nc
    flat = lambda ap: ap.rearrange("p h t -> p (h t)")
    r, k, v = (p[:, j * RT:(j + 1) * RT, :] for j in range(3))
    col = lambda key, t: cols[:, at[key] + t:at[key] + t + 1]
    wflat = m.weights[:, :, :, :].rearrange("p s k c -> p (s k c)")
    w0 = wflat[:, 0:RT * T].rearrange("p (h t) -> p h t", t=T)
    w1 = wflat[:, RT * T:2 * RT * T].rearrange("p (h t) -> p h t", t=T)
    a_bank = lambda n: m.ps[n % 8]
    with ExitStack() as own:
        sb = lambda name, shape, dt=F32: own.enter_context(nc.sbuf_tensor(name, shape, dt))
        A, KK = (sb(f"rk_{x}", [P, RT, T]) for x in ("A", "KK"))
        S, BON = m.hT, m.xT
        elast = sb("rk_elast", [P, RT, RN])
        state = sb("rk_state", [P, RT, RH])
        early = ExitStack()
        ranks = early.enter_context(nc.sbuf_tensor("rk_ranks", [P, D], F32))
        B = early.enter_context(nc.sbuf_tensor("rk_B", [P, RT, T], F32))

        lora_landed = m.sem("rk_lora_landed")
        with nc.Block() as block:

            @block.sync
            def _(sp):
                sp.dma_start(ranks[0:RH, :], w_decay).then_inc(lora_landed, 16)
                sp.dma_start(ranks[RH:P, :], w_a).then_inc(lora_landed, 16)

            @block.gpsimd
            def _(pool):
                m.pool.link(pool, pool.memset(w0[:, :, :], 1.0))
                k4 = flat(w0).rearrange("p (n c) -> p n c", c=RC)
                m.pool.link(pool, pool.memset(k4[:, :, 0:1], 0.0))
                m.pool.mark(pool.memset(state[:, :, :], 0.0))

            @block.vector
            def _(dve):
                c = m.dve
                for j in range(0, R_TILES, RT):
                    n = min(RT, R_TILES - j)
                    c.mark(dve.tensor_tensor(w1[:, 0:n, 1:T], p[:, j:j + n, 0:T - 1], p[:, j:j + n, 1:T], ALU.subtract))
                    c.mark(dve.tensor_scalar(w1[:, 0:n, 0:1], p[:, j:j + n, 0:1], -1.0, None, ALU.mult))
                    c.wait(dve)
                    for t in range(n):
                        c.mark(dve.scalar_tensor_tensor(out=p[:, j + t, :], in0=w1[:, t, :], scalar=col("mu", j + t),
                                                        in1=p[:, j + t, :], op0=ALU.mult, op1=ALU.add))
                    c.wait(dve)

        low, lora_made, lora_kept = m.sem("rk_low"), m.sem("rk_lora_made"), m.sem("rk_lora_kept")
        with nc.Block() as block:

            @block.scalar
            def _(act):
                act.activation(p[0:RH, 24, :], p[0:RH, 24, :], ACT.Tanh).then_inc(low, 1)
                for n in range(2 * RT):
                    t = n % RT
                    act.wait_ge(lora_made, n + 1)
                    act.activation((S if n < RT else A)[:, t, :], a_bank(n)[:, :], ACT.Sigmoid,
                                   bias=col("w0" if n < RT else "a0", t)).then_inc(lora_kept, 1)
                m.act.mark(act.activation(p[:, 25, :], p[:, 25, :], ACT.Sigmoid))

            @block.tensor
            def _(pe):
                pe.wait_ge(lora_landed, 32)
                pe.wait_ge(low, 1)
                for n in range(2 * RT):
                    h, t = n // RT, n % RT
                    if n >= 8:
                        pe.wait_ge(lora_kept, n - 7)
                    q = slice(h * RH, (h + 1) * RH)
                    pe.matmul(a_bank(n)[:, :], ranks[q, t * P:(t + 1) * P], p[q, 24, :],
                              start=True, stop=True).then_inc(lora_made, 1)

            @block.vector
            def _(dve):
                c = m.dve
                dve.wait_ge(lora_kept, RT)
                c.link(dve, dve.tensor_scalar(flat(S), flat(S), -E_HALF, None, ALU.mult))
                c.mark(dve.tensor_tensor_scan(flat(B), flat(w0), flat(S), 0.0, ALU.mult, ALU.add))

        kk_sq, kk_sum, kk_root, bon_in, bon_sum, bon_out = (
            m.sem(f"rk_{x}") for x in ("kk_sq", "kk_sum", "kk_root", "bon_in", "bon_sum", "bon_out"))
        with nc.Block() as block:

            @block.scalar
            def _(act):
                for t in range(RT):
                    act.wait_ge(kk_sq, 2 * t + 1)
                    act.activation(w1[:, t, :], KK[:, t, :], ACT.Square).then_inc(kk_sq, 1)
                for t in range(RT):
                    act.wait_ge(kk_sum, t + 1)
                    act.activation(w0[:, t, :], m.ps[t][:, :], ACT.Sqrt).then_inc(kk_root, 1)

            @block.tensor
            def _(pe):
                for t in range(RT):
                    pe.wait_ge(kk_sq, 2 * t + 2)
                    pe.matmul(m.ps[t][:, :], m.half_ones[:, :], w1[:, t, :], start=True, stop=True).then_inc(kk_sum, 1)
                for t in range(RT):
                    pe.wait_ge(bon_in, t + 1)
                    pe.wait_ge(kk_root, t + 1)
                    pe.matmul(m.ps[t][:, :], m.half_ones[:, :], w1[:, t, :], start=True, stop=True).then_inc(bon_sum, 1)

            @block.vector
            def _(dve):
                c = m.dve
                for t in range(RT):
                    if t:
                        dve.wait_ge(kk_sq, 2 * t)
                    dve.tensor_scalar(KK[:, t, :], k[:, t, :], col("k_k", t), None, ALU.mult).then_inc(kk_sq, 1)
                for t in range(RT):
                    dve.wait_ge(kk_root, t + 1)
                    c.mark(dve.tensor_scalar(w0[:, t, :], w0[:, t, :], 1e-12, None, ALU.max))
                c.wait(dve)
                c.link(dve, dve.reciprocal(flat(w0), flat(w0)))
                c.link(dve, dve.tensor_tensor(flat(KK), flat(KK), flat(w0), ALU.mult))
                for t in range(RT):
                    c.mark(dve.tensor_scalar(w0[:, t, :], A[:, t, :], 1.0, col("k_a", t), ALU.subtract, ALU.mult))
                c.wait(dve)
                c.link(dve, dve.scalar_tensor_tensor(out=flat(k), in0=flat(w0), scalar=1.0, in1=flat(k),
                                                     op0=ALU.add, op1=ALU.mult))
                c.mark(dve.tensor_tensor(flat(A), flat(KK), flat(A), ALU.mult))
                for t in range(RT):
                    dve.scalar_tensor_tensor(out=w1[:, t, :], in0=r[:, t, :], scalar=col("r_k", t), in1=k[:, t, :],
                                             op0=ALU.mult, op1=ALU.mult).then_inc(bon_in, 1)
                for t in range(RT):
                    dve.wait_ge(bon_sum, t + 1)
                    c.mark(dve.tensor_tensor(BON[:, t, :], m.ps[t][:, :], v[:, t, :], ALU.mult))

        exps, shifted = m.sem("rk_exps"), m.sem("rk_shifted")
        bonus_stored, h_back, bonus_back = m.sem("rk_bonus_stored"), m.sem("rk_h_back"), m.sem("rk_bonus_back")
        with nc.Block() as block:

            @block.scalar
            def _(act):
                act.activation(flat(w0), flat(B), ACT.Exp).then_inc(exps, 1)
                act.activation(elast[:, :, :], B[:, :, RC - 1:T:RC], ACT.Exp).then_inc(exps, 1)
                act.wait_ge(shifted, 1)
                act.activation(flat(w1), flat(w1), ACT.Exp).then_inc(exps, 1)
                act.activation(flat(S), flat(B), ACT.Exp, scale=-1.0).then_inc(exps, 1)

            @block.vector
            def _(dve):
                dve.tensor_tensor(flat(w1), flat(B), flat(S), ALU.subtract).then_inc(shifted, 1)

            @block.sync
            def _(sp):
                sp.dma_start(spare.bonus_kept, BON[:, :, :]).then_inc(bonus_stored, 16)
                sp.wait_ge(bonus_stored, 16)
                sp.dma_start(m.xT[:, :, :], spare.h_kept).then_inc(h_back, 16)
                sp.wait_ge(h_back, 16)

        early.close()
        with ExitStack() as late:
            spare.open(late, p[:, 24, :])
            rwkv_chunks(m, late, KK, A, k, r, v, w0, w1, S, elast, state, w0, spare)
        gates = sb("rk_gates", [P, D])
        B = w0

        head_sum, g_made, gates_landed = m.sem("rk_head_sum"), m.sem("rk_g_made"), m.sem("rk_gates_landed")
        with nc.Block() as block:

            @block.sync
            def _(sp):
                sp.dma_start(gates[:, :], w_g).then_inc(gates_landed, 16)
                sp.dma_start(BON[:, :, :], spare.bonus_kept).then_inc(bonus_back, 16)
                sp.wait_ge(bonus_back, 16)

            @block.tensor
            def _(pe):
                for t in range(RT):
                    pe.matmul(m.ps[t][:, :], m.half_ones[:, :], B[:, t, :], start=True, stop=True).then_inc(head_sum, 1)

            @block.vector
            def _(dve):
                for t in range(RT):
                    dve.wait_ge(head_sum, t + 1)
                    m.dve.mark(dve.scalar_tensor_tensor(out=B[:, t, :], in0=m.ps[t][:, :], scalar=-1.0 / RH,
                                                        in1=B[:, t, :], op0=ALU.mult, op1=ALU.add))
        g0 = at["ln_g"]
        group_norm(m, B, yT, cols[:, g0:g0 + RT], RT, 1, m.half_ones, RH, eps=64e-5)
        with nc.Block() as block:

            @block.tensor
            def _(pe):
                pe.wait_ge(gates_landed, 16)
                for t in range(RT):
                    pe.matmul(m.ps[t][:, :], gates[:, t * P:(t + 1) * P], p[:, 25, :], start=True, stop=True).then_inc(g_made, 1)

            @block.vector
            def _(dve):
                c = m.dve
                for t in range(RT):
                    c.mark(dve.scalar_tensor_tensor(out=BON[:, t, :], in0=BON[:, t, :], scalar=col("ln_b", t),
                                                    in1=yT[:, t, :], op0=ALU.add, op1=ALU.add))
                c.wait(dve)
                for t in range(RT):
                    dve.wait_ge(g_made, t + 1)
                    c.mark(dve.tensor_tensor(yT[:, t, :], m.ps[t][:, :], BON[:, t, :], ALU.mult))


def rwkv_chunks(m, own, KK, KA, k, r, v, e, ex, ei, elast, state, out, spare):
    nc = m.nc
    lower, first, after, upto, eye = rwkv_masks(m, own)
    names = ("alpha", "beta", "kappa", "rho", "v")
    with ExitStack() as tmp:
        sb = lambda name: tmp.enter_context(nc.sbuf_tensor(f"rc_{name}", [P, RT, RC], F32))
        st = {x: sb(x) for x in names}
        X, Y, TM, R, U, GAK, GRB, GRK, VT, BT, KT_ = (
            sb(x) for x in ("X", "Y", "TM", "R", "U", "gak", "grb", "grk", "vT", "betaT", "kappaT"))
        NL = tmp.enter_context(nc.sbuf_tensor("rc_NL", [P, R_LEVELS - 1, RT, RC], F32))
        f2 = lambda ap: ap.rearrange("p h t -> p (h t)")
        staged, made, masked, turned_kept, t_made, t_kept, xy_made, xy_kept, tail_made, tail_kept, state_kept = (
            m.sem(f"rc_{x}") for x in ("staged", "products", "masked", "turned_kept", "t_made", "t_kept", "xy_made",
                                       "xy_kept", "tail_made", "tail_kept", "state_kept"))
        over = lambda mask: mask.unsqueeze(1).to_broadcast([P, RT, RC])
        bank3 = lambda b: m.ps[b][:, :].rearrange("p (h t) -> p h t", t=RC)

        def heads(pe, bank, *terms):
            for t in range(RT):
                for h in range(2):
                    q = slice(h * RH, (h + 1) * RH)
                    for n, (lhs, rhs) in enumerate(terms):
                        o, l = bank[q, t * RC:(t + 1) * RC], lhs[q, t, :]
                        rr = rhs[q, t, :] if len(rhs.shape) == 3 else rhs[q, h * RH:(h + 1) * RH]
                        if t == h == n == 0:
                            wide = lhs[q, 0:2, :].rearrange("p a t -> p (a t)")
                            ins = pe.matmul(bank[:, 0:RC], wide, rr, start=True, stop=True)
                            if len(terms) == 1:
                                continue
                        ins = pe.matmul(o, l, rr, start=(n == 0), stop=(n == len(terms) - 1))
            return ins

        with nc.Block() as block:

            @block.vector
            def _(dve):
                with dve.Fori(0, RN) as c:
                    now = lambda ap: ap[:, :, bass.ds(c * RC, RC)]
                    dve.wait_ge(tail_made, 4 * c)
                    dve.wait_ge(tail_kept, 3 * c)
                    dve.wait_ge(state_kept, 2 * c)
                    dve.scalar_tensor_tensor(out=st["alpha"][:, :, :], in0=now(KK), scalar=-1.0, in1=now(ex),
                                             op0=ALU.mult, op1=ALU.mult).then_inc(staged, 1)
                    dve.tensor_tensor(st["beta"][:, :, :], now(KA), now(ei), ALU.mult).then_inc(staged, 1)
                    dve.tensor_tensor(st["kappa"][:, :, :], now(k), now(ei), ALU.mult).then_inc(staged, 1)
                    dve.tensor_tensor(st["rho"][:, :, :], now(r), now(e), ALU.mult).then_inc(staged, 1)
                    dve.tensor_copy(st["v"][:, :, :], now(v)).then_inc(staged, 1)
                    dve.wait_ge(made, 8 * c + 1)
                    dve.tensor_tensor(Y[:, :, :], bank3(0), over(first[:, :]), ALU.mult).then_inc(masked, 1)
                    dve.wait_ge(made, 8 * c + 2)
                    dve.tensor_tensor(X[:, :, :], bank3(1), over(lower[:, 0, :]), ALU.mult).then_inc(masked, 1)
                    dve.wait_ge(masked, 8 * c + 2)
                    dve.tensor_tensor(Y[:, :, :], Y[:, :, :], over(eye[:, :]), ALU.add).then_inc(masked, 1)
                    dve.tensor_tensor(X[:, :, :], X[:, :, :], over(eye[:, :]), ALU.add).then_inc(masked, 1)
                    dve.tensor_tensor(NL[:, :, :, :], bank3(1).unsqueeze(1).to_broadcast([P, R_LEVELS - 1, RT, RC]),
                                      lower[:, 1:R_LEVELS, :].unsqueeze(2).to_broadcast([P, R_LEVELS - 1, RT, RC]),
                                      ALU.mult).then_inc(masked, 1)
                    dve.wait_ge(made, 8 * c + 3)
                    dve.tensor_tensor(GAK[:, :, :], bank3(2), over(after[:, :]), ALU.mult).then_inc(masked, 1)
                    for l in range(1, R_LEVELS):
                        if l in (2, 3):
                            dst = (GRB, GRK)[l - 2]
                            dve.wait_ge(made, 8 * c + 5 + l)
                            dve.tensor_tensor(dst[:, :, :], bank3(l - 1), over(upto[:, :]), ALU.mult).then_inc(masked, 1)
                        for j, dst in enumerate((Y, X)[:2 if l < R_LEVELS - 1 else 1]):
                            dve.wait_ge(xy_made, (2 * R_LEVELS - 3) * c + 2 * (l - 1) + j + 1)
                            dve.tensor_tensor(dst[:, :, :], dst[:, :, :], bank3(5 + j), ALU.add).then_inc(xy_kept, 1)
                    dve.wait_ge(tail_made, 4 * c + 4)
                    dve.tensor_tensor(state[:, :, :], state[:, :, :], bank3(2), ALU.add).then_inc(state_kept, 1)
                    dve.wait_ge(state_kept, 2 * c + 1)
                    dve.tensor_tensor(state[:, :, :], state[:, :, :],
                                      elast[:, :, bass.ds(c, 1)].to_broadcast([P, RT, RH]), ALU.mult).then_inc(state_kept, 1)

            @block.scalar
            def _(act):
                act.sem_inc(spare.kept, 1)
                act.sem_inc(spare.stored, 16)
                with act.Fori(0, RN) as c:
                    for n, dst in enumerate((VT, BT, KT_)):
                        act.wait_ge(made, 8 * c + 4 + n)
                        act.copy(f2(dst), m.ps[5 + n][:, :]).then_inc(turned_kept, 1)
                    spare.keep(act, c, 0)
                    act.wait_ge(tail_made, 4 * c + 1)
                    act.copy(f2(R), m.ps[7][:, :]).then_inc(tail_kept, 1)
                    spare.keep(act, c, 1)
                    for l in range(1, R_LEVELS):
                        act.wait_ge(t_made, (R_LEVELS - 1) * c + l)
                        act.copy(f2(TM), m.ps[0][:, :]).then_inc(t_kept, 1)
                        if l >= 2:
                            spare.keep(act, c, l)
                    act.wait_ge(tail_made, 4 * c + 2)
                    act.copy(f2(U), m.ps[0][:, :]).then_inc(tail_kept, 1)
                    spare.keep(act, c, 6)
                    act.wait_ge(tail_made, 4 * c + 3)
                    act.copy(out[:, :, bass.ds(c * RC, RC)], bank3(1)).then_inc(tail_kept, 1)

            @block.tensor
            def _(pe):
                A, B, K, R_, V = (st[x] for x in names)
                XY = 2 * R_LEVELS - 3
                with pe.Fori(0, RN) as c:
                    i = spare.multiply(pe, c, 0, 8)
                    pe.wait_ge(staged, 5 * c + 5)
                    for b, (l, rr) in ((0, (B, A)), (1, (A, B)), (2, (K, A)),
                                       (5, (V, m.ident)), (6, (B, m.ident)), (7, (K, m.ident))):
                        heads(pe, m.ps[b], (l, rr)).then_inc(made, 1)
                    i = spare.multiply(pe, c, i, 8)
                    pe.wait_ge(masked, 8 * c + 6)
                    pe.wait_ge(turned_kept, 3 * c + 3)
                    heads(pe, m.ps[7], (A, state), (GAK, VT)).then_inc(tail_made, 1)
                    for l in range(1, R_LEVELS):
                        if l >= 2:
                            pe.wait_ge(xy_kept, XY * c + 2 * (l - 1))
                        heads(pe, m.ps[0], (NL[:, l - 1], Y)).then_inc(t_made, 1)
                        if l <= 2:
                            heads(pe, m.ps[l], ((B, K)[l - 1], R_)).then_inc(made, 1)
                        i = spare.multiply(pe, c, i, 2 if l <= 2 else 4)
                        pe.wait_ge(t_kept, (R_LEVELS - 1) * c + l)
                        heads(pe, m.ps[5], (X, TM)).then_inc(xy_made, 1)
                        if l < R_LEVELS - 1:
                            heads(pe, m.ps[6], (TM, X)).then_inc(xy_made, 1)
                        i = spare.multiply(pe, c, i, 4)
                    pe.wait_ge(xy_kept, XY * (c + 1))
                    pe.wait_ge(tail_kept, 3 * c + 1)
                    heads(pe, m.ps[0], (Y, R)).then_inc(tail_made, 1)
                    i = spare.multiply(pe, c, i, 4)
                    assert i == spare.TILES * KT
                    pe.wait_ge(masked, 8 * c + 8)
                    pe.wait_ge(tail_kept, 3 * c + 2)
                    heads(pe, m.ps[1], (state, R_), (U, GRB), (VT, GRK)).then_inc(tail_made, 1)
                    heads(pe, m.ps[2], (BT, U), (KT_, VT)).then_inc(tail_made, 1)

            @block.sync
            def _(sp):
                spare.load(sp, 0, 0)
                spare.load(sp, 0, 1)
                with sp.Fori(0, RN - 1) as c:
                    spare.chunk_loads(sp, c)
                spare.chunk_loads(sp, RN - 1, last=True)
                sp.wait_ge(spare.stored, 16 * (spare.TILES * RN + 1))


def second_columns(m, attn_norm, mu, w0, a0, k_k, k_a, r_k, ln_g, ln_b):
    row = lambda ap: ap.rearrange("(k p) -> k p", p=P)
    return column_rows(m, "cols2", [
        ("attn_norm", row(attn_norm[0])), ("mu", row(mu[0])), ("w0", row(w0[0])), ("a0", row(a0[0])),
        ("k_k", row(k_k[0])), ("k_a", row(k_a[0])),
        ("r_k", r_k[0].rearrange("(k j) c -> k (j c)", j=2)), ("ln_g", row(ln_g[0])), ("ln_b", row(ln_b[0]))])


def copy_out(m, name, pairs):
    done = m.sem(name)
    with m.nc.Block() as block:

        @block.sync
        def _(sp):
            for dst, src in pairs:
                sp.dma_start(dst, src).then_inc(done, 16)
            sp.wait_ge(done, 16 * len(pairs))


def second_rwkv(m, w_in, cols, at, w_decay, w_a, w_g, x_kept, y_kept, spare):
    nc = m.nc
    n0 = at["attn_norm"]
    norm(m, m.xT, m.hT, cols[:, n0:n0 + KT])
    x_stored = m.sem("x_h_stored")

    def store(block):
        @block.scalar
        def _(act):
            act.dma_start(x_kept, m.xT[:, :, :]).then_inc(x_stored, 16)
            act.dma_start(spare.h_kept, m.hT[:, :, :]).then_inc(x_stored, 16)
            act.wait_ge(x_stored, 32)

    with ExitStack() as own:
        p = own.enter_context(nc.sbuf_tensor("proj_rk", [P, R_TILES, T], F32))
        project(m, w_in[0], R_TILES, lambda k: m.hT[:, k, :], KT,
                lambda dve, t, bank: dve.tensor_copy(at_tile(p, t), bank[:, :]), other=store)
        yT = p[:, 0:RT, :]
        rwkv(m, cols, at, p, yT, w_decay[0], w_a[0], w_g[0], spare)
        copy_out(m, "y_kept", [(y_kept, yT), (m.hT[:, :, :], spare.h_kept)])


SH = 32
SG = 4
SC = 128
SN = T // SC
S_TILES = 16
X_TILES = S_TILES + 2 * SG
TAPS = 4
GH = SH // SG


def ssd_conv(m, p, cols, at, source):
    nc = m.nc
    landed = [m.sem(f"sd_x_landed{g}") for g in range(X_TILES // 4)]
    conved, silued = m.sem("sd_conved"), m.sem("sd_silued")
    with ExitStack() as own:
        tmp = own.enter_context(nc.sbuf_tensor("sd_conv", [P, 2, 4, T], F32))
        with nc.Block() as block:

            @block.sync
            def _(sp):
                for g in range(X_TILES // 4):
                    sp.dma_start(p[:, 4 * g:4 * g + 4, :],
                                 source[4 * g:4 * g + 4].rearrange("k p t -> p k t")).then_inc(landed[g], 16)

            @block.vector
            def _(dve):
                c = m.dve
                for g in range(X_TILES // 4):
                    dve.wait_ge(landed[g], 16)
                    if g >= 2:
                        dve.wait_ge(silued, g - 1)
                    for d in range(TAPS):
                        for j in range(4):
                            t = 4 * g + j
                            tap = cols[:, at["conv"] + (TAPS - 1 - d) * X_TILES + t:][:, 0:1]
                            y = tmp[:, g % 2, j, d:]
                            if d == 0:
                                c.mark(dve.tensor_scalar(y, p[:, t, :], tap, cols[:, at["conv_b"] + t:][:, 0:1],
                                                         ALU.mult, ALU.add))
                            else:
                                ins = dve.scalar_tensor_tensor(out=y, in0=p[:, t, :T - d], scalar=tap, in1=y,
                                                               op0=ALU.mult, op1=ALU.add)
                                if d < TAPS - 1:
                                    c.mark(ins)
                                else:
                                    ins.then_inc(conved, 1)
                        c.wait(dve)

            @block.scalar
            def _(act):
                for g in range(X_TILES // 4):
                    act.wait_ge(conved, 4 * (g + 1))
                    act.activation(p[:, 4 * g:4 * g + 4, :], tmp[:, g % 2], ACT.Silu).then_inc(silued, 1)


def ssd(m, p, w_in_dt, dt_bias, a_log, d_skip):
    nc = m.nc
    with ExitStack() as own:
        sb = lambda name, shape, dt=F32: own.enter_context(nc.sbuf_tensor(name, shape, dt))
        w_dt = sb("sd_w_dt", [P, KT, SH])
        small = sb("sd_small", [SH, 4])
        dt, pos, acs, keep = (sb(f"sd_{x}", [SH, T]) for x in ("dt", "pos", "acs", "keep"))
        tok = sb("sd_tok", [P, 2, SN, SH])
        left = sb("sd_left", [P, SN, SH])
        whole = sb("sd_whole", [P, SN, SH])
        last_row = sb("sd_last_row", [P, P])
        upto = sb("sd_upto", [P, SC])
        d_col = sb("sd_d", [P, S_TILES])

        landed, made, soft, turned = (m.sem(f"sd_{x}") for x in ("landed", "dt_made", "soft", "turned"))
        with nc.Block() as block:

            @block.sync
            def _(sp):
                sp.dma_start(w_dt[:, :, :], w_in_dt.rearrange("(k p) n -> p k n", p=P)).then_inc(landed, 16)
                sp.dma_start(small[:, 0:1], dt_bias.rearrange("(h a) -> h a", a=1)).then_inc(landed, 16)
                sp.dma_start(small[:, 1:2], a_log.rearrange("(h a) -> h a", a=1)).then_inc(landed, 16)
                for h in range(2):
                    src = d_skip.rearrange("(a t j) -> a t j", a=1, j=2)[:, :, h]
                    with nc.allow_non_contiguous_dma(reason="32 numbers"):
                        sp.dma_start(d_col[h * RH:(h + 1) * RH, :], src.to_broadcast([RH, S_TILES])).then_inc(landed, 16)

            @block.gpsimd
            def _(pool):
                c = m.pool
                c.mark(pool.memset(keep[:, :], 1.0))
                c.mark(pool.memset(last_row[:, :], 1.0))
                c.mark(pool.memset(upto[:, :], 1.0))
                c.wait(pool)
                c.link(pool, pool.memset(keep[:, 0:T:SC], 0.0))
                c.link(pool, pool.affine_select(out=last_row[:, :], in_=last_row[:, :], compare_op=ALU.is_ge, fill=0.0,
                                                base=-(P - 1), pattern=[[0, P]], channel_multiplier=1))
                c.link(pool, pool.affine_select(out=upto[:, :], in_=upto[:, :], compare_op=ALU.is_ge, fill=0.0,
                                                base=0, pattern=[[1, SC]], channel_multiplier=-1))

            @block.tensor
            def _(pe):
                pe.wait_ge(landed, 80)
                for k in range(KT):
                    ins = pe.matmul(m.ps[0][0:SH, :], w_dt[:, k, :], m.hT[:, k, :], start=(k == 0), stop=(k == KT - 1))
                ins.then_inc(made, 1)
                pe.wait_ge(soft, 9)
                for j, src in enumerate((dt, acs)):
                    for n in range(SN):
                        ins = pe.transpose(m.ps[1][:, (j * SN + n) * SH:(j * SN + n + 1) * SH],
                                           src[:, n * SC:(n + 1) * SC], m.ident[0:SH, 0:SH])
                ins.then_inc(turned, 1)
                pe.wait_ge(soft, 10)
                pe.matmul(m.ps[2][:, 0:SN * SH], last_row[:, :], tok[:, 1].rearrange("p n h -> p (n h)"),
                          start=True, stop=True).then_inc(turned, 1)

            @block.scalar
            def _(act):
                act.wait_ge(landed, 80)
                act.activation(small[:, 2:3], small[:, 1:2], ACT.Exp).then_inc(soft, 1)
                act.wait_ge(soft, 3)
                act.activation(dt[:, :], dt[:, :], ACT.Abs).then_inc(soft, 1)
                act.wait_ge(soft, 4)
                act.activation(dt[:, :], dt[:, :], ACT.Exp, scale=-1.0).then_inc(soft, 1)
                act.wait_ge(soft, 5)
                act.activation(dt[:, :], dt[:, :], ACT.Ln, bias=1.0).then_inc(soft, 1)
                act.wait_ge(soft, 12)
                act.activation(left[:, :, :], left[:, :, :], ACT.Exp).then_inc(soft, 1)
                act.activation(whole[:, :, :], whole[:, :, :], ACT.Exp).then_inc(soft, 1)

            @block.vector
            def _(dve):
                dve.wait_ge(made, 1)
                dve.wait_ge(soft, 1)
                dve.tensor_scalar(dt[:, :], m.ps[0][0:SH, :], small[:, 0:1], None, ALU.add).then_inc(soft, 1)
                dve.tensor_scalar(pos[:, :], m.ps[0][0:SH, :], small[:, 0:1], 0.0, ALU.add, ALU.max).then_inc(soft, 1)
                dve.wait_ge(soft, 6)
                dve.tensor_tensor(dt[:, :], dt[:, :], pos[:, :], ALU.add).then_inc(soft, 1)
                dve.wait_ge(soft, 7)
                dve.tensor_scalar(pos[:, :], dt[:, :], small[:, 2:3], -1.0, ALU.mult, ALU.mult).then_inc(soft, 1)
                dve.wait_ge(soft, 8)
                m.pool.wait(dve)
                dve.tensor_tensor_scan(acs[:, :], keep[:, :], pos[:, :], 0.0, ALU.mult, ALU.add).then_inc(soft, 1)
                dve.wait_ge(turned, 1)
                dve.tensor_copy(tok[:, :, :, :].rearrange("p a n h -> p (a n h)"), m.ps[1][:, 0:2 * SN * SH]).then_inc(soft, 1)
                dve.wait_ge(turned, 2)
                b3 = m.ps[2][:, 0:SN * SH].rearrange("p (n h) -> p n h", h=SH)
                dve.tensor_tensor(left[:, :, :], b3, tok[:, 1], ALU.subtract).then_inc(soft, 1)
                dve.tensor_copy(whole[:, :, :], b3).then_inc(soft, 1)

        state = sb("sd_state", [P, SH * RH])
        xdt = sb("sd_xdt", [P, SH * RH])
        xdts = sb("sd_xdts", [P, SH * RH])
        bt = sb("sd_bt", [P, SG, SC])
        cb = sb("sd_cb", [P, SG, SC])
        dec = sb("sd_dec", [P, 2, GH, SC])
        inn = sb("sd_inn", [P, 2, GH, SC])
        names = ("x_turned", "rows_kept", "cb_made", "spread", "exps", "seg", "scores", "y_made", "y_kept", "s_made", "s_kept", "s_read")
        x_turned, rows_kept, cb_made, spread, exps, seg_made, scores, y_made, y_kept, s_made, s_kept, s_read = (
            m.sem(f"sd_{x}_n") for x in names)
        h3 = lambda ap: ap.rearrange("p (h c) -> p h c", c=RH)

        with nc.Block() as block:

            @block.tensor
            def _(pe):
                for n in range(SN):
                    t = slice(n * SC, (n + 1) * SC)
                    if n:
                        pe.wait_ge(y_kept, 4 * SG * n)
                        pe.wait_ge(s_kept, 2 * SG * n)
                    for b in range(4):
                        for j in range(4):
                            ins = pe.transpose(m.ps[b][:, j * P:(j + 1) * P], p[:, 4 * b + j, t], m.ident[:, :])
                        ins.then_inc(x_turned, 1)
                    for g in range(SG):
                        ins = pe.transpose(m.ps[4][:, g * P:(g + 1) * P], p[:, S_TILES + g, t], m.ident[:, :])
                    ins.then_inc(x_turned, 1)
                    for g in range(SG):
                        ins = pe.matmul(m.ps[5][:, g * P:(g + 1) * P], p[:, S_TILES + g, t], p[:, S_TILES + SG + g, t],
                                        start=True, stop=True)
                    ins.then_inc(x_turned, 1)
                    pe.wait_ge(rows_kept, 14 * (n + 1))
                    for g in range(SG + 1):
                        if g < SG:
                            i = n * SG + g
                            if i >= 2:
                                pe.wait_ge(exps, 3 * (i - 1))
                            for h in range(GH):
                                b = 2 * (i % 2) + h // 4
                                ins = pe.matmul(m.ps[b][:, (h % 4) * SC:(h % 4 + 1) * SC],
                                                m.ident[0:SH, g * GH + h:g * GH + h + 1].to_broadcast([SH, P]), acs[:, t],
                                                start=True, stop=True)
                                if h % 4 == 3:
                                    ins.then_inc(spread, 1)
                        if g >= 1:
                            i = n * SG + g - 1
                            gp = g - 1
                            bank = m.ps[4 + i % 2]
                            pe.wait_ge(scores, 2 * (i + 1))
                            if i >= 2:
                                pe.wait_ge(y_kept, 4 * (i - 1))
                            for h in range(GH):
                                hh = gp * GH + h
                                o = bank[(h % 2) * RH:(h % 2 + 1) * RH, (h // 2) * SC:(h // 2 + 1) * SC]
                                ins = pe.matmul(o, xdt[:, hh * RH:(hh + 1) * RH], dec[:, i % 2, h, :],
                                                start=True, stop=(n == 0))
                                if n:
                                    ins = pe.matmul(o, state[:, hh * RH:(hh + 1) * RH], inn[:, i % 2, h, :],
                                                    start=False, stop=True)
                            ins.then_inc(y_made, 1)
                            if i >= 2:
                                pe.wait_ge(s_kept, 2 * (i - 1))
                            pe.matmul(m.ps[6 + i % 2][:, :], bt[:, gp, :], xdts[:, gp * 512:(gp + 1) * 512],
                                      start=True, stop=True).then_inc(s_made, 1)

            @block.scalar
            def _(act):
                for n in range(SN):
                    for g in range(SG):
                        i = n * SG + g
                        if i >= 2:
                            act.wait_ge(y_made, i - 1)
                        for b in range(2):
                            act.wait_ge(seg_made, GH * i + 4 * (b + 1))
                            bank = m.ps[2 * (i % 2) + b]
                            act.activation(inn[:, i % 2, 4 * b:4 * b + 4, :].rearrange("p h l -> p (h l)"), bank[:, :],
                                           ACT.Exp).then_inc(exps, 1)
                        act.wait_ge(seg_made, GH * (i + 1))
                        act.activation(dec[:, i % 2], dec[:, i % 2], ACT.Exp).then_inc(exps, 1)

            @block.vector
            def _(dve):
                def keep_y(i):
                    n, g = i // SG, i % SG
                    t = slice(n * SC, (n + 1) * SC)
                    bank = m.ps[4 + i % 2]
                    dve.wait_ge(y_made, i + 1)
                    for j in range(4):
                        x = p[:, 4 * g + j, t]
                        dve.scalar_tensor_tensor(out=x, in0=x, scalar=d_col[:, 4 * g + j:4 * g + j + 1],
                                                 in1=bank[:, j * SC:(j + 1) * SC], op0=ALU.mult,
                                                 op1=ALU.add).then_inc(y_kept, 1)
                    dve.wait_ge(s_made, i + 1)
                    s = state[:, g * 512:(g + 1) * 512]
                    if n == 0:
                        dve.tensor_copy(s, m.ps[6 + i % 2][:, :]).then_inc(s_kept, 2)
                    else:
                        dve.tensor_tensor(h3(s), h3(s), whole[:, n, g * GH:(g + 1) * GH].unsqueeze(2)
                                          .to_broadcast([P, GH, RH]), ALU.mult).then_inc(s_kept, 1)
                        dve.wait_ge(s_kept, 2 * i + 1)
                        dve.tensor_tensor(s, s, m.ps[6 + i % 2][:, :], ALU.add).then_inc(s_kept, 1)

                for n in range(SN):
                    if n:
                        dve.wait_ge(y_kept, 4 * SG * n)
                    for b in range(4):
                        q = slice(b * 512, (b + 1) * 512)
                        wide = lambda ap: ap[:, n, b * GH:(b + 1) * GH].unsqueeze(2).to_broadcast([P, GH, RH])
                        dve.wait_ge(x_turned, 6 * n + b + 1)
                        dve.tensor_tensor(h3(xdt[:, q]), h3(m.ps[b][:, :]), wide(tok[:, 0]), ALU.mult).then_inc(rows_kept, 1)
                        dve.wait_ge(rows_kept, 14 * n + 2 * b + 1)
                        dve.tensor_tensor(h3(xdts[:, q]), h3(xdt[:, q]), wide(left), ALU.mult).then_inc(rows_kept, 1)
                    dve.wait_ge(x_turned, 6 * n + 5)
                    dve.tensor_copy(bt[:, :, :].rearrange("p g s -> p (g s)"), m.ps[4][:, :]).then_inc(rows_kept, 1)
                    dve.wait_ge(x_turned, 6 * n + 6)
                    dve.tensor_tensor(cb[:, :, :], m.ps[5][:, :].rearrange("p (g l) -> p g l", l=SC),
                                      upto[:, :].unsqueeze(1).to_broadcast([P, SG, SC]), ALU.mult).then_inc(rows_kept, 5)
                    for g in range(SG):
                        i = n * SG + g
                        if i >= 2:
                            dve.wait_ge(y_made, i - 1)
                        for h in range(GH):
                            if h % 4 == 0:
                                dve.wait_ge(spread, 2 * i + h // 4 + 1)
                            hh = g * GH + h
                            dve.tensor_scalar(dec[:, i % 2, h, :], m.ps[2 * (i % 2) + h // 4][:, (h % 4) * SC:(h % 4 + 1) * SC],
                                              tok[:, 1, n, hh:hh + 1], 0.0, ALU.subtract, ALU.min).then_inc(seg_made, 1)
                        if g >= 1:
                            keep_y(i - 1)
                        dve.wait_ge(exps, 3 * (i + 1))
                        dve.wait_ge(rows_kept, 14 * (n + 1))
                        d = dec[:, i % 2]
                        dve.tensor_tensor(d, d, cb[:, g, :].unsqueeze(1).to_broadcast([P, GH, SC]),
                                          ALU.mult).then_inc(scores, 1)
                        dve.tensor_tensor(inn[:, i % 2], inn[:, i % 2],
                                          p[:, S_TILES + SG + g, n * SC:(n + 1) * SC].unsqueeze(1).to_broadcast([P, GH, SC]),
                                          ALU.mult).then_inc(scores, 1)
                    keep_y(n * SG + SG - 1)


def second_ssd(m, w_dt, cols, at, norms, norms_at, dt_bias, a_log, d_skip, y, projected):
    nc = m.nc
    ssd_conv(m, y, cols, at, projected[S_TILES:S_TILES + X_TILES])
    ssd(m, y, w_dt, dt_bias[0], a_log[0], d_skip[0])
    with ExitStack() as own:
        z = own.enter_context(nc.sbuf_tensor("sd_z", [P, S_TILES, T], F32))
        z_landed = [m.sem(f"sd_z_landed{j}") for j in range(SG)]
        z_silued = m.sem("sd_z_silued")
        with nc.Block() as block:

            @block.sync
            def _(sp):
                for j in range(SG):
                    sp.dma_start(z[:, 4 * j:4 * j + 4, :],
                                 projected[4 * j:4 * j + 4].rearrange("k p t -> p k t")).then_inc(z_landed[j], 16)

            @block.scalar
            def _(act):
                for j in range(SG):
                    act.wait_ge(z_landed[j], 16)
                    act.activation(z[:, 4 * j:4 * j + 4, :], z[:, 4 * j:4 * j + 4, :], ACT.Silu).then_inc(z_silued, 1)

            @block.vector
            def _(dve):
                for j in range(SG):
                    dve.wait_ge(z_silued, j + 1)
                    q = slice(4 * j, 4 * j + 4)
                    m.dve.mark(dve.tensor_tensor(y[:, q, :], y[:, q, :], z[:, q, :], ALU.mult))
    n0 = norms_at["norm_g"]
    group_norm(m, y, y, norms[:, n0:n0 + S_TILES], SG, S_TILES // SG, m.ones, D // 2)


def second_merge(m, cols, at, y, projected, w_up_rwkv, w_up_ssd, w_out, x_kept, y_kept):
    nc = m.nc
    copy_out(m, "ya_back", [(m.xT[:, :, :], y_kept)])
    with ExitStack() as own:
        sb = lambda name, shape, dt=F32: own.enter_context(nc.sbuf_tensor(name, shape, dt))
        up_a = sb("up_a", [P, KT, T])
        gates = sb("mix_gates", [P, 2 * KT, T])
        landed, made, x_back = (m.sem(f"mix_{x}") for x in ("gates_landed", "gate_sigmoid", "x_back"))

        def load_gates(block):
            @block.scalar
            def _(act):
                for j in range(4):
                    act.dma_start(gates[:, 4 * j:4 * j + 4, :],
                                  projected[4 * j:4 * j + 4].rearrange("k p t -> p k t")).then_inc(landed, 16)
                act.wait_ge(landed, 64)
                for t in range(2 * KT):
                    b = at["b_gate"] + t
                    m.act.mark(act.activation(gates[:, t, :], gates[:, t, :], ACT.Sigmoid, bias=cols[:, b:b + 1]))

        def load_x(block):
            @block.scalar
            def _(act):
                act.dma_start(m.xT[:, :, :], x_kept).then_inc(x_back, 16)
                act.wait_ge(x_back, 16)

        up_b = m.hT
        project(m, w_up_rwkv[0], KT, lambda k: m.xT[:, k, :], KT,
                lambda dve, t, bank: dve.tensor_copy(at_tile(up_a, t), bank[:, :]), other=load_gates)
        project(m, w_up_ssd[0][0:D, :], KT, lambda k: y[:, k, :], KT,
                lambda dve, t, bank: dve.tensor_copy(at_tile(up_b, t), bank[:, :]), other=load_x)
        project(m, w_up_ssd[0][D:2 * D, :], KT, lambda k: y[:, KT + k, :], KT,
                lambda dve, t, bank: dve.tensor_tensor(at_tile(up_b, t), bank[:, :], at_tile(up_b, t), ALU.add))
        with nc.Block() as block:

            @block.vector
            def _(dve):
                c = m.dve
                c.mark(dve.tensor_tensor(up_a[:, :, :], up_a[:, :, :], gates[:, 0:KT, :], ALU.mult))
                c.link(dve, dve.tensor_tensor(up_b[:, :, :], up_b[:, :, :], gates[:, KT:2 * KT, :], ALU.mult))
                c.mark(dve.tensor_tensor(up_a[:, :, :], up_a[:, :, :], up_b[:, :, :], ALU.add))

        def keep(dve, t, bank):
            return dve.tensor_tensor(at_tile(m.xT, t), bank[:, :], at_tile(m.xT, t), ALU.add)
        project(m, w_out[0], KT, lambda k: up_a[:, k, :], KT, keep)


NG = 4
EG = 8
NE = NG * EG
DE = 512
TOP = 2
EXTRA = T * TOP // P - 1
BLOCKS = NE + EXTRA


def load_router(m, own, w_rg, b_rg, w_re, b_re):
    w = own.enter_context(m.nc.sbuf_tensor("mo_w", [P, KT, NG + NE], F32))
    b = own.enter_context(m.nc.sbuf_tensor("mo_b", [P, NG + NE], F32))
    parts = []
    for src, bias, c, n in ((w_rg, b_rg, 0, NG), (w_re, b_re, NG, NE)):
        parts.append((w[:, :, c:c + n], src.rearrange("(k p) n -> p k n", p=P)))
        parts.append((b[:, c:c + n], bias.rearrange("(a n) -> a n", a=1).to_broadcast([P, n])))
    copy_out(m, "router_landed", parts)
    return w, b


def route(m, w, bias, gate, dest, extra_expert, slot_token):
    nc = m.nc
    with ExitStack() as tmp:
        sb = lambda name, shape, dt=F32: tmp.enter_context(nc.sbuf_tensor(name, shape, dt))
        logit = sb("mo_logit", [P, TT, NG + NE])
        top = sb("mo_top", [P, TT, 1])
        ex = sb("mo_ex", [P, TT, NG])
        total = sb("mo_total", [P, TT, 1])
        eq = sb("mo_eq", [P, TT, NG])
        grp = sb("mo_grp", [P, TT, 1])
        hot = sb("mo_hot", [P, TT, NG])
        mix = sb("mo_mix", [P, TT, NG, EG])
        sel = sb("mo_sel", [P, TT, EG])
        val8 = sb("mo_val8", [P, TT, 8])
        ind8 = sb("mo_ind8", [P, TT, 8], U32)
        indf = sb("mo_indf", [P, TT, 8])
        e2 = sb("mo_e2", [P, TT, 1])
        inv = sb("mo_inv", [P, TT, 1])
        expert = sb("mo_expert", [P, TT, TOP])
        mask = sb("mo_mask", [P, TT, TOP, NE])
        both = sb("mo_both", [P, TT, NE])
        rank = sb("mo_rank", [P, TT, NE])
        pick = sb("mo_pick", [P, TT, TOP, NE])
        rk = sb("mo_rk", [P, TT, TOP])
        st = sb("mo_st", [P, TT, TOP])
        over = sb("mo_over", [P, TT, TOP])
        base = sb("mo_base", [P, TT, TOP])
        count = sb("mo_count", [P, NE])
        more = sb("mo_more", [P, NE])
        tmp32 = sb("mo_tmp32", [P, NE])
        ends = sb("mo_ends", [P, NE])
        starts = sb("mo_starts", [P, NE])
        ones32 = sb("mo_ones32", [P, NE])
        down4 = sb("mo_down4", [P, NG])
        up32 = sb("mo_up32", [P, NE])
        before = sb("mo_before", [P, P])
        token = sb("mo_token", [P, TT])
        xe = sb("mo_xe", [P, EXTRA, NE])
        upx = sb("mo_upx", [P, EXTRA])
        xf = sb("mo_xf", [P, EXTRA + 1])
        zero = sb("mo_zero", [BLOCKS, P])
        logits_made, ex_made, counted, ready, dest_made = (
            m.sem(f"mo_{x}") for x in ("logits", "exps", "counted", "iotas", "dest_made"))
        zeroed, scattered = m.gathers[16:18]
        with nc.Block() as block:

            @block.gpsimd
            def _(pool):
                c = m.pool
                iota = lambda ap, pat, b, cm: c.link(pool, pool.iota(ap, pat, base=b, channel_multiplier=cm,
                                                                     allow_small_or_imprecise_dtypes=True))
                c.link(pool, pool.memset(zero[:, :], 0.0))
                iota(down4[:, :], [[-1, NG]], NG, 0)
                iota(up32[:, :], [[1, NE]], 0, 0)
                iota(upx[:, :], [[1, EXTRA]], 0, 0)
                iota(token[:, :], [[P, TT]], 0, 1)
                c.link(pool, pool.memset(ones32[:, :], 1.0))
                c.link(pool, pool.memset(before[:, :], 1.0))
                pool.affine_select(out=before[:, :], in_=before[:, :], compare_op=ALU.is_gt, fill=0.0, base=0,
                                   pattern=[[1, P]], channel_multiplier=-1).then_inc(ready, 1)
                pool.wait_ge(ready, 1)
                pool.dma_start(slot_token, zero[:, :]).then_inc(zeroed, 16)
                pool.wait_ge(zeroed, 16)
                pool.wait_ge(dest_made, 1)
                for t in range(TT):
                    for j in range(TOP):
                        n = t * TOP + j
                        pool.indirect_dma_start(
                            out=slot_token.rearrange("b (s a) -> (b s) a", a=1),
                            out_offset=bass.IndirectOffsetOnAxis(ap=dest[:, n:n + 1], axis=0),
                            in_=token[:, t:t + 1], in_offset=None).then_inc(scattered, 16)
                pool.wait_ge(scattered, 16 * TT * TOP)

            @block.tensor
            def _(pe):
                for t in range(TT):
                    for k in range(KT):
                        ins = pe.matmul(m.ps[0][:, t * 64:t * 64 + NG + NE], m.hT[:, k, t * P:(t + 1) * P], w[:, k, :],
                                        start=(k == 0), stop=(k == KT - 1))
                ins.then_inc(logits_made, 1)
                pe.wait_ge(ready, 1)
                pe.wait_ge(counted, 1)
                for t in range(TT):
                    for u in range(t + 1):
                        ins = pe.matmul(m.ps[1][:, t * NE:(t + 1) * NE], (before if u == t else m.ones)[:, :], both[:, u, :],
                                        start=(u == 0), stop=(u == t))
                for u in range(TT):
                    ins = pe.matmul(m.ps[2][:, 0:NE], m.ones[:, :], both[:, u, :], start=(u == 0), stop=(u == TT - 1))
                ins.then_inc(counted, 1)

            @block.scalar
            def _(act):
                act.wait_ge(ex_made, 1)
                act.activation(ex[:, :, :], ex[:, :, :], ACT.Exp).then_inc(ex_made, 1)
                act.wait_ge(ex_made, 3)
                act.activation(e2[:, :, :], e2[:, :, :], ACT.Exp).then_inc(ex_made, 1)

            @block.vector
            def _(dve):
                c = m.dve
                L = lambda ins: c.link(dve, ins)
                bc = lambda ap, shape: ap.to_broadcast(shape)
                dve.wait_ge(ready, 1)
                dve.wait_ge(logits_made, 1)
                b3 = m.ps[0][:, 0:TT * 64].rearrange("p (t n) -> p t n", n=64)[:, :, 0:NG + NE]
                L(dve.tensor_tensor(logit[:, :, :], b3, bias[:, :].unsqueeze(1).to_broadcast([P, TT, NG + NE]), ALU.add))
                g, e = logit[:, :, 0:NG], logit[:, :, NG:NG + NE]
                L(dve.tensor_reduce(top[:, :, :], g, AX.X, ALU.max))
                dve.tensor_tensor(ex[:, :, :], g, bc(top[:, :, :], [P, TT, NG]), ALU.subtract).then_inc(ex_made, 1)
                L(dve.tensor_tensor(eq[:, :, :], g, bc(top[:, :, :], [P, TT, NG]), ALU.is_equal))
                L(dve.tensor_tensor(eq[:, :, :], eq[:, :, :], down4[:, :].unsqueeze(1).to_broadcast([P, TT, NG]), ALU.mult))
                L(dve.tensor_reduce(grp[:, :, :], eq[:, :, :], AX.X, ALU.max))
                L(dve.tensor_tensor(hot[:, :, :], down4[:, :].unsqueeze(1).to_broadcast([P, TT, NG]),
                                    bc(grp[:, :, :], [P, TT, NG]), ALU.is_equal))
                L(dve.tensor_scalar(grp[:, :, :], grp[:, :, :], -1.0, float(NG), ALU.mult, ALU.add))
                L(dve.tensor_tensor(mix[:, :, :, :], e.rearrange("p t (g n) -> p t g n", n=EG),
                                    hot[:, :, :].unsqueeze(3).to_broadcast([P, TT, NG, EG]), ALU.mult))
                L(dve.tensor_reduce(sel[:, :, :], mix[:, :, :, :].rearrange("p t g n -> p t n g"), AX.X, ALU.add))
                for t in range(TT):
                    c.mark(dve.max(val8[:, t, :], sel[:, t, :]))
                c.wait(dve)
                for t in range(TT):
                    c.mark(dve.max_index(ind8[:, t, :], val8[:, t, :], sel[:, t, :]))
                dve.wait_ge(ex_made, 2)
                dve.tensor_tensor(e2[:, :, :], val8[:, :, 1:2], val8[:, :, 0:1], ALU.subtract).then_inc(ex_made, 1)
                L(dve.tensor_reduce(total[:, :, :], ex[:, :, :], AX.X, ALU.add))
                L(dve.tensor_copy(indf[:, :, :], ind8[:, :, :]))
                dve.wait_ge(ex_made, 4)
                L(dve.tensor_scalar(inv[:, :, :], e2[:, :, :], 1.0, None, ALU.add))
                L(dve.tensor_tensor(inv[:, :, :], inv[:, :, :], total[:, :, :], ALU.mult))
                L(dve.reciprocal(inv[:, :, :], inv[:, :, :]))
                g3 = gate[:, :].rearrange("p (t j) -> p t j", j=TOP)
                c.mark(dve.tensor_copy(g3[:, :, 0:1], inv[:, :, :]))
                c.mark(dve.tensor_tensor(g3[:, :, 1:2], inv[:, :, :], e2[:, :, :], ALU.mult))
                L(dve.scalar_tensor_tensor(out=expert[:, :, 0:1], in0=grp[:, :, :], scalar=float(EG), in1=indf[:, :, 0:1],
                                           op0=ALU.mult, op1=ALU.add))
                L(dve.scalar_tensor_tensor(out=expert[:, :, 1:2], in0=grp[:, :, :], scalar=float(EG), in1=indf[:, :, 1:2],
                                           op0=ALU.mult, op1=ALU.add))
                for j in range(TOP):
                    c.mark(dve.tensor_tensor(mask[:, :, j, :], up32[:, :].unsqueeze(1).to_broadcast([P, TT, NE]),
                                             bc(expert[:, :, j:j + 1], [P, TT, NE]), ALU.is_equal))
                c.wait(dve)
                dve.tensor_tensor(both[:, :, :], mask[:, :, 0, :], mask[:, :, 1, :], ALU.add).then_inc(counted, 1)
                dve.wait_ge(counted, 2)
                c.mark(dve.tensor_copy(rank[:, :, :], m.ps[1][:, 0:TT * NE].rearrange("p (t n) -> p t n", n=NE)))
                L(dve.tensor_copy(count[:, :], m.ps[2][:, 0:NE]))
                L(dve.tensor_scalar(more[:, :], count[:, :], float(P), None, ALU.is_gt))
                for q in range(2, T // P):
                    L(dve.tensor_scalar(tmp32[:, :], count[:, :], float(q * P), None, ALU.is_gt))
                    L(dve.tensor_tensor(more[:, :], more[:, :], tmp32[:, :], ALU.add))
                L(dve.tensor_tensor_scan(ends[:, :], ones32[:, :], more[:, :], 0.0, ALU.mult, ALU.add))
                L(dve.tensor_tensor(starts[:, :], ends[:, :], more[:, :], ALU.subtract))
                L(dve.tensor_tensor(xe[:, :, :], ends[:, :].unsqueeze(1).to_broadcast([P, EXTRA, NE]),
                                    upx[:, :].unsqueeze(2).to_broadcast([P, EXTRA, NE]), ALU.is_le))
                L(dve.tensor_reduce(xf[:, 0:EXTRA], xe[:, :, :], AX.X, ALU.add))
                L(dve.tensor_scalar(xf[:, 0:EXTRA], xf[:, 0:EXTRA], float(NE - 1), None, ALU.min))
                L(dve.tensor_copy(xf[:, EXTRA:EXTRA + 1], ends[:, NE - 1:NE]))
                L(dve.tensor_copy(extra_expert[:, :], xf[:, :]))
                for dst, src in ((rk, rank[:, :, :]), (st, starts[:, :].unsqueeze(1).to_broadcast([P, TT, NE]))):
                    for j in range(TOP):
                        c.mark(dve.tensor_tensor(pick[:, :, j, :], mask[:, :, j, :], src, ALU.mult))
                    c.wait(dve)
                    L(dve.tensor_reduce(dst[:, :, :], pick[:, :, :, :], AX.X, ALU.add))
                L(dve.tensor_scalar(over[:, :, :], rk[:, :, :], float(P), None, ALU.is_ge))
                L(dve.tensor_scalar(expert[:, :, :], expert[:, :, :], float(P), None, ALU.mult))
                L(dve.tensor_scalar(base[:, :, :], st[:, :, :], float(P), float((NE - 1) * P), ALU.mult, ALU.add))
                L(dve.tensor_tensor(base[:, :, :], base[:, :, :], expert[:, :, :], ALU.subtract))
                L(dve.tensor_tensor(base[:, :, :], base[:, :, :], over[:, :, :], ALU.mult))
                L(dve.tensor_tensor(base[:, :, :], base[:, :, :], expert[:, :, :], ALU.add))
                dve.tensor_tensor(dest[:, :], base[:, :, :].rearrange("p t j -> p (t j)"),
                                  rk[:, :, :].rearrange("p t j -> p (t j)"), ALU.add).then_inc(dest_made, 1)


def slot_columns(m, slot_token, columns):
    nc = m.nc
    landed, turned = m.sem("slots_landed"), m.sem("slots_turned")
    with ExitStack() as own:
        rows = own.enter_context(nc.sbuf_tensor("slot_rows", [BLOCKS, P], F32))
        with nc.Block() as block:

            @block.sync
            def _(sp):
                sp.dma_start(rows[:, :], slot_token).then_inc(landed, 16)

            @block.tensor
            def _(pe):
                pe.wait_ge(landed, 16)
                pe.transpose(m.ps[0][:, 0:BLOCKS], rows[:, :], m.ident[0:BLOCKS, 0:BLOCKS]).then_inc(turned, 1)

            @block.vector
            def _(dve):
                dve.wait_ge(turned, 1)
                m.dve.mark(dve.memset(columns[:, BLOCKS:BLOCKS + 1], 0))
                m.dve.mark(dve.tensor_copy(columns[:, 0:BLOCKS], m.ps[0][:, 0:BLOCKS]))


def wait(eng, sem, value):
    if not isinstance(value, int) or value > 0:
        eng.wait_ge(sem, value)


class Experts:

    def __init__(self, m, tag, w_gate, w_up, w_down, h_rows, y_rows, bufs, x_landed):
        self.m, self.h_rows, self.y_rows = m, h_rows, y_rows
        self.w = (w_gate.rearrange("e (p k) n -> e p (k n)", k=KT), w_up.rearrange("e (p k) n -> e p (k n)", k=KT),
                  w_down.rearrange("e (p k) n -> e p (k n)", k=DE // P))
        self.gu, self.dn, self.xr, self.xT, self.hs, self.hid, self.hidT, self.yb, self.now = bufs
        sem = lambda x: m.sem(f"{tag}_{x}")
        self.w_landed = [[sem(f"w{j}_landed{s}") for s in range(2)] for j in range(3)]
        self.x_landed = x_landed
        self.y_stored = [sem(f"y_stored{s}") for s in range(2)]
        (self.index_set, self.x_turned, self.x_kept_act, self.x_kept_dve, self.g_made, self.u_made, self.silu_made,
         self.h_made, self.h_turned, self.h_kept, self.y_made, self.y_kept) = (sem(x) for x in (
             "index_set", "x_turned", "x_kept_act", "x_kept_dve", "g_made", "u_made", "silu_made", "h_made", "h_turned",
             "h_kept", "y_made", "y_kept"))

    def load(self, sp, e, n, s, reuse=True):
        for j, (done, k) in enumerate(((self.g_made, 1), (self.u_made, 1), (self.y_made, 2))):
            if reuse:
                wait(sp, done, k * (n - 1))
            dst = self.gu[:, s, j, :] if j < 2 else self.dn[:, s, :]
            src = self.w[j][e] if isinstance(e, int) else self.w[j][bass.ds(e, 1)].rearrange("a p n -> p (a n)")
            sp.dma_start(dst, src).then_inc(self.w_landed[j][s], 16)

    def gather(self, pool, columns, n, slot, s, reuse=True):
        wait(pool, self.index_set, n + 1)
        if reuse:
            wait(pool, self.x_turned, 2 * (n - 1))
        pool.tensor_copy(self.now[:, (slot + 1) % 4:(slot + 1) % 4 + 1],
                         columns[:, bass.ds(n + 1, 1)]).then_inc(self.index_set, 1)
        pool.indirect_dma_start(out=self.xr[:, s, :], out_offset=None, in_=self.h_rows,
                                in_offset=bass.IndirectOffsetOnAxis(ap=self.now[:, slot:slot + 1], axis=0)
                                ).then_inc(self.x_landed[s], 16)

    def turn_x(self, pe, n, s, u):
        m = self.m
        wait(pe, self.x_landed[s], 16 * (u + 1))
        wait(pe, self.x_kept_act, n)
        wait(pe, self.x_kept_dve, n)
        for b in range(2):
            for j in range(4):
                k = 4 * b + j
                ins = pe.transpose(m.ps[b][:, j * P:(j + 1) * P], self.xr[:, s, k:D:KT], m.ident[:, :])
            ins.then_inc(self.x_turned, 1)

    def up(self, pe, n, s, u):
        m = self.m
        wait(pe, self.x_kept_act, n + 1)
        wait(pe, self.x_kept_dve, n + 1)
        wait(pe, self.h_made, n)
        for j, made in enumerate((self.g_made, self.u_made)):
            wait(pe, self.w_landed[j][s], 16 * (u + 1))
            for k in range(KT):
                ins = pe.matmul(m.ps[2 + j][:, :], self.xT[:, k, :], self.gu[:, s, j, k * DE:(k + 1) * DE],
                                start=(k == 0), stop=(k == KT - 1))
            ins.then_inc(made, 1)

    def down(self, pe, n, s, u):
        m = self.m
        wait(pe, self.h_made, n + 1)
        wait(pe, self.h_kept, n)
        for k in range(DE // P):
            ins = pe.transpose(m.ps[4][:, k * P:(k + 1) * P], self.hid[:, k:DE:DE // P], m.ident[:, :])
        ins.then_inc(self.h_turned, 1)
        wait(pe, self.h_kept, n + 1)
        wait(pe, self.y_kept, 2 * n)
        wait(pe, self.w_landed[2][s], 16 * (u + 1))
        for b in range(2):
            for k in range(DE // P):
                ins = pe.matmul(m.ps[5 + b][:, :], self.hidT[:, k, :], self.dn[:, s, k * D + b * 512:k * D + b * 512 + 512],
                                start=(k == 0), stop=(k == DE // P - 1))
            ins.then_inc(self.y_made, 1)

    def act_x(self, act, n):
        wait(act, self.x_turned, 2 * n + 1)
        act.copy(self.xT[:, 0:4, :].rearrange("p k r -> p (k r)"), self.m.ps[0][:, :]).then_inc(self.x_kept_act, 1)

    def act_silu(self, act, n):
        wait(act, self.h_made, n)
        wait(act, self.g_made, n + 1)
        act.activation(self.hs[:, :], self.m.ps[2][:, :], ACT.Silu).then_inc(self.silu_made, 1)

    def act_down(self, act, n, s, u, row):
        wait(act, self.y_stored[s], 16 * u)
        for b in range(2):
            wait(act, self.y_made, 2 * n + b + 1)
            act.copy(self.yb[:, s, b * 512:(b + 1) * 512], self.m.ps[5 + b][:, :]).then_inc(self.y_kept, 1)
        wait(act, self.y_kept, 2 * n + 2)
        act.dma_start(self.y_rows[bass.ds(row, P), :], self.yb[:, s, :]).then_inc(self.y_stored[s], 16)

    def dve_x(self, dve, n):
        wait(dve, self.x_turned, 2 * n + 2)
        dve.tensor_copy(self.xT[:, 4:8, :].rearrange("p k r -> p (k r)"), self.m.ps[1][:, :]).then_inc(self.x_kept_dve, 1)

    def dve_hidden(self, dve, n):
        wait(dve, self.h_turned, n)
        wait(dve, self.silu_made, n + 1)
        wait(dve, self.u_made, n + 1)
        dve.tensor_tensor(self.hid[:, :], self.hs[:, :], self.m.ps[3][:, :], ALU.mult).then_inc(self.h_made, 1)

    def dve_down(self, dve, n):
        wait(dve, self.h_turned, n + 1)
        dve.tensor_copy(self.hidT[:, :, :].rearrange("p k r -> p (k r)"), self.m.ps[4][:, :]).then_inc(self.h_kept, 1)


def run_experts(m, w_gate, w_up, w_down, columns, extra_expert, h_rows, y_rows):
    nc = m.nc
    with ExitStack() as own:
        sb = lambda name, shape, dt=F32: own.enter_context(nc.sbuf_tensor(name, shape, dt))
        bufs = (sb("xp_gu", [P, 2, 2, KT * DE]), sb("xp_dn", [P, 2, (DE // P) * D]), sb("xp_xr", [P, 2, D]),
                sb("xp_xT", [P, KT, P]), sb("xp_hs", [P, DE]), sb("xp_hid", [P, DE]), sb("xp_hidT", [P, DE // P, P]),
                sb("xp_yb", [P, 2, D]), sb("xp_now", [P, 4], U32))
        x = Experts(m, "xp", w_gate, w_up, w_down, h_rows, y_rows, bufs, m.gathers[18:20])
        zero = sb("xp_zero", [P, D])
        zero_set, zero_stored = m.sem("xp_zero_set"), m.sem("xp_zero_stored")
        with nc.Block() as block:

            @block.sync
            def _(sp):
                x.load(sp, 0, 0, 0, reuse=False)
                x.load(sp, 1, 1, 1, reuse=False)
                sp.wait_ge(zero_set, 1)
                for q in range(EXTRA):
                    sp.dma_start(y_rows[(NE + q) * P:(NE + q + 1) * P, :], zero[:, :]).then_inc(zero_stored, 16)
                with sp.Fori(1, NE // 2) as i:
                    for s in range(2):
                        x.load(sp, 2 * i + s, 2 * i + s, s)
                sp.wait_ge(zero_stored, 16 * EXTRA)

            @block.gpsimd
            def _(pool):
                pool.tensor_copy(x.now[:, 0:1], columns[:, 0:1]).then_inc(x.index_set, 1)
                for e in range(4):
                    x.gather(pool, columns, e, e, e % 2, reuse=(e >= 2))
                with pool.Fori(1, NE // 4) as i:
                    for b in range(4):
                        x.gather(pool, columns, 4 * i + b, b, b % 2)

            @block.tensor
            def _(pe):
                def step(e, s, u, u1):
                    x.up(pe, e, s, u)
                    x.turn_x(pe, e + 1, 1 - s, u1)
                    x.down(pe, e - 1, 1 - s, u1 - 1)

                def turn(i):
                    step(2 * i + 1, 1, i, i + 1)
                    step(2 * i + 2, 0, i + 1, i + 1)

                x.turn_x(pe, 0, 0, 0)
                x.up(pe, 0, 0, 0)
                x.turn_x(pe, 1, 1, 0)
                turn(0)
                with pe.Fori(1, NE // 2 - 1) as i:
                    turn(i)
                last = NE // 2 - 1
                x.up(pe, NE - 1, 1, last)
                x.down(pe, NE - 2, 0, last)
                x.down(pe, NE - 1, 1, last)

            @block.scalar
            def _(act):
                def turn(i):
                    for s in range(2):
                        e = 2 * i + s
                        x.act_silu(act, e + 1)
                        x.act_x(act, e + 2)
                        x.act_down(act, e, s, i, (2 * P) * i + s * P)

                x.act_x(act, 0)
                x.act_silu(act, 0)
                x.act_x(act, 1)
                turn(0)
                with act.Fori(1, NE // 2 - 1) as i:
                    turn(i)
                last = NE // 2 - 1
                x.act_silu(act, NE - 1)
                x.act_down(act, NE - 2, 0, last, (NE - 2) * P)
                x.act_down(act, NE - 1, 1, last, (NE - 1) * P)
                for s in range(2):
                    act.wait_ge(x.y_stored[s], 16 * (NE // 2))

            @block.vector
            def _(dve):
                dve.memset(zero[:, :], 0.0).then_inc(zero_set, 1)
                x.dve_x(dve, 0)
                x.dve_hidden(dve, 0)
                x.dve_x(dve, 1)
                with dve.Fori(0, NE // 2 - 1) as i:
                    for s in range(2):
                        e = 2 * i + s
                        x.dve_x(dve, e + 2)
                        x.dve_down(dve, e)
                        x.dve_hidden(dve, e + 1)
                x.dve_down(dve, NE - 2)
                x.dve_hidden(dve, NE - 1)
                x.dve_down(dve, NE - 1)

        y = Experts(m, "xq", w_gate, w_up, w_down, h_rows, y_rows, bufs, m.gathers[20:22])
        some = lambda eng: eng.value_load(extra_expert[0:1, EXTRA:EXTRA + 1], min_val=0, max_val=EXTRA)
        with nc.Block() as block:

            @block.sync
            def _(sp):
                experts = [sp.value_load(extra_expert[0:1, q:q + 1], min_val=0, max_val=NE - 1) for q in range(EXTRA)]
                with sp.If(some(sp) > 0):
                    for q in range(EXTRA):
                        y.load(sp, experts[q], q, q % 2, reuse=(q >= 2))

            @block.gpsimd
            def _(pool):
                with pool.If(some(pool) > 0):
                    for q in range(EXTRA):
                        if q >= 2:
                            pool.wait_ge(y.x_turned, 2 * (q - 1))
                        pool.indirect_dma_start(
                            out=y.xr[:, q % 2, :], out_offset=None, in_=h_rows,
                            in_offset=bass.IndirectOffsetOnAxis(ap=columns[:, NE + q:NE + q + 1], axis=0)
                        ).then_inc(y.x_landed[q % 2], 16)

            @block.tensor
            def _(pe):
                with pe.If(some(pe) > 0):
                    for q in range(EXTRA):
                        y.turn_x(pe, q, q % 2, q // 2)
                        y.up(pe, q, q % 2, q // 2)
                        y.down(pe, q, q % 2, q // 2)

            @block.scalar
            def _(act):
                with act.If(some(act) > 0):
                    for q in range(EXTRA):
                        y.act_x(act, q)
                        y.act_silu(act, q)
                        y.act_down(act, q, q % 2, q // 2, (NE + q) * P)
                    for s in range(2):
                        act.wait_ge(y.y_stored[s], 16 * ((EXTRA + 1 - s) // 2))

            @block.vector
            def _(dve):
                with dve.If(some(dve) > 0):
                    for q in range(EXTRA):
                        y.dve_x(dve, q)
                        y.dve_hidden(dve, q)
                        y.dve_down(dve, q)


def combine(m, gate, dest, x_rows, y_rows, final_norm_g, out):
    nc = m.nc
    with ExitStack() as own:
        sb = lambda name, shape, dt=F32: own.enter_context(nc.sbuf_tensor(name, shape, dt))
        r = sb("cb_r", [P, TT, TOP, D])
        g = sb("cb_g", [P, D])
        sq = sb("cb_sq", [P, D])
        eps = sb("cb_eps", [P, 1])
        mean = sb("cb_mean", [P, TT])
        root = sb("cb_root", [P, TT])
        inv = sb("cb_inv", [P, TT])
        landed = m.gathers[22:22 + TT]
        g_landed, eps_set, summed, squared, rooted, made, stored = (
            m.sem(f"cb_{x}") for x in ("g_landed", "eps_set", "summed", "squared", "rooted", "made", "stored"))
        with nc.Block() as block:

            @block.gpsimd
            def _(pool):
                for t in range(TT):
                    for j in range(TOP):
                        n = t * TOP + j
                        pool.indirect_dma_start(
                            out=r[:, t, j, :], out_offset=None, in_=y_rows,
                            in_offset=bass.IndirectOffsetOnAxis(ap=dest[:, n:n + 1], axis=0)).then_inc(landed[t], 16)

            @block.sync
            def _(sp):
                sp.dma_start(g[:, :], final_norm_g.rearrange("(a n) -> a n", a=1).to_broadcast([P, D])).then_inc(g_landed, 16)
                for t in range(TT):
                    sp.wait_ge(made, t + 1)
                    sp.dma_start(out[t * P:(t + 1) * P, :], x_rows[:, t, :]).then_inc(stored, 16)
                sp.wait_ge(stored, 16 * TT)

            @block.scalar
            def _(act):
                act.wait_ge(eps_set, 1)
                for t in range(TT):
                    act.wait_ge(summed, t + 1)
                    if t:
                        act.wait_ge(squared, t)
                    act.activation(sq[:, :], x_rows[:, t, :], ACT.Square, accum_out=mean[:, t:t + 1]).then_inc(squared, 1)
                act.wait_ge(squared, TT)
                act.activation(root[:, :], mean[:, :], ACT.Sqrt, scale=1.0 / D, bias=eps[:, :]).then_inc(rooted, 1)

            @block.vector
            def _(dve):
                c = m.dve
                dve.memset(eps[:, :], EPS).then_inc(eps_set, 1)
                for t in range(TT):
                    dve.wait_ge(landed[t], 16 * TOP)
                    for j in range(TOP):
                        n = t * TOP + j
                        ins = dve.scalar_tensor_tensor(out=x_rows[:, t, :], in0=r[:, t, j, :], scalar=gate[:, n:n + 1],
                                                       in1=x_rows[:, t, :], op0=ALU.mult, op1=ALU.add)
                        if j < TOP - 1:
                            c.link(dve, ins)
                    ins.then_inc(summed, 1)
                dve.wait_ge(g_landed, 16)
                dve.wait_ge(rooted, 1)
                c.link(dve, dve.reciprocal(inv[:, :], root[:, :]))
                for t in range(TT):
                    dve.scalar_tensor_tensor(out=x_rows[:, t, :], in0=x_rows[:, t, :], scalar=inv[:, t:t + 1], in1=g[:, :],
                                             op0=ALU.mult, op1=ALU.mult).then_inc(made, 1)


def second_experts(m, norm_col, w_rg, b_rg, w_re, b_re, w_gate, w_up, w_down, final_norm_g, h_kept, slot_token, y_rows, out):
    nc = m.nc
    norm(m, m.xT, m.hT, norm_col)
    with ExitStack() as own:
        sb = lambda name, shape, dt=F32: own.enter_context(nc.sbuf_tensor(name, shape, dt))
        gate = sb("mo_gate", [P, TT * TOP])
        dest = sb("mo_dest", [P, TT * TOP], U32)
        extra_expert = sb("mo_extra_expert", [P, EXTRA + 1], I32)
        columns = sb("mo_columns", [P, BLOCKS + 1], U32)
        with ExitStack() as own2:
            w, bias = load_router(m, own2, w_rg, b_rg, w_re, b_re)
            route(m, w, bias, gate, dest, extra_expert, slot_token)
            slot_columns(m, slot_token, columns)
        rows = m.hT[:, :, :].rearrange("p k t -> p (k t)").rearrange("p (t d) -> p t d", t=TT)
        with ExitStack() as own2:
            h_rows = own2.enter_context(nc.sbuf_tensor("mo_h_rows", [P, TT, D], F32))
            turn_back(m, m.hT, h_rows, "h4")
            copy_out(m, "h_stored", [(h_kept.rearrange("(t p) d -> p t d", p=P), h_rows[:, :, :])])
        turn_back(m, m.xT, rows, "x4")
        run_experts(m, w_gate, w_up, w_down, columns, extra_expert, h_kept, y_rows)
        combine(m, gate, dest, rows, y_rows, final_norm_g, out)


def two_blocks(nc, x, c, w_ada, b_ada, norm1_w, w_in, hgrn_lb_logits, hgrn_onorm_w, conv_w, conv_onorm_w, w_out, norm2_w,
               peer_w_query, peer_sub_keys, peer_u, peer_v, final_norm_w, attn_norm_g_2, w_in_2, b_gate_2, rwkv_mu_2,
               rwkv_w0_2, rwkv_w_decay_2, rwkv_a0_2, rwkv_w_a_2, rwkv_w_g_2, rwkv_k_k_2, rwkv_k_a_2, rwkv_r_k_2, rwkv_ln_g_2,
               rwkv_ln_b_2, w_up_rwkv_2, ssd_conv_w_2, ssd_conv_b_2, ssd_dt_bias_2, ssd_a_log_2, ssd_d_2, ssd_norm_g_2,
               w_up_ssd_2, w_out_2, ffn_norm_g_2, w_router_group_2, b_router_group_2, w_router_expert_2, b_router_expert_2,
               w_exp_gate_2, w_exp_up_2, w_exp_down_2, final_norm_g_2, out):
    row = lambda ap: ap.rearrange("(k p) -> k p", p=P)
    kept = lambda name, shape: nc.dram_tensor(name, shape, F32, kind="Internal").ap()
    with ExitStack() as ctx:
        m = setup(nc, ctx)
        constants(m)
        with stage(m):
            cols, at = first_mixer(m, x, c, w_ada, b_ada, norm1_w, w_in, hgrn_lb_logits, hgrn_onorm_w, conv_w,
                                   conv_onorm_w, w_out, norm2_w, final_norm_w)
            first_experts(m, peer_w_query, peer_sub_keys, peer_u, peer_v, cols, at)
        with stage(m):
            x_kept, y_kept = kept("x_kept", [P, KT, T]), kept("ya_kept", [P, KT, T])
            cols, at = second_columns(m, attn_norm_g_2, rwkv_mu_2, rwkv_w0_2, rwkv_a0_2, rwkv_k_k_2, rwkv_k_a_2,
                                      rwkv_r_k_2, rwkv_ln_g_2, rwkv_ln_b_2)
            c0 = 3 * D + 2 * P
            dt0 = c0 + (S_TILES + X_TILES) * P
            projected = kept("projected", [RN * Spare.TILES, P, T])
            spare = Spare(m, w_in_2[0], c0, dt0 + SH, projected, kept("h_kept2", [P, KT, T]),
                          kept("bonus_kept", [P, KT, T]))
            second_rwkv(m, w_in_2, cols, at, rwkv_w_decay_2, rwkv_w_a_2, rwkv_w_g_2, x_kept, y_kept, spare)
        with stage(m):
            cols3, at3 = column_rows(m, "cols3", [
                ("conv", ssd_conv_w_2[0].rearrange("j (k p) -> (j k) p", p=P)), ("conv_b", row(ssd_conv_b_2[0]))])
            cols4, at4 = column_rows(m, "cols4", [
                ("norm_g", row(ssd_norm_g_2[0])), ("b_gate", row(b_gate_2[0])), ("ffn_norm", row(ffn_norm_g_2[0]))])
            with ExitStack() as own:
                y = own.enter_context(nc.sbuf_tensor("ssd_y", [P, X_TILES, T], F32))
                second_ssd(m, w_in_2[0][:, dt0:dt0 + SH], cols3, at3, cols4, at4, ssd_dt_bias_2, ssd_a_log_2, ssd_d_2, y,
                           projected)
                second_merge(m, cols4, at4, y, projected[S_TILES + X_TILES:], w_up_rwkv_2, w_up_ssd_2, w_out_2, x_kept,
                             y_kept)
            second_experts(m, cols4[:, at4["ffn_norm"]:at4["ffn_norm"] + KT], w_router_group_2[0], b_router_group_2[0],
                           w_router_expert_2[0], b_router_expert_2[0], w_exp_gate_2[0], w_exp_up_2[0], w_exp_down_2[0],
                           final_norm_g_2, kept("h_kept", [T, D]), kept("slot_token", [BLOCKS, P]),
                           kept("y_rows", [BLOCKS * P, D]), out[0])


_INS = ['x', 'c', 'w_ada', 'b_ada', 'norm1_w', 'w_in', 'hgrn_lb_logits', 'hgrn_onorm_w', 'conv_w',
        'conv_onorm_w', 'w_out', 'norm2_w', 'peer_w_query', 'peer_sub_keys', 'peer_u', 'peer_v', 'final_norm_w',
        'attn_norm_g_2', 'w_in_2', 'b_gate_2', 'rwkv_mu_2', 'rwkv_w0_2', 'rwkv_w_decay_2', 'rwkv_a0_2',
        'rwkv_w_a_2', 'rwkv_w_g_2', 'rwkv_k_k_2', 'rwkv_k_a_2', 'rwkv_r_k_2', 'rwkv_ln_g_2', 'rwkv_ln_b_2',
        'w_up_rwkv_2', 'ssd_conv_w_2', 'ssd_conv_b_2', 'ssd_dt_bias_2', 'ssd_a_log_2', 'ssd_d_2', 'ssd_norm_g_2',
        'w_up_ssd_2', 'w_out_2', 'ffn_norm_g_2', 'w_router_group_2', 'b_router_group_2', 'w_router_expert_2',
        'b_router_expert_2', 'w_exp_gate_2', 'w_exp_up_2', 'w_exp_down_2', 'final_norm_g_2']


def kernel(**inputs):
    import numpy as _np
    import concourse.bacc as _bacc
    from concourse import mybir as _mybir
    from concourse.bass_utils import run_bass_kernel_spmd as _run

    nc = _bacc.Bacc("TRN2", target_bir_lowering=False, num_devices=1)
    arrays, args = {}, []
    for name in _INS:
        a = _np.ascontiguousarray(inputs[name])
        arrays[f"in_{name}_dram"] = a
        args.append(nc.dram_tensor(f"in_{name}_dram", a.shape, _mybir.dt.from_np(a.dtype), kind="ExternalInput").ap())
    out = nc.dram_tensor("out_0_dram", (1, T, D), F32, kind="ExternalOutput").ap()
    two_blocks(nc, *args, out)
    r = _run(nc, [arrays], core_ids=[0])
    return r.results[0]["out_0_dram"]
```

```python
from contextlib import ExitStack, contextmanager

import concourse.bass as bass
from concourse import mybir

P = 128
F32 = mybir.dt.float32
I32 = mybir.dt.int32
U32 = mybir.dt.uint32
ALU = mybir.AluOpType
ACT = mybir.ActivationFunctionType
AX = mybir.AxisListType
EPS = 1e-6

T = 512
D = 1024
KT = D // P
TT = T // P
HG = 4
HC = 128
CG = 4
HGRN_LEVELS = 7
SLOTS = 4
SLOT_COLS = 256


class Chain:

    def __init__(self, sem):
        self.sem = sem
        self.n = 0
        self.off = 0

    def link(self, eng, ins):
        self.mark(ins)
        self.wait(eng)

    def mark(self, ins):
        ins.then_inc(self.sem, 1)
        self.n += 1

    def wait(self, eng):
        eng.wait_ge(self.sem, self.off + self.n)

    def enter(self, i, steps):
        self.base = self.n
        self.steps = steps
        self.off = i * steps

    def leave(self, turns):
        assert self.n - self.base == self.steps, (self.n, self.base, self.steps)
        self.off = 0
        self.n = self.base + self.steps * turns


class Mem:
    pass


def setup(nc, ctx):
    m = Mem()
    m.nc = nc
    m.ctx = ctx
    m.ps = [ctx.enter_context(nc.psum_tensor(f"bank{i}", [P, 512], F32)) for i in range(8)]
    m.sem = lambda name: ctx.enter_context(nc.semaphore(name))
    m.dve = Chain(m.sem("dve_steps"))
    m.act = Chain(m.sem("act_steps"))
    m.pool = Chain(m.sem("pool_steps"))
    m.pe = Chain(m.sem("pe_steps"))
    sb = lambda name, shape, dt=F32: ctx.enter_context(nc.sbuf_tensor(name, shape, dt))
    m.sb = sb
    m.gathers = [m.sem(f"gathered{s}") for s in range(26)]
    m.ready = m.sem("constants_ready")
    m.ident = sb("ident", [P, P])
    m.ones = sb("ones", [P, P])
    m.half_ones = sb("half_ones", [P, P])
    m.weights = sb("weights", [P, SLOTS, KT, SLOT_COLS])
    m.xT = sb("xT", [P, KT, T])
    m.hT = sb("hT", [P, KT, T])
    m.w_landed = [m.sem(f"w_landed{i}") for i in range(SLOTS)]
    m.w_landed_n = [0] * SLOTS
    m.tile_made = m.sem("tile_made")
    m.tile_made_n = 0
    m.tile_kept = m.sem("tile_kept")
    m.tile_kept_n = 0
    m.ahead = 0
    m.sq_made = m.sem("sq_made")
    m.sq_made_n = 0
    m.sq_summed = m.sem("sq_summed")
    m.sq_summed_n = 0
    m.rstd_made = m.sem("rstd_made")
    m.rstd_made_n = 0
    m.scaled = m.sem("scaled")
    m.scaled_n = 0
    m.spread = m.sem("spread")
    m.spread_n = 0
    return m


@contextmanager
def stage(m):
    nc, outer, taken = m.nc, m.sem, []
    with ExitStack() as own:
        def sem(name):
            taken.append(own.enter_context(nc.semaphore(name)))
            return taken[-1]

        m.sem = sem
        yield
        m.sem = outer
        with nc.Block() as block:

            @block.gpsimd
            def _(pool):
                for s in taken:
                    pool.sem_clear(s)


def constants(m):
    nc = m.nc
    with nc.Block() as block:

        @block.gpsimd
        def _(pool):
            c = m.pool
            c.mark(pool.memset(m.ones[:], 1.0))
            c.mark(pool.memset(m.half_ones[:], 1.0))
            c.mark(pool.memset(m.ident[:], 0.0))
            c.wait(pool)
            c.link(pool, pool.affine_select(out=m.ident[:], in_=m.ident[:], compare_op=ALU.not_equal, fill=1.0,
                                            base=0, pattern=[[-1, P]], channel_multiplier=1))
            c.link(pool, pool.memset(m.half_ones[0:64, 64:P], 0.0))
            c.link(pool, pool.memset(m.half_ones[64:P, 0:64], 0.0))
            pool.sem_inc(m.ready, 1)


class Columns:

    def __init__(self, m, sets):
        self.m, self.sets = m, sets
        count = lambda rows: sum(ap.shape[0] for _, ap in rows)
        self.cols = [m.sb(f"cols{i}", [P, count(rows)]) for i, rows in enumerate(sets)]
        self.at = []
        for rows in sets:
            at, r = {}, 0
            for key, ap in rows:
                at[key] = r
                r += ap.shape[0]
            assert r <= P
            self.at.append(at)

    def open(self, own):
        self.raw = own.enter_context(self.m.nc.sbuf_tensor("cols_raw", [P, len(self.sets), P], F32))
        self.landed, self.turned = self.m.sem("cols_landed"), self.m.sem("cols_turned")

    def load(self, eng):
        for i, rows in enumerate(self.sets):
            for key, ap in rows:
                r = self.at[i][key]
                eng.dma_start(self.raw[r:r + ap.shape[0], i, :], ap).then_inc(self.landed, 16)

    def turn(self, pe, bank):
        pe.wait_ge(self.landed, 16 * sum(len(rows) for rows in self.sets))
        for i, cols in enumerate(self.cols):
            n = cols.shape[1]
            ins = pe.transpose(bank[:, i * P:i * P + n], self.raw[0:n, i, :], self.m.ident[0:n, 0:n])
        ins.then_inc(self.turned, 1)

    def keep(self, dve, bank):
        dve.wait_ge(self.turned, 1)
        for i, cols in enumerate(self.cols):
            self.m.dve.mark(dve.tensor_copy(cols[:, :], bank[:, i * P:i * P + cols.shape[1]]))


def prefetch(m, sp, w, n_tiles, col0=0, done=None):
    wv = w.rearrange("(k p) n -> p k n", p=P)
    m.ahead = min(SLOTS, n_tiles * P // SLOT_COLS)
    for s in range(m.ahead):
        if done:
            sp.wait_ge(m.tile_made, done(s))
        sp.dma_start(m.weights[:, s, 0:wv.shape[1], :],
                     wv[:, :, s * SLOT_COLS + col0:(s + 1) * SLOT_COLS + col0]).then_inc(m.w_landed[s], 16)


def project(m, w, n_tiles, rhs, k_tiles, keep, other=None, setup=None, col0=0, then=None):
    nc = m.nc
    wv = w.rearrange("(k p) n -> p k n", p=P)
    per_slot = SLOT_COLS // P
    chunks = n_tiles // per_slot
    turns = chunks // SLOTS
    assert n_tiles % per_slot == 0
    made0, kept0 = m.tile_made_n, m.tile_kept_n
    ahead, m.ahead = m.ahead, 0
    landed0 = list(m.w_landed_n)
    per_turn = SLOTS * per_slot

    def turns_of(eng, body, first=0):
        if turns > first:
            with eng.Fori(first, turns) as i:
                body(i, SLOTS)
        if chunks % SLOTS:
            body(turns, chunks % SLOTS)

    with nc.Block() as block:

        @block.sync
        def _(sp):
            def load(i, s):
                sp.dma_start(m.weights[:, s, 0:k_tiles, :],
                             wv[:, :, bass.ds((i * SLOTS + s) * SLOT_COLS + col0, SLOT_COLS)]).then_inc(m.w_landed[s], 16)

            def body(i, slots):
                for s in range(slots):
                    sp.wait_ge(m.tile_made, made0 + (i - 1) * per_turn + (s + 1) * per_slot)
                    load(i, s)

            for s in range(ahead, min(SLOTS, chunks)):
                load(0, s)
            if turns >= 1:
                turns_of(sp, body, first=1)
            if then:
                last = lambda s: (chunks - 1 - s) // SLOTS * SLOTS + s
                prefetch(m, sp, *then, done=lambda s: made0 + (last(s) + 1) * per_slot)

        @block.tensor
        def _(pe):
            def body(i, slots, first_turn=False):
                for s in range(slots):
                    pe.wait_ge(m.w_landed[s], landed0[s] + 16 * i + 16)
                    for c in range(per_slot):
                        b = s * per_slot + c
                        if not first_turn:
                            pe.wait_ge(m.tile_kept, kept0 + (i - 1) * per_turn + b + 1)
                        for k in range(k_tiles):
                            ins = pe.matmul(m.ps[b][:, :], m.weights[:, s, k, c * P:(c + 1) * P], rhs(k),
                                            start=(k == 0), stop=(k == k_tiles - 1))
                        ins.then_inc(m.tile_made, 1)

            if turns >= 1:
                body(0, SLOTS, first_turn=True)
                turns_of(pe, body, first=1)
            else:
                body(0, chunks, first_turn=True)

        @block.vector
        def _(dve):
            def body(i, slots):
                for b in range(slots * per_slot):
                    dve.wait_ge(m.tile_made, made0 + i * per_turn + b + 1)
                    keep(dve, i * per_turn + b, m.ps[b]).then_inc(m.tile_kept, 1)

            if setup:
                setup(dve)
            turns_of(dve, body)

        if other:
            other(block)

    m.tile_made_n += n_tiles
    m.tile_kept_n += n_tiles
    for s in range(SLOTS):
        m.w_landed_n[s] += 16 * len([c for c in range(chunks) if c % SLOTS == s])


def norm(m, src, dst, scale, shift=None, sq=None):
    nc = m.nc
    sq = dst if sq is None else sq
    made0, summed0, rstd0, scaled0 = m.sq_made_n, m.sq_summed_n, m.rstd_made_n, m.scaled_n
    with ExitStack() as own:
        rstd = own.enter_context(nc.sbuf_tensor(f"rstd{made0}", [P, T], F32))
        with nc.Block() as block:

            @block.scalar
            def _(act):
                for k in range(KT):
                    act.activation(sq[:, k, :], src[:, k, :], ACT.Square).then_inc(m.sq_made, 1)
                act.wait_ge(m.rstd_made, rstd0 + 1)
                act.activation(rstd[:, :], rstd[:, :], ACT.Sqrt).then_inc(m.rstd_made, 1)
                if shift is not None:
                    for k in range(KT):
                        act.wait_ge(m.scaled, scaled0 + k + 1)
                        m.act.mark(act.activation(dst[:, k, :], dst[:, k, :], ACT.Identity, bias=shift[:, k:k + 1]))

            @block.tensor
            def _(pe):
                for k in range(KT):
                    pe.wait_ge(m.sq_made, made0 + k + 1)
                    ins = pe.matmul(m.ps[0][:, :], m.ones[:, :], sq[:, k, :], start=(k == 0), stop=(k == KT - 1))
                ins.then_inc(m.sq_summed, 1)

            @block.vector
            def _(dve):
                dve.wait_ge(m.sq_summed, summed0 + 1)
                dve.tensor_scalar(rstd[:, :], m.ps[0][:, :], 1.0 / D, EPS, ALU.mult, ALU.add).then_inc(m.rstd_made, 1)
                dve.wait_ge(m.rstd_made, rstd0 + 2)
                m.dve.link(dve, dve.reciprocal(rstd[:, :], rstd[:, :]))
                for k in range(KT):
                    dve.scalar_tensor_tensor(out=dst[:, k, :], in0=src[:, k, :], scalar=scale[:, k:k + 1],
                                             in1=rstd[:, :], op0=ALU.mult, op1=ALU.mult).then_inc(m.scaled, 1)

    m.sq_made_n += KT
    m.sq_summed_n += 1
    m.rstd_made_n += 2
    m.scaled_n += KT


def load_tokens(m, x, ada, columns):
    nc = m.nc
    landed = m.sem("x_landed")
    turned, kept = m.sem("x_turned"), m.sem("x_turned_kept")
    with ExitStack() as own:
        rows = own.enter_context(nc.sbuf_tensor("x_rows", [P, TT, D], F32))
        columns.open(own)
        with nc.Block() as block:

            @block.sync
            def _(sp):
                sp.dma_start(rows[:, :, :], x.rearrange("(t p) d -> p t d", p=P)).then_inc(landed, 16)
                for n in range(ada.BUFS):
                    ada.load(sp, n)

            @block.scalar
            def _(act):
                columns.load(act)

            @block.tensor
            def _(pe):
                pe.wait_ge(landed, 16)
                for k in range(KT):
                    for t in range(TT):
                        ins = pe.transpose(m.ps[k][:, t * P:(t + 1) * P], rows[:, t, k * P:(k + 1) * P], m.ident[:, :])
                    ins.then_inc(turned, 1)
                pe.wait_ge(kept, 1)
                columns.turn(pe, m.ps[0])

            @block.vector
            def _(dve):
                for k in range(KT):
                    dve.wait_ge(turned, k + 1)
                    dve.tensor_copy(m.xT[:, k, :], m.ps[k][:, :]).then_inc(kept, 1)
                columns.keep(dve, m.ps[0])


class Modulation:
    HALVES, BUFS = 2, 4

    def __init__(self, m, own, w_ada):
        self.m, self.w_ada = m, w_ada
        self.width = w_ada.shape[1]
        self.H = self.width // self.HALVES
        self.landed = [m.sem(f"ada_landed{b}") for b in range(self.BUFS)]
        self.rows = own.enter_context(m.nc.sbuf_tensor("ada_rows", [P, self.BUFS, self.H], F32))
        self.acc = own.enter_context(m.nc.sbuf_tensor("ada_acc", [P, self.width], F32))

    def load(self, sp, n):
        k, h, b = n // self.HALVES, n % self.HALVES, n % self.BUFS
        sp.dma_start(self.rows[:, b, :],
                     self.w_ada[k * P:(k + 1) * P, h * self.H:(h + 1) * self.H]).then_inc(self.landed[b], 16)

    def run(self, cols, at, mod, lead, then):
        m, H, rows, acc, halves, bufs = self.m, self.H, self.rows, self.acc, self.HALVES, self.BUFS
        n_tiles = self.width // P
        added, summed = m.sem("ada_added"), m.sem("ada_summed")
        with m.nc.Block() as block:

            @block.sync
            def _(sp):
                for n in range(bufs, KT * halves):
                    sp.wait_ge(added, n - bufs + 1)
                    self.load(sp, n)
                prefetch(m, sp, *then)

            @block.scalar
            def _(act):
                m.act.mark(act.activation(lead[:, :], cols[:, at["c"]:at["c"] + KT], ACT.Silu))

            @block.vector
            def _(dve):
                m.act.wait(dve)
                for n in range(KT * halves):
                    k, h = n // halves, n % halves
                    a, row = acc[:, h * H:(h + 1) * H], rows[:, n % bufs, :]
                    dve.wait_ge(self.landed[n % bufs], 16 * (n // bufs + 1))
                    if k == 0:
                        ins = dve.tensor_scalar(a, row, lead[:, 0:1], None, ALU.mult)
                    else:
                        dve.wait_ge(added, n - halves + 1)
                        ins = dve.scalar_tensor_tensor(out=a, in0=row, scalar=lead[:, k:k + 1], in1=a,
                                                       op0=ALU.mult, op1=ALU.add)
                    ins.then_inc(added, 1)
                dve.wait_ge(summed, 1)
                b0 = at["b_ada"]
                m.dve.mark(dve.tensor_tensor(mod[:, :], m.ps[0][:, 0:n_tiles], cols[:, b0:b0 + n_tiles], ALU.add))

            @block.tensor
            def _(pe):
                for n in range(n_tiles):
                    if n % (n_tiles // halves) == 0:
                        pe.wait_ge(added, halves * (KT - 1) + n // (n_tiles // halves) + 1)
                    ins = pe.matmul(m.ps[0][:, n:n + 1], acc[:, n * P:(n + 1) * P], m.ones[:, 0:1], start=True, stop=True)
                ins.then_inc(summed, 1)


def level_masks(m, own, name, n, levels):
    nc = m.nc
    masks = own.enter_context(nc.sbuf_tensor(name, [P, levels + 1, n], I32))
    with ExitStack() as own:
        s_of = own.enter_context(nc.sbuf_tensor(f"{name}_s", [P, n], I32))
        t_of = own.enter_context(nc.sbuf_tensor(f"{name}_t", [P, n], I32))
        late = own.enter_context(nc.sbuf_tensor(f"{name}_late", [P, n], I32))
        x = own.enter_context(nc.sbuf_tensor(f"{name}_x", [P, n], I32))
        with nc.Block() as block:

            @block.gpsimd
            def _(pool):
                c = m.pool
                for h in range(P // n):
                    c.mark(pool.iota(s_of[h * n:(h + 1) * n, :], [[0, n]], base=0, channel_multiplier=1))
                c.mark(pool.iota(t_of[:, :], [[1, n]], base=0, channel_multiplier=0))

            @block.vector
            def _(dve):
                c = m.dve
                m.pool.wait(dve)
                c.mark(dve.tensor_tensor(late[:, :], t_of[:, :], s_of[:, :], ALU.is_gt))
                c.mark(dve.tensor_tensor(masks[:, levels, :], t_of[:, :], s_of[:, :], ALU.is_equal))
                c.link(dve, dve.tensor_tensor(x[:, :], t_of[:, :], s_of[:, :], ALU.bitwise_xor))
                c.link(dve, dve.tensor_tensor(x[:, :], x[:, :], late[:, :], ALU.mult))
                for l in range(levels):
                    c.link(dve, dve.tensor_scalar(s_of[:, :], x[:, :], l, None, ALU.logical_shift_right))
                    c.link(dve, dve.tensor_scalar(masks[:, l, :], s_of[:, :], 1, None, ALU.is_equal))
    return masks


class Rows:

    def __init__(self, m, own, name, groups, per_group, halves):
        self.per_group, self.halves = per_group, halves
        self.n = groups * (2 if halves else 1)
        self.strip = own.enter_context(m.nc.sbuf_tensor(f"{name}_strip", [P, 2 * self.n], F32))
        self.back = own.enter_context(m.nc.sbuf_tensor(f"{name}_back", [self.n, groups, P], F32))
        self.groups = groups

    def build(self, m, pool):
        c, n = m.pool, self.n
        c.mark(pool.memset(self.strip[:, :], 0.0))
        c.mark(pool.memset(self.back[:, :, :], 0.0))
        c.wait(pool)
        if self.halves:
            c.mark(pool.memset(self.strip[0:64, n:n + 1], 1.0))
            c.mark(pool.memset(self.strip[64:P, n + 1:n + 2], 1.0))
            pattern = [[-2, self.groups], [-1, 2], [0, 64]]
        else:
            c.mark(pool.memset(self.strip[:, n:n + 1], 1.0))
            pattern = [[-1, self.groups], [0, P]]
        back = self.back[:, :, :].rearrange("r g (a p) -> r g a p", a=2) if self.halves else self.back[:, :, :]
        c.mark(pool.affine_select(out=back, in_=back, compare_op=ALU.not_equal, fill=1.0, base=0,
                                  pattern=pattern, channel_multiplier=1))

    def sum_of(self, tile):
        row = 2 * tile if self.halves else tile // self.per_group
        return self.strip[:, self.n - row:2 * self.n - row]


def group_norm(m, src, dst, w, groups, per_group, ones, mean_of, eps=EPS, gate=None, sq=None):
    nc = m.nc
    src_of = src if callable(src) else lambda n: src[:, n, :]
    made0, summed0, rstd0, spread0 = m.sq_made_n, m.sq_summed_n, m.rstd_made_n, m.spread_n
    tiles = groups * per_group
    with ExitStack() as own:
        if sq is None:
            sq = own.enter_context(nc.sbuf_tensor(f"gn_sq{made0}", [P, 2, T], F32))
        rows = Rows(m, own, f"gn{made0}", groups, per_group, ones is m.half_ones)
        R = rows.n
        rstd = own.enter_context(nc.sbuf_tensor(f"gn_rstd{made0}", [R, T], F32))
        with nc.Block() as block:

            @block.gpsimd
            def _(pool):
                rows.build(m, pool)

            @block.scalar
            def _(act):
                for n in range(tiles):
                    if n >= 2:
                        act.wait_ge(m.sq_summed, summed0 + n - 1)
                    act.activation(sq[:, n % 2, :], src_of(n), ACT.Square).then_inc(m.sq_made, 1)
                act.wait_ge(m.rstd_made, rstd0 + 1)
                act.activation(rstd[:, :], rstd[:, :], ACT.Sqrt).then_inc(m.rstd_made, 1)

            @block.tensor
            def _(pe):
                m.pool.wait(pe)
                for n in range(tiles):
                    pe.wait_ge(m.sq_made, made0 + n + 1)
                    pe.matmul(m.ps[7][0:R, :], rows.sum_of(n), sq[:, n % 2, :],
                              start=(n == 0), stop=(n == tiles - 1)).then_inc(m.sq_summed, 1)
                pe.wait_ge(m.rstd_made, rstd0 + 3)
                for g in range(groups):
                    pe.matmul(m.ps[g][:, :], rows.back[:, g, :], rstd[:, :], start=True, stop=True).then_inc(m.spread, 1)

            @block.vector
            def _(dve):
                c = m.dve
                dve.wait_ge(m.sq_summed, summed0 + tiles)
                dve.tensor_scalar(rstd[:, :], m.ps[7][0:R, :], 1.0 / mean_of, eps, ALU.mult, ALU.add).then_inc(m.rstd_made, 1)
                dve.wait_ge(m.rstd_made, rstd0 + 2)
                dve.reciprocal(rstd[:, :], rstd[:, :]).then_inc(m.rstd_made, 1)
                for n in range(tiles):
                    if n % per_group == 0:
                        dve.wait_ge(m.spread, spread0 + n // per_group + 1)
                    c.mark(dve.scalar_tensor_tensor(out=dst[:, n, :], in0=src_of(n), scalar=w[:, n:n + 1],
                                                    in1=m.ps[n // per_group][:, :], op0=ALU.mult, op1=ALU.mult))
                    if gate is not None and n < gate.shape[1]:
                        c.wait(dve)
                        c.mark(dve.tensor_tensor(dst[:, n, :], dst[:, n, :], gate[:, n, :], ALU.mult))

    m.sq_made_n += tiles
    m.sq_summed_n += tiles
    m.rstd_made_n += 3
    m.spread_n += groups


def hgrn(m, cols, at, proj, yT, masks, conv):
    nc = m.nc
    H, C = HG, HC
    NCH = T // C
    W = H * T
    L = HGRN_LEVELS
    flat = lambda ap: ap.rearrange("p h t -> p (h t)")
    q, f_raw, v, g = (proj[:, j * H:(j + 1) * H, :] for j in range(4))
    with ExitStack() as own:
        sb = lambda name, shape, dt=F32: own.enter_context(nc.sbuf_tensor(name, shape, dt))
        lb = sb("hg_lb", [P, H])
        lb1 = sb("hg_lb1", [P, H])
        kk = sb("hg_k", [P, H, T])
        b = sb("hg_b", [P, H, T])
        pair = sb("hg_pair", [P, 2, H, T])
        scores = sb("hg_scores", [P, H, T])
        dist = sb("hg_dist", [P, 2, H, T])
        keep = dist[:, 0]
        f = dist[:, 1]

        diff_made, sig_made, f_made, ready = (m.sem(f"hg_{x}") for x in ("diff", "sig", "f", "ready"))
        with nc.Block() as block:

            @block.gpsimd
            def _(pool):
                m.pool.mark(pool.memset(scores[:, :, :], 0.0))
                m.pool.link(pool, pool.memset(keep[:, :, :], 1.0))
                k4 = flat(keep).rearrange("p (n c) -> p n c", c=C)
                pool.memset(k4[:, :, 0:1], 0.0).then_inc(ready, 1)

            @block.scalar
            def _(act):
                act.wait_ge(diff_made, 1)
                act.activation(lb[:, :], lb1[:, :], ACT.Sigmoid).then_inc(sig_made, 1)
                act.activation(flat(f), flat(f_raw), ACT.Sigmoid).then_inc(sig_made, 1)
                act.activation(flat(kk), flat(f_raw), ACT.Sigmoid, scale=-1.0).then_inc(sig_made, 1)
                act.wait_ge(f_made, H)
                act.activation(flat(f), flat(f), ACT.Ln).then_inc(sig_made, 1)

            @block.vector
            def _(dve):
                c = m.dve
                a0 = at["lb"]
                dve.tensor_tensor(lb1[:, :], cols[:, a0:a0 + H], cols[:, a0 + H:a0 + 2 * H], ALU.subtract).then_inc(diff_made, 1)
                dve.wait_ge(sig_made, 1)
                c.link(dve, dve.tensor_scalar(lb1[:, :], lb[:, :], -1.0, 1.0, ALU.mult, ALU.add))
                dve.wait_ge(sig_made, 3)
                for h in range(H):
                    dve.tensor_scalar(f[:, h, :], f[:, h, :], lb1[:, h:h + 1], lb[:, h:h + 1],
                                      ALU.mult, ALU.add).then_inc(f_made, 1)
                for h in range(H):
                    c.mark(dve.tensor_scalar(kk[:, h, :], kk[:, h, :], lb1[:, h:h + 1], None, ALU.mult))
                dve.wait_ge(sig_made, 4)
                dve.wait_ge(ready, 1)
                c.mark(dve.tensor_tensor_scan(flat(b), flat(keep), flat(f), 0.0, ALU.mult, ALU.add))

        dist_made, decay_made, pair_made, level_made, folded = (
            m.sem(f"hg_{x}") for x in ("dist_made", "decay_made", "pair_made", "level_made", "folded"))
        blocks = lambda ap, l: flat(ap).rearrange("p (n c) -> p n c", c=2 << l)
        halves = lambda ap, l, j: flat(ap).rearrange("p (n j c) -> p n j c", j=2, c=1 << l)[:, :, j, :]
        with nc.Block() as block:

            @block.scalar
            def _(act):
                for l in range(L):
                    act.wait_ge(dist_made, l + 1)
                    act.activation(flat(dist[:, l % 2]), flat(dist[:, l % 2]), ACT.Abs).then_inc(decay_made, 1)
                    act.wait_ge(decay_made, 2 * l + 1)
                    act.activation(flat(dist[:, l % 2]), flat(dist[:, l % 2]), ACT.Exp, scale=-1.0).then_inc(decay_made, 1)

            @block.tensor
            def _(pe):
                for l in range(L + 1):
                    if l < L:
                        pe.wait_ge(pair_made, 2 * l + 2)
                    if l >= 2:
                        pe.wait_ge(folded, H * (l - 1))
                    for h in range(H):
                        for n in range(NCH):
                            t = slice(n * C, (n + 1) * C)
                            k_, q_ = (pair[:, l % 2, h, t],) * 2 if l < L else (kk[:, h, t], q[:, h, t])
                            ins = pe.matmul(m.ps[4 * (l % 2) + h][:, t], k_, q_, start=True, stop=True)
                    ins.then_inc(level_made, 1)

            @block.vector
            def _(dve):
                for l in range(L + 3):
                    if l < L:
                        if l >= 2:
                            dve.wait_ge(pair_made, 2 * l - 2)
                        mid = blocks(b, l)[:, :, (1 << l) - 1:1 << l].to_broadcast([P, W // (2 << l), 2 << l])
                        dve.tensor_tensor(blocks(dist[:, l % 2], l), blocks(b, l), mid, ALU.subtract).then_inc(dist_made, 1)
                    if 1 <= l <= L:
                        p = l - 1
                        dve.wait_ge(decay_made, 2 * p + 2)
                        if p >= 2:
                            dve.wait_ge(level_made, p - 1)
                        for j, src in enumerate((kk, q)):
                            dve.tensor_tensor(halves(pair[:, p % 2], p, j), halves(dist[:, p % 2], p, j),
                                              halves(src, p, j), ALU.mult).then_inc(pair_made, 1)
                    if l >= 2:
                        p = l - 2
                        dve.wait_ge(level_made, p + 1)
                        if p >= 1:
                            dve.wait_ge(folded, H * p)
                        for h in range(H):
                            mask = masks[:, p:p + 1, :].to_broadcast([P, NCH, C])
                            dve.copy_predicated(scores[:, h, :].rearrange("p (n t) -> p n t", t=C), mask,
                                                m.ps[4 * (p % 2) + h][:, :].rearrange("p (n t) -> p n t", t=C)).then_inc(folded, 1)

        vrow, krow = dist[:, 0], dist[:, 1]
        with ExitStack() as last:
            elast = last.enter_context(nc.sbuf_tensor("hg_elast", [P, H, NCH], F32))
            state = last.enter_context(nc.sbuf_tensor("hg_state", [P, H, P], F32))
            eb = m.hT[:, 0:H, :]
            v_turned, k_turned, e_made, k_decayed, rows_kept, update_made, state_made, out_kept = (
                m.sem(f"hg_{x}") for x in ("v_turned", "k_turned", "e_made", "k_decayed", "rows_kept", "update_made",
                                           "state_made", "out_kept"))
            with nc.Block() as block:

                @block.scalar
                def _(act):
                    act.activation(flat(eb), flat(b), ACT.Exp).then_inc(e_made, 1)
                    act.activation(elast[:, :, :], b[:, :, C - 1:T:C], ACT.Exp).then_inc(e_made, 1)
                    act.wait_ge(k_decayed, 1)
                    act.activation(flat(pair[:, 1]), flat(pair[:, 1]), ACT.Exp, scale=-1.0).then_inc(e_made, 1)
                    for h in range(H):
                        act.wait_ge(v_turned, h + 1)
                        act.copy(vrow[:, h, :], m.ps[h][:, :]).then_inc(rows_kept, 1)
                    for h in range(H):
                        act.wait_ge(k_turned, h + 1)
                        act.copy(krow[:, h, :], m.ps[4 + h][:, :]).then_inc(rows_kept, 1)
                    m.act.mark(act.activation(flat(kk), flat(g), ACT.Silu))

                @block.tensor
                def _(pe):
                    for h in range(H):
                        for n in range(NCH):
                            ins = pe.transpose(m.ps[h][:, n * C:(n + 1) * C], v[:, h, n * C:(n + 1) * C], m.ident[:, :])
                        ins.then_inc(v_turned, 1)
                    pe.wait_ge(k_decayed, 3)
                    for h in range(H):
                        for n in range(NCH):
                            ins = pe.transpose(m.ps[4 + h][:, n * C:(n + 1) * C], pair[:, 1, h, n * C:(n + 1) * C], m.ident[:, :])
                        ins.then_inc(k_turned, 1)
                    pe.wait_ge(rows_kept, 2 * H)
                    for n in range(NCH):
                        t = slice(n * C, (n + 1) * C)
                        for h in range(H):
                            pe.matmul(m.ps[h][:, t], vrow[:, h, t], scores[:, h, t], start=True, stop=(n == 0))
                            if n > 0:
                                pe.wait_ge(state_made, (n - 1) * H + h + 1)
                                ins = pe.matmul(m.ps[h][:, t], state[:, h, :], pair[:, 0, h, t], start=False, stop=True)
                            if n < NCH - 1:
                                ins = pe.matmul(m.ps[4 + h][:, t], krow[:, h, t], vrow[:, h, t], start=True, stop=True)
                            ins.then_inc(update_made, 1)

                @block.vector
                def _(dve):
                    bv = flat(b).rearrange("p (n c) -> p n c", c=C)
                    last_b = bv[:, :, C - 1:C].to_broadcast([P, H * NCH, C])
                    kd = flat(pair[:, 1])
                    dve.tensor_tensor(kd.rearrange("p (n c) -> p n c", c=C), bv, last_b, ALU.subtract).then_inc(k_decayed, 1)
                    dve.wait_ge(e_made, 2)
                    dve.tensor_tensor(flat(pair[:, 0]), flat(eb), flat(q), ALU.mult).then_inc(k_decayed, 1)
                    dve.wait_ge(e_made, 3)
                    dve.tensor_tensor(kd, kd, flat(kk), ALU.mult).then_inc(k_decayed, 1)
                    for n in range(NCH - 1):
                        for h in range(H):
                            u = m.ps[4 + h][:, n * C:(n + 1) * C]
                            dve.wait_ge(update_made, n * H + h + 1)
                            if n == 0:
                                dve.tensor_copy(state[:, h, :], u).then_inc(state_made, 1)
                            else:
                                dve.wait_ge(state_made, (n - 1) * H + h + 1)
                                dve.scalar_tensor_tensor(out=state[:, h, :], in0=state[:, h, :], scalar=elast[:, h, n:n + 1],
                                                         in1=u, op0=ALU.mult, op1=ALU.add).then_inc(state_made, 1)
                    for h in range(H):
                        dve.wait_ge(update_made, (NCH - 1) * H + h + 1)
                        m.dve.mark(dve.tensor_copy(b[:, h, :], m.ps[h][:, :]))

        w0 = at["hgrn_w"]
        group_norm(m, lambda n: b[:, n, :] if n < H else conv[:, n - H, :], yT, cols[:, w0:w0 + H + CG], H + CG, 1,
                   m.ones, P, gate=kk, sq=proj[:, 20:22, :])


def short_conv(m, dve, cols, at, proj):
    bg, cg, xin = (proj[:, 16 + 4 * j:20 + 4 * j, :] for j in range(3))
    c0 = at["conv_w"]
    c = m.dve
    c.link(dve, dve.tensor_tensor(xin, cg, xin, ALU.mult))
    for j in range(2, -1, -1):
        for g in range(CG):
            tap = cols[:, c0 + j * CG + g:c0 + j * CG + g + 1]
            u, y, d = xin[:, g, :], cg[:, g, :], 2 - j
            if d == 0:
                c.mark(dve.tensor_scalar(y, u, tap, None, ALU.mult))
            else:
                c.mark(dve.scalar_tensor_tensor(out=y[:, d:], in0=u[:, :T - d], scalar=tap, in1=y[:, d:],
                                                op0=ALU.mult, op1=ALU.add))
        c.wait(dve)
    c.mark(dve.tensor_tensor(bg, cg, bg, ALU.mult))


def first_rows(c, b_ada, norm1_w, lb_logits, hgrn_w, conv_w, conv_norm_w, norm2_w, final_norm_w):
    row = lambda ap: ap.rearrange("(k p) -> k p", p=P)
    return [
        ("c", row(c[0])), ("b_ada", row(b_ada[0])), ("norm1", row(norm1_w[0])),
        ("lb", lb_logits.rearrange("l (k p) -> (l k) p", p=P)), ("hgrn_w", row(hgrn_w[0])),
        ("conv_norm", row(conv_norm_w[0])), ("conv_w", conv_w[0].rearrange("j (k p) -> (j k) p", p=P)),
        ("norm2", row(norm2_w[0])), ("final", row(final_norm_w))]


def first_mixer(m, x, columns, w_ada, w_in, w_out, then):
    nc = m.nc
    cols, at = columns.cols[0], columns.at[0]
    mod = m.sb("mod", [P, 6 * KT])
    m.mod = mod
    scale1 = m.sb("scale1", [P, KT])
    m.scale2 = m.sb("scale2", [P, KT])
    silu_c = m.sb("silu_c", [P, KT])
    with ExitStack() as own:
        ada = Modulation(m, own, w_ada[0])
        load_tokens(m, x[0], ada, columns)
        ada.run(cols, at, mod, silu_c, (w_in[0], 12, 16 * P))
        with nc.Block() as block:

            @block.vector
            def _(dve):
                for j, key, dst in ((1, "norm1", scale1), (4, "norm2", m.scale2)):
                    m.dve.mark(dve.scalar_tensor_tensor(out=dst[:, :], in0=mod[:, j * KT:(j + 1) * KT], scalar=1.0,
                                                        in1=cols[:, at[key]:at[key] + KT], op0=ALU.add, op1=ALU.mult))
    norm(m, m.xT, m.hT, scale1, mod[:, 0:KT])
    with ExitStack() as own:
        proj = own.enter_context(nc.sbuf_tensor("proj1", [P, 28, T], F32))
        yT = own.enter_context(nc.sbuf_tensor("y1T", [P, KT, T], F32))
        project(m, w_in[0], 12, lambda k: m.hT[:, k, :], KT,
                lambda dve, t, bank: dve.tensor_copy(at_tile(proj, t + 16), bank[:, :]), col0=16 * P, then=(w_in[0], 16))
        project(m, w_in[0], 16, lambda k: m.hT[:, k, :], KT,
                lambda dve, t, bank: dve.tensor_copy(at_tile(proj, t), bank[:, :]),
                setup=lambda dve: short_conv(m, dve, cols, at, proj), then=(w_out[0], KT))
        with ExitStack() as own2:
            masks = level_masks(m, own2, "pairs128", HC, HGRN_LEVELS)
            hgrn(m, cols, at, proj, yT, masks, proj[:, 16:16 + CG, :])
        add_projected(m, w_out[0], yT, KT, mod[:, 2 * KT:3 * KT], then)


def at_tile(t3, t):
    return t3[:, t, :] if isinstance(t, int) else t3[:, bass.ds(t, 1), :].rearrange("p a t -> p (a t)")


def add_projected(m, w, rhs, k_tiles, gate, then):
    def keep(dve, t, bank):
        scalar = gate[:, t:t + 1] if isinstance(t, int) else gate[:, bass.ds(t, 1)]
        x = at_tile(m.xT, t)
        return dve.scalar_tensor_tensor(out=x, in0=bank[:, :], scalar=scalar, in1=x, op0=ALU.mult, op1=ALU.add)
    project(m, w, KT, lambda k: rhs[:, k, :], k_tiles, keep, then=then)


PH = 8
NK = 128
TOPK = 16
PICKS = PH * TOPK
RING = 16
GROUP = 4
GROUPS = PICKS // GROUP
BUFS = 2 * RING // GROUP
LOWEST = -3.0e38


def turn_back(m, src, dst, name, other=None):
    nc = m.nc
    turned = m.sem(f"{name}_turned")
    kept = m.sem(f"{name}_kept")
    halves = D // 512
    with nc.Block() as block:

        @block.tensor
        def _(pe):
            for t in range(TT):
                for h in range(halves):
                    for j in range(4):
                        ins = pe.transpose(m.ps[t * halves + h][:, j * P:(j + 1) * P],
                                           src[:, 4 * h + j, t * P:(t + 1) * P], m.ident[:, :])
                    ins.then_inc(turned, 1)

        @block.vector
        def _(dve):
            for n in range(TT * halves):
                dve.wait_ge(turned, n + 1)
                m.dve.mark(dve.tensor_copy(dst[:, n // halves, (n % halves) * 512:(n % halves + 1) * 512], m.ps[n][:, :]))

        if other:
            other(block)


def turn_forward(m, src, name, keep, then):
    nc = m.nc
    turned = m.sem(f"{name}_turned")
    with nc.Block() as block:

        @block.sync
        def _(sp):
            prefetch(m, sp, *then)

        @block.tensor
        def _(pe):
            for k in range(KT):
                for t in range(TT):
                    ins = pe.transpose(m.ps[k][:, t * P:(t + 1) * P], src[:, t, k * P:(k + 1) * P], m.ident[:, :])
                ins.then_inc(turned, 1)

        @block.vector
        def _(dve):
            for k in range(KT):
                dve.wait_ge(turned, k + 1)
                m.dve.mark(keep(dve, k, m.ps[k]))


def key_scores(m, sub_keys, qT, s_all):
    nc = m.nc
    HP = 2 * PH
    landed, turned, kept, made, s_kept = (m.sem(f"keys_{x}") for x in ("landed", "turned", "kept", "made", "s_kept"))
    with ExitStack() as own:
        raw = own.enter_context(nc.sbuf_tensor("keys_raw", [P, HP, P], F32))
        kT = own.enter_context(nc.sbuf_tensor("keysT", [P, HP, P], F32))
        with nc.Block() as block:

            @block.sync
            def _(sp):
                keys = sub_keys.rearrange("h j n k -> n (h j) k")
                for b in range(4):
                    sp.dma_start(raw[:, 4 * b:4 * b + 4, :], keys[:, 4 * b:4 * b + 4, :]).then_inc(landed, 16)

            @block.tensor
            def _(pe):
                pe.wait_ge(landed, 64)
                for b in range(4):
                    for j in range(4):
                        ins = pe.transpose(m.ps[b][:, j * P:(j + 1) * P], raw[:, 4 * b + j, :], m.ident[:, :])
                    ins.then_inc(turned, 1)
                pe.wait_ge(kept, 4)
                for t in range(TT):
                    for b in range(4):
                        n = t * 4 + b
                        if n >= 8:
                            pe.wait_ge(s_kept, n - 7)
                        for j in range(4):
                            hp = 4 * b + j
                            ins = pe.matmul(m.ps[n % 8][:, j * P:(j + 1) * P], qT[:, hp, t * P:(t + 1) * P], kT[:, hp, :],
                                            start=True, stop=True)
                        ins.then_inc(made, 1)

            @block.vector
            def _(dve):
                for b in range(4):
                    dve.wait_ge(turned, b + 1)
                    dve.tensor_copy(kT[:, 4 * b:4 * b + 4, :].rearrange("p j n -> p (j n)"), m.ps[b][:, :]).then_inc(kept, 1)
                for n in range(4 * TT):
                    dve.wait_ge(made, n + 1)
                    dve.tensor_copy(s_all[:, n // 4, (n % 4) * 512:(n % 4 + 1) * 512], m.ps[n % 8][:, :]).then_inc(s_kept, 1)


class Picker:
    PARTS = 14

    def __init__(self, m, own, s_all, index, gate):
        self.m, self.s_all, self.index, self.gate = m, s_all, index, gate
        self.shifted, self.exps, self.picked = m.sem("gate_shifted"), m.sem("gate_exps"), m.sem("tiles_picked")
        HP = 2 * PH
        sb = lambda name, shape, dt=F32: own.enter_context(m.nc.sbuf_tensor(name, shape, dt))
        self.s = sb("pk_s", [P, HP, NK])
        self.s2 = sb("pk_s2", [P, HP, NK])
        self.val = sb("pk_val", [P, HP, TOPK])
        self.ind = sb("pk_ind", [P, HP, TOPK], U32)
        self.indf = sb("pk_indf", [P, HP, TOPK])
        self.cand = sb("pk_cand", [P, PH, TOPK * TOPK])
        self.cand2 = sb("pk_cand2", [P, PH, TOPK * TOPK])
        self.best = sb("pk_best", [P, PH, TOPK])
        self.pos = sb("pk_pos", [P, PH, TOPK], U32)
        self.digit = sb("pk_digit", [P, 2, PH * TOPK], U32)
        self.digitf = sb("pk_digitf", [P, 2, PH * TOPK])
        self.which = sb("pk_which", [P, PH, TOPK, TOPK])
        self.found = sb("pk_found", [P, 2, PH * TOPK])
        self.count = sb("pk_count", [P, TOPK])
        self.total = sb("pk_total", [P, PH])
        self.ex = sb("pk_ex", [P, PH, TOPK])
        self.pad = sb("pk_pad", [P, 1])
        self.STEPS = 1 + (5 * HP + 4) + 2 + (5 * PH + 4) + 3 + 2 * 3 + 1 + 2

    def start(self, pool):
        m = self.m
        m.pool.mark(pool.memset(self.index[:, TT, :], 0))
        m.pool.mark(pool.iota(self.count[:, :], [[1, TOPK]], base=0, channel_multiplier=0,
                              allow_small_or_imprecise_dtypes=True))

    def exp(self, act, i):
        act.wait_ge(self.shifted, i + 1)
        act.activation(self.ex[:, :, :], self.ex[:, :, :], ACT.Exp).then_inc(self.exps, 1)

    def carried(self, dve):
        c = self.m.dve
        c.wait(dve)
        c.mark(dve.memset(self.pad[:, :], 0.0))

    def largest8(self, dve, vals, src, half, n):
        for r in range(n):
            self.m.dve.mark(dve.max(vals[:, r, 8 * half:8 * half + 8], src[:, r, :]))

    def places8(self, dve, inds, vals, src, half, n):
        for r in range(n):
            self.m.dve.mark(dve.max_index(inds[:, r, 8 * half:8 * half + 8], vals[:, r, 8 * half:8 * half + 8], src[:, r, :]))

    def strike8(self, dve, spare, vals, src, n):
        for r in range(n):
            self.m.dve.mark(dve.match_replace(spare[:, r, :], vals[:, r, 0:8], src[:, r, :], LOWEST))

    def look_up(self, dve, j, step):
        c = self.m.dve
        w3 = self.which[:, :, :, :].rearrange("p h k n -> p (h k) n")
        i4 = self.indf[:, :, :].rearrange("p (h j) k -> p h j k", j=2)
        if step == 0:
            c.link(dve, dve.tensor_tensor(w3, self.count[:, :].unsqueeze(1).to_broadcast([P, PH * TOPK, TOPK]),
                                          self.digitf[:, j, :].unsqueeze(2).to_broadcast([P, PH * TOPK, TOPK]),
                                          ALU.is_equal))
        elif step == 1:
            c.link(dve, dve.tensor_tensor(self.which[:, :, :, :], self.which[:, :, :, :],
                                          i4[:, :, j, :].unsqueeze(2).to_broadcast([P, PH, TOPK, TOPK]), ALU.mult))
        else:
            c.link(dve, dve.tensor_reduce(self.found[:, j, :], w3, AX.X, ALU.add))

    def part(self, dve, n, i):
        c, HP = self.m.dve, 2 * PH
        s, s2, val, ind, cand, cand2, best, pos = (
            self.s, self.s2, self.val, self.ind, self.cand, self.cand2, self.best, self.pos)
        if n == 0:
            c.link(dve, dve.tensor_copy(s[:, :, :].rearrange("p h n -> p (h n)"),
                                        self.s_all[:, bass.ds(i, 1), :].rearrange("p a n -> p (a n)")))
            self.carried(dve)
            self.largest8(dve, val, s, 0, HP)
        elif n == 1:
            self.carried(dve)
            self.places8(dve, ind, val, s, 0, HP)
        elif n == 2:
            self.strike8(dve, s2, val, s, HP)
        elif n == 3:
            self.carried(dve)
            self.largest8(dve, val, s2, 1, HP)
        elif n == 4:
            self.carried(dve)
            self.places8(dve, ind, val, s2, 1, HP)
        elif n == 5:
            c.wait(dve)
            c.mark(dve.tensor_copy(self.indf[:, :, :], ind[:, :, :]))
            v4 = val[:, :, :].rearrange("p (h j) k -> p h j k", j=2)
            c.link(dve, dve.tensor_tensor(
                cand[:, :, :].rearrange("p h (a b) -> p h a b", b=TOPK),
                v4[:, :, 0, :].unsqueeze(3).to_broadcast([P, PH, TOPK, TOPK]),
                v4[:, :, 1, :].unsqueeze(2).to_broadcast([P, PH, TOPK, TOPK]), ALU.add))
        elif n == 6:
            self.carried(dve)
            self.largest8(dve, best, cand, 0, PH)
            self.carried(dve)
            self.places8(dve, pos, best, cand, 0, PH)
        elif n == 7:
            self.strike8(dve, cand2, best, cand, PH)
            self.carried(dve)
            self.largest8(dve, best, cand2, 1, PH)
        elif n == 8:
            self.carried(dve)
            self.places8(dve, pos, best, cand2, 1, PH)
            c.wait(dve)
            flat_pos = pos[:, :, :].rearrange("p h k -> p (h k)")
            c.mark(dve.tensor_scalar(self.digit[:, 0, :], flat_pos, 4, None, ALU.logical_shift_right))
            c.mark(dve.tensor_scalar(self.digit[:, 1, :], flat_pos, 15, None, ALU.bitwise_and))
            dve.tensor_tensor(self.ex[:, :, :], best[:, :, :], best[:, :, 0:1].to_broadcast([P, PH, TOPK]),
                              ALU.subtract).then_inc(self.shifted, 1)
            c.wait(dve)
            c.link(dve, dve.tensor_copy(self.digitf[:, :, :], self.digit[:, :, :]))
        elif n == 9:
            self.look_up(dve, 0, 0)
        elif n == 10:
            self.look_up(dve, 0, 1)
            self.look_up(dve, 0, 2)
        elif n == 11:
            self.look_up(dve, 1, 0)
        elif n == 12:
            self.look_up(dve, 1, 1)
            self.look_up(dve, 1, 2)
        else:
            dve.scalar_tensor_tensor(out=self.index[:, bass.ds(i, 1), :].rearrange("p a n -> p (a n)"),
                                     in0=self.found[:, 0, :], scalar=float(NK), in1=self.found[:, 1, :],
                                     op0=ALU.mult, op1=ALU.add).then_inc(self.picked, 1)
            dve.wait_ge(self.exps, i + 1)
            c.link(dve, dve.tensor_reduce(self.total[:, :], self.ex[:, :, :], AX.X, ALU.add))
            c.link(dve, dve.reciprocal(self.total[:, :], self.total[:, :]))
            c.mark(dve.tensor_tensor(self.gate[:, bass.ds(i, 1), :].rearrange("p a (h k) -> p (a h) k", k=TOPK),
                                     self.ex[:, :, :], self.total[:, :].unsqueeze(2).to_broadcast([P, PH, TOPK]), ALU.mult))


def apply_experts(m, table_u, table_v, s_all, rows, index, gate, out):
    nc = m.nc
    TURNS = PICKS // RING
    landed = m.gathers[0:RING]
    free, index_set, dots_made, act_made, coef_made = (
        m.sem(x) for x in ("rows_free", "index_set", "dots_made", "act_made", "coef_made"))
    with ExitStack() as own:
        sb = lambda name, shape, dt=F32: own.enter_context(nc.sbuf_tensor(name, shape, dt))
        ring = sb("ring", [P, RING, D])
        now = sb("index_now", [P, BUFS, GROUP], U32)
        flat_index = index[:, :, :].rearrange("p t n -> p (t n)")
        dots = sb("dots", [P, PICKS])
        coef = sb("coef", [P, PICKS])
        acc = sb("acc", [P, D])
        picker = Picker(m, own, s_all, index, gate)
        one = lambda ap3, i: ap3[:, bass.ds(i, 1), :].rearrange("p a n -> p (a n)")
        with nc.Block() as block:

            @block.gpsimd
            def _(pool):
                def groups(i, half, table, body):
                    for b in range(BUFS):
                        g = body * BUFS + b
                        n = (i * 2 + half) * GROUPS + g
                        pool.wait_ge(index_set, n + 1)
                        pool.wait_ge(free, (n + 1) * GROUP)
                        after = i * PICKS + g * GROUP + GROUP
                        last = b == BUFS - 1
                        if last and half == 0:
                            after = i * PICKS + (body + 1) % (GROUPS // BUFS) * (BUFS * GROUP)
                        if last and half == 1 and isinstance(body, int):
                            pool.wait_ge(picker.picked, i + 2)
                        pool.tensor_copy(now[:, (b + 1) % BUFS, :],
                                         flat_index[:, bass.ds(after, GROUP)]).then_inc(index_set, 1)
                        for j in range(GROUP):
                            s = (b * GROUP + j) % RING
                            pool.indirect_dma_start(
                                out=ring[:, s, :], out_offset=None, in_=table,
                                in_offset=bass.IndirectOffsetOnAxis(ap=now[:, b, j:j + 1], axis=0)).then_inc(landed[s], 16)

                picker.start(pool)
                pool.wait_ge(picker.picked, 1)
                pool.tensor_copy(now[:, 0, :], flat_index[:, 0:GROUP]).then_inc(index_set, 1)
                with pool.Fori(0, TT) as i:
                    with pool.Fori(0, GROUPS // BUFS) as body:
                        groups(i, 0, table_u, body)
                    with pool.Fori(0, GROUPS // BUFS - 1) as body:
                        groups(i, 1, table_v, body)
                    groups(i, 1, table_v, GROUPS // BUFS - 1)

            @block.scalar
            def _(act):
                picker.exp(act, 0)
                with act.Fori(0, TT - 1) as i:
                    act.wait_ge(dots_made, (i + 1) * PICKS)
                    act.activation(coef[:, :], dots[:, :], ACT.Gelu).then_inc(act_made, 1)
                    picker.exp(act, i + 1)
                act.wait_ge(dots_made, TT * PICKS)
                act.activation(coef[:, :], dots[:, :], ACT.Gelu).then_inc(act_made, 1)

            @block.vector
            def _(dve):
                c = m.dve

                def dot(i, g):
                    for s in range(RING):
                        dve.wait_ge(landed[s], (i * (2 * TURNS) + g + 1) * 16)
                        dve.scalar_tensor_tensor(out=ring[:, s, :], in0=ring[:, s, :], scalar=1.0, in1=one(rows, i),
                                                 op0=ALU.mult, op1=ALU.mult,
                                                 accum_out=dots[:, bass.ds(g * RING + s, 1)]).then_inc(free, 1)

                def add(i, g):
                    v0 = i * (2 * TURNS) + TURNS
                    for s in range(RING):
                        dve.wait_ge(landed[s], (v0 + g + 1) * 16)
                        dve.wait_ge(free, (v0 + g + 1) * RING + s)
                        dve.scalar_tensor_tensor(out=acc[:, :], in0=ring[:, s, :],
                                                 scalar=coef[:, bass.ds(g * RING + s, 1)], in1=acc[:, :],
                                                 op0=ALU.mult, op1=ALU.add).then_inc(free, 1)

                def coefficients(i):
                    dve.wait_ge(free, RING + (i * (2 * TURNS) + TURNS) * RING)
                    dve.nop().then_inc(dots_made, PICKS)
                    dve.wait_ge(act_made, i + 1)
                    c.mark(dve.tensor_tensor(coef[:, :], coef[:, :], one(gate, i), ALU.mult))
                    c.mark(dve.memset(acc[:, :], 0.0))
                    c.wait(dve)
                    c.mark(dve.memset(picker.pad[:, :], 0.0))

                def keep(i):
                    dve.wait_ge(free, (i * 2 + 2) * TURNS * RING + RING)
                    c.mark(dve.tensor_copy(one(out, i), acc[:, :]))

                dve.sem_inc(free, RING)
                m.pool.wait(dve)
                for n in range(picker.PARTS):
                    picker.part(dve, n, 0)
                c.wait(dve)
                c.mark(dve.memset(picker.pad[:, :], 0.0))
                with dve.Fori(0, TT - 1) as i:
                    c.enter(i, picker.STEPS + 4)
                    for g in range(TURNS):
                        dot(i, g)
                        picker.part(dve, g, i + 1)
                    coefficients(i)
                    for g in range(TURNS):
                        add(i, g)
                        if TURNS + g < picker.PARTS:
                            picker.part(dve, TURNS + g, i + 1)
                    keep(i)
                    c.leave(TT - 1)
                dve.sem_inc(picker.picked, 1)
                with dve.Fori(0, TURNS) as g:
                    dot(TT - 1, g)
                coefficients(TT - 1)
                with dve.Fori(0, TURNS) as g:
                    add(TT - 1, g)
                keep(TT - 1)


def first_experts(m, w_query, sub_keys, table_u, table_v, cols, at, then):
    nc = m.nc
    norm(m, m.xT, m.hT, m.scale2, m.mod[:, 3 * KT:4 * KT])
    with ExitStack() as own:
        index = own.enter_context(nc.sbuf_tensor("index", [P, TT + 1, PICKS], U32))
        gate = own.enter_context(nc.sbuf_tensor("gate", [P, TT, PICKS], F32))
        rows = own.enter_context(nc.sbuf_tensor("h_rows", [P, TT, D], F32))
        turn_back(m, m.hT, rows, "h2")
        s_all = m.weights[:, :, :, :].rearrange("p s k c -> p (s k c)").rearrange("p (t n) -> p t n", t=TT)
        out = m.hT[:, :, :].rearrange("p k t -> p (k t)").rearrange("p (t d) -> p t d", t=TT)
        with ExitStack() as own2:
            qT = own2.enter_context(nc.sbuf_tensor("qT", [P, 2 * PH, T], F32))
            project(m, w_query[0], 2 * PH, lambda k: m.hT[:, k, :], KT,
                    lambda dve, t, bank: dve.tensor_copy(at_tile(qT, t), bank[:, :]))
            key_scores(m, sub_keys[0], qT, s_all)
        apply_experts(m, table_u[0], table_v[0], s_all, rows, index, gate, out)
        g0 = 5 * KT
        turn_forward(m, out, "peer", lambda dve, k, bank: dve.scalar_tensor_tensor(
            out=m.xT[:, k, :], in0=bank[:, :], scalar=m.mod[:, g0 + k:g0 + k + 1], in1=m.xT[:, k, :],
            op0=ALU.mult, op1=ALU.add), then)
    norm(m, m.xT, m.xT, cols[:, at["final"]:at["final"] + KT], sq=m.hT)


RH = 64
RC = 64
RT = 8
RN = T // RC
R_TILES = 3 * RT + 2
R_LEVELS = 6
E_HALF = 0.6065306597126334


def rwkv_masks(m, own):
    nc = m.nc
    sb = lambda ctx, name, shape, dt=F32: ctx.enter_context(nc.sbuf_tensor(name, shape, dt))
    lower = sb(own, "rk_lower", [P, R_LEVELS, RC])
    first = sb(own, "rk_first", [P, RC])
    after = sb(own, "rk_after", [P, RC])
    upto = sb(own, "rk_upto", [P, RC])
    eye = sb(own, "rk_eye", [P, RC])
    with ExitStack() as tmp:
        a = sb(tmp, "rk_a", [P, RC], I32)
        b = sb(tmp, "rk_b", [P, RC], I32)
        x = sb(tmp, "rk_x", [P, RC], I32)
        y = sb(tmp, "rk_y", [P, RC], I32)
        z = sb(tmp, "rk_z", [P, RC], I32)
        with nc.Block() as block:

            @block.gpsimd
            def _(pool):
                for h in range(2):
                    m.pool.link(pool, pool.iota(a[h * RC:(h + 1) * RC, :], [[0, RC]], base=0, channel_multiplier=1))
                m.pool.mark(pool.iota(b[:, :], [[1, RC]], base=0, channel_multiplier=0))

            @block.vector
            def _(dve):
                c = m.dve
                m.pool.wait(dve)
                c.mark(dve.tensor_tensor(after[:, :], b[:, :], a[:, :], ALU.is_gt))
                c.mark(dve.tensor_tensor(upto[:, :], b[:, :], a[:, :], ALU.is_ge))
                c.mark(dve.tensor_tensor(eye[:, :], b[:, :], a[:, :], ALU.is_equal))
                c.mark(dve.tensor_tensor(y[:, :], a[:, :], b[:, :], ALU.is_gt))
                c.link(dve, dve.tensor_tensor(x[:, :], a[:, :], b[:, :], ALU.bitwise_xor))
                c.link(dve, dve.tensor_scalar(z[:, :], x[:, :], 1, None, ALU.is_equal))
                c.link(dve, dve.tensor_tensor(first[:, :], z[:, :], after[:, :], ALU.mult))
                c.link(dve, dve.tensor_tensor(x[:, :], x[:, :], y[:, :], ALU.mult))
                for l in range(R_LEVELS):
                    c.link(dve, dve.tensor_scalar(z[:, :], x[:, :], l, None, ALU.logical_shift_right))
                    c.link(dve, dve.tensor_scalar(lower[:, l, :], z[:, :], 1, None, ALU.is_equal))
    return lower, first, after, upto, eye


class Spare:
    Z, X, G = 2, 3, 2
    TILES = Z + X + G
    TAPS = 4

    def __init__(self, m, w, z0, gate0, conv, gate_bias, dest, h_kept, bonus_kept):
        self.m, self.z0, self.gate0, self.dest = m, z0, gate0, dest
        self.taps, self.conv_bias = conv
        self.gate_bias = gate_bias
        self.h_kept, self.bonus_kept = h_kept, bonus_kept
        self.w = w.rearrange("(k p) n -> p k n", p=P)
        self.landed = [m.sem(f"spare_landed{s}") for s in range(2)]
        self.made, self.kept, self.stored, self.conved = (m.sem(f"spare_{x}") for x in ("made", "kept", "stored", "conved"))

    def open(self, own, leaving):
        self.weights = own.enter_context(self.m.nc.sbuf_tensor("spare_weights", [P, 2, KT, P], F32))
        self.leaving = leaving

    def kind(self, c, j):
        if j < self.Z:
            return "z", self.Z * c + j
        if j < self.Z + self.X:
            return "x", self.X * c + j - self.Z
        return "gate", self.G * c + j - self.Z - self.X

    def place(self, c, j):
        kind, n = self.kind(c, j)
        if kind == "gate":
            return self.gate0 + n * P, RN * (self.Z + self.X) + n
        n = n + (RN * self.Z if kind == "x" else 0)
        return self.z0 + n * P, n

    def load(self, sp, c, j):
        sp.dma_start(self.weights[:, j % 2], self.w[:, :, bass.ds(self.place(c, j)[0], P)]).then_inc(self.landed[j % 2], 16)

    def store(self, sp, c, j):
        sp.wait_ge(self.kept, self.TILES * c + j + 2)
        n = self.place(c, j)[1]
        dst = self.dest[n] if isinstance(n, int) else self.dest[bass.ds(n, 1)].rearrange("a p t -> p (a t)")
        sp.dma_start(dst, self.leaving).then_inc(self.stored, 16)

    def chunk_loads(self, sp, c, last=False):
        for j in range(self.TILES):
            self.store(sp, c, j)
            if j + 2 < self.TILES:
                self.load(sp, c, j + 2)
            elif not last:
                self.load(sp, c + 1, j % 2)

    def multiply(self, pe, c, i, count):
        for x in range(i, i + count):
            j, k = x // KT, x % KT
            if k == 0:
                use = (self.TILES + 1 - j % 2) // 2 * c + j // 2
                pe.wait_ge(self.landed[j % 2], 16 * (use + 1))
                pe.wait_ge(self.kept, self.TILES * c + 1 + max(0, j - 1))
            ins = pe.matmul(self.m.ps[3 + j % 2][:, :], self.weights[:, j % 2, k, :], self.m.xT[:, k, :],
                            start=(k == 0), stop=(k == KT - 1))
            if k == KT - 1:
                ins.then_inc(self.made, 1)
        return i + count

    def ready(self, eng, c, j):
        eng.wait_ge(self.made, self.TILES * c + j + 1)
        eng.wait_ge(self.stored, 16 * (self.TILES * c + j + 1))

    def convolve(self, dve, c, j):
        n = self.kind(c, j)[1]
        tiles = RN * self.X
        bank, y = self.m.ps[3 + j % 2], self.leaving
        done = self.TAPS * (self.X * c + j - self.Z)
        self.ready(dve, c, j)
        for d in range(self.TAPS):
            tap = self.taps[:, bass.ds((self.TAPS - 1 - d) * tiles + n, 1)]
            if d == 0:
                ins = dve.tensor_scalar(y, bank[:, :], tap, self.conv_bias[:, bass.ds(n, 1)], ALU.mult, ALU.add)
            else:
                dve.wait_ge(self.conved, done + d)
                ins = dve.scalar_tensor_tensor(out=y[:, d:], in0=bank[:, :T - d], scalar=tap, in1=y[:, d:],
                                               op0=ALU.mult, op1=ALU.add)
            ins.then_inc(self.conved, 1)

    def keep(self, act, c, j):
        kind, n = self.kind(c, j)
        bank = self.m.ps[3 + j % 2]
        if kind == "x":
            act.wait_ge(self.conved, self.TAPS * (self.X * c + j - self.Z + 1))
            ins = act.activation(self.leaving, self.leaving, ACT.Silu)
        else:
            self.ready(act, c, j)
            if kind == "z":
                ins = act.activation(self.leaving, bank[:, :], ACT.Silu)
            else:
                ins = act.activation(self.leaving, bank[:, :], ACT.Sigmoid, bias=self.gate_bias[:, bass.ds(n, 1)])
        ins.then_inc(self.kept, 1)


def rwkv(m, cols, at, p, yT, w_decay, w_a, w_g, spare):
    nc = m.nc
    flat = lambda ap: ap.rearrange("p h t -> p (h t)")
    r, k, v = (p[:, j * RT:(j + 1) * RT, :] for j in range(3))
    col = lambda key, t: cols[:, at[key] + t:at[key] + t + 1]
    wflat = m.weights[:, :, :, :].rearrange("p s k c -> p (s k c)")
    w0 = wflat[:, 0:RT * T].rearrange("p (h t) -> p h t", t=T)
    w1 = wflat[:, RT * T:2 * RT * T].rearrange("p (h t) -> p h t", t=T)
    a_bank = lambda n: m.ps[n % 8]
    with ExitStack() as own:
        sb = lambda name, shape, dt=F32: own.enter_context(nc.sbuf_tensor(name, shape, dt))
        A, KK = (sb(f"rk_{x}", [P, RT, T]) for x in ("A", "KK"))
        S, BON = m.hT, m.xT
        elast = sb("rk_elast", [P, RT, RN])
        state = sb("rk_state", [P, RT, RH])
        early = ExitStack()
        ranks = early.enter_context(nc.sbuf_tensor("rk_ranks", [P, D], F32))
        B = early.enter_context(nc.sbuf_tensor("rk_B", [P, RT, T], F32))

        lora_landed = m.sem("rk_lora_landed")
        with nc.Block() as block:

            @block.sync
            def _(sp):
                sp.dma_start(ranks[0:RH, :], w_decay).then_inc(lora_landed, 16)
                sp.dma_start(ranks[RH:P, :], w_a).then_inc(lora_landed, 16)

            @block.gpsimd
            def _(pool):
                m.pool.link(pool, pool.memset(w0[:, :, :], 1.0))
                k4 = flat(w0).rearrange("p (n c) -> p n c", c=RC)
                m.pool.link(pool, pool.memset(k4[:, :, 0:1], 0.0))
                m.pool.mark(pool.memset(state[:, :, :], 0.0))

        low, lora_made, lora_kept = m.sem("rk_low"), m.sem("rk_lora_made"), m.sem("rk_lora_kept")
        with nc.Block() as block:

            @block.scalar
            def _(act):
                act.activation(p[0:RH, 24, :], p[0:RH, 24, :], ACT.Tanh).then_inc(low, 1)
                for n in range(2 * RT):
                    t = n % RT
                    act.wait_ge(lora_made, n + 1)
                    act.activation((S if n < RT else A)[:, t, :], a_bank(n)[:, :], ACT.Sigmoid,
                                   bias=col("w0" if n < RT else "a0", t)).then_inc(lora_kept, 1)
                m.act.mark(act.activation(p[:, 25, :], p[:, 25, :], ACT.Sigmoid))

            @block.tensor
            def _(pe):
                pe.wait_ge(lora_landed, 32)
                pe.wait_ge(low, 1)
                for n in range(2 * RT):
                    h, t = n // RT, n % RT
                    if n >= 8:
                        pe.wait_ge(lora_kept, n - 7)
                    q = slice(h * RH, (h + 1) * RH)
                    pe.matmul(a_bank(n)[:, :], ranks[q, t * P:(t + 1) * P], p[q, 24, :],
                              start=True, stop=True).then_inc(lora_made, 1)

            @block.vector
            def _(dve):
                c = m.dve
                dve.wait_ge(lora_kept, RT)
                c.link(dve, dve.tensor_scalar(flat(S), flat(S), -E_HALF, None, ALU.mult))
                c.mark(dve.tensor_tensor_scan(flat(B), flat(w0), flat(S), 0.0, ALU.mult, ALU.add))

        kk_sq, kk_sum, kk_root, bon_in, bon_sum, bon_out = (
            m.sem(f"rk_{x}") for x in ("kk_sq", "kk_sum", "kk_root", "bon_in", "bon_sum", "bon_out"))
        rows = Rows(m, early, "kk", RT, 1, True)
        root = early.enter_context(nc.sbuf_tensor("rk_root", [2 * RT, T], F32))
        with nc.Block() as block:

            @block.gpsimd
            def _(pool):
                rows.build(m, pool)

            @block.scalar
            def _(act):
                for t in range(RT):
                    act.wait_ge(kk_sq, 2 * t + 1)
                    act.activation(w1[:, t, :], KK[:, t, :], ACT.Square).then_inc(kk_sq, 1)
                act.wait_ge(kk_sum, 1)
                act.activation(root[:, :], m.ps[7][0:2 * RT, :], ACT.Sqrt).then_inc(kk_root, 1)

            @block.tensor
            def _(pe):
                m.pool.wait(pe)
                for t in range(RT):
                    pe.wait_ge(kk_sq, 2 * t + 2)
                    ins = pe.matmul(m.ps[7][0:2 * RT, :], rows.sum_of(t), w1[:, t, :], start=(t == 0), stop=(t == RT - 1))
                ins.then_inc(kk_sum, 1)
                pe.wait_ge(kk_root, 3)
                for t in range(RT):
                    pe.matmul(m.ps[t][:, :], rows.back[:, t, :], root[:, :], start=True, stop=True).then_inc(kk_sum, 1)
                for t in range(RT):
                    pe.wait_ge(bon_in, t + 1)
                    pe.matmul(m.ps[t][:, :], m.half_ones[:, :], w1[:, t, :], start=True, stop=True).then_inc(bon_sum, 1)

            @block.vector
            def _(dve):
                c = m.dve
                for t in range(RT):
                    if t:
                        dve.wait_ge(kk_sq, 2 * t)
                    dve.tensor_scalar(KK[:, t, :], k[:, t, :], col("k_k", t), None, ALU.mult).then_inc(kk_sq, 1)
                dve.wait_ge(kk_root, 1)
                dve.tensor_scalar(root[:, :], root[:, :], 1e-12, None, ALU.max).then_inc(kk_root, 1)
                dve.wait_ge(kk_root, 2)
                dve.reciprocal(root[:, :], root[:, :]).then_inc(kk_root, 1)
                for t in range(RT):
                    dve.wait_ge(kk_sum, t + 2)
                    c.mark(dve.tensor_tensor(KK[:, t, :], KK[:, t, :], m.ps[t][:, :], ALU.mult))
                for t in range(RT):
                    c.mark(dve.tensor_scalar(w0[:, t, :], A[:, t, :], 1.0, col("k_a", t), ALU.subtract, ALU.mult))
                c.wait(dve)
                c.link(dve, dve.scalar_tensor_tensor(out=flat(k), in0=flat(w0), scalar=1.0, in1=flat(k),
                                                     op0=ALU.add, op1=ALU.mult))
                c.mark(dve.tensor_tensor(flat(A), flat(KK), flat(A), ALU.mult))
                for t in range(RT):
                    dve.scalar_tensor_tensor(out=w1[:, t, :], in0=r[:, t, :], scalar=col("r_k", t), in1=k[:, t, :],
                                             op0=ALU.mult, op1=ALU.mult).then_inc(bon_in, 1)
                for t in range(RT):
                    dve.wait_ge(bon_sum, t + 1)
                    c.mark(dve.tensor_tensor(BON[:, t, :], m.ps[t][:, :], v[:, t, :], ALU.mult))

        exps, shifted = m.sem("rk_exps"), m.sem("rk_shifted")
        bonus_stored, h_back, bonus_back = m.sem("rk_bonus_stored"), m.sem("rk_h_back"), m.sem("rk_bonus_back")
        with nc.Block() as block:

            @block.scalar
            def _(act):
                act.activation(flat(w0), flat(B), ACT.Exp).then_inc(exps, 1)
                act.activation(elast[:, :, :], B[:, :, RC - 1:T:RC], ACT.Exp).then_inc(exps, 1)
                act.wait_ge(shifted, 1)
                act.activation(flat(w1), flat(w1), ACT.Exp).then_inc(exps, 1)
                act.activation(flat(S), flat(B), ACT.Exp, scale=-1.0).then_inc(exps, 1)

            @block.vector
            def _(dve):
                dve.tensor_tensor(flat(w1), flat(B), flat(S), ALU.subtract).then_inc(shifted, 1)

            @block.sync
            def _(sp):
                sp.dma_start(spare.bonus_kept, BON[:, :, :]).then_inc(bonus_stored, 16)
                sp.wait_ge(bonus_stored, 16)
                sp.dma_start(m.xT[:, :, :], spare.h_kept).then_inc(h_back, 16)
                sp.wait_ge(h_back, 16)

        early.close()
        with ExitStack() as late:
            spare.open(late, p[:, 24, :])
            rwkv_chunks(m, late, KK, A, k, r, v, w0, w1, S, elast, state, w0, spare)
        gates = sb("rk_gates", [P, D])
        B = w0

        head_sum, g_made, gates_landed = m.sem("rk_head_sum"), m.sem("rk_g_made"), m.sem("rk_gates_landed")
        with nc.Block() as block:

            @block.sync
            def _(sp):
                sp.dma_start(gates[:, :], w_g).then_inc(gates_landed, 16)
                sp.dma_start(BON[:, :, :], spare.bonus_kept).then_inc(bonus_back, 16)
                sp.wait_ge(bonus_back, 16)

            @block.tensor
            def _(pe):
                for t in range(RT):
                    pe.matmul(m.ps[t][:, :], m.half_ones[:, :], B[:, t, :], start=True, stop=True).then_inc(head_sum, 1)

            @block.vector
            def _(dve):
                for t in range(RT):
                    dve.wait_ge(head_sum, t + 1)
                    m.dve.mark(dve.scalar_tensor_tensor(out=B[:, t, :], in0=m.ps[t][:, :], scalar=-1.0 / RH,
                                                        in1=B[:, t, :], op0=ALU.mult, op1=ALU.add))
        g0 = at["ln_g"]
        group_norm(m, B, yT, cols[:, g0:g0 + RT], RT, 1, m.half_ones, RH, eps=64e-5)
        with nc.Block() as block:

            @block.sync
            def _(sp):
                sp.dma_start(m.hT[:, :, :], spare.h_kept).then_inc(h_back, 16)
                sp.wait_ge(h_back, 32)

            @block.tensor
            def _(pe):
                pe.wait_ge(gates_landed, 16)
                for t in range(RT):
                    pe.matmul(m.ps[t][:, :], gates[:, t * P:(t + 1) * P], p[:, 25, :], start=True, stop=True).then_inc(g_made, 1)

            @block.vector
            def _(dve):
                c = m.dve
                for t in range(RT):
                    c.mark(dve.scalar_tensor_tensor(out=BON[:, t, :], in0=BON[:, t, :], scalar=col("ln_b", t),
                                                    in1=yT[:, t, :], op0=ALU.add, op1=ALU.add))
                c.wait(dve)
                for t in range(RT):
                    dve.wait_ge(g_made, t + 1)
                    c.mark(dve.tensor_tensor(BON[:, t, :], m.ps[t][:, :], BON[:, t, :], ALU.mult))


def rwkv_chunks(m, own, KK, KA, k, r, v, e, ex, ei, elast, state, out, spare):
    nc = m.nc
    lower, first, after, upto, eye = rwkv_masks(m, own)
    names = ("alpha", "beta", "kappa", "rho", "v")
    with ExitStack() as tmp:
        sb = lambda name: tmp.enter_context(nc.sbuf_tensor(f"rc_{name}", [P, RT, RC], F32))
        st = {x: sb(x) for x in names}
        X, Y, TM, R, U, GAK, GRB, GRK, VT, BT, KT_ = (
            sb(x) for x in ("X", "Y", "TM", "R", "U", "gak", "grb", "grk", "vT", "betaT", "kappaT"))
        NL = tmp.enter_context(nc.sbuf_tensor("rc_NL", [P, R_LEVELS - 1, RT, RC], F32))
        f2 = lambda ap: ap.rearrange("p h t -> p (h t)")
        staged, made, masked, turned_kept, t_made, t_kept, xy_made, xy_kept, tail_made, tail_kept, state_kept = (
            m.sem(f"rc_{x}") for x in ("staged", "products", "masked", "turned_kept", "t_made", "t_kept", "xy_made",
                                       "xy_kept", "tail_made", "tail_kept", "state_kept"))
        over = lambda mask: mask.unsqueeze(1).to_broadcast([P, RT, RC])
        bank3 = lambda b: m.ps[b][:, :].rearrange("p (h t) -> p h t", t=RC)

        def heads(pe, bank, *terms):
            for t in range(RT):
                for h in range(2):
                    q = slice(h * RH, (h + 1) * RH)
                    for n, (lhs, rhs) in enumerate(terms):
                        o, l = bank[q, t * RC:(t + 1) * RC], lhs[q, t, :]
                        rr = rhs[q, t, :] if len(rhs.shape) == 3 else rhs[q, h * RH:(h + 1) * RH]
                        if t == h == n == 0:
                            wide = lhs[q, 0:2, :].rearrange("p a t -> p (a t)")
                            ins = pe.matmul(bank[:, 0:RC], wide, rr, start=True, stop=True)
                            if len(terms) == 1:
                                continue
                        ins = pe.matmul(o, l, rr, start=(n == 0), stop=(n == len(terms) - 1))
            return ins

        with nc.Block() as block:

            @block.vector
            def _(dve):
                with dve.Fori(0, RN) as c:
                    now = lambda ap: ap[:, :, bass.ds(c * RC, RC)]
                    dve.wait_ge(tail_made, 4 * c)
                    dve.wait_ge(tail_kept, 3 * c)
                    dve.wait_ge(state_kept, 2 * c)
                    dve.scalar_tensor_tensor(out=st["alpha"][:, :, :], in0=now(KK), scalar=-1.0, in1=now(ex),
                                             op0=ALU.mult, op1=ALU.mult).then_inc(staged, 1)
                    dve.tensor_tensor(st["beta"][:, :, :], now(KA), now(ei), ALU.mult).then_inc(staged, 1)
                    dve.tensor_tensor(st["kappa"][:, :, :], now(k), now(ei), ALU.mult).then_inc(staged, 1)
                    dve.tensor_tensor(st["rho"][:, :, :], now(r), now(e), ALU.mult).then_inc(staged, 1)
                    dve.tensor_copy(st["v"][:, :, :], now(v)).then_inc(staged, 1)
                    dve.wait_ge(made, 8 * c + 1)
                    dve.tensor_tensor(Y[:, :, :], bank3(0), over(first[:, :]), ALU.mult).then_inc(masked, 1)
                    dve.wait_ge(made, 8 * c + 2)
                    dve.tensor_tensor(X[:, :, :], bank3(1), over(lower[:, 0, :]), ALU.mult).then_inc(masked, 1)
                    dve.wait_ge(masked, 8 * c + 2)
                    dve.tensor_tensor(Y[:, :, :], Y[:, :, :], over(eye[:, :]), ALU.add).then_inc(masked, 1)
                    dve.tensor_tensor(X[:, :, :], X[:, :, :], over(eye[:, :]), ALU.add).then_inc(masked, 1)
                    dve.tensor_tensor(NL[:, :, :, :], bank3(1).unsqueeze(1).to_broadcast([P, R_LEVELS - 1, RT, RC]),
                                      lower[:, 1:R_LEVELS, :].unsqueeze(2).to_broadcast([P, R_LEVELS - 1, RT, RC]),
                                      ALU.mult).then_inc(masked, 1)
                    dve.wait_ge(made, 8 * c + 3)
                    dve.tensor_tensor(GAK[:, :, :], bank3(2), over(after[:, :]), ALU.mult).then_inc(masked, 1)
                    for l in range(1, R_LEVELS):
                        if l in (2, 3):
                            dst = (GRB, GRK)[l - 2]
                            dve.wait_ge(made, 8 * c + 5 + l)
                            dve.tensor_tensor(dst[:, :, :], bank3(l - 1), over(upto[:, :]), ALU.mult).then_inc(masked, 1)
                        for j, dst in enumerate((Y, X)[:2 if l < R_LEVELS - 1 else 1]):
                            dve.wait_ge(xy_made, (2 * R_LEVELS - 3) * c + 2 * (l - 1) + j + 1)
                            dve.tensor_tensor(dst[:, :, :], dst[:, :, :], bank3(5 + j), ALU.add).then_inc(xy_kept, 1)
                        if 2 <= l <= 4:
                            spare.convolve(dve, c, l)
                    dve.wait_ge(tail_made, 4 * c + 4)
                    dve.tensor_tensor(state[:, :, :], state[:, :, :], bank3(2), ALU.add).then_inc(state_kept, 1)
                    dve.wait_ge(state_kept, 2 * c + 1)
                    dve.tensor_tensor(state[:, :, :], state[:, :, :],
                                      elast[:, :, bass.ds(c, 1)].to_broadcast([P, RT, RH]), ALU.mult).then_inc(state_kept, 1)

            @block.scalar
            def _(act):
                act.sem_inc(spare.kept, 1)
                act.sem_inc(spare.stored, 16)
                with act.Fori(0, RN) as c:
                    for n, dst in enumerate((VT, BT, KT_)):
                        act.wait_ge(made, 8 * c + 4 + n)
                        act.copy(f2(dst), m.ps[5 + n][:, :]).then_inc(turned_kept, 1)
                    spare.keep(act, c, 0)
                    act.wait_ge(tail_made, 4 * c + 1)
                    act.copy(f2(R), m.ps[7][:, :]).then_inc(tail_kept, 1)
                    spare.keep(act, c, 1)
                    for l in range(1, R_LEVELS):
                        act.wait_ge(t_made, (R_LEVELS - 1) * c + l)
                        act.copy(f2(TM), m.ps[0][:, :]).then_inc(t_kept, 1)
                        if l >= 2:
                            spare.keep(act, c, l)
                    act.wait_ge(tail_made, 4 * c + 2)
                    act.copy(f2(U), m.ps[0][:, :]).then_inc(tail_kept, 1)
                    spare.keep(act, c, 6)
                    act.wait_ge(tail_made, 4 * c + 3)
                    act.copy(out[:, :, bass.ds(c * RC, RC)], bank3(1)).then_inc(tail_kept, 1)

            @block.tensor
            def _(pe):
                A, B, K, R_, V = (st[x] for x in names)
                XY = 2 * R_LEVELS - 3
                with pe.Fori(0, RN) as c:
                    i = spare.multiply(pe, c, 0, 8)
                    pe.wait_ge(staged, 5 * c + 5)
                    for b, (l, rr) in ((0, (B, A)), (1, (A, B)), (2, (K, A)),
                                       (5, (V, m.ident)), (6, (B, m.ident)), (7, (K, m.ident))):
                        heads(pe, m.ps[b], (l, rr)).then_inc(made, 1)
                    i = spare.multiply(pe, c, i, 8)
                    pe.wait_ge(masked, 8 * c + 6)
                    pe.wait_ge(turned_kept, 3 * c + 3)
                    heads(pe, m.ps[7], (A, state), (GAK, VT)).then_inc(tail_made, 1)
                    for l in range(1, R_LEVELS):
                        if l >= 2:
                            pe.wait_ge(xy_kept, XY * c + 2 * (l - 1))
                        heads(pe, m.ps[0], (NL[:, l - 1], Y)).then_inc(t_made, 1)
                        if l <= 2:
                            heads(pe, m.ps[l], ((B, K)[l - 1], R_)).then_inc(made, 1)
                        i = spare.multiply(pe, c, i, 2 if l <= 2 else 4)
                        pe.wait_ge(t_kept, (R_LEVELS - 1) * c + l)
                        heads(pe, m.ps[5], (X, TM)).then_inc(xy_made, 1)
                        if l < R_LEVELS - 1:
                            heads(pe, m.ps[6], (TM, X)).then_inc(xy_made, 1)
                        i = spare.multiply(pe, c, i, 4)
                    pe.wait_ge(xy_kept, XY * (c + 1))
                    pe.wait_ge(tail_kept, 3 * c + 1)
                    heads(pe, m.ps[0], (Y, R)).then_inc(tail_made, 1)
                    i = spare.multiply(pe, c, i, 4)
                    assert i == spare.TILES * KT
                    pe.wait_ge(masked, 8 * c + 8)
                    pe.wait_ge(tail_kept, 3 * c + 2)
                    heads(pe, m.ps[1], (state, R_), (U, GRB), (VT, GRK)).then_inc(tail_made, 1)
                    heads(pe, m.ps[2], (BT, U), (KT_, VT)).then_inc(tail_made, 1)

            @block.sync
            def _(sp):
                spare.load(sp, 0, 0)
                spare.load(sp, 0, 1)
                with sp.Fori(0, RN - 1) as c:
                    spare.chunk_loads(sp, c)
                spare.chunk_loads(sp, RN - 1, last=True)
                sp.wait_ge(spare.stored, 16 * (spare.TILES * RN + 1))


def rwkv_rows(attn_norm, mu, w0, a0, k_k, k_a, r_k, ln_g, ln_b):
    row = lambda ap: ap.rearrange("(k p) -> k p", p=P)
    return [
        ("attn_norm", row(attn_norm[0])), ("mu", row(mu[0])), ("w0", row(w0[0])), ("a0", row(a0[0])),
        ("k_k", row(k_k[0])), ("k_a", row(k_a[0])),
        ("r_k", r_k[0].rearrange("(k j) c -> k (j c)", j=2)), ("ln_g", row(ln_g[0])), ("ln_b", row(ln_b[0]))]


def copy_out(m, name, pairs):
    done = m.sem(name)
    with m.nc.Block() as block:

        @block.sync
        def _(sp):
            for dst, src in pairs:
                sp.dma_start(dst, src).then_inc(done, 16)
            sp.wait_ge(done, 16 * len(pairs))


def second_rwkv(m, w_in, cols, at, w_decay, w_a, w_g, x_kept, spare):
    nc = m.nc
    n0 = at["attn_norm"]
    norm(m, m.xT, m.hT, cols[:, n0:n0 + KT])
    x_stored = m.sem("x_h_stored")

    def store(block):
        @block.scalar
        def _(act):
            act.dma_start(x_kept, m.xT[:, :, :]).then_inc(x_stored, 16)
            act.dma_start(spare.h_kept, m.hT[:, :, :]).then_inc(x_stored, 16)
            act.wait_ge(x_stored, 32)

    with ExitStack() as own:
        p = own.enter_context(nc.sbuf_tensor("proj_rk", [P, R_TILES, T], F32))
        own2 = ExitStack()
        earlier = own2.enter_context(nc.sbuf_tensor("rk_earlier", [P, 2, T], F32))
        keep_mu = own2.enter_context(nc.sbuf_tensor("rk_keep_mu", [P, R_TILES], F32))
        shifted = m.sem("rk_token_shifted")
        mu0 = at["mu"]

        def less_mu(dve):
            m.dve.link(dve, dve.tensor_scalar(keep_mu[:, :], cols[:, mu0:mu0 + R_TILES], -1.0, 1.0, ALU.mult, ALU.add))

        def keep(dve, t, bank):
            one = lambda ap, n: ap[:, n:n + 1] if isinstance(n, int) else ap[:, bass.ds(n, 1)]
            e = earlier[:, m.ps.index(bank) % 2, :]
            dve.tensor_scalar(e, bank[:, :], one(cols, mu0 + t), None, ALU.mult).then_inc(shifted, 1)
            dve.tensor_scalar(at_tile(p, t)[:, 0:1], bank[:, 0:1], one(keep_mu, t), None, ALU.mult)
            dve.wait_ge(shifted, t + 1)
            return dve.scalar_tensor_tensor(out=at_tile(p, t)[:, 1:T], in0=bank[:, 1:T], scalar=one(keep_mu, t),
                                            in1=e[:, 0:T - 1], op0=ALU.mult, op1=ALU.add)

        project(m, w_in[0], R_TILES, lambda k: m.hT[:, k, :], KT, keep, other=store, setup=less_mu)
        own2.close()
        yT = p[:, 0:RT, :]
        rwkv(m, cols, at, p, yT, w_decay[0], w_a[0], w_g[0], spare)


SH = 32
SG = 4
SC = 128
SN = T // SC
S_TILES = 16
X_TILES = S_TILES + 2 * SG
GH = SH // SG


def ssd(m, p, w_in_dt, dt_bias, a_log, d_skip, load_tiles):
    nc = m.nc
    with ExitStack() as own:
        sb = lambda name, shape, dt=F32: own.enter_context(nc.sbuf_tensor(name, shape, dt))
        w_dt = sb("sd_w_dt", [P, KT, SH])
        small = sb("sd_small", [SH, 4])
        dt, pos, acs, keep = (sb(f"sd_{x}", [SH, T]) for x in ("dt", "pos", "acs", "keep"))
        tok = sb("sd_tok", [P, 2, SN, SH])
        left = sb("sd_left", [P, SN, SH])
        whole = sb("sd_whole", [P, SN, SH])
        last_row = sb("sd_last_row", [P, P])
        upto = sb("sd_upto", [P, SC])
        d_col = sb("sd_d", [P, S_TILES])

        landed, made, soft, turned = (m.sem(f"sd_{x}") for x in ("landed", "dt_made", "soft", "turned"))
        with nc.Block() as block:

            @block.sync
            def _(sp):
                sp.dma_start(w_dt[:, :, :], w_in_dt.rearrange("(k p) n -> p k n", p=P)).then_inc(landed, 16)
                sp.dma_start(small[:, 0:1], dt_bias.rearrange("(h a) -> h a", a=1)).then_inc(landed, 16)
                sp.dma_start(small[:, 1:2], a_log.rearrange("(h a) -> h a", a=1)).then_inc(landed, 16)
                for h in range(2):
                    src = d_skip.rearrange("(a t j) -> a t j", a=1, j=2)[:, :, h]
                    with nc.allow_non_contiguous_dma(reason="32 numbers"):
                        sp.dma_start(d_col[h * RH:(h + 1) * RH, :], src.to_broadcast([RH, S_TILES])).then_inc(landed, 16)

            @block.gpsimd
            def _(pool):
                c = m.pool
                c.mark(pool.memset(keep[:, :], 1.0))
                c.mark(pool.memset(last_row[:, :], 1.0))
                c.mark(pool.memset(upto[:, :], 1.0))
                c.wait(pool)
                c.link(pool, pool.memset(keep[:, 0:T:SC], 0.0))
                c.link(pool, pool.affine_select(out=last_row[:, :], in_=last_row[:, :], compare_op=ALU.is_ge, fill=0.0,
                                                base=-(P - 1), pattern=[[0, P]], channel_multiplier=1))
                c.link(pool, pool.affine_select(out=upto[:, :], in_=upto[:, :], compare_op=ALU.is_ge, fill=0.0,
                                                base=0, pattern=[[1, SC]], channel_multiplier=-1))

            @block.tensor
            def _(pe):
                pe.wait_ge(landed, 80)
                for k in range(KT):
                    ins = pe.matmul(m.ps[0][0:SH, :], w_dt[:, k, :], m.hT[:, k, :], start=(k == 0), stop=(k == KT - 1))
                ins.then_inc(made, 1)
                pe.wait_ge(soft, 9)
                for j, src in enumerate((dt, acs)):
                    for n in range(SN):
                        ins = pe.transpose(m.ps[1][:, (j * SN + n) * SH:(j * SN + n + 1) * SH],
                                           src[:, n * SC:(n + 1) * SC], m.ident[0:SH, 0:SH])
                ins.then_inc(turned, 1)
                pe.wait_ge(soft, 10)
                pe.matmul(m.ps[2][:, 0:SN * SH], last_row[:, :], tok[:, 1].rearrange("p n h -> p (n h)"),
                          start=True, stop=True).then_inc(turned, 1)

            @block.scalar
            def _(act):
                tiles_landed = load_tiles(act)
                act.wait_ge(landed, 80)
                act.activation(small[:, 2:3], small[:, 1:2], ACT.Exp).then_inc(soft, 1)
                act.wait_ge(soft, 3)
                act.activation(dt[:, :], dt[:, :], ACT.Abs).then_inc(soft, 1)
                act.wait_ge(soft, 4)
                act.activation(dt[:, :], dt[:, :], ACT.Exp, scale=-1.0).then_inc(soft, 1)
                act.wait_ge(soft, 5)
                act.activation(dt[:, :], dt[:, :], ACT.Ln, bias=1.0).then_inc(soft, 1)
                act.wait_ge(soft, 12)
                act.activation(left[:, :, :], left[:, :, :], ACT.Exp).then_inc(soft, 1)
                act.activation(whole[:, :, :], whole[:, :, :], ACT.Exp).then_inc(soft, 1)
                tiles_landed()

            @block.vector
            def _(dve):
                dve.wait_ge(made, 1)
                dve.wait_ge(soft, 1)
                dve.tensor_scalar(dt[:, :], m.ps[0][0:SH, :], small[:, 0:1], None, ALU.add).then_inc(soft, 1)
                dve.tensor_scalar(pos[:, :], m.ps[0][0:SH, :], small[:, 0:1], 0.0, ALU.add, ALU.max).then_inc(soft, 1)
                dve.wait_ge(soft, 6)
                dve.tensor_tensor(dt[:, :], dt[:, :], pos[:, :], ALU.add).then_inc(soft, 1)
                dve.wait_ge(soft, 7)
                dve.tensor_scalar(pos[:, :], dt[:, :], small[:, 2:3], -1.0, ALU.mult, ALU.mult).then_inc(soft, 1)
                dve.wait_ge(soft, 8)
                m.pool.wait(dve)
                dve.tensor_tensor_scan(acs[:, :], keep[:, :], pos[:, :], 0.0, ALU.mult, ALU.add).then_inc(soft, 1)
                dve.wait_ge(turned, 1)
                dve.tensor_copy(tok[:, :, :, :].rearrange("p a n h -> p (a n h)"), m.ps[1][:, 0:2 * SN * SH]).then_inc(soft, 1)
                dve.wait_ge(turned, 2)
                b3 = m.ps[2][:, 0:SN * SH].rearrange("p (n h) -> p n h", h=SH)
                dve.tensor_tensor(left[:, :, :], b3, tok[:, 1], ALU.subtract).then_inc(soft, 1)
                dve.tensor_copy(whole[:, :, :], b3).then_inc(soft, 1)

        state = sb("sd_state", [P, SH * RH])
        xdt = sb("sd_xdt", [P, SH * RH])
        xdts = sb("sd_xdts", [P, SH * RH])
        bt = sb("sd_bt", [P, SG, SC])
        cb = sb("sd_cb", [P, SG, SC])
        dec = sb("sd_dec", [P, 2, GH, SC])
        inn = sb("sd_inn", [P, 2, GH, SC])
        names = ("x_turned", "rows_kept", "cb_made", "spread", "exps", "seg", "scores", "y_made", "y_kept", "s_made", "s_kept", "s_read")
        x_turned, rows_kept, cb_made, spread, exps, seg_made, scores, y_made, y_kept, s_made, s_kept, s_read = (
            m.sem(f"sd_{x}_n") for x in names)
        h3 = lambda ap: ap.rearrange("p (h c) -> p h c", c=RH)

        with nc.Block() as block:

            @block.tensor
            def _(pe):
                for n in range(SN):
                    t = slice(n * SC, (n + 1) * SC)
                    if n:
                        pe.wait_ge(y_kept, 4 * SG * n)
                        pe.wait_ge(s_kept, 2 * SG * n)
                    for b in range(4):
                        for j in range(4):
                            ins = pe.transpose(m.ps[b][:, j * P:(j + 1) * P], p[:, 4 * b + j, t], m.ident[:, :])
                        ins.then_inc(x_turned, 1)
                    for g in range(SG):
                        ins = pe.transpose(m.ps[4][:, g * P:(g + 1) * P], p[:, S_TILES + g, t], m.ident[:, :])
                    ins.then_inc(x_turned, 1)
                    for g in range(SG):
                        ins = pe.matmul(m.ps[5][:, g * P:(g + 1) * P], p[:, S_TILES + g, t], p[:, S_TILES + SG + g, t],
                                        start=True, stop=True)
                    ins.then_inc(x_turned, 1)
                    pe.wait_ge(rows_kept, 14 * (n + 1))
                    for g in range(SG + 1):
                        if g < SG:
                            i = n * SG + g
                            if i >= 2:
                                pe.wait_ge(exps, 3 * (i - 1))
                            for h in range(GH):
                                b = 2 * (i % 2) + h // 4
                                ins = pe.matmul(m.ps[b][:, (h % 4) * SC:(h % 4 + 1) * SC],
                                                m.ident[0:SH, g * GH + h:g * GH + h + 1].to_broadcast([SH, P]), acs[:, t],
                                                start=True, stop=True)
                                if h % 4 == 3:
                                    ins.then_inc(spread, 1)
                        if g >= 1:
                            i = n * SG + g - 1
                            gp = g - 1
                            bank = m.ps[4 + i % 2]
                            pe.wait_ge(scores, 2 * (i + 1))
                            if i >= 2:
                                pe.wait_ge(y_kept, 4 * (i - 1))
                            for h in range(GH):
                                hh = gp * GH + h
                                o = bank[(h % 2) * RH:(h % 2 + 1) * RH, (h // 2) * SC:(h // 2 + 1) * SC]
                                ins = pe.matmul(o, xdt[:, hh * RH:(hh + 1) * RH], dec[:, i % 2, h, :],
                                                start=True, stop=(n == 0))
                                if n:
                                    ins = pe.matmul(o, state[:, hh * RH:(hh + 1) * RH], inn[:, i % 2, h, :],
                                                    start=False, stop=True)
                            ins.then_inc(y_made, 1)
                            if i >= 2:
                                pe.wait_ge(s_kept, 2 * (i - 1))
                            pe.matmul(m.ps[6 + i % 2][:, :], bt[:, gp, :], xdts[:, gp * 512:(gp + 1) * 512],
                                      start=True, stop=True).then_inc(s_made, 1)

            @block.scalar
            def _(act):
                for n in range(SN):
                    for g in range(SG):
                        i = n * SG + g
                        if i >= 2:
                            act.wait_ge(y_made, i - 1)
                        for b in range(2):
                            act.wait_ge(seg_made, GH * i + 4 * (b + 1))
                            bank = m.ps[2 * (i % 2) + b]
                            act.activation(inn[:, i % 2, 4 * b:4 * b + 4, :].rearrange("p h l -> p (h l)"), bank[:, :],
                                           ACT.Exp).then_inc(exps, 1)
                        act.wait_ge(seg_made, GH * (i + 1))
                        act.activation(dec[:, i % 2], dec[:, i % 2], ACT.Exp).then_inc(exps, 1)

            @block.vector
            def _(dve):
                def keep_y(i):
                    n, g = i // SG, i % SG
                    t = slice(n * SC, (n + 1) * SC)
                    bank = m.ps[4 + i % 2]
                    dve.wait_ge(y_made, i + 1)
                    for j in range(4):
                        x = p[:, 4 * g + j, t]
                        dve.scalar_tensor_tensor(out=x, in0=x, scalar=d_col[:, 4 * g + j:4 * g + j + 1],
                                                 in1=bank[:, j * SC:(j + 1) * SC], op0=ALU.mult,
                                                 op1=ALU.add).then_inc(y_kept, 1)
                    dve.wait_ge(s_made, i + 1)
                    s = state[:, g * 512:(g + 1) * 512]
                    if n == 0:
                        dve.tensor_copy(s, m.ps[6 + i % 2][:, :]).then_inc(s_kept, 2)
                    else:
                        dve.tensor_tensor(h3(s), h3(s), whole[:, n, g * GH:(g + 1) * GH].unsqueeze(2)
                                          .to_broadcast([P, GH, RH]), ALU.mult).then_inc(s_kept, 1)
                        dve.wait_ge(s_kept, 2 * i + 1)
                        dve.tensor_tensor(s, s, m.ps[6 + i % 2][:, :], ALU.add).then_inc(s_kept, 1)

                for n in range(SN):
                    if n:
                        dve.wait_ge(y_kept, 4 * SG * n)
                    for b in range(4):
                        q = slice(b * 512, (b + 1) * 512)
                        wide = lambda ap: ap[:, n, b * GH:(b + 1) * GH].unsqueeze(2).to_broadcast([P, GH, RH])
                        dve.wait_ge(x_turned, 6 * n + b + 1)
                        dve.tensor_tensor(h3(xdt[:, q]), h3(m.ps[b][:, :]), wide(tok[:, 0]), ALU.mult).then_inc(rows_kept, 1)
                        dve.wait_ge(rows_kept, 14 * n + 2 * b + 1)
                        dve.tensor_tensor(h3(xdts[:, q]), h3(xdt[:, q]), wide(left), ALU.mult).then_inc(rows_kept, 1)
                    dve.wait_ge(x_turned, 6 * n + 5)
                    dve.tensor_copy(bt[:, :, :].rearrange("p g s -> p (g s)"), m.ps[4][:, :]).then_inc(rows_kept, 1)
                    dve.wait_ge(x_turned, 6 * n + 6)
                    dve.tensor_tensor(cb[:, :, :], m.ps[5][:, :].rearrange("p (g l) -> p g l", l=SC),
                                      upto[:, :].unsqueeze(1).to_broadcast([P, SG, SC]), ALU.mult).then_inc(rows_kept, 5)
                    for g in range(SG):
                        i = n * SG + g
                        if i >= 2:
                            dve.wait_ge(y_made, i - 1)
                        for h in range(GH):
                            if h % 4 == 0:
                                dve.wait_ge(spread, 2 * i + h // 4 + 1)
                            hh = g * GH + h
                            dve.tensor_scalar(dec[:, i % 2, h, :], m.ps[2 * (i % 2) + h // 4][:, (h % 4) * SC:(h % 4 + 1) * SC],
                                              tok[:, 1, n, hh:hh + 1], 0.0, ALU.subtract, ALU.min).then_inc(seg_made, 1)
                        dve.wait_ge(exps, 3 * (i + 1))
                        dve.wait_ge(rows_kept, 14 * (n + 1))
                        d = dec[:, i % 2]
                        dve.tensor_tensor(d, d, cb[:, g, :].unsqueeze(1).to_broadcast([P, GH, SC]),
                                          ALU.mult).then_inc(scores, 1)
                        dve.tensor_tensor(inn[:, i % 2], inn[:, i % 2],
                                          p[:, S_TILES + SG + g, n * SC:(n + 1) * SC].unsqueeze(1).to_broadcast([P, GH, SC]),
                                          ALU.mult).then_inc(scores, 1)
                        if g >= 1:
                            keep_y(i - 1)
                    keep_y(n * SG + SG - 1)


def second_ssd(m, w_dt, norms, norms_at, dt_bias, a_log, d_skip, y, projected, then):
    nc = m.nc
    y_landed = m.sem("sd_x_landed")

    def load_tiles(act):
        for g in range(X_TILES // 4):
            act.dma_start(y[:, 4 * g:4 * g + 4, :],
                          projected[S_TILES + 4 * g:S_TILES + 4 * g + 4].rearrange("k p t -> p k t")).then_inc(y_landed, 16)
        return lambda: act.wait_ge(y_landed, 16 * (X_TILES // 4))

    ssd(m, y, w_dt, dt_bias[0], a_log[0], d_skip[0], load_tiles)
    with ExitStack() as own:
        z = own.enter_context(nc.sbuf_tensor("sd_z", [P, S_TILES, T], F32))
        z_landed = [m.sem(f"sd_z_landed{j}") for j in range(SG)]
        with nc.Block() as block:

            @block.sync
            def _(sp):
                for j in range(SG):
                    sp.dma_start(z[:, 4 * j:4 * j + 4, :],
                                 projected[4 * j:4 * j + 4].rearrange("k p t -> p k t")).then_inc(z_landed[j], 16)
                prefetch(m, sp, *then)

            @block.vector
            def _(dve):
                for j in range(SG):
                    dve.wait_ge(z_landed[j], 16)
                    q = slice(4 * j, 4 * j + 4)
                    m.dve.mark(dve.tensor_tensor(y[:, q, :], y[:, q, :], z[:, q, :], ALU.mult))
    n0 = norms_at["norm_g"]
    group_norm(m, y, y, norms[:, n0:n0 + S_TILES], SG, S_TILES // SG, m.ones, D // 2)


def second_merge(m, y, projected, w_up_rwkv, w_up_ssd, w_out, x_kept):
    nc = m.nc
    with ExitStack() as own:
        sb = lambda name, shape, dt=F32: own.enter_context(nc.sbuf_tensor(name, shape, dt))
        merged = sb("mix_merged", [P, KT, T])
        gates = sb("mix_gates", [P, 2 * KT, T])
        landed, x_back, steps = (m.sem(f"mix_{x}") for x in ("gates_landed", "x_back", "steps"))
        up_b = m.hT

        def load_gates(block):
            @block.scalar
            def _(act):
                for j in range(4):
                    act.dma_start(gates[:, 4 * j:4 * j + 4, :],
                                  projected[4 * j:4 * j + 4].rearrange("k p t -> p k t")).then_inc(landed, 16)

        def load_x(block):
            @block.scalar
            def _(act):
                act.dma_start(m.xT[:, :, :], x_kept).then_inc(x_back, 16)
                act.wait_ge(x_back, 16)

        def gated_a(dve, t, bank):
            return dve.tensor_tensor(at_tile(merged, t), bank[:, :], at_tile(gates, t), ALU.mult)

        def gated_b(dve, t, bank):
            b = at_tile(up_b, t)
            dve.tensor_tensor(b, bank[:, :], b, ALU.add).then_inc(steps, 1)
            dve.wait_ge(steps, 2 * t + 1)
            dve.tensor_tensor(b, b, at_tile(gates, t + KT), ALU.mult).then_inc(steps, 1)
            dve.wait_ge(steps, 2 * t + 2)
            return dve.tensor_tensor(at_tile(merged, t), b, at_tile(merged, t), ALU.add)

        up = w_up_ssd[0]
        project(m, w_up_rwkv[0], KT, lambda k: m.xT[:, k, :], KT, gated_a, other=load_gates,
                setup=lambda dve: dve.wait_ge(landed, 64), then=(up[0:D, :], KT))
        project(m, up[0:D, :], KT, lambda k: y[:, k, :], KT,
                lambda dve, t, bank: dve.tensor_copy(at_tile(up_b, t), bank[:, :]), other=load_x, then=(up[D:2 * D, :], KT))
        project(m, up[D:2 * D, :], KT, lambda k: y[:, KT + k, :], KT, gated_b, then=(w_out[0], KT))

        def keep(dve, t, bank):
            return dve.tensor_tensor(at_tile(m.xT, t), bank[:, :], at_tile(m.xT, t), ALU.add)
        project(m, w_out[0], KT, lambda k: merged[:, k, :], KT, keep)


NG = 4
EG = 8
NE = NG * EG
DE = 512
TOP = 2
EXTRA = T * TOP // P - 1
BLOCKS = NE + EXTRA


def load_router(m, own, w_rg, b_rg, w_re, b_re):
    w = own.enter_context(m.nc.sbuf_tensor("mo_w", [P, KT, NG + NE], F32))
    b = own.enter_context(m.nc.sbuf_tensor("mo_b", [P, NG + NE], F32))
    parts = []
    for src, bias, c, n in ((w_rg, b_rg, 0, NG), (w_re, b_re, NG, NE)):
        parts.append((w[:, :, c:c + n], src.rearrange("(k p) n -> p k n", p=P)))
        parts.append((b[:, c:c + n], bias.rearrange("(a n) -> a n", a=1).to_broadcast([P, n])))
    landed = m.sem("router_landed")

    def load(block):
        @block.sync
        def _(sp):
            for dst, src in parts:
                sp.dma_start(dst, src).then_inc(landed, 16)
            sp.wait_ge(landed, 16 * len(parts))
    return w, b, load


def route(m, w, bias, gate, dest, extra_expert, slot_token, meanwhile):
    nc = m.nc
    with ExitStack() as tmp:
        sb = lambda name, shape, dt=F32: tmp.enter_context(nc.sbuf_tensor(name, shape, dt))
        logit = sb("mo_logit", [P, TT, NG + NE])
        top = sb("mo_top", [P, TT, 1])
        ex = sb("mo_ex", [P, TT, NG])
        total = sb("mo_total", [P, TT, 1])
        eq = sb("mo_eq", [P, TT, NG])
        grp = sb("mo_grp", [P, TT, 1])
        hot = sb("mo_hot", [P, TT, NG])
        mix = sb("mo_mix", [P, TT, NG, EG])
        sel = sb("mo_sel", [P, TT, EG])
        val8 = sb("mo_val8", [P, TT, 8])
        ind8 = sb("mo_ind8", [P, TT, 8], U32)
        indf = sb("mo_indf", [P, TT, 8])
        e2 = sb("mo_e2", [P, TT, 1])
        inv = sb("mo_inv", [P, TT, 1])
        expert = sb("mo_expert", [P, TT, TOP])
        mask = sb("mo_mask", [P, TT, TOP, NE])
        both = sb("mo_both", [P, TT, NE])
        rank = sb("mo_rank", [P, TT, NE])
        pick = sb("mo_pick", [P, TT, TOP, NE])
        rk = sb("mo_rk", [P, TT, TOP])
        st = sb("mo_st", [P, TT, TOP])
        over = sb("mo_over", [P, TT, TOP])
        base = sb("mo_base", [P, TT, TOP])
        count = sb("mo_count", [P, NE])
        more = sb("mo_more", [P, NE])
        tmp32 = sb("mo_tmp32", [P, NE])
        ends = sb("mo_ends", [P, NE])
        starts = sb("mo_starts", [P, NE])
        ones32 = sb("mo_ones32", [P, NE])
        down4 = sb("mo_down4", [P, NG])
        up32 = sb("mo_up32", [P, NE])
        before = sb("mo_before", [P, P])
        token = sb("mo_token", [P, TT])
        xe = sb("mo_xe", [P, EXTRA, NE])
        upx = sb("mo_upx", [P, EXTRA])
        xf = sb("mo_xf", [P, EXTRA + 1])
        zero = sb("mo_zero", [BLOCKS, P])
        logits_made, ex_made, counted, ready, dest_made = (
            m.sem(f"mo_{x}") for x in ("logits", "exps", "counted", "iotas", "dest_made"))
        zeroed, scattered = m.gathers[16:18]
        with nc.Block() as block:

            @block.sync
            def _(sp):
                meanwhile(sp)

            @block.gpsimd
            def _(pool):
                c = m.pool
                iota = lambda ap, pat, b, cm: c.link(pool, pool.iota(ap, pat, base=b, channel_multiplier=cm,
                                                                     allow_small_or_imprecise_dtypes=True))
                c.link(pool, pool.memset(zero[:, :], 0.0))
                iota(down4[:, :], [[-1, NG]], NG, 0)
                iota(up32[:, :], [[1, NE]], 0, 0)
                iota(upx[:, :], [[1, EXTRA]], 0, 0)
                iota(token[:, :], [[P, TT]], 0, 1)
                c.link(pool, pool.memset(ones32[:, :], 1.0))
                c.link(pool, pool.memset(before[:, :], 1.0))
                pool.affine_select(out=before[:, :], in_=before[:, :], compare_op=ALU.is_gt, fill=0.0, base=0,
                                   pattern=[[1, P]], channel_multiplier=-1).then_inc(ready, 1)
                pool.wait_ge(ready, 1)
                pool.dma_start(slot_token, zero[:, :]).then_inc(zeroed, 16)
                pool.wait_ge(zeroed, 16)
                pool.wait_ge(dest_made, 1)
                for t in range(TT):
                    for j in range(TOP):
                        n = t * TOP + j
                        pool.indirect_dma_start(
                            out=slot_token.rearrange("b (s a) -> (b s) a", a=1),
                            out_offset=bass.IndirectOffsetOnAxis(ap=dest[:, n:n + 1], axis=0),
                            in_=token[:, t:t + 1], in_offset=None).then_inc(scattered, 16)
                pool.wait_ge(scattered, 16 * TT * TOP)

            @block.tensor
            def _(pe):
                for t in range(TT):
                    for k in range(KT):
                        ins = pe.matmul(m.ps[0][:, t * 64:t * 64 + NG + NE], m.hT[:, k, t * P:(t + 1) * P], w[:, k, :],
                                        start=(k == 0), stop=(k == KT - 1))
                ins.then_inc(logits_made, 1)
                pe.wait_ge(ready, 1)
                pe.wait_ge(counted, 1)
                for t in range(TT):
                    for u in range(t + 1):
                        ins = pe.matmul(m.ps[1][:, t * NE:(t + 1) * NE], (before if u == t else m.ones)[:, :], both[:, u, :],
                                        start=(u == 0), stop=(u == t))
                for u in range(TT):
                    ins = pe.matmul(m.ps[2][:, 0:NE], m.ones[:, :], both[:, u, :], start=(u == 0), stop=(u == TT - 1))
                ins.then_inc(counted, 1)

            @block.scalar
            def _(act):
                act.wait_ge(ex_made, 1)
                act.activation(ex[:, :, :], ex[:, :, :], ACT.Exp).then_inc(ex_made, 1)
                act.wait_ge(ex_made, 3)
                act.activation(e2[:, :, :], e2[:, :, :], ACT.Exp).then_inc(ex_made, 1)

            @block.vector
            def _(dve):
                c = m.dve
                L = lambda ins: c.link(dve, ins)
                bc = lambda ap, shape: ap.to_broadcast(shape)
                dve.wait_ge(ready, 1)
                dve.wait_ge(logits_made, 1)
                b3 = m.ps[0][:, 0:TT * 64].rearrange("p (t n) -> p t n", n=64)[:, :, 0:NG + NE]
                L(dve.tensor_tensor(logit[:, :, :], b3, bias[:, :].unsqueeze(1).to_broadcast([P, TT, NG + NE]), ALU.add))
                g, e = logit[:, :, 0:NG], logit[:, :, NG:NG + NE]
                L(dve.tensor_reduce(top[:, :, :], g, AX.X, ALU.max))
                dve.tensor_tensor(ex[:, :, :], g, bc(top[:, :, :], [P, TT, NG]), ALU.subtract).then_inc(ex_made, 1)
                L(dve.tensor_tensor(eq[:, :, :], g, bc(top[:, :, :], [P, TT, NG]), ALU.is_equal))
                L(dve.tensor_tensor(eq[:, :, :], eq[:, :, :], down4[:, :].unsqueeze(1).to_broadcast([P, TT, NG]), ALU.mult))
                L(dve.tensor_reduce(grp[:, :, :], eq[:, :, :], AX.X, ALU.max))
                L(dve.tensor_tensor(hot[:, :, :], down4[:, :].unsqueeze(1).to_broadcast([P, TT, NG]),
                                    bc(grp[:, :, :], [P, TT, NG]), ALU.is_equal))
                L(dve.tensor_scalar(grp[:, :, :], grp[:, :, :], -1.0, float(NG), ALU.mult, ALU.add))
                L(dve.tensor_tensor(mix[:, :, :, :], e.rearrange("p t (g n) -> p t g n", n=EG),
                                    hot[:, :, :].unsqueeze(3).to_broadcast([P, TT, NG, EG]), ALU.mult))
                L(dve.tensor_reduce(sel[:, :, :], mix[:, :, :, :].rearrange("p t g n -> p t n g"), AX.X, ALU.add))
                for t in range(TT):
                    c.mark(dve.max(val8[:, t, :], sel[:, t, :]))
                c.wait(dve)
                for t in range(TT):
                    c.mark(dve.max_index(ind8[:, t, :], val8[:, t, :], sel[:, t, :]))
                dve.wait_ge(ex_made, 2)
                dve.tensor_tensor(e2[:, :, :], val8[:, :, 1:2], val8[:, :, 0:1], ALU.subtract).then_inc(ex_made, 1)
                L(dve.tensor_reduce(total[:, :, :], ex[:, :, :], AX.X, ALU.add))
                L(dve.tensor_copy(indf[:, :, :], ind8[:, :, :]))
                dve.wait_ge(ex_made, 4)
                L(dve.tensor_scalar(inv[:, :, :], e2[:, :, :], 1.0, None, ALU.add))
                L(dve.tensor_tensor(inv[:, :, :], inv[:, :, :], total[:, :, :], ALU.mult))
                L(dve.reciprocal(inv[:, :, :], inv[:, :, :]))
                g3 = gate[:, :].rearrange("p (t j) -> p t j", j=TOP)
                c.mark(dve.tensor_copy(g3[:, :, 0:1], inv[:, :, :]))
                c.mark(dve.tensor_tensor(g3[:, :, 1:2], inv[:, :, :], e2[:, :, :], ALU.mult))
                L(dve.scalar_tensor_tensor(out=expert[:, :, 0:1], in0=grp[:, :, :], scalar=float(EG), in1=indf[:, :, 0:1],
                                           op0=ALU.mult, op1=ALU.add))
                L(dve.scalar_tensor_tensor(out=expert[:, :, 1:2], in0=grp[:, :, :], scalar=float(EG), in1=indf[:, :, 1:2],
                                           op0=ALU.mult, op1=ALU.add))
                for j in range(TOP):
                    c.mark(dve.tensor_tensor(mask[:, :, j, :], up32[:, :].unsqueeze(1).to_broadcast([P, TT, NE]),
                                             bc(expert[:, :, j:j + 1], [P, TT, NE]), ALU.is_equal))
                c.wait(dve)
                dve.tensor_tensor(both[:, :, :], mask[:, :, 0, :], mask[:, :, 1, :], ALU.add).then_inc(counted, 1)
                dve.wait_ge(counted, 2)
                c.mark(dve.tensor_copy(rank[:, :, :], m.ps[1][:, 0:TT * NE].rearrange("p (t n) -> p t n", n=NE)))
                L(dve.tensor_copy(count[:, :], m.ps[2][:, 0:NE]))
                L(dve.tensor_scalar(more[:, :], count[:, :], float(P), None, ALU.is_gt))
                for q in range(2, T // P):
                    L(dve.tensor_scalar(tmp32[:, :], count[:, :], float(q * P), None, ALU.is_gt))
                    L(dve.tensor_tensor(more[:, :], more[:, :], tmp32[:, :], ALU.add))
                L(dve.tensor_tensor_scan(ends[:, :], ones32[:, :], more[:, :], 0.0, ALU.mult, ALU.add))
                L(dve.tensor_tensor(starts[:, :], ends[:, :], more[:, :], ALU.subtract))
                L(dve.tensor_tensor(xe[:, :, :], ends[:, :].unsqueeze(1).to_broadcast([P, EXTRA, NE]),
                                    upx[:, :].unsqueeze(2).to_broadcast([P, EXTRA, NE]), ALU.is_le))
                L(dve.tensor_reduce(xf[:, 0:EXTRA], xe[:, :, :], AX.X, ALU.add))
                L(dve.tensor_scalar(xf[:, 0:EXTRA], xf[:, 0:EXTRA], float(NE - 1), None, ALU.min))
                L(dve.tensor_copy(xf[:, EXTRA:EXTRA + 1], ends[:, NE - 1:NE]))
                L(dve.tensor_copy(extra_expert[:, :], xf[:, :]))
                for dst, src in ((rk, rank[:, :, :]), (st, starts[:, :].unsqueeze(1).to_broadcast([P, TT, NE]))):
                    for j in range(TOP):
                        c.mark(dve.tensor_tensor(pick[:, :, j, :], mask[:, :, j, :], src, ALU.mult))
                    c.wait(dve)
                    L(dve.tensor_reduce(dst[:, :, :], pick[:, :, :, :], AX.X, ALU.add))
                L(dve.tensor_scalar(over[:, :, :], rk[:, :, :], float(P), None, ALU.is_ge))
                L(dve.tensor_scalar(expert[:, :, :], expert[:, :, :], float(P), None, ALU.mult))
                L(dve.tensor_scalar(base[:, :, :], st[:, :, :], float(P), float((NE - 1) * P), ALU.mult, ALU.add))
                L(dve.tensor_tensor(base[:, :, :], base[:, :, :], expert[:, :, :], ALU.subtract))
                L(dve.tensor_tensor(base[:, :, :], base[:, :, :], over[:, :, :], ALU.mult))
                L(dve.tensor_tensor(base[:, :, :], base[:, :, :], expert[:, :, :], ALU.add))
                dve.tensor_tensor(dest[:, :], base[:, :, :].rearrange("p t j -> p (t j)"),
                                  rk[:, :, :].rearrange("p t j -> p (t j)"), ALU.add).then_inc(dest_made, 1)


def slot_columns(m, slot_token, columns):
    nc = m.nc
    landed, turned = m.sem("slots_landed"), m.sem("slots_turned")
    with ExitStack() as own:
        rows = own.enter_context(nc.sbuf_tensor("slot_rows", [BLOCKS, P], F32))
        with nc.Block() as block:

            @block.sync
            def _(sp):
                sp.dma_start(rows[:, :], slot_token).then_inc(landed, 16)

            @block.tensor
            def _(pe):
                pe.wait_ge(landed, 16)
                pe.transpose(m.ps[0][:, 0:BLOCKS], rows[:, :], m.ident[0:BLOCKS, 0:BLOCKS]).then_inc(turned, 1)

            @block.vector
            def _(dve):
                dve.wait_ge(turned, 1)
                m.dve.mark(dve.memset(columns[:, BLOCKS:BLOCKS + 1], 0))
                m.dve.mark(dve.tensor_copy(columns[:, 0:BLOCKS], m.ps[0][:, 0:BLOCKS]))


def wait(eng, sem, value):
    if not isinstance(value, int) or value > 0:
        eng.wait_ge(sem, value)


class Experts:

    def __init__(self, m, tag, w_gate, w_up, w_down, h_rows, y_rows, bufs, x_landed):
        self.m, self.h_rows, self.y_rows = m, h_rows, y_rows
        self.w = (w_gate.rearrange("e (p k) n -> e p (k n)", k=KT), w_up.rearrange("e (p k) n -> e p (k n)", k=KT),
                  w_down.rearrange("e (p k) n -> e p (k n)", k=DE // P))
        self.gu, self.dn, self.xr, self.xT, self.hs, self.hid, self.hidT, self.yb, self.now = bufs
        sem = lambda x: m.sem(f"{tag}_{x}")
        self.w_landed = [[sem(f"w{j}_landed{s}") for s in range(2)] for j in range(3)]
        self.x_landed = x_landed
        self.y_stored = [sem(f"y_stored{s}") for s in range(2)]
        (self.index_set, self.x_turned, self.x_kept_act, self.x_kept_dve, self.g_made, self.u_made, self.silu_made,
         self.h_made, self.h_turned, self.h_kept, self.y_made, self.y_kept) = (sem(x) for x in (
             "index_set", "x_turned", "x_kept_act", "x_kept_dve", "g_made", "u_made", "silu_made", "h_made", "h_turned",
             "h_kept", "y_made", "y_kept"))

    def load(self, sp, e, n, s, reuse=True):
        for j, (done, k) in enumerate(((self.g_made, 1), (self.u_made, 1), (self.y_made, 2))):
            if reuse:
                wait(sp, done, k * (n - 1))
            dst = self.gu[:, s, j, :] if j < 2 else self.dn[:, s, :]
            src = self.w[j][e] if isinstance(e, int) else self.w[j][bass.ds(e, 1)].rearrange("a p n -> p (a n)")
            sp.dma_start(dst, src).then_inc(self.w_landed[j][s], 16)

    def gather(self, pool, columns, n, slot, s, reuse=True):
        wait(pool, self.index_set, n + 1)
        if reuse:
            wait(pool, self.x_turned, 2 * (n - 1))
        pool.tensor_copy(self.now[:, (slot + 1) % 4:(slot + 1) % 4 + 1],
                         columns[:, bass.ds(n + 1, 1)]).then_inc(self.index_set, 1)
        pool.indirect_dma_start(out=self.xr[:, s, :], out_offset=None, in_=self.h_rows,
                                in_offset=bass.IndirectOffsetOnAxis(ap=self.now[:, slot:slot + 1], axis=0)
                                ).then_inc(self.x_landed[s], 16)

    def turn_x(self, pe, n, s, u):
        m = self.m
        wait(pe, self.x_landed[s], 16 * (u + 1))
        wait(pe, self.x_kept_act, n)
        wait(pe, self.x_kept_dve, n)
        for b in range(2):
            for j in range(4):
                k = 4 * b + j
                ins = pe.transpose(m.ps[b][:, j * P:(j + 1) * P], self.xr[:, s, k:D:KT], m.ident[:, :])
            ins.then_inc(self.x_turned, 1)

    def up(self, pe, n, s, u, between=None):
        m = self.m
        wait(pe, self.x_kept_act, n + 1)
        wait(pe, self.x_kept_dve, n + 1)
        wait(pe, self.h_made, n)
        for j, made in enumerate((self.g_made, self.u_made)):
            wait(pe, self.w_landed[j][s], 16 * (u + 1))
            for k in range(KT):
                ins = pe.matmul(m.ps[2 + j][:, :], self.xT[:, k, :], self.gu[:, s, j, k * DE:(k + 1) * DE],
                                start=(k == 0), stop=(k == KT - 1))
            ins.then_inc(made, 1)
            if between and j == 0:
                between()

    def turn_hidden(self, pe, n):
        m = self.m
        wait(pe, self.h_made, n + 1)
        wait(pe, self.h_kept, n)
        for k in range(DE // P):
            ins = pe.transpose(m.ps[4][:, k * P:(k + 1) * P], self.hid[:, k:DE:DE // P], m.ident[:, :])
        ins.then_inc(self.h_turned, 1)

    def down(self, pe, n, s, u):
        m = self.m
        wait(pe, self.h_kept, n + 1)
        wait(pe, self.y_kept, 2 * n)
        wait(pe, self.w_landed[2][s], 16 * (u + 1))
        for b in range(2):
            for k in range(DE // P):
                ins = pe.matmul(m.ps[5 + b][:, :], self.hidT[:, k, :], self.dn[:, s, k * D + b * 512:k * D + b * 512 + 512],
                                start=(k == 0), stop=(k == DE // P - 1))
            ins.then_inc(self.y_made, 1)

    def act_x(self, act, n):
        wait(act, self.x_turned, 2 * n + 1)
        act.copy(self.xT[:, 0:4, :].rearrange("p k r -> p (k r)"), self.m.ps[0][:, :]).then_inc(self.x_kept_act, 1)

    def act_silu(self, act, n):
        wait(act, self.h_made, n)
        wait(act, self.g_made, n + 1)
        act.activation(self.hs[:, :], self.m.ps[2][:, :], ACT.Silu).then_inc(self.silu_made, 1)

    def act_down(self, act, n, s, u, row):
        wait(act, self.y_stored[s], 16 * u)
        for b in range(2):
            wait(act, self.y_made, 2 * n + b + 1)
            act.copy(self.yb[:, s, b * 512:(b + 1) * 512], self.m.ps[5 + b][:, :]).then_inc(self.y_kept, 1)
        wait(act, self.y_kept, 2 * n + 2)
        act.dma_start(self.y_rows[bass.ds(row, P), :], self.yb[:, s, :]).then_inc(self.y_stored[s], 16)

    def dve_x(self, dve, n):
        wait(dve, self.x_turned, 2 * n + 2)
        dve.tensor_copy(self.xT[:, 4:8, :].rearrange("p k r -> p (k r)"), self.m.ps[1][:, :]).then_inc(self.x_kept_dve, 1)

    def dve_hidden(self, dve, n):
        wait(dve, self.h_turned, n)
        wait(dve, self.silu_made, n + 1)
        wait(dve, self.u_made, n + 1)
        dve.tensor_tensor(self.hid[:, :], self.hs[:, :], self.m.ps[3][:, :], ALU.mult).then_inc(self.h_made, 1)

    def dve_down(self, dve, n):
        wait(dve, self.h_turned, n + 1)
        dve.tensor_copy(self.hidT[:, :, :].rearrange("p k r -> p (k r)"), self.m.ps[4][:, :]).then_inc(self.h_kept, 1)


def expert_buffers(m, own):
    sb = lambda name, shape, dt=F32: own.enter_context(m.nc.sbuf_tensor(name, shape, dt))
    return (sb("xp_gu", [P, 2, 2, KT * DE]), sb("xp_dn", [P, 2, (DE // P) * D]), sb("xp_xr", [P, 2, D]),
            sb("xp_xT", [P, KT, P]), sb("xp_hs", [P, DE]), sb("xp_hid", [P, DE]), sb("xp_hidT", [P, DE // P, P]),
            sb("xp_yb", [P, 2, D]), sb("xp_now", [P, 4], U32))


def run_experts(m, x, y, columns, extra_expert, y_rows):
    nc = m.nc
    with ExitStack() as own:
        sb = lambda name, shape, dt=F32: own.enter_context(nc.sbuf_tensor(name, shape, dt))
        zero = sb("xp_zero", [P, D])
        zero_set, zero_stored = m.sem("xp_zero_set"), m.sem("xp_zero_stored")
        with nc.Block() as block:

            @block.sync
            def _(sp):
                sp.wait_ge(zero_set, 1)
                for q in range(EXTRA):
                    sp.dma_start(y_rows[(NE + q) * P:(NE + q + 1) * P, :], zero[:, :]).then_inc(zero_stored, 16)
                with sp.Fori(1, NE // 2) as i:
                    for s in range(2):
                        x.load(sp, 2 * i + s, 2 * i + s, s)
                sp.wait_ge(zero_stored, 16 * EXTRA)

            @block.gpsimd
            def _(pool):
                pool.tensor_copy(x.now[:, 0:1], columns[:, 0:1]).then_inc(x.index_set, 1)
                for e in range(4):
                    x.gather(pool, columns, e, e, e % 2, reuse=(e >= 2))
                with pool.Fori(1, NE // 4) as i:
                    for b in range(4):
                        x.gather(pool, columns, 4 * i + b, b, b % 2)

            @block.tensor
            def _(pe):
                def step(e, s, u, u1):
                    x.up(pe, e, s, u, between=lambda: x.turn_hidden(pe, e - 1))
                    x.turn_x(pe, e + 1, 1 - s, u1)
                    x.down(pe, e - 1, 1 - s, u1 - 1)

                def turn(i):
                    step(2 * i + 1, 1, i, i + 1)
                    step(2 * i + 2, 0, i + 1, i + 1)

                x.turn_x(pe, 0, 0, 0)
                x.up(pe, 0, 0, 0)
                x.turn_x(pe, 1, 1, 0)
                turn(0)
                with pe.Fori(1, NE // 2 - 1) as i:
                    turn(i)
                last = NE // 2 - 1
                x.up(pe, NE - 1, 1, last, between=lambda: x.turn_hidden(pe, NE - 2))
                x.down(pe, NE - 2, 0, last)
                x.turn_hidden(pe, NE - 1)
                x.down(pe, NE - 1, 1, last)

            @block.scalar
            def _(act):
                def turn(i):
                    for s in range(2):
                        e = 2 * i + s
                        x.act_silu(act, e + 1)
                        x.act_x(act, e + 2)
                        x.act_down(act, e, s, i, (2 * P) * i + s * P)

                x.act_x(act, 0)
                x.act_silu(act, 0)
                x.act_x(act, 1)
                turn(0)
                with act.Fori(1, NE // 2 - 1) as i:
                    turn(i)
                last = NE // 2 - 1
                x.act_silu(act, NE - 1)
                x.act_down(act, NE - 2, 0, last, (NE - 2) * P)
                x.act_down(act, NE - 1, 1, last, (NE - 1) * P)
                for s in range(2):
                    act.wait_ge(x.y_stored[s], 16 * (NE // 2))

            @block.vector
            def _(dve):
                dve.memset(zero[:, :], 0.0).then_inc(zero_set, 1)
                x.dve_x(dve, 0)
                x.dve_hidden(dve, 0)
                x.dve_x(dve, 1)
                with dve.Fori(0, NE // 2 - 1) as i:
                    for s in range(2):
                        e = 2 * i + s
                        x.dve_down(dve, e)
                        x.dve_hidden(dve, e + 1)
                        x.dve_x(dve, e + 2)
                x.dve_down(dve, NE - 2)
                x.dve_hidden(dve, NE - 1)
                x.dve_down(dve, NE - 1)

        some = lambda eng: eng.value_load(extra_expert[0:1, EXTRA:EXTRA + 1], min_val=0, max_val=EXTRA)
        with nc.Block() as block:

            @block.sync
            def _(sp):
                experts = [sp.value_load(extra_expert[0:1, q:q + 1], min_val=0, max_val=NE - 1) for q in range(EXTRA)]
                with sp.If(some(sp) > 0):
                    for q in range(EXTRA):
                        y.load(sp, experts[q], q, q % 2, reuse=(q >= 2))

            @block.gpsimd
            def _(pool):
                with pool.If(some(pool) > 0):
                    for q in range(EXTRA):
                        if q >= 2:
                            pool.wait_ge(y.x_turned, 2 * (q - 1))
                        pool.indirect_dma_start(
                            out=y.xr[:, q % 2, :], out_offset=None, in_=y.h_rows,
                            in_offset=bass.IndirectOffsetOnAxis(ap=columns[:, NE + q:NE + q + 1], axis=0)
                        ).then_inc(y.x_landed[q % 2], 16)

            @block.tensor
            def _(pe):
                with pe.If(some(pe) > 0):
                    for q in range(EXTRA):
                        y.turn_x(pe, q, q % 2, q // 2)
                        y.up(pe, q, q % 2, q // 2)
                        y.turn_hidden(pe, q)
                        y.down(pe, q, q % 2, q // 2)

            @block.scalar
            def _(act):
                with act.If(some(act) > 0):
                    for q in range(EXTRA):
                        y.act_x(act, q)
                        y.act_silu(act, q)
                        y.act_down(act, q, q % 2, q // 2, (NE + q) * P)
                    for s in range(2):
                        act.wait_ge(y.y_stored[s], 16 * ((EXTRA + 1 - s) // 2))

            @block.vector
            def _(dve):
                with dve.If(some(dve) > 0):
                    for q in range(EXTRA):
                        y.dve_x(dve, q)
                        y.dve_hidden(dve, q)
                        y.dve_down(dve, q)


def combine(m, gate, dest, x_rows, y_rows, final_norm_g, out):
    nc = m.nc
    with ExitStack() as own:
        sb = lambda name, shape, dt=F32: own.enter_context(nc.sbuf_tensor(name, shape, dt))
        r = sb("cb_r", [P, TT, TOP, D])
        g = sb("cb_g", [P, D])
        sq = sb("cb_sq", [P, D])
        eps = sb("cb_eps", [P, 1])
        mean = sb("cb_mean", [P, TT])
        root = sb("cb_root", [P, TT])
        inv = sb("cb_inv", [P, TT])
        landed = m.gathers[22:22 + TT]
        g_landed, eps_set, summed, squared, rooted, made, stored = (
            m.sem(f"cb_{x}") for x in ("g_landed", "eps_set", "summed", "squared", "rooted", "made", "stored"))
        with nc.Block() as block:

            @block.gpsimd
            def _(pool):
                for t in range(TT):
                    for j in range(TOP):
                        n = t * TOP + j
                        pool.indirect_dma_start(
                            out=r[:, t, j, :], out_offset=None, in_=y_rows,
                            in_offset=bass.IndirectOffsetOnAxis(ap=dest[:, n:n + 1], axis=0)).then_inc(landed[t], 16)

            @block.sync
            def _(sp):
                sp.dma_start(g[:, :], final_norm_g.rearrange("(a n) -> a n", a=1).to_broadcast([P, D])).then_inc(g_landed, 16)
                for t in range(TT):
                    sp.wait_ge(made, t + 1)
                    sp.dma_start(out[t * P:(t + 1) * P, :], x_rows[:, t, :]).then_inc(stored, 16)
                sp.wait_ge(stored, 16 * TT)

            @block.scalar
            def _(act):
                act.wait_ge(eps_set, 1)
                for t in range(TT):
                    act.wait_ge(summed, t + 1)
                    if t:
                        act.wait_ge(squared, t)
                    act.activation(sq[:, :], x_rows[:, t, :], ACT.Square, accum_out=mean[:, t:t + 1]).then_inc(squared, 1)
                act.wait_ge(squared, TT)
                act.activation(root[:, :], mean[:, :], ACT.Sqrt, scale=1.0 / D, bias=eps[:, :]).then_inc(rooted, 1)

            @block.vector
            def _(dve):
                c = m.dve
                dve.memset(eps[:, :], EPS).then_inc(eps_set, 1)
                for t in range(TT):
                    dve.wait_ge(landed[t], 16 * TOP)
                    for j in range(TOP):
                        n = t * TOP + j
                        ins = dve.scalar_tensor_tensor(out=x_rows[:, t, :], in0=r[:, t, j, :], scalar=gate[:, n:n + 1],
                                                       in1=x_rows[:, t, :], op0=ALU.mult, op1=ALU.add)
                        if j < TOP - 1:
                            c.link(dve, ins)
                    ins.then_inc(summed, 1)
                dve.wait_ge(g_landed, 16)
                dve.wait_ge(rooted, 1)
                c.link(dve, dve.reciprocal(inv[:, :], root[:, :]))
                for t in range(TT):
                    dve.scalar_tensor_tensor(out=x_rows[:, t, :], in0=x_rows[:, t, :], scalar=inv[:, t:t + 1], in1=g[:, :],
                                             op0=ALU.mult, op1=ALU.mult).then_inc(made, 1)


def second_experts(m, norm_col, w_rg, b_rg, w_re, b_re, w_gate, w_up, w_down, final_norm_g, h_kept, slot_token, y_rows, out):
    nc = m.nc
    norm(m, m.xT, m.hT, norm_col)
    with ExitStack() as own:
        sb = lambda name, shape, dt=F32: own.enter_context(nc.sbuf_tensor(name, shape, dt))
        gate = sb("mo_gate", [P, TT * TOP])
        dest = sb("mo_dest", [P, TT * TOP], U32)
        extra_expert = sb("mo_extra_expert", [P, EXTRA + 1], I32)
        columns = sb("mo_columns", [P, BLOCKS + 1], U32)
        rows = m.hT[:, :, :].rearrange("p k t -> p (k t)").rearrange("p (t d) -> p t d", t=TT)
        with ExitStack() as own2:
            bufs = expert_buffers(m, own2)
            work = [Experts(m, tag, w_gate, w_up, w_down, h_kept, y_rows, bufs, m.gathers[g:g + 2])
                    for tag, g in (("xp", 18), ("xq", 20))]
            h_stored = m.sem("h_stored")
            h_rows = m.weights[:, :, :, :].rearrange("p s k c -> p (s k c)")[:, 0:TT * D].rearrange("p (t d) -> p t d", t=TT)

            def meanwhile(sp):
                sp.dma_start(h_kept.rearrange("(t p) d -> p t d", p=P), h_rows).then_inc(h_stored, 16)
                for e in range(2):
                    work[0].load(sp, e, e, e, reuse=False)
                sp.wait_ge(h_stored, 16)

            with ExitStack() as own3:
                w, bias, load = load_router(m, own3, w_rg, b_rg, w_re, b_re)
                turn_back(m, m.hT, h_rows, "h4", other=load)
                route(m, w, bias, gate, dest, extra_expert, slot_token, meanwhile)
                slot_columns(m, slot_token, columns)
            turn_back(m, m.xT, rows, "x4")
            run_experts(m, *work, columns, extra_expert, y_rows)
        combine(m, gate, dest, rows, y_rows, final_norm_g, out)


def two_blocks(nc, x, c, w_ada, b_ada, norm1_w, w_in, hgrn_lb_logits, hgrn_onorm_w, conv_w, conv_onorm_w, w_out, norm2_w,
               peer_w_query, peer_sub_keys, peer_u, peer_v, final_norm_w, attn_norm_g_2, w_in_2, b_gate_2, rwkv_mu_2,
               rwkv_w0_2, rwkv_w_decay_2, rwkv_a0_2, rwkv_w_a_2, rwkv_w_g_2, rwkv_k_k_2, rwkv_k_a_2, rwkv_r_k_2, rwkv_ln_g_2,
               rwkv_ln_b_2, w_up_rwkv_2, ssd_conv_w_2, ssd_conv_b_2, ssd_dt_bias_2, ssd_a_log_2, ssd_d_2, ssd_norm_g_2,
               w_up_ssd_2, w_out_2, ffn_norm_g_2, w_router_group_2, b_router_group_2, w_router_expert_2, b_router_expert_2,
               w_exp_gate_2, w_exp_up_2, w_exp_down_2, final_norm_g_2, out):
    row = lambda ap: ap.rearrange("(k p) -> k p", p=P)
    kept = lambda name, shape: nc.dram_tensor(name, shape, F32, kind="Internal").ap()
    with ExitStack() as ctx:
        m = setup(nc, ctx)
        constants(m)
        columns = Columns(m, [
            first_rows(c, b_ada, norm1_w, hgrn_lb_logits, hgrn_onorm_w, conv_w, conv_onorm_w, norm2_w, final_norm_w),
            rwkv_rows(attn_norm_g_2, rwkv_mu_2, rwkv_w0_2, rwkv_a0_2, rwkv_k_k_2, rwkv_k_a_2, rwkv_r_k_2, rwkv_ln_g_2,
                      rwkv_ln_b_2),
            [("conv", ssd_conv_w_2[0].rearrange("j (k p) -> (j k) p", p=P)), ("conv_b", row(ssd_conv_b_2[0]))],
            [("norm_g", row(ssd_norm_g_2[0])), ("b_gate", row(b_gate_2[0])), ("ffn_norm", row(ffn_norm_g_2[0]))]])
        with stage(m):
            first_mixer(m, x, columns, w_ada, w_in, w_out, (peer_w_query[0], 2 * PH))
            first_experts(m, peer_w_query, peer_sub_keys, peer_u, peer_v, columns.cols[0], columns.at[0],
                          (w_in_2[0], R_TILES))
        with stage(m):
            x_kept = kept("x_kept", [P, KT, T])
            (_, cols, cols3, cols4), (_, at, at3, at4) = columns.cols, columns.at
            c0 = 3 * D + 2 * P
            dt0 = c0 + (S_TILES + X_TILES) * P
            projected = kept("projected", [RN * Spare.TILES, P, T])
            spare = Spare(m, w_in_2[0], c0, dt0 + SH,
                          (cols3[:, at3["conv"]:at3["conv"] + Spare.TAPS * X_TILES], cols3[:, at3["conv_b"]:at3["conv_b"] + X_TILES]),
                          cols4[:, at4["b_gate"]:at4["b_gate"] + 2 * KT],
                          projected, kept("h_kept2", [P, KT, T]), kept("bonus_kept", [P, KT, T]))
            second_rwkv(m, w_in_2, cols, at, rwkv_w_decay_2, rwkv_w_a_2, rwkv_w_g_2, x_kept, spare)
        with stage(m):
            with ExitStack() as own:
                y = own.enter_context(nc.sbuf_tensor("ssd_y", [P, X_TILES, T], F32))
                second_ssd(m, w_in_2[0][:, dt0:dt0 + SH], cols4, at4, ssd_dt_bias_2, ssd_a_log_2, ssd_d_2, y,
                           projected, (w_up_rwkv_2[0], KT))
                second_merge(m, y, projected[S_TILES + X_TILES:], w_up_rwkv_2, w_up_ssd_2, w_out_2, x_kept)
            second_experts(m, cols4[:, at4["ffn_norm"]:at4["ffn_norm"] + KT], w_router_group_2[0], b_router_group_2[0],
                           w_router_expert_2[0], b_router_expert_2[0], w_exp_gate_2[0], w_exp_up_2[0], w_exp_down_2[0],
                           final_norm_g_2, kept("h_kept", [T, D]), kept("slot_token", [BLOCKS, P]),
                           kept("y_rows", [BLOCKS * P, D]), out[0])


_INS = ['x', 'c', 'w_ada', 'b_ada', 'norm1_w', 'w_in', 'hgrn_lb_logits', 'hgrn_onorm_w', 'conv_w',
        'conv_onorm_w', 'w_out', 'norm2_w', 'peer_w_query', 'peer_sub_keys', 'peer_u', 'peer_v', 'final_norm_w',
        'attn_norm_g_2', 'w_in_2', 'b_gate_2', 'rwkv_mu_2', 'rwkv_w0_2', 'rwkv_w_decay_2', 'rwkv_a0_2',
        'rwkv_w_a_2', 'rwkv_w_g_2', 'rwkv_k_k_2', 'rwkv_k_a_2', 'rwkv_r_k_2', 'rwkv_ln_g_2', 'rwkv_ln_b_2',
        'w_up_rwkv_2', 'ssd_conv_w_2', 'ssd_conv_b_2', 'ssd_dt_bias_2', 'ssd_a_log_2', 'ssd_d_2', 'ssd_norm_g_2',
        'w_up_ssd_2', 'w_out_2', 'ffn_norm_g_2', 'w_router_group_2', 'b_router_group_2', 'w_router_expert_2',
        'b_router_expert_2', 'w_exp_gate_2', 'w_exp_up_2', 'w_exp_down_2', 'final_norm_g_2']


def kernel(**inputs):
    import numpy as _np
    import concourse.bacc as _bacc
    from concourse import mybir as _mybir
    from concourse.bass_utils import run_bass_kernel_spmd as _run

    nc = _bacc.Bacc("TRN2", target_bir_lowering=False, num_devices=1)
    arrays, args = {}, []
    for name in _INS:
        a = _np.ascontiguousarray(inputs[name])
        arrays[f"in_{name}_dram"] = a
        args.append(nc.dram_tensor(f"in_{name}_dram", a.shape, _mybir.dt.from_np(a.dtype), kind="ExternalInput").ap())
    out = nc.dram_tensor("out_0_dram", (1, T, D), F32, kind="ExternalOutput").ap()
    two_blocks(nc, *args, out)
    r = _run(nc, [arrays], core_ids=[0])
    return r.results[0]["out_0_dram"]
```
